# Optimizing a Trainium2 kernel written in Bass

```python
import jax, jax.numpy as jnp
from jax import lax
import numpy as np
import jax
import jax.numpy as jnp
import math

D_MODEL = 1024
BATCH = 1
SEQ = 256
DEPTH = 2

N_MIXERS = 2
N_A_LAYERS = (DEPTH + 1) // 2
N_B_LAYERS = DEPTH // 2
D_FF = ((8 * D_MODEL // 3 + 127) // 128) * 128
CHUNK = 128
A_DIM = 2 * D_MODEL
A_HEADS = 8
A_HEAD_DIM = A_DIM // A_HEADS
POOL_WINDOWS = (2, 4, 8, 16)
B_GROUPS = len(POOL_WINDOWS)
B_DIM = D_MODEL
B_GROUP_DIM = B_DIM // B_GROUPS
EPS = 1e-6


def rmsnorm(x, g):
    xf = x.astype(jnp.float32)
    y = xf * lax.rsqrt(jnp.mean(xf * xf, axis=-1, keepdims=True) + EPS)
    return (y * g.astype(jnp.float32)).astype(x.dtype)

def swiglu(h, w_in, w_out):
    gate, up = jnp.split(h @ w_in, 2, axis=-1)
    return (jax.nn.silu(gate) * up) @ w_out

def chunked_sgu(h, w_in, v_norm, w_s, b_s, w_out):
    bsz, seq, _ = h.shape
    z = jax.nn.gelu(h @ w_in)
    u, v = jnp.split(z, 2, axis=-1)
    v = rmsnorm(v, v_norm)
    v = v.reshape(bsz, seq // CHUNK, CHUNK, A_HEADS, A_HEAD_DIM)
    causal = jnp.tril(jnp.ones((CHUNK, CHUNK), dtype=bool))
    ws = jnp.where(causal[None], w_s, jnp.zeros_like(w_s))
    gate = jnp.einsum('hts,bcshd->bcthd', ws, v) + b_s.T[None, None, :, :, None]
    gate = gate.reshape(bsz, seq, A_DIM)
    return (u * gate) @ w_out

def causal_mean(x, window):
    seq = x.shape[1]
    c = jnp.cumsum(x.astype(jnp.float32), axis=1)
    c_prev = jnp.pad(c, ((0, 0), (window, 0), (0, 0)))[:, :seq]
    cnt = jnp.minimum(jnp.arange(1, seq + 1), window).astype(jnp.float32)[None, :, None]
    return ((c - c_prev) / cnt).astype(x.dtype)

def pool_mixer(h, w_in, w_grp, scale, w_out):
    bsz, seq, _ = h.shape
    p = h @ w_in
    groups = jnp.split(p, B_GROUPS, axis=-1)
    pooled = jnp.stack([causal_mean(g, w) - g for g, w in zip(groups, POOL_WINDOWS)], axis=2)
    y = jnp.einsum('bsgc,gcd->bsgd', pooled, w_grp).reshape(bsz, seq, B_DIM)
    return (y * scale) @ w_out

def first_inputs(seed: int = 0) -> dict:
    key = jax.random.key(seed)
    ks = jax.random.split(key, 16)
    f32 = jnp.float32
    nrm = lambda k, shape, fan_in: jax.random.normal(k, shape, f32) * (fan_in ** -0.5)
    gain = lambda k, shape: 1.0 + 0.02 * jax.random.normal(k, shape, f32)
    return {
        "x": jax.random.normal(ks[0], (BATCH, SEQ, D_MODEL), f32),
        "ffn_norm": gain(ks[1], (DEPTH, 2, D_MODEL)),
        "ffn_w_in": nrm(ks[2], (DEPTH, 2, D_MODEL, 2 * D_FF), D_MODEL),
        "ffn_w_out": nrm(ks[3], (DEPTH, 2, D_FF, D_MODEL), D_FF),
        "mix_norm": gain(ks[4], (DEPTH, D_MODEL)),
        "a_w_in": nrm(ks[5], (N_A_LAYERS, D_MODEL, 2 * A_DIM), D_MODEL),
        "a_v_norm": gain(ks[6], (N_A_LAYERS, A_DIM)),
        "a_w_s": nrm(ks[7], (N_A_LAYERS, A_HEADS, CHUNK, CHUNK), CHUNK),
        "a_b_s": 1.0 + 0.02 * jax.random.normal(ks[8], (N_A_LAYERS, A_HEADS, CHUNK), f32),
        "a_w_out": nrm(ks[9], (N_A_LAYERS, A_DIM, D_MODEL), A_DIM),
        "b_w_in": nrm(ks[10], (N_B_LAYERS, D_MODEL, B_DIM), D_MODEL),
        "b_w_grp": nrm(ks[11], (N_B_LAYERS, B_GROUPS, B_GROUP_DIM, B_GROUP_DIM), B_GROUP_DIM),
        "b_scale": gain(ks[12], (N_B_LAYERS, B_DIM)),
        "b_w_out": nrm(ks[13], (N_B_LAYERS, B_DIM, D_MODEL), B_DIM),
        "final_norm": gain(ks[14], (D_MODEL,)),
    }

def first_block(x, ffn_norm, ffn_w_in, ffn_w_out, mix_norm, a_w_in, a_v_norm, a_w_s, a_b_s,
              a_w_out, b_w_in, b_w_grp, b_scale, b_w_out, final_norm):
    for i in range(DEPTH):
        x = x + 0.5 * swiglu(rmsnorm(x, ffn_norm[i, 0]), ffn_w_in[i, 0], ffn_w_out[i, 0])
        h = rmsnorm(x, mix_norm[i])
        j = i // N_MIXERS
        if i % N_MIXERS == 0:
            x = x + chunked_sgu(h, a_w_in[j], a_v_norm[j], a_w_s[j], a_b_s[j], a_w_out[j])
        else:
            x = x + pool_mixer(h, b_w_in[j], b_w_grp[j], b_scale[j], b_w_out[j])
        x = x + 0.5 * swiglu(rmsnorm(x, ffn_norm[i, 1]), ffn_w_in[i, 1], ffn_w_out[i, 1])
    return rmsnorm(x, final_norm)


_first_inputs = first_inputs


def first_inputs(seed=0):
    import zlib

    import numpy as np

    out = dict(_first_inputs(seed))
    spreads = {}
    factors = {'ffn_norm': 3.848,
     'mix_norm': 3.021,
     'a_v_norm': 7.393,
     'a_b_s': 5.636,
     'b_scale': 5.43,
     'final_norm': 2.873}
    for name, (base, spread) in spreads.items():
        noise = np.random.default_rng([zlib.crc32(name.encode()), seed]).standard_normal(out[name].shape)
        drawn = base * np.exp(spread * noise) if base else spread * noise
        out[name] = __import__('jax').numpy.asarray(drawn.astype(out[name].dtype))
    for name, factor in factors.items():
        out[name] = (out[name] * factor).astype(out[name].dtype)
    return out


_narrow_inputs = first_inputs


def first_inputs(seed=0):

    out = dict(_narrow_inputs(seed))
    wider = {'a_v_norm': 4.45, 'a_b_s': 4.11, 'b_scale': 5.43, 'final_norm': 3.24}
    for name, times in wider.items():
        mean = out[name].mean()
        out[name] = (mean + times * (out[name] - mean)).astype(out[name].dtype)
    return out


DEPTH_2 = 1

MLA_HEADS = 8
MLA_Q_RANK = 256
MLA_KV_RANK = 128
MLA_NOPE = 64
MLA_ROPE = 32
MLA_V = 64
ROPE_THETA = 10000.0
DSA_HEADS = 8
DSA_KV_HEADS = 2
DSA_HEAD_DIM = 64
IDX_HEADS = 8
IDX_DIM = 32
IDX_TOPK_MAX = 256
N_EXPERTS = 32
TOP_K = 4
D_EXPERT = D_MODEL
SWIGLU_ALPHA = 1.702
SWIGLU_LIMIT = 7.0

NORM_EPS = 1e-6
NEG_INF = -1e30
Q_BLOCK = 128
MOE_BLOCK = 128

MIX_WIDTH = MLA_HEADS * MLA_V + DSA_HEADS * DSA_HEAD_DIM
IN_SPLITS = (MLA_Q_RANK, MLA_KV_RANK, MLA_ROPE,
             DSA_HEADS * DSA_HEAD_DIM, DSA_KV_HEADS * DSA_HEAD_DIM, DSA_KV_HEADS * DSA_HEAD_DIM,
             IDX_HEADS * IDX_DIM, IDX_DIM, IDX_HEADS)
IN_WIDTH = sum(IN_SPLITS)


def rms_norm(x, g):
    xf = x.astype(jnp.float32)
    y = xf * lax.rsqrt(jnp.mean(xf * xf, axis=-1, keepdims=True) + NORM_EPS)
    return (y * g.astype(jnp.float32)).astype(x.dtype)

def rope(x, pos):
    half = x.shape[-1] // 2
    freqs = ROPE_THETA ** (-jnp.arange(half, dtype=jnp.float32) / half)
    ang = pos.astype(jnp.float32)[..., None] * freqs
    ang = ang.reshape(ang.shape[:2] + (1,) * (x.ndim - 3) + (half,))
    cos, sin = jnp.cos(ang), jnp.sin(ang)
    x1 = x[..., :half].astype(jnp.float32)
    x2 = x[..., half:].astype(jnp.float32)
    return jnp.concatenate([x1 * cos - x2 * sin, x2 * cos + x1 * sin], axis=-1).astype(x.dtype)

def to_blocks(a):
    b, s = a.shape[:2]
    return jnp.moveaxis(a.reshape((b, s // Q_BLOCK, Q_BLOCK) + a.shape[2:]), 1, 0)

def from_blocks(a):
    a = jnp.moveaxis(a, 0, 1)
    return a.reshape((a.shape[0], a.shape[1] * a.shape[2]) + a.shape[3:])

def mla_attention(c_q, c_kv, k_rope_in, pos, g_q_a, g_kv_a, w_q_b, w_kv_b):
    b, s, _ = c_q.shape
    q = (rms_norm(c_q, g_q_a) @ w_q_b).reshape(b, s, MLA_HEADS, MLA_NOPE + MLA_ROPE)
    q_nope = q[..., :MLA_NOPE]
    q_rope = rope(q[..., MLA_NOPE:], pos)
    kv = (rms_norm(c_kv, g_kv_a) @ w_kv_b).reshape(b, s, MLA_HEADS, MLA_NOPE + MLA_V)
    k_nope, v = kv[..., :MLA_NOPE], kv[..., MLA_NOPE:]
    k_rope = rope(k_rope_in, pos)
    scale = (MLA_NOPE + MLA_ROPE) ** -0.5
    key_idx = jnp.arange(s)

    def block(args):
        qn, qr, qi = args
        sc = (jnp.einsum('bqhd,bkhd->bhqk', qn, k_nope)
              + jnp.einsum('bqhd,bkd->bhqk', qr, k_rope)).astype(jnp.float32) * scale
        sc = jnp.where(key_idx[None, None, None, :] <= qi[None, None, :, None], sc, NEG_INF)
        p = jax.nn.softmax(sc, axis=-1).astype(v.dtype)
        return jnp.einsum('bhqk,bkhd->bqhd', p, v)

    q_ids = jnp.arange(s).reshape(-1, Q_BLOCK)
    out = lax.map(block, (to_blocks(q_nope), to_blocks(q_rope), q_ids))
    return from_blocks(out).reshape(b, s, MLA_HEADS * MLA_V)

def dsa_attention(q, k, v, q_i, k_i, w_i, pos):
    b, s, _ = q.shape
    grp = DSA_HEADS // DSA_KV_HEADS
    q = q.reshape(b, s, DSA_KV_HEADS, grp, DSA_HEAD_DIM)
    k = k.reshape(b, s, DSA_KV_HEADS, DSA_HEAD_DIM)
    v = v.reshape(b, s, DSA_KV_HEADS, DSA_HEAD_DIM)
    q_i = q_i.reshape(b, s, IDX_HEADS, IDX_DIM) * (IDX_DIM ** -0.5)
    w_i = w_i * (IDX_HEADS ** -0.5)
    n_sel = min(IDX_TOPK_MAX, s // 4)
    key_idx = jnp.arange(s)
    slopes = jnp.exp2(-8.0 * jnp.arange(1, DSA_HEADS + 1, dtype=jnp.float32) / DSA_HEADS)
    slopes = slopes.reshape(DSA_KV_HEADS, grp)
    gather = jax.vmap(lambda a, i: a[i])

    def block(args):
        qb, qib, wib, posb, ti = args
        rel = jax.nn.relu(jnp.einsum('bqhd,bsd->bqsh', qib, k_i).astype(jnp.float32))
        idx_score = jnp.einsum('bqsh,bqh->bqs', rel, wib.astype(jnp.float32))
        idx_score = jnp.where(key_idx[None, None, :] <= ti[None, :, None], idx_score, NEG_INF)
        _, sel = lax.top_k(idx_score, n_sel)
        k_sel = gather(k, sel)
        v_sel = gather(v, sel)
        pos_sel = gather(pos, sel)
        sc = jnp.einsum('bqhgd,bqnhd->bqhgn', qb, k_sel).astype(jnp.float32) * (DSA_HEAD_DIM ** -0.5)
        dist = jnp.abs(posb[:, :, None] - pos_sel).astype(jnp.float32)
        sc = sc - slopes[None, None, :, :, None] * dist[:, :, None, None, :]
        valid = sel <= ti[None, :, None]
        sc = jnp.where(valid[:, :, None, None, :], sc, NEG_INF)
        p = jax.nn.softmax(sc, axis=-1).astype(v.dtype)
        return jnp.einsum('bqhgn,bqnhd->bqhgd', p, v_sel)

    q_ids = jnp.arange(s).reshape(-1, Q_BLOCK)
    out = lax.map(block, (to_blocks(q), to_blocks(q_i), to_blocks(w_i), to_blocks(pos), q_ids))
    return from_blocks(out).reshape(b, s, DSA_HEADS * DSA_HEAD_DIM)

def moe_ffn(h, w_router, b_router, w_mlp1, b_mlp1, w_mlp2, b_mlp2):
    b, s, d = h.shape
    xf = h.reshape(-1, d)
    n = xf.shape[0]
    logits = (xf @ w_router + b_router).astype(jnp.float32)
    top_val, top_idx = lax.top_k(logits, TOP_K)
    gates = jax.nn.softmax(top_val, axis=-1)
    n_assign = n * TOP_K
    flat_e = top_idx.reshape(-1)
    flat_tok = jnp.arange(n_assign, dtype=jnp.int32) // TOP_K
    flat_gate = gates.reshape(-1)
    order = jnp.argsort(flat_e)
    e_sorted = flat_e[order]
    counts = jnp.bincount(flat_e, length=N_EXPERTS)
    start = jnp.cumsum(counts) - counts
    padded = (counts + MOE_BLOCK - 1) // MOE_BLOCK * MOE_BLOCK
    pad_end = jnp.cumsum(padded)
    pad_start = pad_end - padded
    dest = pad_start[e_sorted] + jnp.arange(n_assign) - start[e_sorted]
    n_slots = (n_assign + MOE_BLOCK - 1) // MOE_BLOCK * MOE_BLOCK + N_EXPERTS * MOE_BLOCK
    n_blocks = n_slots // MOE_BLOCK
    slot_tok = jnp.full((n_slots,), n, jnp.int32).at[dest].set(flat_tok[order])
    slot_gate = jnp.zeros((n_slots,), jnp.float32).at[dest].set(flat_gate[order])
    block_e = jnp.minimum(
        jnp.searchsorted(pad_end, jnp.arange(n_blocks) * MOE_BLOCK, side='right'), N_EXPERTS - 1)
    x_pad = jnp.concatenate([xf, jnp.zeros((1, d), xf.dtype)], axis=0)
    x_slots = x_pad[slot_tok].reshape(n_blocks, MOE_BLOCK, d)

    def expert_block(args):
        xb, e = args
        hid = xb @ w_mlp1[e] + b_mlp1[e]
        glu = jnp.minimum(hid[..., ::2], SWIGLU_LIMIT)
        lin = jnp.clip(hid[..., 1::2], -SWIGLU_LIMIT, SWIGLU_LIMIT)
        act = glu * jax.nn.sigmoid(SWIGLU_ALPHA * glu) * (lin + 1.0)
        return act @ w_mlp2[e] + b_mlp2[e]

    y = lax.map(expert_block, (x_slots, block_e)).reshape(n_slots, d)
    y = y * slot_gate[:, None].astype(y.dtype)
    out = jax.ops.segment_sum(y, slot_tok, num_segments=n + 1)[:n]
    return out.reshape(b, s, d)

def second_inputs(seed: int = 0) -> dict:
    key = jax.random.key(seed)
    ks = jax.random.split(key, 24)
    f32 = jnp.float32
    L, D, F, E = DEPTH_2, D_MODEL, D_EXPERT, N_EXPERTS

    def nrm(k, shape, scale):
        return jax.random.normal(k, shape, f32) * scale

    def gain(k, width):
        return 1.0 + nrm(k, (L, width), 0.02)

    x = nrm(ks[0], (BATCH, SEQ, D), 1.0)
    c = nrm(ks[1], (BATCH, D), 1.0)
    offsets = jax.random.randint(ks[2], (BATCH, 1), 0, 4096, dtype=jnp.int32)
    positions = offsets + jnp.arange(SEQ, dtype=jnp.int32)[None, :]
    return {
        "x": x,
        "c": c,
        "positions": positions,
        "w_ada": nrm(ks[3], (L, D, 6 * D), 0.2 * D ** -0.5),
        "b_ada": nrm(ks[4], (L, 6 * D), 0.01),
        "g_pre_mix": gain(ks[5], D),
        "g_post_mix": gain(ks[6], D),
        "g_pre_ffn": gain(ks[7], D),
        "g_post_ffn": gain(ks[8], D),
        "w_in": nrm(ks[9], (L, D, IN_WIDTH), D ** -0.5),
        "g_q_a": gain(ks[10], MLA_Q_RANK),
        "g_kv_a": gain(ks[11], MLA_KV_RANK),
        "w_q_b": nrm(ks[12], (L, MLA_Q_RANK, MLA_HEADS * (MLA_NOPE + MLA_ROPE)), MLA_Q_RANK ** -0.5),
        "w_kv_b": nrm(ks[13], (L, MLA_KV_RANK, MLA_HEADS * (MLA_NOPE + MLA_V)), MLA_KV_RANK ** -0.5),
        "w_o": nrm(ks[14], (L, MIX_WIDTH, D), MIX_WIDTH ** -0.5),
        "w_router": nrm(ks[15], (L, D, E), D ** -0.5),
        "b_router": nrm(ks[16], (L, E), 0.01),
        "w_mlp1": nrm(ks[17], (L, E, D, 2 * F), D ** -0.5),
        "b_mlp1": nrm(ks[18], (L, E, 2 * F), 0.01),
        "w_mlp2": nrm(ks[19], (L, E, F, D), F ** -0.5),
        "b_mlp2": nrm(ks[20], (L, E, D), 0.01),
    }

def second_block(x, c, positions, w_ada, b_ada, g_pre_mix, g_post_mix, g_pre_ffn, g_post_ffn,
              w_in, g_q_a, g_kv_a, w_q_b, w_kv_b, w_o, w_router, b_router,
              w_mlp1, b_mlp1, w_mlp2, b_mlp2):
    split_at = np.cumsum(IN_SPLITS)[:-1].tolist()
    cond = jax.nn.silu(c)
    for l in range(DEPTH_2):
        mod = cond @ w_ada[l] + b_ada[l]
        sh1, sc1, gt1, sh2, sc2, gt2 = [m[:, None, :] for m in jnp.split(mod, 6, axis=-1)]

        h = rms_norm(x, g_pre_mix[l]) * (1.0 + sc1) + sh1
        proj = h @ w_in[l]
        (c_q, c_kv, k_rope, q_d, k_d, v_d, q_idx, k_idx, w_idx) = jnp.split(proj, split_at, axis=-1)
        y_mla = mla_attention(c_q, c_kv, k_rope, positions, g_q_a[l], g_kv_a[l], w_q_b[l], w_kv_b[l])
        y_dsa = dsa_attention(q_d, k_d, v_d, q_idx, k_idx, w_idx, positions)
        mix = jnp.concatenate([y_mla, y_dsa], axis=-1) @ w_o[l]
        x = x + gt1 * rms_norm(mix, g_post_mix[l])

        h2 = rms_norm(x, g_pre_ffn[l]) * (1.0 + sc2) + sh2
        ffn = moe_ffn(h2, w_router[l], b_router[l], w_mlp1[l], b_mlp1[l], w_mlp2[l], b_mlp2[l])
        x = x + gt2 * rms_norm(ffn, g_post_ffn[l])
    return x


DEPTH_3 = 1

CHUNK_3 = 64
SB_HEAD_DIM = 64
SB_HEADS = D_MODEL // 128
SB_WIDTH = SB_HEADS * SB_HEAD_DIM
SSM_WIDTH = D_MODEL // 2
SSM_GROUP = 16
SSM_GROUPS = SSM_WIDTH // SSM_GROUP
SSM_STATE = 64
N_MEM = 256
XA_HEADS = 4
XA_HEAD_DIM = D_MODEL // XA_HEADS
D_FF_3 = 11 * D_MODEL // 4
CONV_WIDTH = 3
RMS_EPS = 1e-6
IN_WIDTH_3 = 3 * SB_WIDTH + SSM_WIDTH + 2 * D_MODEL


def rms_norm_3(x, gain):
    xf = x.astype(jnp.float32)
    y = xf * lax.rsqrt(jnp.mean(xf * xf, axis=-1, keepdims=True) + RMS_EPS)
    return (y * gain.astype(jnp.float32)).astype(x.dtype)

def stick_breaking_attention(q, k, v):
    b, s, _ = q.shape
    n_blk = s // Q_BLOCK
    qh = q.reshape(b, n_blk, Q_BLOCK, SB_HEADS, SB_HEAD_DIM).transpose(1, 0, 3, 2, 4)
    kh = k.reshape(b, s, SB_HEADS, SB_HEAD_DIM).transpose(0, 2, 1, 3)
    vh = v.reshape(b, s, SB_HEADS, SB_HEAD_DIM).transpose(0, 2, 1, 3)
    key_pos = jnp.arange(s, dtype=jnp.int32)
    scale = SB_HEAD_DIM ** -0.5

    def one_block(args):
        q_blk, blk = args
        z = jnp.einsum('bhqd,bhkd->bhqk', q_blk, kh).astype(jnp.float32) * scale
        q_pos = blk * Q_BLOCK + jnp.arange(Q_BLOCK, dtype=jnp.int32)
        causal = key_pos[None, :] < q_pos[:, None]
        log_fail = jnp.where(causal, jax.nn.log_sigmoid(-z), 0.0)
        log_remain = lax.cumsum(log_fail, axis=3, reverse=True) - log_fail
        w = jnp.where(causal, jnp.exp(jax.nn.log_sigmoid(z) + log_remain), 0.0)
        return jnp.einsum('bhqk,bhkd->bhqd', w.astype(vh.dtype), vh)

    out = lax.map(one_block, (qh, jnp.arange(n_blk, dtype=jnp.int32)))
    return out.transpose(1, 0, 3, 2, 4).reshape(b, s, SB_WIDTH)

def _linear_recurrence_combine(e_i, e_j):
    a_i, b_i = e_i
    a_j, b_j = e_j
    return a_j * a_i, a_j * b_i + b_j

def s5_branch(u, a_re, a_im, log_dt, b_re, b_im, c_re, c_im, d_skip, w_glu, b_glu):
    b, s, _ = u.shape
    f32 = jnp.float32
    ug = u.astype(f32).reshape(b, s, SSM_GROUPS, SSM_GROUP)
    lam = lax.complex(a_re.astype(f32), a_im.astype(f32))
    dt = jnp.exp(log_dt.astype(f32))[:, None]
    lam_bar = jnp.exp(lam * dt)
    b_mat = lax.complex(b_re.astype(f32), b_im.astype(f32))
    b_bar = ((lam_bar - 1.0) / lam)[:, :, None] * b_mat
    bu = jnp.einsum('gpc,bsgc->bsgp', b_bar, ug.astype(jnp.complex64))
    decay = jnp.broadcast_to(lam_bar, (1, s, SSM_GROUPS, SSM_STATE))
    _, states = lax.associative_scan(_linear_recurrence_combine, (decay, bu), axis=1)
    c_mat = lax.complex(c_re.astype(f32), c_im.astype(f32))
    y = jnp.einsum('gcp,bsgp->bsgc', c_mat, states).real
    y = y + d_skip.astype(f32).reshape(SSM_GROUPS, SSM_GROUP) * ug
    y = jax.nn.gelu(y.reshape(b, s, SSM_WIDTH)).astype(u.dtype)
    return y * jax.nn.sigmoid(y @ w_glu + b_glu)

def memory_cross_attention(h, mem_n, wq, wk, wv, wo):
    b, s, _ = h.shape
    m = mem_n.shape[1]
    q = (h @ wq).reshape(b, s, XA_HEADS, XA_HEAD_DIM)
    k = (mem_n @ wk).reshape(b, m, XA_HEADS, XA_HEAD_DIM)
    v = (mem_n @ wv).reshape(b, m, XA_HEADS, XA_HEAD_DIM)
    scores = jnp.einsum('bqhd,bmhd->bhqm', q, k).astype(jnp.float32) * (XA_HEAD_DIM ** -0.5)
    p = jax.nn.softmax(scores, axis=-1).astype(v.dtype)
    o = jnp.einsum('bhqm,bmhd->bqhd', p, v).reshape(b, s, D_MODEL)
    return o @ wo

def conv_ffn(h, w_up, conv_w, conv_b, w_down):
    up = h @ w_up
    up = lax.conv_general_dilated(
        up, conv_w[:, None, :].astype(up.dtype), window_strides=(1,),
        padding=[(CONV_WIDTH - 1, 0)], dimension_numbers=('NWC', 'WIO', 'NWC'),
        feature_group_count=2 * D_FF_3) + conv_b
    gate, val = jnp.split(up, 2, axis=-1)
    return (jax.nn.gelu(gate) * val) @ w_down

def _normal(key, shape, scale):
    return jax.random.normal(key, shape, jnp.float32) * scale

def third_inputs(seed: int = 0) -> dict:
    key = jax.random.key(seed)
    ks = jax.random.split(key, 32)
    L, D, G, P, C = DEPTH_3, D_MODEL, SSM_GROUPS, SSM_STATE, SSM_GROUP
    gain = lambda k: 1.0 + _normal(k, (L, D), 0.05)
    return {
        "x": _normal(ks[0], (BATCH, SEQ, D), 1.0),
        "mem": _normal(ks[1], (BATCH, N_MEM, D), 1.0),
        "norm_mix_pre": gain(ks[2]),
        "norm_mix_post": gain(ks[3]),
        "w_in": _normal(ks[4], (L, D, IN_WIDTH_3), D ** -0.5),
        "b_gate": _normal(ks[5], (L, 2 * D), 0.01),
        "ssm_a_re": -0.5 + _normal(ks[6], (L, G, P), 0.01),
        "ssm_a_im": jnp.pi * jnp.arange(P, dtype=jnp.float32)[None, None, :] + _normal(ks[7], (L, G, P), 0.01),
        "ssm_log_dt": jax.random.uniform(ks[8], (L, G), jnp.float32, math.log(1e-3), math.log(1e-1)),
        "ssm_b_re": _normal(ks[9], (L, G, P, C), (2 * C) ** -0.5),
        "ssm_b_im": _normal(ks[10], (L, G, P, C), (2 * C) ** -0.5),
        "ssm_c_re": _normal(ks[11], (L, G, C, P), (2 * P) ** -0.5),
        "ssm_c_im": _normal(ks[12], (L, G, C, P), (2 * P) ** -0.5),
        "ssm_d": _normal(ks[13], (L, SSM_WIDTH), 1.0),
        "ssm_w_glu": _normal(ks[14], (L, SSM_WIDTH, SSM_WIDTH), SSM_WIDTH ** -0.5),
        "ssm_b_glu": _normal(ks[15], (L, SSM_WIDTH), 0.01),
        "w_branch_attn": _normal(ks[16], (L, SB_WIDTH, D), SB_WIDTH ** -0.5),
        "w_branch_ssm": _normal(ks[17], (L, SSM_WIDTH, D), SSM_WIDTH ** -0.5),
        "w_out": _normal(ks[18], (L, D, D), D ** -0.5),
        "norm_xa_pre": gain(ks[19]),
        "norm_xa_post": gain(ks[20]),
        "norm_mem": gain(ks[21]),
        "xa_wq": _normal(ks[22], (L, D, D), D ** -0.5),
        "xa_wk": _normal(ks[23], (L, D, D), D ** -0.5),
        "xa_wv": _normal(ks[24], (L, D, D), D ** -0.5),
        "xa_wo": _normal(ks[25], (L, D, D), D ** -0.5),
        "norm_ffn_pre": gain(ks[26]),
        "norm_ffn_post": gain(ks[27]),
        "ffn_w_up": _normal(ks[28], (L, D, 2 * D_FF_3), D ** -0.5),
        "ffn_conv_w": _normal(ks[29], (L, CONV_WIDTH, 2 * D_FF_3), CONV_WIDTH ** -0.5),
        "ffn_conv_b": _normal(ks[30], (L, 2 * D_FF_3), 0.01),
        "ffn_w_down": _normal(ks[31], (L, D_FF_3, D), D_FF_3 ** -0.5),
    }

def third_block(x, mem, norm_mix_pre, norm_mix_post, w_in, b_gate,
              ssm_a_re, ssm_a_im, ssm_log_dt, ssm_b_re, ssm_b_im, ssm_c_re, ssm_c_im,
              ssm_d, ssm_w_glu, ssm_b_glu, w_branch_attn, w_branch_ssm, w_out,
              norm_xa_pre, norm_xa_post, norm_mem, xa_wq, xa_wk, xa_wv, xa_wo,
              norm_ffn_pre, norm_ffn_post, ffn_w_up, ffn_conv_w, ffn_conv_b, ffn_w_down):
    splits = (SB_WIDTH, 2 * SB_WIDTH, 3 * SB_WIDTH, 3 * SB_WIDTH + SSM_WIDTH)
    for l in range(DEPTH_3):
        h = rms_norm_3(x, norm_mix_pre[l])
        proj = h @ w_in[l]
        q, k, v, u, gate_logits = jnp.split(proj, splits, axis=-1)
        gate_attn, gate_ssm = jnp.split(jax.nn.sigmoid(gate_logits + b_gate[l]), 2, axis=-1)
        o_attn = stick_breaking_attention(q, k, v)
        o_ssm = s5_branch(u, ssm_a_re[l], ssm_a_im[l], ssm_log_dt[l], ssm_b_re[l], ssm_b_im[l],
                          ssm_c_re[l], ssm_c_im[l], ssm_d[l], ssm_w_glu[l], ssm_b_glu[l])
        merged = gate_attn * (o_attn @ w_branch_attn[l]) + gate_ssm * (o_ssm @ w_branch_ssm[l])
        x = x + rms_norm_3(merged @ w_out[l], norm_mix_post[l])
        h = rms_norm_3(x, norm_xa_pre[l])
        mem_n = rms_norm_3(mem, norm_mem[l])
        xa = memory_cross_attention(h, mem_n, xa_wq[l], xa_wk[l], xa_wv[l], xa_wo[l])
        x = x + rms_norm_3(xa, norm_xa_post[l])
        h = rms_norm_3(x, norm_ffn_pre[l])
        f = conv_ffn(h, ffn_w_up[l], ffn_conv_w[l], ffn_conv_b[l], ffn_w_down[l])
        x = x + rms_norm_3(f, norm_ffn_post[l])
    return x


def setup_inputs(seed=0):
    out = dict(first_inputs(seed))
    for name, value in second_inputs(seed + 1).items():
        if name != "x":
            out[name + "_2"] = value
    for name, value in third_inputs(seed + 2).items():
        if name != "x":
            out[name + "_3"] = value
    return out


def reference(
    x, ffn_norm, ffn_w_in, ffn_w_out, mix_norm, a_w_in, a_v_norm, a_w_s, a_b_s, a_w_out, b_w_in,
    b_w_grp, b_scale, b_w_out, final_norm, c_2, positions_2, w_ada_2, b_ada_2, g_pre_mix_2,
    g_post_mix_2, g_pre_ffn_2, g_post_ffn_2, w_in_2, g_q_a_2, g_kv_a_2, w_q_b_2, w_kv_b_2,
    w_o_2, w_router_2, b_router_2, w_mlp1_2, b_mlp1_2, w_mlp2_2, b_mlp2_2, mem_3,
    norm_mix_pre_3, norm_mix_post_3, w_in_3, b_gate_3, ssm_a_re_3, ssm_a_im_3, ssm_log_dt_3,
    ssm_b_re_3, ssm_b_im_3, ssm_c_re_3, ssm_c_im_3, ssm_d_3, ssm_w_glu_3, ssm_b_glu_3,
    w_branch_attn_3, w_branch_ssm_3, w_out_3, norm_xa_pre_3, norm_xa_post_3, norm_mem_3,
    xa_wq_3, xa_wk_3, xa_wv_3, xa_wo_3, norm_ffn_pre_3, norm_ffn_post_3, ffn_w_up_3,
    ffn_conv_w_3, ffn_conv_b_3, ffn_w_down_3,
):
    x = first_block(
        x, ffn_norm, ffn_w_in, ffn_w_out, mix_norm, a_w_in, a_v_norm, a_w_s, a_b_s, a_w_out,
        b_w_in, b_w_grp, b_scale, b_w_out, final_norm,
    )
    x = second_block(
        x, c_2, positions_2, w_ada_2, b_ada_2, g_pre_mix_2, g_post_mix_2, g_pre_ffn_2,
        g_post_ffn_2, w_in_2, g_q_a_2, g_kv_a_2, w_q_b_2, w_kv_b_2, w_o_2, w_router_2,
        b_router_2, w_mlp1_2, b_mlp1_2, w_mlp2_2, b_mlp2_2,
    )
    return third_block(
        x, mem_3, norm_mix_pre_3, norm_mix_post_3, w_in_3, b_gate_3, ssm_a_re_3, ssm_a_im_3,
        ssm_log_dt_3, ssm_b_re_3, ssm_b_im_3, ssm_c_re_3, ssm_c_im_3, ssm_d_3, ssm_w_glu_3,
        ssm_b_glu_3, w_branch_attn_3, w_branch_ssm_3, w_out_3, norm_xa_pre_3, norm_xa_post_3,
        norm_mem_3, xa_wq_3, xa_wk_3, xa_wv_3, xa_wo_3, norm_ffn_pre_3, norm_ffn_post_3,
        ffn_w_up_3, ffn_conv_w_3, ffn_conv_b_3, ffn_w_down_3,
    )


_drawn_inputs = setup_inputs


def setup_inputs(seed=0):
    import zlib

    import numpy as np

    out = dict(_drawn_inputs(seed))
    spreads = {}
    factors = {'b_ada_2': 7.181,
     'g_pre_mix_2': 8.0,
     'g_post_mix_2': 8.0,
     'g_pre_ffn_2': 8.0,
     'g_post_ffn_2': 24.262,
     'g_q_a_2': 8.0,
     'g_kv_a_2': 8.0,
     'w_q_b_2': 4.879,
     'b_router_2': 8.0,
     'b_mlp1_2': 27.789,
     'b_mlp2_2': 64.0,
     'norm_mix_pre_3': 2.737,
     'norm_mix_post_3': 3.339,
     'b_gate_3': 26.876,
     'ssm_a_re_3': 64.0,
     'ssm_a_im_3': 44.136,
     'ssm_log_dt_3': 53.48,
     'ssm_b_re_3': 64.0,
     'ssm_b_im_3': 64.0,
     'ssm_c_re_3': 64.0,
     'ssm_c_im_3': 63.392,
     'ssm_b_glu_3': 39.221,
     'norm_xa_pre_3': 3.504,
     'norm_xa_post_3': 3.411,
     'norm_ffn_post_3': 3.904,
     'ffn_conv_b_3': 8.0}
    for name, (base, spread) in spreads.items():
        noise = np.random.default_rng([zlib.crc32(name.encode()), seed]).standard_normal(out[name].shape)
        drawn = base * np.exp(spread * noise) if base else spread * noise
        out[name] = jnp.asarray(drawn.astype(out[name].dtype))
    for name, factor in factors.items():
        out[name] = (out[name] * factor).astype(out[name].dtype)
    return out
```

```python
import math
from contextlib import ExitStack

import numpy as np

import concourse.bass as bass
from concourse import mybir

F32 = mybir.dt.float32
F32R = mybir.dt.float32r
I32 = mybir.dt.int32
U32 = mybir.dt.uint32
ALU = mybir.AluOpType
ACT = mybir.ActivationFunctionType
AX = mybir.AxisListType

P = 128
S = 256
D = 1024
DT = D // P
TB = S // P
FF = 2816
SLOT = 2048
SLOTS = 12
EPS = 1e-6
NEG = -1e30
TWO_PI = 2 * math.pi
ROUND = 1.5 * 2.0 ** 23


class Signal:

    def __init__(self, nc, name, primed=0):
        self.sem, self.base = nc.alloc_semaphore(name), primed

    def __call__(self, n):
        return self.sem, self.base + n

    def done(self, n):
        self.base += n


class Steps:

    def __init__(self, nc, name, primed=0):
        self.sem, self.n, self.shift, self.eng = nc.alloc_semaphore(name), primed, 0, None

    def link(self, instruction):
        self.n += 1
        instruction.then_inc(self.sem, 1)
        self.eng.wait_ge(self.sem, self.n + self.shift)

    def loop(self, i, per):
        self.shift, self.at = i * per, self.n

    def end(self, trips, per):
        assert self.n - self.at == per, (self.n - self.at, per)
        self.shift, self.n = 0, self.n + (trips - 1) * per


class Ring:

    def __init__(self, nc, memory):
        self.memory = memory
        self.loaded = [nc.alloc_semaphore(f"slot{i}_loaded") for i in range(SLOTS)]
        self.used = [nc.alloc_semaphore(f"slot{i}_used") for i in range(SLOTS)]
        self.fills = [0] * SLOTS
        self.uses = [0] * SLOTS
        self.last = [None] * SLOTS
        self.next = 0

    def slot(self, s):
        return self.memory[:, s * SLOT:(s + 1) * SLOT]

    def take(self, trips=1):
        s = self.next
        self.next = (s + 1) % SLOTS
        fill = self.fills[s]
        self.fills[s] += trips
        return s, fill, self.last[s]

    def freed_by_use(self, s, trips=1):
        n = self.uses[s]
        self.uses[s] += trips
        self.last[s] = (self.used[s], n + trips)
        return n

    def freed_by(self, s, semaphore, value):
        self.last[s] = (semaphore, value)

    def vacant(self, eng, unit):
        if unit[2] is not None:
            eng.wait_ge(*unit[2])

    def arrived(self, eng, unit):
        eng.wait_ge(self.loaded[unit[0]], unit[1] * 16 + 16)


class Banks:

    def __init__(self, nc):
        self.ps = [nc.alloc_psum_tensor(f"bank{i}", [P, 512], F32) for i in range(8)]
        self.full = [nc.alloc_semaphore(f"bank{i}_full") for i in range(8)]
        self.free = [nc.alloc_semaphore(f"bank{i}_free") for i in range(8)]
        self.fulls = [0] * 8
        self.frees = [0] * 8

    def take(self, b, trips=1, signals=True):
        at = b, self.frees[b], self.fulls[b]
        self.frees[b] += trips
        if signals:
            self.fulls[b] += trips
        return at

    def vacant(self, eng, at):
        eng.wait_ge(self.free[at[0]], at[1] + 1)

    def ready(self, eng, at):
        eng.wait_ge(self.full[at[0]], at[2] + 1)

    def read(self, eng, at):
        eng.wait_ge(self.free[at[0]], at[1] + 2)


class Kit:

    def __init__(self, nc, const_at, const_width):
        self.nc = nc
        self.const_at = const_at
        self.consts = nc.alloc_sbuf_tensor("consts", [P, const_width], F32)
        self.ring = Ring(nc, nc.alloc_sbuf_tensor("weight_slots", [P, SLOTS * SLOT], F32))
        self.banks = Banks(nc)
        self.ps = self.banks.ps
        self.x = nc.alloc_sbuf_tensor("x_residual", [P, DT, S], F32)
        self.h = nc.alloc_sbuf_tensor("h_normed", [P, DT, S], F32)
        self.ident = self.const("ident", P)
        self.ones = self.const("ones", P)
        self.causal_rows = self.const("seen", 2 * P)
        self.earlier_rows = self.const("all_earlier", 2 * P)
        self.negmax = nc.alloc_sbuf_tensor("negative_maxima", [P, 8], F32)
        self.sums = nc.alloc_sbuf_tensor("exponential_sums", [P, 8], F32)
        self.squares = Signal(nc, "squares_written")
        self.hidden, self.gelus = Signal(nc, "hidden_written"), Signal(nc, "gelu_written")
        self.weights = Signal(nc, "attention_weights_written")
        self.maxima = Signal(nc, "maxima_written")
        self.exps = Signal(nc, "exponentials_written")
        self.pool_done = Signal(nc, "pool_steps")
        self.scaled = Signal(nc, "operand_scaled")
        self.vsteps = Steps(nc, "vector_steps")
        self.asteps = Steps(nc, "scalar_steps")

    def const(self, name, width):
        return self.consts[:, self.const_at[name]:self.const_at[name] + width]

    def col(self, name):
        return self.const(name, 1)

    def param(self, name, t=0, n=1):
        at = self.param_at[name] + t
        return self.params[:, bass.ds(at, n)]


def constant_table():
    at, parts = {}, []

    def add(name, a):
        at[name] = sum(p.shape[1] for p in parts)
        parts.append(np.broadcast_to(np.asarray(a, np.float32), (P, np.shape(a)[-1])))

    i = np.arange(P)
    add("ident", np.eye(P))
    add("before", i[:, None] < i[None, :])
    add("upto", i[:, None] <= i[None, :])
    add("iota", i[None, :])
    add("seen", np.zeros((1, P)))
    add("causal", np.where(i[None, :] <= i[:, None], 0.0, NEG))
    add("all_earlier", np.ones((1, P)))
    add("earlier", i[None, :] < i[:, None])
    t = np.arange(1, S + 1)
    for w in (2, 4, 8, 16):
        add(f"per{w}", (1.0 / np.minimum(t, w))[None, :])
    freq = 10000.0 ** (-np.arange(16, dtype=np.float32) / 16)
    add("freq", np.concatenate([np.zeros(64), freq, freq])[None, :])
    add("times", np.arange(S)[None, :])
    add("sign", np.where(i < 80, -1.0, 1.0)[:, None])
    add("ones", np.ones((1, P)))
    add("index", i[:, None])
    add("half_pi", np.full((1, 1), math.pi / 2))
    add("eps", np.full((1, 1), EPS))
    return np.ascontiguousarray(np.concatenate(parts, 1)), at


def parameter_rows(a):
    rows = []

    def add(name, ap, pattern="(r p) -> r p"):
        rows.append((name, ap.rearrange(pattern, p=P)))

    add("ffn_norm", a["ffn_norm"], "a b (r p) -> (a b r) p")
    add("mix_norm", a["mix_norm"], "a (r p) -> (a r) p")
    add("a_v_norm", a["a_v_norm"][0])
    add("b_scale", a["b_scale"][0])
    add("final_norm", a["final_norm"])
    add("c", a["c_2"][0])
    add("b_ada", a["b_ada_2"][0])
    for n in ("g_pre_mix", "g_post_mix", "g_pre_ffn", "g_post_ffn", "g_q_a", "g_kv_a"):
        add(n, a[n + "_2"][0])
    for n in ("norm_mix_pre", "norm_mix_post", "norm_xa_pre", "norm_xa_post", "norm_mem",
              "norm_ffn_pre", "norm_ffn_post", "b_gate", "ssm_d", "ssm_b_glu", "ffn_conv_b"):
        add(n, a[n + "_3"][0])
    add("conv_w", a["ffn_conv_w_3"][0], "w (r p) -> (w r) p")
    rows.append(("ssm_a_re", a["ssm_a_re_3"][0].rearrange("(j g) n -> j (g n)", g=2)))
    rows.append(("ssm_a_im", a["ssm_a_im_3"][0].rearrange("(j g) n -> j (g n)", g=2)))
    return rows



def transpose_tokens(K, pe, src, banks, width=DT):
    nc = K.nc
    for j, at in enumerate(banks):
        b = at[0]
        K.banks.vacant(pe, at)
        for tile in (2 * j, 2 * j + 1):
            for blk in range(TB):
                col = (tile % 2) * S + blk * P
                last = nc.tensor.transpose(K.ps[b][:, col:col + P], src[:, blk, tile * P:(tile + 1) * P], K.ident)
        last.then_inc(K.banks.full[b], 1)


def rmsnorm(K, src, dst, gain, tiles, shift=None, add_to=None):
    nc = K.nc
    bank = K.banks.take(7)
    with nc.sbuf_tensor([P, tiles, S], F32) as squares, nc.sbuf_tensor([P, S], F32) as rms, \
            nc.sbuf_tensor([P, S], F32) as rstd, nc.Block() as block:

        @block.scalar
        def _(act):
            nc.scalar.activation(squares[:, :, :], src, ACT.Square).then_inc(K.squares.sem, 1)
            K.banks.ready(act, bank)
            nc.scalar.activation(rms[:, :], K.ps[7][:, 0:S], ACT.Sqrt, bias=K.col("eps"),
                                 scale=1.0 / (tiles * P)).then_inc(K.banks.free[7], 1)

        @block.tensor
        def _(pe):
            pe.wait_ge(*K.squares(1))
            K.banks.vacant(pe, bank)
            for t in range(tiles):
                last = nc.tensor.matmul(K.ps[7][:, 0:S], K.ones, squares[:, t, :], start=t == 0, stop=t == tiles - 1)
            last.then_inc(K.banks.full[7], 1)

        @block.vector
        def _(dve):
            K.vsteps.eng = dve
            K.banks.read(dve, bank)
            K.vsteps.link(nc.vector.reciprocal(rstd[:, :], rms[:, :]))
            if add_to is None and shift is None:
                for t in range(tiles):
                    nc.vector.scalar_tensor_tensor(dst[:, t, :], src[:, t, :], gain(t), rstd[:, :], ALU.mult, ALU.mult)
                return
            for t in range(tiles):
                last = nc.vector.scalar_tensor_tensor(squares[:, t, :], src[:, t, :], gain(t), rstd[:, :],
                                                      ALU.mult, ALU.mult)
            K.vsteps.link(last)
            if add_to is not None:
                nc.vector.tensor_tensor(add_to, add_to, squares[:, :, :], ALU.add)
            else:
                for t in range(tiles):
                    nc.vector.tensor_scalar(dst[:, t, :], squares[:, t, :], shift(t), None, ALU.add)
    K.squares.done(1)


def take_accumulators(K, signals=True):
    return [K.banks.take(b, signals=signals and b == 3) for b in range(4)]


def read_accumulators(K, dve, out, finish):
    K.vsteps.eng = dve
    for j, (b, _, _) in enumerate(out):
        finish(dve, j, K.ps[b]).then_inc(K.banks.free[b], 1)


def dense_down(K, src, weights, tiles, finish):
    nc, ring, banks = K.nc, K.ring, K.banks
    view = weights.rearrange("(t p) n -> p t n", p=P)
    units = []
    for u in range(tiles // 2):
        units.append(ring.take())
        ring.freed_by_use(units[-1][0])
    out = take_accumulators(K)
    ring.uses[units[-1][0]] -= 1
    ring.freed_by(units[-1][0], banks.full[3], banks.fulls[3])
    with nc.Block() as block:

        @block.sync
        def _(sp):
            for u, unit in enumerate(units):
                ring.vacant(sp, unit)
                sp.dma_start(ring.slot(unit[0]).rearrange("p (t n) -> p t n", t=2), view[:, 2 * u:2 * u + 2, :])\
                    .then_inc(ring.loaded[unit[0]], 16)

        @block.tensor
        def _(pe):
            for at in out:
                banks.vacant(pe, at)
            for u, unit in enumerate(units):
                ring.arrived(pe, unit)
                last = down_unit(K, ring.slot(unit[0]), lambda kk: src[:, 2 * u + kk, :], u == 0, u == len(units) - 1)
                last.then_inc(ring.used[unit[0]] if u < len(units) - 1 else banks.full[3], 1)

        @block.vector
        def _(dve):
            banks.ready(dve, out[3])
            read_accumulators(K, dve, out, finish)


def down_unit(K, slot, moving, first, last):
    for kk in range(2):
        for c in range(DT):
            m = K.nc.tensor.matmul(K.ps[c // 2][:, (c % 2) * S:(c % 2 + 1) * S],
                                   slot[:, kk * D + c * P:kk * D + (c + 1) * P], moving(kk),
                                   start=first and kk == 0 and c % 2 == 0, stop=last and kk == 1,
                                   skip_group_check=True)
    return m


def add_residual(K, scale=None):
    def finish(dve, j, ps):
        x = K.x[:, 2 * j:2 * j + 2, :].rearrange("p t s -> p (t s)")
        if scale is None:
            return K.nc.vector.tensor_tensor(x, ps[:, :], x, ALU.add)
        return K.nc.vector.scalar_tensor_tensor(x, ps[:, :], scale, x, ALU.mult, ALU.add)
    return finish


def store_to(K, dst):
    def finish(dve, j, ps):
        return K.nc.vector.tensor_copy(dst[:, 2 * j:2 * j + 2, :].rearrange("p t s -> p (t s)"), ps[:, :])
    return finish


def dense_up(K, src, tiles, jobs):
    nc, ring, banks = K.nc, K.ring, K.banks
    units, out = [], []
    for j in range(len(jobs)):
        units.append(ring.take())
        out.append(banks.take(4 + j % 4))
        ring.freed_by(units[j][0], banks.full[out[j][0]], out[j][2] + 1)

    def finish_on(eng, which):
        for (_, _, engine, finish), at in zip(jobs, out):
            if engine == which:
                banks.ready(eng, at)
                finish(K.ps[at[0]]).then_inc(banks.free[at[0]], 1)

    with nc.Block() as block:

        @block.sync
        def _(sp):
            for (w, _, _, _), unit in zip(jobs, units):
                ring.vacant(sp, unit)
                sp.dma_start(ring.slot(unit[0])[:, 0:tiles * 256].rearrange("p (t n) -> p t n", n=256),
                             w.rearrange("(t p) n -> p t n", p=P)).then_inc(ring.loaded[unit[0]], 16)

        @block.tensor
        def _(pe):
            for (_, by_token, _, _), unit, at in zip(jobs, units, out):
                ring.arrived(pe, unit)
                banks.vacant(pe, at)
                up_unit(K, ring.slot(unit[0]), src, tiles, K.ps[at[0]], by_token).then_inc(banks.full[at[0]], 1)

        @block.scalar
        def _(act):
            finish_on(act, "act")

        @block.vector
        def _(dve):
            finish_on(dve, "dve")


def up_unit(K, slot, src, tiles, ps, by_token=False):
    for half in range(2):
        for k in range(tiles):
            if by_token:
                a, m = src[:, k, half * P:(half + 1) * P], slot[:, k * 256:(k + 1) * 256]
            else:
                a, m = slot[:, k * 256 + half * P:k * 256 + (half + 1) * P], src[:, k, :]
            last = K.nc.tensor.matmul(ps[:, half * 256:(half + 1) * 256], a, m, start=k == 0, stop=k == tiles - 1)
    return last


def feed_forward(K, w_in, w_out, middle, finish):
    nc, ring, banks = K.nc, K.ring, K.banks
    pairs = FF // 256
    trips = (pairs - 1) // 2
    w_in_v = w_in.rearrange("(t p) n -> p t n", p=P)
    w_out_v = w_out.rearrange("(t p) n -> p t n", p=P)

    def plan(first_bank, trips=1):
        units, at = [], []
        for b in (first_bank, first_bank + 1):
            units.append(ring.take(trips))
            at.append(banks.take(b, trips))
            ring.freed_by(units[-1][0], banks.full[b], at[-1][2] + trips)
        return units, at

    first_up = plan(4)
    loop_up = [plan(6, trips), plan(4, trips)]
    body = (pairs - 1) // 2
    first_down = ring.take()
    first_use = ring.freed_by_use(first_down[0])
    loop_down, loop_uses = [], []
    for _ in range(body):
        loop_down.append(ring.take(2))
        loop_uses.append(ring.freed_by_use(loop_down[-1][0], 2))
    out = take_accumulators(K, signals=False)

    with nc.sbuf_tensor([P, FF // P, S], F32) as hid, nc.Block() as block:

        def load_up(sp, unit, column):
            sp.dma_start(ring.slot(unit[0]).rearrange("p (t n) -> p t n", n=256),
                         w_in_v[:, :, bass.ds(column, 256)]).then_inc(ring.loaded[unit[0]], 16)

        def load_down(sp, u, unit):
            sp.dma_start(ring.slot(unit[0]).rearrange("p (t n) -> p t n", t=2),
                         w_out_v[:, bass.ds(u * 2, 2), :]).then_inc(ring.loaded[unit[0]], 16)

        @block.sync
        def _(sp):
            for pair, (units, _) in enumerate([first_up] + loop_up):
                for g, unit in enumerate(units):
                    ring.vacant(sp, unit)
                    load_up(sp, unit, pair * 256 + g * FF)
            with sp.Fori(1, trips) as i:
                for b, (units, at) in enumerate(loop_up):
                    for g, (unit, bank) in enumerate(zip(units, at)):
                        column = sp.snap(i * 512 + ((1 + b) * 256 + g * FF))
                        sp.wait_ge(banks.full[bank[0]], i + bank[2])
                        load_up(sp, unit, column)
            ring.vacant(sp, first_down)
            load_down(sp, 0, first_down)
            for u, unit in enumerate(loop_down):
                ring.vacant(sp, unit)
                load_down(sp, 1 + u, unit)
            for u, (unit, uses) in enumerate(zip(loop_down, loop_uses)):
                sp.wait_ge(ring.used[unit[0]], uses + 1)
                load_down(sp, 1 + body + u, unit)

        @block.tensor
        def _(pe):
            def up_pair(i, units, at):
                for unit, bank in zip(units, at):
                    pe.wait_ge(ring.loaded[unit[0]], i * 16 + (unit[1] * 16 + 16))
                    pe.wait_ge(banks.free[bank[0]], i + (bank[1] + 1))
                    up_unit(K, ring.slot(unit[0]), K.h, DT, K.ps[bank[0]]).then_inc(banks.full[bank[0]], 1)

            up_pair(0, *first_up)
            with pe.Fori(0, trips) as i:
                for units, at in loop_up:
                    up_pair(i, units, at)
            for at in out:
                banks.vacant(pe, at)
            pe.wait_ge(*middle.written(loop_up[1][1], trips, pairs))
            ring.arrived(pe, first_down)
            down_unit(K, ring.slot(first_down[0]), lambda kk: hid[:, kk, :], True, False)\
                .then_inc(ring.used[first_down[0]], 1)
            with pe.Fori(0, 2) as i:
                for u, unit in enumerate(loop_down):
                    pe.wait_ge(ring.loaded[unit[0]], i * 16 + (unit[1] * 16 + 16))
                    down_unit(K, ring.slot(unit[0]), lambda kk: hid[:, bass.ds(i * (2 * body) + (2 + 2 * u + kk), 1), :],
                              False, False).then_inc(ring.used[unit[0]], 1)

        @block.scalar
        def _(act):
            middle.act(act, 0, 2, first_up[1])
            with act.Fori(0, trips) as i:
                for b, (_, at) in enumerate(loop_up):
                    middle.act(act, i, b, at)

        @block.vector
        def _(dve):
            K.vsteps.eng = dve
            middle.dve(dve, 0, 0, 2, first_up[1], hid)
            with dve.Fori(0, trips) as i:
                K.vsteps.loop(i, 2 * middle.links)
                for b, (_, at) in enumerate(loop_up):
                    middle.dve(dve, i, dve.snap(i * 2 + (1 + b)), b, at, hid)
                K.vsteps.end(trips, 2 * middle.links)
            dve.wait_ge(ring.used[loop_down[-1][0]], loop_uses[-1] + 2)
            read_accumulators(K, dve, out, finish)


class SiluGate:
    links = 0

    def written(self, at, trips, pairs):
        return self.K.banks.free[at[1][0]], at[1][1] + trips + 1

    def __init__(self, K, buffer):
        self.K, self.silu = K, buffer

    def act(self, act, i, b, at):
        K, banks, ((gate, _, gate_full), (up, up_free, _)) = self.K, self.K.banks, at
        act.wait_ge(banks.full[gate], i + (gate_full + 1))
        act.wait_ge(banks.free[up], i + (up_free + 1))
        K.nc.scalar.activation(self.silu[:, b, :], K.ps[gate][:, :], ACT.Silu).then_inc(banks.free[gate], 1)

    def dve(self, dve, i, pair, b, at, hid):
        K, banks, ((gate, gate_free, _), (up, _, up_full)) = self.K, self.K.banks, at
        dve.wait_ge(banks.full[up], i + (up_full + 1))
        dve.wait_ge(banks.free[gate], i + (gate_free + 2))
        K.nc.vector.tensor_tensor(hid[:, bass.ds(pair * 2, 2), :], self.silu[:, b, :].rearrange("p (t s) -> p t s", t=2),
                                  K.ps[up][:, :].rearrange("p (t s) -> p t s", t=2), ALU.mult)\
            .then_inc(banks.free[up], 1)


def swiglu(K, w_in, w_out, norm_at):
    rmsnorm(K, K.x[:, :, :], K.h, lambda t: K.param("ffn_norm", norm_at + t), DT)
    with K.nc.sbuf_tensor([P, 3, 512], F32) as silu:
        feed_forward(K, w_in, w_out, SiluGate(K, silu), add_residual(K, 0.5))


class ConvGate:
    links = 2

    def written(self, at, trips, pairs):
        return self.K.hidden(pairs)

    def __init__(self, K, buffer):
        self.K, self.buf = K, buffer

    def act(self, act, i, b, at):
        K, (gate, gate_free, _) = self.K, at[0]
        act.wait_ge(K.banks.free[gate], i + (gate_free + 2))
        part = self.buf[:, b, 0:2, :]
        K.nc.scalar.activation(part, part, ACT.Gelu_apprx_tanh).then_inc(K.gelus.sem, 1)

    def dve(self, dve, i, pair, b, at, hid):
        K, v, banks, ((gate, _, gate_full), (up, _, up_full)) = self.K, self.K.nc.vector, self.K.banks, at
        dve.wait_ge(banks.full[gate], i + (gate_full + 1))
        dve.wait_ge(banks.full[up], i + (up_full + 1))
        tiles = [(self.buf[:, b, 2 * g + half, :], K.ps[(gate, up)[g]][:, half * S:(half + 1) * S],
                  dve.snap(pair * 2 + (g * (FF // P) + half))) for g in range(2) for half in range(2)]
        for out, ps, tile in tiles:
            m = v.tensor_scalar(out, ps, K.param("conv_w", tile + 2 * 2 * FF // P), K.param("ffn_conv_b", tile),
                                ALU.mult, ALU.add)
        K.vsteps.link(m)
        for out, ps, tile in tiles:
            m = v.scalar_tensor_tensor(out[:, 1:], ps[:, 0:S - 1], K.param("conv_w", tile + 2 * FF // P), out[:, 1:],
                                       ALU.mult, ALU.add)
        K.vsteps.link(m)
        for n, (out, ps, tile) in enumerate(tiles):
            m = v.scalar_tensor_tensor(out[:, 2:], ps[:, 0:S - 2], K.param("conv_w", tile), out[:, 2:], ALU.mult, ALU.add)
            if n % 2:
                m.then_inc(banks.free[(gate, up)[n // 2]], 1)
        dve.wait_ge(banks.free[up], i + (at[1][1] + 2))
        dve.wait_ge(K.gelus.sem, pair + (K.gelus.base + 1))
        v.tensor_tensor(hid[:, bass.ds(pair * 2, 2), :], self.buf[:, b, 0:2, :], self.buf[:, b, 2:4, :], ALU.mult)\
            .then_inc(K.hidden.sem, 1)


def conv_feed_forward(K, a):
    rmsnorm(K, K.x[:, :, :], K.h, lambda t: K.param("norm_ffn_pre", t), DT)
    with K.nc.sbuf_tensor([P, 3, 4, S], F32) as conv:
        feed_forward(K, a["ffn_w_up_3"][0], a["ffn_w_down_3"][0], ConvGate(K, conv), store_to(K, K.h))
    K.gelus.done(FF // 256)
    rmsnorm(K, K.h[:, :, :], None, lambda t: K.param("norm_ffn_post", t), DT, add_to=K.x[:, :, :])


def setup(K, a, const):
    nc, banks = K.nc, K.banks
    rows = parameter_rows(a)
    total = sum(r.shape[0] for _, r in rows)
    groups = -(-total // P)
    K.params = nc.alloc_sbuf_tensor("params", [P, groups * P], F32)
    K.param_at, at, pieces = {}, 0, []
    for name, r in rows:
        K.param_at[name] = at
        done = 0
        while done < r.shape[0]:
            n = min(r.shape[0] - done, P - at % P)
            pieces.append((at // P, at % P, n, r[done:done + n, :]))
            done, at = done + n, at + n
    param_banks = [banks.take(g) for g in range(-(-groups // 4))]
    x_banks = [banks.take(4 + j) for j in range(4)]
    consts_in, x_in, zeroed = (nc.alloc_semaphore(n) for n in ("consts_in", "x_in", "rows_zeroed"))
    rows_in = [nc.alloc_semaphore(f"rows_in{i}") for i in range(4)]
    with nc.sbuf_tensor([P, groups, P], F32) as raw, nc.sbuf_tensor([P, TB, D], F32) as tokens, nc.Block() as block:

        def load_rows(eng, which):
            eng.wait_ge(zeroed, 1)
            for k, (g, p, n, src) in enumerate(pieces[which::4]):
                if k:
                    eng.wait_ge(rows_in[which], 16 * k)
                eng.dma_start(raw[p:p + n, g, :], src).then_inc(rows_in[which], 16)

        @block.sync
        def _(sp):
            sp.dma_start(K.consts[:, :], const).then_inc(consts_in, 16)
            sp.dma_start(tokens[:, :, :], a["x"][0].rearrange("(b p) d -> p b d", p=P)).then_inc(x_in, 16)
            load_rows(sp, 0)
            load_rows(sp, 1)

        @block.gpsimd
        def _(pool):
            nc.gpsimd.memset(raw[:, :, :], 0.0).then_inc(zeroed, 1)
            for sem in banks.free:
                pool.sem_inc(sem, 1)

        @block.scalar
        def _(act):
            load_rows(act, 2)
            load_rows(act, 3)
            for j, at in enumerate(x_banks):
                banks.ready(act, at)
                nc.scalar.activation(K.x[:, 2 * j:2 * j + 2, :].rearrange("p t s -> p (t s)"), K.ps[at[0]][:, :],
                                     ACT.Copy).then_inc(banks.free[at[0]], 1)

        @block.tensor
        def _(pe):
            pe.wait_ge(consts_in, 16)
            pe.wait_ge(x_in, 16)
            transpose_tokens(K, pe, tokens, x_banks)
            for which in range(4):
                pe.wait_ge(rows_in[which], 16 * len(pieces[which::4]))
            for g in range(groups):
                at = param_banks[g // 4]
                if g % 4 == 0:
                    banks.vacant(pe, at)
                m = nc.tensor.transpose(K.ps[at[0]][:, g % 4 * P:(g % 4 + 1) * P], raw[:, g, :], K.ident)
                if g % 4 == 3 or g == groups - 1:
                    m.then_inc(banks.full[at[0]], 1)

        @block.vector
        def _(dve):
            for k, at in enumerate(param_banks):
                banks.ready(dve, at)
                n = min(4, groups - 4 * k) * P
                nc.vector.tensor_copy(K.params[:, k * 512:k * 512 + n], K.ps[at[0]][:, 0:n])\
                    .then_inc(banks.free[at[0]], 1)


def store_output(K, out):
    nc, banks = K.nc, K.banks
    at = [banks.take(j) for j in range(4)]
    out_written = [nc.alloc_semaphore(f"out_written{b}") for b in range(TB)]
    with nc.sbuf_tensor([P, TB, D], F32) as tokens, nc.Block() as block:

        @block.tensor
        def _(pe):
            for j in range(4):
                banks.vacant(pe, at[j])
                for q in range(4):
                    t, blk = (4 * j + q) % DT, j // 2
                    m = nc.tensor.transpose(K.ps[j][:, q * P:(q + 1) * P], K.x[:, t, blk * P:(blk + 1) * P], K.ident)
                m.then_inc(banks.full[j], 1)

        @block.vector
        def _(dve):
            for j in range(4):
                banks.ready(dve, at[j])
                nc.vector.tensor_copy(tokens[:, j // 2, (j % 2) * 512:(j % 2 + 1) * 512], K.ps[j][:, :])\
                    .then_inc(banks.free[j], 1)

        @block.sync
        def _(sp):
            for blk in range(TB):
                banks.read(sp, at[2 * blk + 1])
                sp.dma_start(out[0, blk * P:(blk + 1) * P, :], tokens[:, blk, :]).then_inc(out_written[blk], 16)
            for blk in range(TB):
                sp.wait_ge(out_written[blk], 16)


def spatial_gate(K, a):
    nc, banks = K.nc, K.banks
    heads, wide = 8, 2048
    tiles = wide // P
    rmsnorm(K, K.x[:, :, :], K.h, lambda t: K.param("mix_norm", t), DT)
    w_in, w_s, b_s = a["a_w_in"][0], a["a_w_s"][0], a["a_b_s"][0]
    mix_in, bias_in = nc.alloc_semaphore("mixing_loaded"), nc.alloc_semaphore("mixing_bias_loaded")
    mixed_steps, v_steps = K.vsteps, K.asteps
    with nc.sbuf_tensor([P, tiles, S], F32) as u, nc.sbuf_tensor([P, TB, wide], F32) as v, \
            nc.sbuf_tensor([P, heads, P], F32) as mix:
        jobs = []
        for j in range(8):
            jobs.append((w_in[:, j * 256:(j + 1) * 256], False, "act", lambda ps, j=j: nc.scalar.activation(
                u[:, 2 * j:2 * j + 2, :].rearrange("p t s -> p (t s)"), ps[:, :], ACT.Gelu_apprx_tanh)))
        for j in range(8):
            jobs.append((w_in[:, wide + j * 256:wide + (j + 1) * 256], True, "act",
                         lambda ps, j=j: nc.scalar.activation(v[:, :, j * 256:(j + 1) * 256],
                                                              ps[:, :].rearrange("p (b n) -> p b n", b=TB),
                                                              ACT.Gelu_apprx_tanh)))
        dense_up(K, K.h, DT, jobs)
        mix_at = [banks.take(0), banks.take(1)]
        gate_at = [banks.take(2 + h % 6) for h in range(heads)]
        with nc.sbuf_tensor([P, heads, P], F32) as raw, nc.sbuf_tensor([P, heads, P], F32) as bias, \
                nc.sbuf_tensor([P, wide], F32) as squares, nc.sbuf_tensor([P, TB], F32) as ssq, \
                nc.sbuf_tensor([P, 2, 2, S], F32) as gated, nc.Block() as block:

            @block.sync
            def _(sp):
                sp.dma_start(raw[:, :, :], w_s.rearrange("h t s -> t h s")).then_inc(mix_in, 16)
                sp.dma_start(bias[:, :, :], b_s.unsqueeze(0).broadcast_to([P, heads, P])).then_inc(bias_in, 16)

            @block.scalar
            def _(act):
                v_steps.eng = act
                for b in range(TB):
                    v_steps.link(nc.scalar.activation(squares[:, :], v[:, b, :], ACT.Square, accum_out=ssq[:, b:b + 1]))
                nc.scalar.activation(ssq[:, :], ssq[:, :], ACT.Sqrt, bias=K.col("eps"), scale=1.0 / wide)\
                    .then_inc(K.squares.sem, 1)

            @block.tensor
            def _(pe):
                pe.wait_ge(mix_in, 16)
                for g, at in enumerate(mix_at):
                    banks.vacant(pe, at)
                    for h in range(4):
                        m = nc.tensor.transpose(K.ps[at[0]][:, h * P:(h + 1) * P], raw[:, 4 * g + h, :], K.ident)
                    m.then_inc(banks.full[at[0]], 1)
                banks.read(pe, mix_at[1])
                pe.wait_ge(K.scaled.sem, K.scaled.base + 1)
                for h, at in enumerate(gate_at):
                    banks.vacant(pe, at)
                    for half in range(2):
                        for c in range(TB):
                            m = nc.tensor.matmul(K.ps[at[0]][:, half * S + c * P:half * S + (c + 1) * P],
                                                 v[:, c, h * 256 + half * P:h * 256 + (half + 1) * P], mix[:, h, :],
                                                 start=True, stop=True)
                    m.then_inc(banks.full[at[0]], 1)

            @block.vector
            def _(dve):
                mixed_steps.eng = dve
                for g, at in enumerate(mix_at):
                    banks.ready(dve, at)
                    nc.vector.tensor_tensor(mix[:, 4 * g:4 * g + 4, :],
                                            K.ps[at[0]][:, :].rearrange("p (h t) -> p h t", h=4),
                                            K.const("upto", P).unsqueeze(1).broadcast_to([P, 4, P]), ALU.mult)\
                        .then_inc(banks.free[at[0]], 1)
                dve.wait_ge(*K.squares(1))
                mixed_steps.link(nc.vector.reciprocal(ssq[:, :], ssq[:, :]))
                for b in range(TB):
                    m = nc.vector.tensor_scalar(v[:, b, :], v[:, b, :], ssq[:, b:b + 1], None, ALU.mult)
                m.then_inc(K.scaled.sem, 1)
                dve.wait_ge(bias_in, 16)
                for h, at in enumerate(gate_at):
                    banks.ready(dve, at)
                    for half in range(2):
                        m = nc.vector.scalar_tensor_tensor(
                            gated[:, h % 2, half, :].rearrange("p (c t) -> p c t", c=TB),
                            K.ps[at[0]][:, half * S:(half + 1) * S].rearrange("p (c t) -> p c t", c=TB),
                            K.param("a_v_norm", 2 * h + half),
                            bias[:, h, :].unsqueeze(1).broadcast_to([P, TB, P]), ALU.mult, ALU.add)
                    m.then_inc(banks.free[at[0]], 1)
                    banks.read(dve, at)
                    nc.vector.tensor_tensor(u[:, 2 * h:2 * h + 2, :], u[:, 2 * h:2 * h + 2, :], gated[:, h % 2, :, :],
                                            ALU.mult)
        K.squares.done(1)
        K.scaled.done(1)
        dense_down(K, u, a["a_w_out"][0], tiles, add_residual(K))


def pool_mixer(K, a):
    nc, banks = K.nc, K.banks
    windows = (2, 4, 8, 16)
    rmsnorm(K, K.x[:, :, :], K.h, lambda t: K.param("mix_norm", DT + t), DT)
    with nc.sbuf_tensor([P, DT, S], F32) as p, nc.sbuf_tensor([P, DT, S], F32) as y:
        dense_down(K, K.h, a["b_w_in"][0], DT, store_to(K, p))
        grp_in = nc.alloc_semaphore("group_weights_loaded")
        group_at = [banks.take(g) for g in range(4)]
        with nc.sbuf_tensor([P, DT, S], F32) as even, nc.sbuf_tensor([P, DT, S], F32) as odd, \
                nc.sbuf_tensor([P, 4, 2, 256], F32) as w, nc.Block() as block:

            @block.sync
            def _(sp):
                sp.dma_start(w[:, :, :, :], a["b_w_grp"][0].rearrange("g (k p) d -> p g k d", p=P)).then_inc(grp_in, 16)

            @block.vector
            def _(dve):
                K.vsteps.eng = dve
                link = K.vsteps.link
                src = p
                for g, window in enumerate(windows):
                    back, dst = window // 2, (even, odd)[g % 2]
                    first = 2 * g
                    nc.vector.tensor_copy(dst[:, first:, 0:back], src[:, first:, 0:back])
                    link(nc.vector.tensor_tensor(dst[:, first:, back:], src[:, first:, back:], src[:, first:, 0:S - back],
                                                 ALU.add))
                    mean = dst[:, first:first + 2, :]
                    link(nc.vector.tensor_tensor(mean, mean, K.const(f"per{window}", S).unsqueeze(1)
                                                 .broadcast_to([P, 2, S]), ALU.mult))
                    nc.vector.tensor_tensor(mean, mean, p[:, first:first + 2, :], ALU.subtract)\
                        .then_inc(K.scaled.sem, 1)
                    src = dst
                for g, at in enumerate(group_at):
                    banks.ready(dve, at)
                    for half in range(2):
                        m = nc.vector.tensor_scalar(y[:, 2 * g + half, :], K.ps[at[0]][:, half * S:(half + 1) * S],
                                                    K.param("b_scale", 2 * g + half), None, ALU.mult)
                    m.then_inc(banks.free[at[0]], 1)

            @block.tensor
            def _(pe):
                pe.wait_ge(grp_in, 16)
                for g, at in enumerate(group_at):
                    pe.wait_ge(*K.scaled(g + 1))
                    banks.vacant(pe, at)
                    pooled = (even, odd)[g % 2]
                    for half in range(2):
                        for k in range(2):
                            m = nc.tensor.matmul(K.ps[at[0]][:, half * S:(half + 1) * S],
                                                 w[:, g, k, half * P:(half + 1) * P], pooled[:, 2 * g + k, :],
                                                 start=k == 0, stop=k == 1)
                    m.then_inc(banks.full[at[0]], 1)
        K.scaled.done(4)
        dense_down(K, y, a["b_w_out"][0], DT, add_residual(K))


def adaptive_columns(K, a):
    nc, ring, banks = K.nc, K.ring, K.banks
    tiles = 6 * DT
    trips, per = tiles // 8, 4
    units = []
    for _ in range(per):
        units.append(ring.take(trips))
    uses = [ring.freed_by_use(u[0], trips) for u in units]
    at = banks.take(4, signals=False)
    w = a["w_ada_2"][0].rearrange("(t p) n -> p t n", p=P)
    mod = nc.alloc_sbuf_tensor("mod_columns", [P, tiles], F32)
    K.gain1, K.gain2, K.gate1, K.gate2 = (nc.alloc_sbuf_tensor(n, [P, DT], F32) for n in
                                          ("gain_mix", "gain_ffn", "gate_mix", "gate_ffn"))
    K.shift1, K.shift2 = mod[:, 0:DT], mod[:, 3 * DT:4 * DT]
    with nc.sbuf_tensor([P, DT], F32) as cond, nc.Block() as block:

        @block.sync
        def _(sp):
            for b, unit in enumerate(units):
                ring.vacant(sp, unit)
                sp.dma_start(ring.slot(unit[0]).rearrange("p (t n) -> p t n", n=256), w[:, :, b * 256:(b + 1) * 256])\
                    .then_inc(ring.loaded[unit[0]], 16)
            with sp.Fori(1, trips) as i:
                for b, (unit, n) in enumerate(zip(units, uses)):
                    column = sp.snap(i * (per * 256) + b * 256)
                    sp.wait_ge(ring.used[unit[0]], i + n)
                    sp.dma_start(ring.slot(unit[0]).rearrange("p (t n) -> p t n", n=256),
                                 w[:, :, bass.ds(column, 256)]).then_inc(ring.loaded[unit[0]], 16)

        @block.scalar
        def _(act):
            nc.scalar.activation(cond[:, :], K.param("c", 0, DT), ACT.Silu).then_inc(K.squares.sem, 1)

        @block.tensor
        def _(pe):
            pe.wait_ge(*K.squares(1))
            banks.vacant(pe, at)
            with pe.Fori(0, trips) as i:
                for b, unit in enumerate(units):
                    pe.wait_ge(ring.loaded[unit[0]], i * 16 + (unit[1] * 16 + 16))
                    for half in range(2):
                        for k in range(DT):
                            m = nc.tensor.matmul(K.ps[4][:, bass.ds(i * 8 + (2 * b + half), 1)],
                                                 ring.slot(unit[0])[:, k * 256 + half * P:k * 256 + (half + 1) * P],
                                                 cond[:, k:k + 1], start=k == 0, stop=k == DT - 1)
                    m.then_inc(ring.used[unit[0]], 1)

        @block.vector
        def _(dve):
            K.vsteps.eng = dve
            dve.wait_ge(ring.used[units[-1][0]], uses[-1] + trips)
            K.vsteps.link(nc.vector.tensor_tensor(mod[:, :], K.ps[4][:, 0:tiles], K.param("b_ada", 0, tiles), ALU.add))
            for out, g, q in ((K.gain1, "g_pre_mix", 1), (K.gain2, "g_pre_ffn", 4)):
                nc.vector.scalar_tensor_tensor(out[:, :], mod[:, q * DT:(q + 1) * DT], 1.0, K.param(g, 0, DT),
                                               ALU.add, ALU.mult)
            for out, g, q in ((K.gate1, "g_post_mix", 2), (K.gate2, "g_post_ffn", 5)):
                m = nc.vector.tensor_tensor(out[:, :], mod[:, q * DT:(q + 1) * DT], K.param(g, 0, DT), ALU.mult)
            m.then_inc(banks.free[4], 1)
    K.squares.done(1)


def attention(K, qb, heads, keys, scores, weights, values, halves, out, order=range(8)):
    nc, banks = K.nc, K.banks
    blocks = keys // P
    per_bank = 512 // keys
    score_at = [banks.take(b) for b in range(-(-heads // per_bank))]
    turned = heads * blocks
    turned_at = [banks.take(4 + b) for b in range(turned // 4)]
    out_banks = 1 if halves == 1 else 2
    out_at = [banks.take(b) for b in range(out_banks)]
    with nc.sbuf_tensor([P, heads, keys], F32) as w, nc.sbuf_tensor([P, turned, P], F32) as w_t, nc.Block() as block:
        weights.begin(K, qb, heads, keys, w, score_at)

        @block.tensor
        def _(pe):
            for b, at in enumerate(score_at):
                banks.vacant(pe, at)
                for h in range(b * per_bank, min(heads, (b + 1) * per_bank)):
                    ops = scores(order[h])
                    col = (h - b * per_bank) * keys
                    for k, (lhs, rhs) in enumerate(ops):
                        m = nc.tensor.matmul(K.ps[at[0]][:, col:col + keys], lhs, rhs, start=k == 0,
                                             stop=k == len(ops) - 1)
                m.then_inc(banks.full[at[0]], 1)
            pe.wait_ge(*K.weights(1))
            for b, at in enumerate(turned_at):
                banks.vacant(pe, at)
                for q in range(4):
                    h, kb = divmod(4 * b + q, blocks)
                    m = nc.tensor.transpose(K.ps[at[0]][:, q * P:(q + 1) * P], w[:, h, kb * P:(kb + 1) * P], K.ident)
                m.then_inc(banks.full[at[0]], 1)
            for at in turned_at:
                banks.read(pe, at)
            for at in out_at:
                banks.vacant(pe, at)
            for h in range(heads):
                for half in range(halves):
                    if halves == 1:
                        row, tile = order[h] % 2, order[h] // 2
                        ps = K.ps[0][64 * row:64 * row + 64, tile * P:(tile + 1) * P]
                    else:
                        tile = 2 * h + half
                        ps = K.ps[tile // 4][:, tile % 4 * P:(tile % 4 + 1) * P]
                    for kb in range(blocks):
                        m = nc.tensor.matmul(ps, values(order[h], kb, half), w_t[:, h * blocks + kb, :], start=kb == 0,
                                             stop=kb == blocks - 1)
                if h == heads - 1 or halves == 2 and h % 2:
                    m.then_inc(banks.full[0 if halves == 1 else h // 2], 1)

        @block.scalar
        def _(act):
            weights.act(act)
            for b, at in enumerate(turned_at):
                banks.ready(act, at)
                nc.scalar.activation(w_t[:, 4 * b:4 * b + 4, :].rearrange("p a q -> p (a q)"), K.ps[at[0]][:, :],
                                     ACT.Copy).then_inc(banks.free[at[0]], 1)

        @block.gpsimd
        def _(pool):
            weights.pool(pool)

        @block.vector
        def _(dve):
            K.vsteps.eng = dve
            weights.dve(dve)
            for at, (dst, src) in zip(out_at, out([K.ps[at[0]] for at in out_at])):
                banks.ready(dve, at)
                nc.vector.tensor_copy(dst, src).then_inc(banks.free[at[0]], 1)
    K.weights.done(1)
    weights.end()


class Softmax:

    def __init__(self, scale, bias=None, slopes=None, distance=None):
        self.scale, self.bias, self.slopes, self.distance = scale, bias, slopes, distance

    def begin(self, K, qb, heads, keys, w, at):
        self.K, self.qb, self.heads, self.keys, self.w, self.at = K, qb, heads, keys, w, at

    def pool(self, pool):
        pass

    def act(self, act):
        K, nc = self.K, self.K.nc
        act.wait_ge(*K.maxima(1))
        for h in range(self.heads):
            m = nc.scalar.activation(self.w[:, h, :], self.w[:, h, :], ACT.Exp, bias=K.negmax[:, h:h + 1],
                                     accum_out=K.sums[:, h:h + 1])
        m.then_inc(K.exps.sem, 1)

    def dve(self, dve):
        K, nc, w, keys = self.K, self.K.nc, self.w, self.keys
        link = K.vsteps.link
        per_bank = 512 // keys
        if self.slopes is not None:
            for h in range(self.heads):
                m = nc.vector.scalar_tensor_tensor(w[:, h, :], self.distance[:, self.qb, 0:keys], -self.slopes[h],
                                                   self.bias[:, self.qb, 0:keys], ALU.mult, ALU.add)
            link(m)
        for b, at in enumerate(self.at):
            K.banks.ready(dve, at)
            h0, n = b * per_bank, min(per_bank, self.heads - b * per_bank)
            ps = K.ps[at[0]][:, 0:n * keys].rearrange("p (h k) -> p h k", h=n)
            part = w[:, h0:h0 + n, :]
            if self.slopes is not None:
                m = nc.vector.scalar_tensor_tensor(part, ps, self.scale, part, ALU.mult, ALU.add)
            elif self.bias is not None:
                m = nc.vector.scalar_tensor_tensor(part, ps, self.scale, self.bias[self.qb].unsqueeze(1)
                                                   .broadcast_to([P, n, keys]), ALU.mult, ALU.add)
            else:
                m = nc.vector.tensor_scalar(part, ps, self.scale, None, ALU.mult)
            m.then_inc(K.banks.free[at[0]], 1)
        K.banks.read(dve, self.at[-1])
        nc.vector.tensor_reduce(K.negmax[:, 0:self.heads], w[:, :, :], AX.X, ALU.max, negate=True)\
            .then_inc(K.maxima.sem, 1)
        dve.wait_ge(*K.exps(1))
        link(nc.vector.reciprocal(K.sums[:, 0:self.heads], K.sums[:, 0:self.heads]))
        nc.vector.tensor_tensor(w[:, :, :], w[:, :, :], K.sums[:, 0:self.heads].unsqueeze(2)
                                .broadcast_to([P, self.heads, keys]), ALU.mult).then_inc(K.weights.sem, 1)

    def end(self):
        self.K.maxima.done(1)
        self.K.exps.done(1)


def reduce_angle(K, dve, angle, turns):
    nc, link = K.nc, K.vsteps.link
    c1 = 6.28125
    c2 = float(np.float32(np.round((TWO_PI - c1) * 2 ** 21) / 2 ** 21))
    c3 = float(np.float32(TWO_PI - c1 - c2))
    link(nc.vector.tensor_scalar(turns, angle, 1.0 / TWO_PI, ROUND, ALU.mult, ALU.add))
    link(nc.vector.tensor_scalar(turns, turns, ROUND, None, ALU.subtract))
    for c in (c1, c2, c3):
        link(nc.vector.scalar_tensor_tensor(angle, turns, -c, angle, ALU.mult, ALU.add))
    limit = 3.1415925
    return nc.vector.tensor_scalar(angle, angle, limit, -limit, ALU.min, ALU.max)


def mixed_attention(K, a):
    nc, banks = K.nc, K.banks
    rmsnorm(K, K.x[:, :, :], K.h, lambda t: K.gain1[:, t:t + 1], DT, shift=lambda t: K.shift1[:, t:t + 1])
    heads, width = 8, 1480
    memory = K.ring.memory
    at = [0]

    def part(n, pattern, **sizes):
        at[0] += n
        return memory[:, at[0] - n:at[0]].rearrange(pattern, **sizes)

    w_in = part(DT * width, "p (k n) -> p k n", k=DT)
    w_q = part(2 * 768, "p (k n) -> p k n", k=2)
    w_q_swapped = part(2 * 768, "p (k n) -> p k n", k=2)
    w_kv = part(1024, "p (k n) -> p k n", k=1)
    w_k_swapped = part(DT * 96, "p (k n) -> p k n", k=DT)
    w_q_pairs = part(DT * 512, "p (k n) -> p k n", k=DT)
    w_k_four = part(DT * P, "p (k n) -> p k n", k=DT)
    with ExitStack() as stack:
        def buffer(name, *shape):
            return stack.enter_context(nc.sbuf_tensor(name, [P, *shape], F32))

        c_q, c_kv = buffer("c_q", 2, S), buffer("c_kv", 1, S)
        q, k, v = buffer("mla_q", heads, S), buffer("mla_k", heads, S), buffer("mla_v", TB, 512)
        q_d, k_d, v_d = buffer("sparse_q", 4, S), buffer("sparse_k", S), buffer("sparse_v", TB, P)
        q_i, k_i, w_i = buffer("index_q", 2, S), buffer("index_k", S), buffer("index_w", TB, 8)
        mix, cos, sin = buffer("mixed", DT, S), buffer("rotary_cos", S), buffer("rotary_sin", S)
        distance, selected = buffer("distance", TB, S), buffer("selected", TB, S)
        project_inputs(K, a, heads, w_in, w_q, w_q_swapped, w_kv, w_k_swapped, w_q_pairs, w_k_four, c_q, c_kv, k, q_d, k_d, v_d,
                       q_i, k_i, w_i, cos, sin, distance)
        rmsnorm(K, c_q[:, :, :], c_q, lambda t: K.param("g_q_a", t), 2)
        rmsnorm(K, c_kv[:, :, :], c_kv, lambda t: K.param("g_kv_a", t), 1)
        expand_latents(K, heads, w_q, w_q_swapped, w_kv, c_q, c_kv, cos, sin, q, k, v)
        select_keys(K, q_i, k_i, w_i, selected)
        causal = {0: K.const("causal", P), 1: K.causal_rows}
        for qb in range(TB):
            keys = (qb + 1) * P
            tokens = slice(qb * P, (qb + 1) * P)
            attention(K, qb, heads, keys, lambda h: [(q[0:96, h, tokens], k[0:96, h, 0:keys])],
                      Softmax(96 ** -0.5, bias=causal), lambda h, kb, half: v[:, kb, h * 64:(h + 1) * 64], 1,
                      lambda ps: [(mix[:, 0:4, tokens], ps[0][:, :].rearrange("p (t q) -> p t q", t=4))])
            slopes = [2.0 ** (-8.0 * (h + 1) / heads) for h in range(heads)]

            def sparse_scores(h):
                g, j = divmod(h, 4)
                rows = slice(64 * g, 64 * g + 64)
                return [(q_d[rows, j, tokens], k_d[rows, 0:keys])]

            attention(K, qb, heads, keys, sparse_scores,
                      Softmax(64 ** -0.5, bias=selected, slopes=slopes, distance=distance),
                      lambda h, kb, half: v_d[:, kb, (h // 4) * 64:(h // 4 + 1) * 64], 1,
                      lambda ps: [(mix[:, 4:8, tokens], ps[0][:, :].rearrange("p (t q) -> p t q", t=4))])
        dense_down(K, mix, a["w_o_2"][0], DT, store_to(K, K.h))
    rmsnorm(K, K.h[:, :, :], None, lambda t: K.gate1[:, t:t + 1], DT, add_to=K.x[:, :, :])


def project_inputs(K, a, heads, w_in, w_q, w_q_swapped, w_kv, w_k_swapped, w_q_pairs, w_k_four, c_q, c_kv, k, q_d, k_d, v_d,
                   q_i, k_i, w_i, cos, sin, distance):
    nc, banks = K.nc, K.banks
    w_in_loaded = [nc.alloc_semaphore(f"w_in_loaded{i}") for i in range(2)]
    w_q_loaded, w_kv_loaded, pos_loaded, row_loaded = (nc.alloc_semaphore(n) for n in (
        "w_q_loaded", "w_kv_loaded", "positions_loaded", "position_row_loaded"))
    arranged = nc.alloc_semaphore("projection_weights_arranged")
    pos_done, angle_done, abs_done = (nc.alloc_semaphore(n) for n in ("positions_float", "angles_reduced", "abs_angle"))
    with nc.sbuf_tensor([P, S], I32) as pos_int, nc.sbuf_tensor([P, S], F32) as pos, \
            nc.sbuf_tensor([P, TB], F32) as pos_col, nc.sbuf_tensor([P, S], F32) as turns, \
            nc.sbuf_tensor([P, 2, S], F32) as k_rope:
        angle_at = [banks.take(7), banks.take(6)]
        result_at = [banks.take(b) for b in range(6)] + [banks.take(6), banks.take(7)]
        with nc.Block() as block:

            @block.sync
            def _(sp):
                view = a["w_in_2"][0].rearrange("(t p) n -> p t n", p=P)
                sp.dma_start(pos_int[:, :], a["positions_2"].broadcast_to([P, S])).then_inc(pos_loaded, 16)
                for i in range(2):
                    sp.dma_start(w_in[:, 4 * i:4 * i + 4, :], view[:, 4 * i:4 * i + 4, :]).then_inc(w_in_loaded[i], 16)
                sp.dma_start(w_q, a["w_q_b_2"][0].rearrange("(t p) n -> p t n", p=P)).then_inc(w_q_loaded, 16)
                sp.dma_start(w_kv, a["w_kv_b_2"][0].rearrange("(t p) n -> p t n", p=P)).then_inc(w_kv_loaded, 16)

            @block.tensor
            def _(pe):
                pe.wait_ge(pos_done, 1)
                for b in angle_at:
                    banks.vacant(pe, b)
                nc.tensor.matmul(K.ps[7][0:96, 0:S], K.const("freq", 96)[0:1, :], pos[0:1, :], start=True, stop=True)\
                    .then_inc(banks.full[7], 1)
                for b in range(TB):
                    m = nc.tensor.matmul(K.ps[6][:, b:b + 1], pos[0:1, b * P:(b + 1) * P], K.ones[0:1, 0:1],
                                         start=True, stop=True)
                m.then_inc(banks.full[6], 1)

                def project(ps, cols, by_token=None):
                    for t in range(DT):
                        lhs, rhs = (cols(t), K.h[:, t, :]) if by_token is None else \
                            (K.h[:, t, by_token * P:(by_token + 1) * P], cols(t))
                        m = nc.tensor.matmul(ps, lhs, rhs, start=t == 0, stop=t == DT - 1)
                    return m

                def columns(lo, n):
                    return lambda t: w_in[:, t, lo:lo + n]

                for i in range(2):
                    pe.wait_ge(w_in_loaded[i], 16)
                for at_ in result_at[:6]:
                    banks.vacant(pe, at_)
                ps = K.ps
                project(ps[0][:, 0:S], columns(0, P))
                project(ps[0][:, S:2 * S], columns(P, P)).then_inc(banks.full[0], 1)
                project(ps[1][:, 0:S], columns(256, P))
                project(ps[1][0:96, S:2 * S], columns(320, 96)).then_inc(banks.full[1], 1)
                pe.wait_ge(*K.scaled(1))
                project(ps[2][0:96, 0:S], lambda t: w_k_swapped[:, t, :])
                project(ps[2][:, S:2 * S], columns(928, P)).then_inc(banks.full[2], 1)
                pe.wait_ge(arranged, 1)
                for j in range(4):
                    m = project(ps[3 + j // 2][:, (j % 2) * S:(j % 2 + 1) * S],
                                lambda t: w_q_pairs[:, t, j * P:(j + 1) * P])
                    if j % 2:
                        m.then_inc(banks.full[3 + j // 2], 1)
                for b in range(TB):
                    m = project(ps[5][:, b * P:(b + 1) * P], columns(1056, P), b)
                m.then_inc(banks.full[5], 1)
                for at_ in result_at[6:]:
                    banks.vacant(pe, at_)
                project(ps[6][:, 0:S], columns(1184, P))
                project(ps[6][:, S:2 * S], columns(1312, P)).then_inc(banks.full[6], 1)
                project(ps[7][:, 0:S], lambda t: w_k_four[:, t, :])
                for b in range(TB):
                    m = project(ps[7][:, S + 8 * b:S + 8 * b + 8], columns(1472, 8), b)
                m.then_inc(banks.full[7], 1)
                pe.wait_ge(w_kv_loaded, 16)

            @block.gpsimd
            def _(pool):
                for i in range(2):
                    pool.wait_ge(w_in_loaded[i], 16)
                pairs = w_q_pairs.rearrange("p k (j g d) -> p k j g d", j=4, g=2)
                own = w_in[:, :, 416:928].rearrange("p k (g j d) -> p k g j d", g=2, j=4)
                for j in range(4):
                    nc.gpsimd.tensor_copy(pairs[:, :, j], own[:, :, :, j])
                nc.gpsimd.tensor_copy(w_k_four.rearrange("p k (r d) -> p k r d", r=4),
                                      w_in[:, :, 1440:1472].unsqueeze(2).broadcast_to([P, DT, 4, 32])).then_inc(arranged, 1)

            @block.scalar
            def _(act):
                for b in range(TB):
                    act.wait_ge(*K.maxima(b + 1))
                    nc.scalar.activation(distance[:, b, :], distance[:, b, :], ACT.Abs)
                act.wait_ge(angle_done, 1)
                nc.scalar.activation(turns[0:96, :], sin[0:96, :], ACT.Abs).then_inc(abs_done, 1)
                act.wait_ge(abs_done, 1)
                nc.scalar.activation(cos[0:96, :], turns[0:96, :], ACT.Sin, bias=K.col("half_pi")[0:96, :], scale=-1.0)
                nc.scalar.activation(sin[0:96, :], sin[0:96, :], ACT.Sin).then_inc(abs_done, 1)
                for b, at_, dst, src in (
                        (0, result_at[0], c_q[:, :, :].rearrange("p t s -> p (t s)"), K.ps[0][:, :]),
                        (3, result_at[3], q_d[:, 0:2, :].rearrange("p t s -> p (t s)"), K.ps[3][:, :]),
                        (4, result_at[4], q_d[:, 2:4, :].rearrange("p t s -> p (t s)"), K.ps[4][:, :]),
                        (5, result_at[5], v_d[:, :, :].rearrange("p t s -> p (t s)"), K.ps[5][:, 0:2 * P])):
                    banks.ready(act, at_)
                    nc.scalar.activation(dst, src, ACT.Copy).then_inc(banks.free[b], 1)

            @block.vector
            def _(dve):
                K.vsteps.eng = dve
                link = K.vsteps.link
                dve.wait_ge(pos_loaded, 16)
                nc.vector.tensor_copy(pos[:, :], pos_int[:, :]).then_inc(pos_done, 1)
                for i in range(2):
                    dve.wait_ge(w_in_loaded[i], 16)
                nc.vector.tensor_copy(w_k_swapped[:, :, 0:64], w_in[:, :, 320:384])
                nc.vector.tensor_copy(w_k_swapped[:, :, 64:80], w_in[:, :, 400:416])
                nc.vector.tensor_copy(w_k_swapped[:, :, 80:96], w_in[:, :, 384:400]).then_inc(K.scaled.sem, 1)
                banks.ready(dve, angle_at[0])
                nc.vector.tensor_copy(sin[0:96, :], K.ps[7][0:96, 0:S]).then_inc(banks.free[7], 1)
                banks.ready(dve, angle_at[1])
                nc.vector.tensor_copy(pos_col[:, :], K.ps[6][:, 0:TB]).then_inc(banks.free[6], 1)
                banks.read(dve, angle_at[1])
                for b in range(TB):
                    nc.vector.tensor_scalar(distance[:, b, :], pos[:, :], pos_col[:, b:b + 1], None, ALU.subtract)\
                        .then_inc(K.maxima.sem, 1)
                reduce_angle(K, dve, sin[0:96, :], turns[0:96, :]).then_inc(angle_done, 1)
                dve.wait_ge(w_q_loaded, 16)
                own, swapped = (w.rearrange("p k (h n) -> p (k h) n", n=96) for w in (w_q, w_q_swapped))
                nc.vector.tensor_copy(swapped[:, :, 0:64], own[:, :, 0:64])
                nc.vector.tensor_copy(swapped[:, :, 64:80], own[:, :, 80:96])
                nc.vector.tensor_copy(swapped[:, :, 80:96], own[:, :, 64:80])
                dve.wait_ge(abs_done, 2)
                link(nc.vector.tensor_scalar(sin[0:96, :], sin[0:96, :], K.col("sign")[0:96, :], None, ALU.mult))
                banks.ready(dve, result_at[1])
                nc.vector.tensor_copy(c_kv[:, 0, :], K.ps[1][:, 0:S])
                nc.vector.tensor_tensor(k_rope[64:96, 0, :], K.ps[1][64:96, S:2 * S], cos[64:96, :], ALU.mult)\
                    .then_inc(banks.free[1], 1)
                banks.ready(dve, result_at[2])
                nc.vector.tensor_copy(k_d[:, :], K.ps[2][:, S:2 * S])
                nc.vector.tensor_tensor(k_rope[64:96, 1, :], K.ps[2][64:96, 0:S], sin[64:96, :], ALU.mult)\
                    .then_inc(banks.free[2], 1)
                banks.read(dve, result_at[2])
                for h in range(heads):
                    nc.vector.tensor_tensor(k[64:96, h, :], k_rope[64:96, 0, :], k_rope[64:96, 1, :], ALU.add)
                banks.ready(dve, result_at[6])
                nc.vector.tensor_scalar(q_i[:, :, :].rearrange("p t s -> p (t s)"), K.ps[6][:, :], 32 ** -0.5, None,
                                        ALU.mult).then_inc(banks.free[6], 1)
                banks.ready(dve, result_at[7])
                nc.vector.tensor_copy(k_i[:, :], K.ps[7][:, 0:S])
                nc.vector.tensor_scalar(w_i[:, :, :].rearrange("p b h -> p (b h)"), K.ps[7][:, S:S + 16], 8 ** -0.5,
                                        None, ALU.mult).then_inc(banks.free[7], 1)
        K.scaled.done(1)
        K.maxima.done(TB)


def expand_latents(K, heads, w_q, w_q_swapped, w_kv, c_q, c_kv, cos, sin, q, k, v):
    nc, banks = K.nc, K.banks
    plain_at = [banks.take(b) for b in (0, 1, 2, 3)]
    swapped_at = [banks.take(b) for b in (4, 5, 6, 7)]
    k_at = [banks.take(b) for b in (0, 1, 2, 3)]
    v_at = [banks.take(b) for b in (4, 5)]
    with nc.sbuf_tensor([P, 2, 2, S], F32) as turned, nc.Block() as block:

        @block.tensor
        def _(pe):
            for w, at in ((w_q, plain_at), (w_q_swapped, swapped_at)):
                for j in range(4):
                    banks.vacant(pe, at[j])
                    for i in range(2):
                        h = 2 * j + i
                        for t in range(2):
                            m = nc.tensor.matmul(K.ps[at[j][0]][0:96, i * S:(i + 1) * S], w[:, t, h * 96:(h + 1) * 96],
                                                 c_q[:, t, :], start=t == 0, stop=t == 1)
                    m.then_inc(banks.full[at[j][0]], 1)
            for j in range(4):
                banks.vacant(pe, k_at[j])
                for i in range(2):
                    h = 2 * j + i
                    m = nc.tensor.matmul(K.ps[j][0:64, i * S:(i + 1) * S], w_kv[:, 0, h * P:h * P + 64], c_kv[:, 0, :],
                                         start=True, stop=True)
                m.then_inc(banks.full[j], 1)
            for b, at in enumerate(v_at):
                banks.vacant(pe, at)
                nc.tensor.matmul(K.ps[at[0]][:, :], c_kv[:, 0, b * P:(b + 1) * P],
                                 w_kv[:, 0, :].rearrange("p (h n) -> p h n", h=heads)[:, :, 64:P],
                                 start=True, stop=True).then_inc(banks.full[at[0]], 1)

        @block.vector
        def _(dve):
            K.vsteps.eng = dve
            link = K.vsteps.link

            def table(t):
                return t[64:96, :].unsqueeze(1).broadcast_to([32, 2, S])
            for j in range(4):
                banks.ready(dve, plain_at[j])
                ps = K.ps[j][:, :].rearrange("p (h s) -> p h s", h=2)
                nc.vector.tensor_copy(q[0:64, 2 * j:2 * j + 2, :], ps[0:64])
                nc.vector.tensor_tensor(turned[64:96, 0, :, :], ps[64:96], table(cos), ALU.mult)\
                    .then_inc(banks.free[j], 1)
                banks.ready(dve, swapped_at[j])
                nc.vector.tensor_tensor(turned[64:96, 1, :, :],
                                        K.ps[4 + j][:, :].rearrange("p (h s) -> p h s", h=2)[64:96], table(sin),
                                        ALU.mult).then_inc(banks.free[4 + j], 1)
                banks.read(dve, swapped_at[j])
                link(nc.vector.tensor_tensor(q[64:96, 2 * j:2 * j + 2, :], turned[64:96, 0, :, :],
                                             turned[64:96, 1, :, :], ALU.add))
            for b, at in enumerate(v_at):
                banks.ready(dve, at)
                nc.vector.tensor_copy(v[:, b, :], K.ps[at[0]][:, :]).then_inc(banks.free[at[0]], 1)

        @block.scalar
        def _(act):
            for j in range(4):
                banks.ready(act, k_at[j])
                nc.scalar.activation(k[0:64, 2 * j:2 * j + 2, :], K.ps[j][0:64, :].rearrange("p (h s) -> p h s", h=2),
                                     ACT.Copy).then_inc(banks.free[j], 1)


def select_keys(K, q_i, k_i, w_i, selected):
    nc, banks = K.nc, K.banks
    taken = -3e38
    at = [[banks.take(4 * (qb % 2) + r) for r in range(4)] for qb in range(TB)]
    with nc.sbuf_tensor([P, TB, 8, S], F32) as rel, nc.sbuf_tensor([P, TB, S], F32) as score, \
            nc.sbuf_tensor([P, TB, 8], F32) as top, nc.Block() as block:

        @block.tensor
        def _(pe):
            for qb in range(TB):
                keys = (qb + 1) * P
                for r in range(4):
                    banks.vacant(pe, at[qb][r])
                    for i in range(2):
                        rows = slice(32 * r, 32 * r + 32)
                        m = nc.tensor.matmul(K.ps[at[qb][r][0]][:, i * keys:(i + 1) * keys],
                                             q_i[rows, i, qb * P:(qb + 1) * P], k_i[rows, 0:keys], start=True, stop=True)
                    m.then_inc(banks.full[at[qb][r][0]], 1)

        @block.scalar
        def _(act):
            for qb in range(TB):
                keys = (qb + 1) * P
                for r in range(4):
                    banks.ready(act, at[qb][r])
                    nc.scalar.activation(rel[:, qb, 2 * r:2 * r + 2, 0:keys],
                                         K.ps[at[qb][r][0]][:, 0:2 * keys].rearrange("p (h s) -> p h s", h=2),
                                         ACT.Relu).then_inc(banks.free[at[qb][r][0]], 1)

        @block.vector
        def _(dve):
            K.vsteps.eng = dve
            link = K.vsteps.link
            for qb in range(TB):
                keys = (qb + 1) * P
                acc = score[:, qb, 0:keys]
                for r in range(4):
                    banks.read(dve, at[qb][r])
                    for i in range(2):
                        w = w_i[:, qb, 4 * i + r:4 * i + r + 1]
                        part = rel[:, qb, 2 * r + i, 0:keys]
                        if r == i == 0:
                            link(nc.vector.tensor_scalar(acc, part, w, 0.0, ALU.mult, ALU.add))
                        else:
                            link(nc.vector.scalar_tensor_tensor(acc, part, w, acc, ALU.mult, ALU.add))
                causal = K.const("causal", P) if qb == 0 else K.causal_rows
                link(nc.vector.tensor_tensor(acc, acc, causal, ALU.add))
                for _ in range(64 // 8):
                    link(nc.vector.max(top[:, qb, :], acc))
                    link(nc.vector.match_replace(acc, top[:, qb, :], acc, taken))
                link(nc.vector.tensor_scalar(acc, acc, taken / 2, NEG, ALU.is_gt, ALU.mult))
                nc.vector.tensor_tensor(selected[:, qb, 0:keys], acc, causal, ALU.add)


EXPERTS, CHOSEN = 32, 4
CAP = 128
ITEMS = 48


def route(K, a, M):
    nc, banks = K.nc, K.banks
    router_in, bias_in, b1_in, b2_in = (nc.alloc_semaphore(n) for n in (
        "router_loaded", "router_bias_loaded", "expert_b1_loaded", "expert_b2_loaded"))
    chosen, softmaxed, tables = (nc.alloc_semaphore(n) for n in ("experts_chosen", "gates_exp", "item_tables"))
    logits_at = banks.take(0)
    token_at = [banks.take(4 + j) for j in range(4)]
    rank_at, turn_at, start_at, item_at, b1_at = banks.take(1), banks.take(2), banks.take(3), banks.take(0), banks.take(1)
    b2_at = [banks.take(4 + j) for j in range(4)]
    E = EXPERTS
    with ExitStack() as stack:
        def buffer(name, *shape, dt=F32):
            return stack.enter_context(nc.sbuf_tensor(name, list(shape), dt))

        w, bias = buffer("router_w", P, DT, E), buffer("router_b", P, E)
        b1, b2 = buffer("b1_rows", E, 2 * D), buffer("b2_rows", E, D)
        logits, top, negtop = buffer("logits", P, TB, E), buffer("top_logits", P, TB, 8), buffer("neg_top", P, TB)
        index_u, index = buffer("top_index", P, TB, 8, dt=U32), buffer("top_index_f", P, TB, 8)
        gates4, total = buffer("gates4", P, TB, CHOSEN), buffer("gate_sums", P, TB)
        hit, mask, gates = buffer("hit", P, TB, E), buffer("expert_mask", P, TB, E), buffer("expert_gates", P, TB, E)
        ranks = buffer("ranks", P, TB, E)
        rank_t, gate_t = buffer("rank_t", E, S), buffer("gate_t", E, S)
        count, items, over, start = (buffer(n, E, 1) for n in ("expert_counts", "expert_items", "over", "first_item"))
        since, inside, offset = (buffer(n, E, ITEMS) for n in ("since_first", "item_of_expert", "slot_offset"))
        block = stack.enter_context(nc.Block())

        @block.sync
        def _(sp):
            sp.dma_start(w[:, :, :], a["w_router_2"][0].rearrange("(t p) n -> p t n", p=P)).then_inc(router_in, 16)
            sp.dma_start(bias[:, :], a["b_router_2"].broadcast_to([P, E])).then_inc(bias_in, 16)
            sp.dma_start(b1[:, :], a["b_mlp1_2"][0]).then_inc(b1_in, 16)
            sp.dma_start(b2[:, :], a["b_mlp2_2"][0]).then_inc(b2_in, 16)

        @block.tensor
        def _(pe):
            ps = K.ps
            pe.wait_ge(router_in, 16)
            banks.vacant(pe, logits_at)
            for b in range(TB):
                for t in range(DT):
                    m = nc.tensor.matmul(ps[0][:, b * E:(b + 1) * E], K.h[:, t, b * P:(b + 1) * P], w[:, t, :],
                                         start=t == 0, stop=t == DT - 1)
            m.then_inc(banks.full[0], 1)
            for j, at in enumerate(token_at):
                banks.vacant(pe, at)
                for q in range(4):
                    t = 4 * (j % 2) + q
                    m = nc.tensor.transpose(ps[4 + j][:, q * P:(q + 1) * P], K.h[:, t, j // 2 * P:(j // 2 + 1) * P], K.ident)
                m.then_inc(banks.full[4 + j], 1)
            pe.wait_ge(chosen, 1)
            banks.vacant(pe, rank_at)
            before = K.const("before", P)
            nc.tensor.matmul(ps[1][:, 0:E], before, mask[:, 0, :], start=True, stop=True)
            nc.tensor.matmul(ps[1][:, E:2 * E], before, mask[:, 1, :], start=True, stop=False)
            nc.tensor.matmul(ps[1][:, E:2 * E], K.ones, mask[:, 0, :], start=False, stop=True)
            for b in range(TB):
                m = nc.tensor.matmul(ps[1][0:E, 2 * E:2 * E + 1], mask[:, b, :], K.ones[:, 0:1], start=b == 0, stop=b == TB - 1)
            m.then_inc(banks.full[1], 1)
            pe.wait_ge(chosen, 2)
            banks.vacant(pe, turn_at)
            for b in range(TB):
                nc.tensor.transpose(ps[2][0:E, b * P:(b + 1) * P], ranks[:, b, :], K.ident)
                m = nc.tensor.transpose(ps[2][0:E, S + b * P:S + (b + 1) * P], gates[:, b, :], K.ident)
            m.then_inc(banks.full[2], 1)
            pe.wait_ge(chosen, 3)
            banks.vacant(pe, start_at)
            nc.tensor.matmul(ps[3][0:E, 0:1], before[0:E, 0:E], items[:, :], start=True, stop=True)
            nc.tensor.matmul(ps[3][0:1, 1:2], items[:, :], K.ones[0:E, 0:1], start=True, stop=True)\
                .then_inc(banks.full[3], 1)
            pe.wait_ge(b1_in, 16)
            banks.vacant(pe, b1_at)
            pairs = b1[:, :].rearrange("e (t p two) -> e two t p", two=2, p=P)
            for q in range(2 * DT):
                m = nc.tensor.transpose(ps[1][:, q * E:(q + 1) * E], pairs[:, q // DT, q % DT, :], K.ident[0:E, 0:E])
            m.then_inc(banks.full[1], 1)
            pe.wait_ge(tables, 1)
            banks.vacant(pe, item_at)
            for b in range(TB):
                tokens = slice(b * P, (b + 1) * P)
                nc.tensor.matmul(ps[0][:, b * ITEMS:(b + 1) * ITEMS], rank_t[:, tokens], inside[:, :], start=True, stop=False)
                nc.tensor.matmul(ps[0][:, b * ITEMS:(b + 1) * ITEMS], K.ones[0:E, :], offset[:, :], start=False, stop=True)
                nc.tensor.matmul(ps[0][:, (2 + b) * ITEMS:(3 + b) * ITEMS], gate_t[:, tokens], inside[:, :], start=True, stop=True)
            nc.tensor.matmul(ps[0][0:1, 4 * ITEMS:5 * ITEMS], K.col("index")[0:E, :], inside[:, :], start=True, stop=True)\
                .then_inc(banks.full[0], 1)
            pe.wait_ge(b2_in, 16)
            for j, at in enumerate(b2_at):
                banks.vacant(pe, at)
                for i in range(2):
                    t = 2 * j + i
                    m = nc.tensor.matmul(ps[4 + j][:, i * S:(i + 1) * S], b2[:, t * P:(t + 1) * P], gate_t[:, :],
                                         start=True, stop=True)
                m.then_inc(banks.full[4 + j], 1)

        @block.scalar
        def _(act):
            for j, at in enumerate(token_at):
                banks.ready(act, at)
                nc.scalar.activation(M.tokens[:, j // 2, (j % 2) * 512:(j % 2 + 1) * 512], K.ps[4 + j][:, :], ACT.Copy)\
                    .then_inc(banks.free[4 + j], 1)
            act.wait_ge(softmaxed, 1)
            for b in range(TB):
                m = nc.scalar.activation(gates4[:, b, :], top[:, b, 0:CHOSEN], ACT.Exp, bias=negtop[:, b:b + 1],
                                         accum_out=total[:, b:b + 1])
            m.then_inc(softmaxed, 1)

        @block.vector
        def _(dve):
            K.vsteps.eng = dve
            link, v = K.vsteps.link, nc.vector
            dve.wait_ge(bias_in, 16)
            banks.ready(dve, logits_at)
            v.tensor_tensor(logits[:, :, :], K.ps[0][:, 0:TB * E].rearrange("p (b e) -> p b e", b=TB),
                            bias[:, :].unsqueeze(1).broadcast_to([P, TB, E]), ALU.add).then_inc(banks.free[0], 1)
            banks.read(dve, logits_at)
            for b in range(TB):
                link(v.max(top[:, b, :], logits[:, b, :]))
                link(v.max_index(index_u[:, b, :], top[:, b, :], logits[:, b, :]))
            v.tensor_scalar(negtop[:, :], top[:, :, 0], -1.0, None, ALU.mult).then_inc(softmaxed, 1)
            link(v.tensor_copy(index[:, :, :], index_u[:, :, :]))
            dve.wait_ge(softmaxed, 2)
            link(v.reciprocal(total[:, :], total[:, :]))
            link(v.tensor_tensor(gates4[:, :, :], gates4[:, :, :], total[:, :].unsqueeze(2).broadcast_to([P, TB, CHOSEN]), ALU.mult))
            number = K.const("iota", E)
            for b in range(TB):
                for k in range(CHOSEN):
                    pick = index[:, b, k:k + 1]
                    if k == 0:
                        v.tensor_scalar(mask[:, b, :], number, pick, None, ALU.is_equal)
                        link(v.tensor_scalar(gates[:, b, :], number, pick, gates4[:, b, k:k + 1], ALU.is_equal, ALU.mult))
                        continue
                    v.scalar_tensor_tensor(mask[:, b, :], number, pick, mask[:, b, :], ALU.is_equal, ALU.add)
                    link(v.tensor_scalar(hit[:, b, :], number, pick, gates4[:, b, k:k + 1], ALU.is_equal, ALU.mult))
                    link(v.tensor_tensor(gates[:, b, :], gates[:, b, :], hit[:, b, :], ALU.add))
            v.tensor_copy(hit[:, :, :], mask[:, :, :]).then_inc(chosen, 1)
            banks.ready(dve, rank_at)
            link(v.tensor_copy(count[:, :], K.ps[1][0:E, 2 * E:2 * E + 1]))
            link(v.scalar_tensor_tensor(ranks[:, :, :], K.ps[1][:, 0:TB * E].rearrange("p (b e) -> p b e", b=TB), 1000.0,
                                        mask[:, :, :], ALU.add, ALU.mult))
            v.tensor_scalar(ranks[:, :, :], ranks[:, :, :], -1000.0, None, ALU.add).then_inc(banks.free[1], 1)
            banks.read(dve, rank_at)
            v.tensor_copy(hit[:, :, :], ranks[:, :, :]).then_inc(chosen, 1)
            link(v.tensor_scalar(items[:, :], count[:, :], 0.0, None, ALU.is_gt))
            for r in range(1, S // CAP):
                link(v.tensor_scalar(over[:, :], count[:, :], float(r * CAP), None, ALU.is_gt))
                link(v.tensor_tensor(items[:, :], items[:, :], over[:, :], ALU.add))
            v.tensor_copy(over[:, :], items[:, :]).then_inc(chosen, 1)
            banks.ready(dve, turn_at)
            v.tensor_copy(rank_t[:, :], K.ps[2][0:E, 0:S])
            v.tensor_copy(gate_t[:, :], K.ps[2][0:E, S:2 * S]).then_inc(banks.free[2], 1)
            banks.ready(dve, start_at)
            link(v.tensor_copy(start[:, :], K.ps[3][0:E, 0:1]))
            v.tensor_copy(M.number[0:1, :], K.ps[3][0:1, 1:2]).then_inc(banks.free[3], 1)
            item = K.const("iota", ITEMS)[0:E, :]
            link(v.tensor_scalar(since[:, :], item, start[:, :], None, ALU.subtract))
            link(v.tensor_scalar(inside[:, :], since[:, :], 0.0, None, ALU.is_ge))
            link(v.scalar_tensor_tensor(inside[:, :], since[:, :], items[:, :], inside[:, :], ALU.is_lt, ALU.mult))
            banks.read(dve, turn_at)
            v.scalar_tensor_tensor(offset[:, :], since[:, :], -float(CAP), inside[:, :], ALU.mult, ALU.mult)\
                .then_inc(tables, 1)
            banks.ready(dve, b1_at)
            v.tensor_copy(M.b1[:, :], K.ps[1][:, :]).then_inc(banks.free[1], 1)
            banks.ready(dve, item_at)
            v.tensor_copy(M.rank[:, :, :], K.ps[0][:, 0:2 * ITEMS].rearrange("p (b j) -> p b j", b=TB))
            v.tensor_copy(M.gate[:, :, :], K.ps[0][:, 2 * ITEMS:4 * ITEMS].rearrange("p (b j) -> p b j", b=TB))
            v.tensor_copy(M.expert[0:1, :], K.ps[0][0:1, 4 * ITEMS:5 * ITEMS]).then_inc(banks.free[0], 1)
            for j, at in enumerate(b2_at):
                banks.ready(dve, at)
                v.tensor_copy(M.sum[:, 2 * j:2 * j + 2, :].rearrange("p t s -> p (t s)"), K.ps[4 + j][:, :])\
                    .then_inc(banks.free[4 + j], 1)


def experts(K, a):
    nc = K.nc
    rmsnorm(K, K.x[:, :, :], K.h, lambda t: K.gain2[:, t:t + 1], DT, shift=lambda t: K.shift2[:, t:t + 1])
    with ExitStack() as stack:
        def buffer(name, *shape, dt=F32):
            return stack.enter_context(nc.sbuf_tensor(name, list(shape), dt))

        M = ExpertMemory(
            tokens=buffer("h_by_token", P, TB, D), number=buffer("item_number", P, 1, dt=I32),
            rank=buffer("item_rank", P, TB, ITEMS), gate=buffer("item_gate", P, TB, ITEMS),
            expert=buffer("item_expert", P, ITEMS, dt=I32), b1=buffer("b1_columns", P, 2 * DT * EXPERTS),
            sum=buffer("expert_sum", P, DT, S))
        route(K, a, M)
        run_items(K, a, M)
        rmsnorm(K, M.sum[:, :, :], None, lambda t: K.gate2[:, t:t + 1], DT, add_to=K.x[:, :, :])


class ExpertMemory:

    def __init__(self, tokens, number, rank, gate, expert, b1, sum):
        self.tokens, self.number, self.rank, self.gate = tokens, number, rank, gate
        self.expert, self.b1, self.sum = expert, b1, sum


class ItemSignals:

    def __init__(self, nc):
        self.slots_selected = nc.alloc_semaphore("item_slots_selected")
        self.gathered = nc.alloc_semaphore("item_gathered")
        self.gathered_written = nc.alloc_semaphore("item_gathered_written")
        self.hidden_done = nc.alloc_semaphore("item_hidden_done")
        self.hidden_written = nc.alloc_semaphore("item_hidden_written")
        self.gated_turned = nc.alloc_semaphore("item_gated_turned")
        self.linear_turned = nc.alloc_semaphore("item_linear_turned")
        self.gated_biased = nc.alloc_semaphore("item_gated_biased")
        self.gated_ready = nc.alloc_semaphore("item_gated_ready")
        self.sigmoid_written = nc.alloc_semaphore("item_sigmoid_written")
        self.act_written = nc.alloc_semaphore("item_act_written")
        self.gate_rows_written = nc.alloc_semaphore("item_gate_rows_written")
        self.gates_turned = nc.alloc_semaphore("item_gates_turned")
        self.gates_written = nc.alloc_semaphore("item_gates_written")
        self.output_done = nc.alloc_semaphore("item_output_done")
        self.output_written = nc.alloc_semaphore("item_output_written")
        self.scattered = nc.alloc_semaphore("item_scattered")
        self.added = nc.alloc_semaphore("item_added")


def run_items(K, a, M):
    nc, ring, ps = K.nc, K.ring, K.ps
    w1 = a["w_mlp1_2"][0].rearrange("e (t p) n -> e p t n", p=P)
    w2 = a["w_mlp2_2"][0].rearrange("e (t p) n -> e p t n", p=P)
    sem = ItemSignals(nc)
    loaded = [nc.alloc_semaphore(f"expert_slot{s}_loaded") for s in range(SLOTS)]
    used = [nc.alloc_semaphore(f"expert_slot{s}_used") for s in range(SLOTS)]
    used[7], used[11] = sem.hidden_done, sem.output_done
    steps = Steps(nc, "item_vector_steps")
    with ExitStack() as stack:
        def buffer(name, *shape):
            return stack.enter_context(nc.sbuf_tensor(name, [P, *shape], F32))

        x, hid, act_t, y = buffer("item_x", DT, CAP), buffer("item_hidden", 2 * D), buffer("item_act", DT, CAP), buffer("item_y", D)
        sel, gated_sel, gates_t = buffer("item_select", TB, CAP), buffer("item_gated_select", TB, CAP), buffer("item_gates_t", S)
        glu, sig, lin = buffer("item_glu", DT, CAP), buffer("item_sigmoid", DT, CAP), buffer("item_linear", DT, CAP)
        block = stack.enter_context(nc.Block())

        def number_of(eng):
            return eng.value_load(M.number[0:1, 0:1], min_val=CHOSEN, max_val=ITEMS - 1)

        def expert_of(eng, i):
            return eng.value_load(M.expert[0:1, bass.ds(i, 1)], min_val=0, max_val=EXPERTS - 1)

        @block.sync
        def _(sp):
            n = number_of(sp)

            def load_first(i):
                e = expert_of(sp, i)
                for s in range(8):
                    if not isinstance(i, int):
                        sp.wait_ge(used[s], i)
                    sp.dma_start(ring.slot(s), w1[bass.ds(e, 1), :, s, :].rearrange("e p n -> p (e n)")).then_inc(loaded[s], 16)

            def load_second(i, wait=True):
                e = expert_of(sp, i)
                for s in range(8, 12):
                    if wait:
                        sp.wait_ge(used[s], i)
                    sp.dma_start(ring.slot(s).rearrange("p (t n) -> p t n", t=2),
                                 w2[bass.ds(e, 1), :, 2 * (s - 8):2 * (s - 8) + 2, :].rearrange("e p t n -> p (e t) n"))\
                        .then_inc(loaded[s], 16)

            load_first(0)
            load_second(0, wait=False)
            with sp.Fori(1, n) as i:
                load_first(i)
                load_second(i)

        @block.tensor
        def _(pe):
            def gather(i):
                pe.wait_ge(sem.slots_selected, i + 1)
                if not isinstance(i, int):
                    pe.wait_ge(sem.added, i * 4)
                for t in range(DT):
                    for b in range(TB):
                        m = nc.tensor.matmul(ps[4 + t // 4][:, t % 4 * CAP:(t % 4 + 1) * CAP],
                                             M.tokens[:, b, t * P:(t + 1) * P], sel[:, b, :], start=b == 0, stop=b == TB - 1)
                m.then_inc(sem.gathered, 1)

            def first_product(i):
                pe.wait_ge(sem.gathered_written, i + 1)
                for s in range(8):
                    pe.wait_ge(loaded[s], i * 16 + 16)
                    for c in range(4):
                        m = nc.tensor.matmul(ps[c][0:CAP, :], x[:, s, :], ring.slot(s)[:, c * 512:(c + 1) * 512],
                                             start=s == 0, stop=s == 7)
                    m.then_inc(used[s], 1)

            def turn_hidden(i):
                pairs = hid[0:CAP, :].rearrange("s (t p two) -> s two t p", two=2, p=P)
                pe.wait_ge(sem.hidden_written, i)
                for q in range(2):
                    for t in range(DT):
                        m = nc.tensor.transpose(ps[(6, 4)[q] + t // 4][:, t % 4 * CAP:(t % 4 + 1) * CAP], pairs[:, q, t, :],
                                                K.ident[0:CAP, 0:CAP])
                    m.then_inc((sem.gated_turned, sem.linear_turned)[q], 1)

            def finish_item(i):
                pe.wait_ge(sem.gated_biased, i)
                pe.wait_ge(sem.gate_rows_written, i)
                for b in range(TB):
                    m = nc.tensor.transpose(ps[6][0:CAP, b * P:(b + 1) * P], gated_sel[:, b, :], K.ident)
                m.then_inc(sem.gates_turned, 1)
                pe.wait_ge(sem.act_written, i)
                for s in range(8, 12):
                    pe.wait_ge(loaded[s], i * 16)
                    for kk in range(2):
                        for c in range(2):
                            k = 2 * (s - 8) + kk
                            m = nc.tensor.matmul(ps[4 + c][0:CAP, :], act_t[:, k, :],
                                                 ring.slot(s)[:, kk * D + c * 512:kk * D + (c + 1) * 512],
                                                 start=k == 0, stop=k == 7)
                    m.then_inc(used[s], 1)
                pe.wait_ge(sem.output_written, i)
                pe.wait_ge(sem.gates_written, i)
                for j, b in enumerate((4, 5, 7, 6)):
                    for half in range(2):
                        t = 2 * j + half
                        m = nc.tensor.matmul(ps[b][:, half * S:(half + 1) * S], y[0:CAP, t * P:(t + 1) * P], gates_t[0:CAP, :],
                                             start=True, stop=True)
                    m.then_inc(sem.scattered, 1)

            n = number_of(pe)
            pe.sem_inc(sem.scattered, 4)
            gather(0)
            first_product(0)
            with pe.Fori(1, n) as i:
                gather(i)
                pe.wait_ge(sem.gathered_written, i + 1)
                turn_hidden(i)
                first_product(i)
                finish_item(i)
            pe.wait_ge(sem.added, n * 4)
            turn_hidden(n)
            finish_item(n)

        @block.scalar
        def _(act):
            copy = ACT.Copy

            def write_gathered(i):
                act.wait_ge(sem.gathered, i + 1)
                for q in range(2):
                    m = nc.scalar.activation(x[:, 4 * q:4 * q + 4, :].rearrange("p t s -> p (t s)"), ps[4 + q][:, 0:4 * CAP], copy)
                m.then_inc(sem.gathered_written, 1)

            def write_hidden(i):
                act.wait_ge(sem.hidden_done, i + 1)
                for c in range(4):
                    m = nc.scalar.activation(hid[0:CAP, c * 512:(c + 1) * 512], ps[c][0:CAP, :], copy)
                m.then_inc(sem.hidden_written, 1)

            def sigmoid(i):
                act.wait_ge(sem.gated_ready, i)
                nc.scalar.activation(sig[:, :, :], glu[:, :, :], ACT.Sigmoid, scale=1.702).then_inc(sem.sigmoid_written, 1)

            def write_output(i):
                act.wait_ge(sem.gates_turned, i)
                nc.scalar.activation(gates_t[0:CAP, :], ps[6][0:CAP, 0:S], copy).then_inc(sem.gates_written, 1)
                act.wait_ge(sem.output_done, i)
                for c in range(2):
                    m = nc.scalar.activation(y[0:CAP, c * 512:(c + 1) * 512], ps[4 + c][0:CAP, :], copy)
                m.then_inc(sem.output_written, 1)

            n = number_of(act)
            write_gathered(0)
            write_hidden(0)
            with act.Fori(1, n) as i:
                write_gathered(i)
                sigmoid(i)
                write_hidden(i)
                write_output(i)
            sigmoid(n)
            write_output(n)

        @block.vector
        def _(dve):
            v = nc.vector
            steps.eng = dve
            link = steps.link

            def select(i, wait=True):
                if wait:
                    dve.wait_ge(sem.gathered, i)
                for b in range(TB):
                    m = v.tensor_scalar(sel[:, b, :], K.const("iota", CAP), M.rank[:, b, bass.ds(i, 1)], None, ALU.is_equal)
                m.then_inc(sem.slots_selected, 1)

            def finish_item(i, last=False):
                before = dve.snap(i - 1)
                bias_at = dve.value_load(M.expert[0:1, bass.ds(before, 1)], min_val=0, max_val=EXPERTS - 1)
                columns = M.b1[:, :].rearrange("p (q t e) -> p q t e", q=2, e=EXPERTS)

                def bias(q):
                    return columns[:, q, :, bass.ds(bias_at, 1)].broadcast_to([P, DT, CAP])

                dve.wait_ge(sem.gated_turned, i)
                for b in range(TB):
                    m = v.tensor_scalar(gated_sel[:, b, :], K.const("iota", CAP), M.rank[:, b, bass.ds(before, 1)],
                                        M.gate[:, b, bass.ds(before, 1)], ALU.is_equal, ALU.mult)
                m.then_inc(sem.gate_rows_written, 1)
                for q in range(2):
                    m = v.tensor_tensor(glu[:, 4 * q:4 * q + 4, :], ps[6 + q][:, 0:4 * CAP].rearrange("p (t s) -> p t s", t=4),
                                        bias(0)[:, 4 * q:4 * q + 4], ALU.add)
                m.then_inc(sem.gated_biased, 1)
                dve.wait_ge(sem.gated_biased, i)
                v.tensor_scalar(glu[:, :, :], glu[:, :, :], 7.0, None, ALU.min).then_inc(sem.gated_ready, 1)
                dve.wait_ge(sem.linear_turned, i)
                for q in range(2):
                    m = v.tensor_tensor(lin[:, 4 * q:4 * q + 4, :], ps[4 + q][:, 0:4 * CAP].rearrange("p (t s) -> p t s", t=4),
                                        bias(1)[:, 4 * q:4 * q + 4], ALU.add)
                link(m)
                link(v.tensor_scalar(lin[:, :, :], lin[:, :, :], -7.0, 7.0, ALU.max, ALU.min))
                link(v.scalar_tensor_tensor(lin[:, :, :], lin[:, :, :], 1.0, glu[:, :, :], ALU.add, ALU.mult))
                dve.wait_ge(sem.sigmoid_written, i)
                v.tensor_tensor(act_t[:, :, :], lin[:, :, :], sig[:, :, :], ALU.mult).then_inc(sem.act_written, 1)
                if not last:
                    select(i + 1)
                for j, b in enumerate((4, 5, 7, 6)):
                    dve.wait_ge(sem.scattered, i * 4 + (j + 1))
                    part = M.sum[:, 2 * j:2 * j + 2, :].rearrange("p t s -> p (t s)")
                    v.tensor_tensor(part, ps[b][:, :], part, ALU.add).then_inc(sem.added, 1)

            n = number_of(dve)
            dve.sem_inc(sem.added, 4)
            dve.sem_inc(steps.sem, 3)
            select(0, wait=False)
            select(1)
            with dve.Fori(1, n) as i:
                steps.loop(i, 3)
                finish_item(i)
                steps.end(1, 3)
            steps.n -= 3
            steps.loop(n, 3)
            finish_item(n, last=True)


class StickBreaking:

    def __init__(self, K, scale, buffer, keep):
        self.K, self.scale, self.fail_buffer, self.keep_buffer = K, scale, buffer, keep

    def begin(self, K, qb, heads, keys, w, at):
        self.qb, self.heads, self.keys, self.w, self.at = qb, heads, keys, w, at
        self.fail = self.fail_buffer[:, 0:heads * keys].rearrange("p (h k) -> p h k", h=heads)
        self.keep = self.keep_buffer[:, 0:heads * keys].rearrange("p (h k) -> p h k", h=heads)

    def pool(self, pool):
        K, nc = self.K, self.K.nc
        nc.gpsimd.memset(self.keep, 1.0).then_inc(K.pool_done.sem, 1)
        pool.wait_ge(*K.pool_done(1))
        nc.gpsimd.memset(self.keep[:, :, self.keys - 1:self.keys], 0.0).then_inc(K.pool_done.sem, 1)
        pool.wait_ge(*K.exps(2))
        nc.gpsimd.affine_select(out=self.w[:, :, :], in_=self.w[:, :, :], compare_op=ALU.is_gt, fill=0.0,
                                base=self.qb * P, pattern=[[0, self.heads], [-1, self.keys]], channel_multiplier=1)\
            .then_inc(K.weights.sem, 1)

    def act(self, act):
        K, nc = self.K, self.K.nc
        K.asteps.eng = act
        link = K.asteps.link
        act.wait_ge(*K.maxima(1))
        link(nc.scalar.activation(self.fail, self.w[:, :, :], ACT.Abs))
        link(nc.scalar.activation(self.fail, self.fail, ACT.Exp, scale=-1.0))
        nc.scalar.activation(self.fail, self.fail, ACT.Ln, bias=K.ones[:, 0:1]).then_inc(K.exps.sem, 1)
        act.wait_ge(*K.maxima(2))
        nc.scalar.activation(self.w[:, :, :], self.w[:, :, :], ACT.Exp).then_inc(K.exps.sem, 1)

    def dve(self, dve):
        K, v, w, keys, fail = self.K, self.K.nc.vector, self.w, self.keys, self.fail
        link = K.vsteps.link
        per_bank = 512 // keys
        for b, at in enumerate(self.at):
            K.banks.ready(dve, at)
            v.tensor_scalar(w[:, b * per_bank:(b + 1) * per_bank, :].rearrange("p h k -> p (h k)"), K.ps[at[0]][:, :],
                            self.scale, None, ALU.mult).then_inc(K.banks.free[at[0]], 1)
        K.banks.read(dve, self.at[-1])
        v.tensor_copy(K.sums[:, 0:1], K.ones[:, 0:1]).then_inc(K.maxima.sem, 1)
        dve.wait_ge(*K.exps(1))
        link(v.scalar_tensor_tensor(fail, w[:, :, :], 0.0, fail, ALU.max, ALU.add))
        earlier = K.const("earlier", P) if self.qb == 0 else K.earlier_rows
        link(v.scalar_tensor_tensor(fail, fail, -1.0, earlier.unsqueeze(1).broadcast_to([P, self.heads, keys]),
                                    ALU.mult, ALU.mult))
        dve.wait_ge(*K.pool_done(2))
        n = self.heads * keys
        total = self.total[:, 0:n]
        link(v.tensor_tensor_scan(total[:, ::-1], self.keep_buffer[:, 0:n][:, ::-1], self.fail_buffer[:, 0:n][:, ::-1],
                                  0.0, ALU.mult, ALU.add))
        v.tensor_tensor(w[:, :, :], w[:, :, :], total.rearrange("p (h k) -> p h k", h=self.heads), ALU.add)\
            .then_inc(K.maxima.sem, 1)

    def end(self):
        self.K.pool_done.done(2)
        self.K.maxima.done(2)
        self.K.exps.done(2)


def exact_exp(K, x, out, minus_one, s):
    v, link = K.nc.vector, K.vsteps.link
    k, r, power = s
    ln2_hi = 0.693359375
    ln2_lo = math.log(2.0) - ln2_hi
    link(v.tensor_scalar(r, x, -87.0, 88.0, ALU.max, ALU.min))
    link(v.tensor_scalar(k, r, 1.0 / math.log(2.0), ROUND, ALU.mult, ALU.add))
    link(v.tensor_scalar(k, k, ROUND, None, ALU.subtract))
    link(v.scalar_tensor_tensor(r, k, -ln2_hi, r, ALU.mult, ALU.add))
    link(v.scalar_tensor_tensor(r, k, -ln2_lo, r, ALU.mult, ALU.add))
    link(v.tensor_scalar(power, k, 127.0, 2.0 ** 23, ALU.add, ALU.mult))
    link(v.tensor_scalar(k, r, 1.0 / math.factorial(8), None, ALU.mult))
    for n in range(7, 0, -1):
        link(v.scalar_tensor_tensor(k, k, 1.0 / math.factorial(n), r, ALU.add, ALU.mult))
    scale = power.bitcast(F32)
    if out is not None:
        link(v.scalar_tensor_tensor(out, k, 1.0, scale, ALU.add, ALU.mult))
    if minus_one is not None:
        link(v.tensor_tensor(k, k, scale, ALU.mult))
        link(v.scalar_tensor_tensor(minus_one, scale, -1.0, k, ALU.add, ALU.add))


class S5Operands:

    def __init__(self, b, c, phase, decay):
        self.b, self.c, self.phase, self.decay = b, c, phase, decay


def s5_matrices(K, a, T):
    nc, banks = K.nc, K.banks
    J, Q = 16, 4
    in_sem = {n: nc.alloc_semaphore("s5_" + n + "_loaded") for n in ("dt", "b_re", "b_im", "c_re", "c_im")}
    dt_ready, angles, sines, zeroed, natural = (nc.alloc_semaphore("s5_" + n) for n in (
        "dt_rows", "angles_reduced", "sines_written", "zeroed", "natural_ready"))
    dt_at = banks.take(0)
    b_at, c_at = [banks.take(1), banks.take(2)], [banks.take(3), banks.take(4)]
    with ExitStack() as stack:
        def buffer(name, *shape, dt=F32):
            return stack.enter_context(nc.sbuf_tensor(name, list(shape), dt))

        dt_pair, dt_rows = buffer("dt_pairs", J, 2), buffer("dt_rows", J, 2, 64)
        small = {n: buffer("s5_" + n, P, J) for n in (
            "dt", "a", "k", "r", "em1", "sin", "half", "cos", "cosm1", "lre", "lim", "fre", "fim", "inv", "t")}
        power = buffer("s5_power", P, J, dt=I32)
        b_in = [buffer(f"s5_b_in{i}", P, J, 16) for i in range(2)]
        b_tmp = [buffer(f"s5_b_tmp{i}", P, J, 16) for i in range(2)]
        b_nat = [buffer(f"s5_b_natural{i}", P, Q, 4, 2, 16) for i in range(2)]
        c_in = [buffer(f"s5_c_in{i}", P, Q, 2, 64) for i in range(2)]
        block = stack.enter_context(nc.Block())

        @block.sync
        def _(sp):
            sp.dma_start(dt_pair[:, :], a["ssm_log_dt_3"][0].rearrange("(j g) -> j g", g=2)).then_inc(in_sem["dt"], 16)
            for i, n in enumerate(("b_re", "b_im")):
                for g in range(2):
                    sp.dma_start(b_in[i][64 * g:64 * g + 64, :, :], a[f"ssm_{n}_3"][0].rearrange("(j g) n c -> g n j c", g=2)[g])\
                        .then_inc(in_sem[n], 16)
                    sp.wait_ge(in_sem[n], 16 * (g + 1))
            for i, n in enumerate(("c_re", "c_im")):
                for g in range(2):
                    sp.dma_start(c_in[i][:, :, g, :], a[f"ssm_{n}_3"][0].rearrange("(q g) c n -> (g c) q n", q=Q))\
                        .then_inc(in_sem[n], 16)
                    sp.wait_ge(in_sem[n], 16 * (g + 1))

        @block.gpsimd
        def _(pool):
            for i in range(2):
                nc.gpsimd.memset(b_nat[i][:, :, :, :, :], 0.0)
                m = nc.gpsimd.memset(T.c[i][:, :, :, :, :], 0.0)
            m.then_inc(zeroed, 1)

        @block.tensor
        def _(pe):
            pe.wait_ge(dt_ready, 1)
            banks.vacant(pe, dt_at)
            nc.tensor.transpose(K.ps[0][:, 0:J], dt_rows[:, :, :].rearrange("j g n -> j (g n)"), K.ident[0:J, 0:J])\
                .then_inc(banks.full[0], 1)
            for i, n in enumerate(("c_re", "c_im")):
                pe.wait_ge(in_sem[n], 32)
                banks.vacant(pe, c_at[i])
                for q in range(Q):
                    m = nc.tensor.transpose(K.ps[3 + i][:, q * P:(q + 1) * P], c_in[i][:, q, :, :].rearrange("p g n -> p (g n)"),
                                            K.ident)
                m.then_inc(banks.full[3 + i], 1)
            pe.wait_ge(natural, 1)
            for i in range(2):
                banks.vacant(pe, b_at[i])
                for q in range(Q):
                    m = nc.tensor.transpose(K.ps[1 + i][:, q * P:(q + 1) * P],
                                            b_nat[i][:, q, :, :, :].rearrange("p j g c -> p (j g c)"), K.ident)
                m.then_inc(banks.full[1 + i], 1)

        @block.scalar
        def _(act):
            act.wait_ge(angles, 1)
            nc.scalar.activation(small["half"][:, :], T.phase[:, :], ACT.Sin, scale=0.5)
            nc.scalar.activation(small["sin"][:, :], T.phase[:, :], ACT.Sin).then_inc(sines, 1)

        @block.vector
        def _(dve):
            K.vsteps.eng = dve
            link, v = K.vsteps.link, nc.vector
            a_re, a_im = K.param("ssm_a_re", 0, J), K.param("ssm_a_im", 0, J)
            t = {n: b[:, :] for n, b in small.items()}
            scratch = (t["k"], t["r"], power[:, :])
            dve.wait_ge(in_sem["dt"], 16)
            v.tensor_copy(dt_rows[:, :, :], dt_pair[:, :].unsqueeze(2).broadcast_to([J, 2, 64])).then_inc(dt_ready, 1)
            banks.ready(dve, dt_at)
            v.tensor_copy(t["dt"], K.ps[0][:, 0:J]).then_inc(banks.free[0], 1)
            banks.read(dve, dt_at)
            exact_exp(K, t["dt"], t["dt"], None, scratch)
            link(v.tensor_tensor(T.phase[:, :], a_im, t["dt"], ALU.mult))
            link(v.tensor_tensor(t["a"], a_re, t["dt"], ALU.mult))
            reduce_angle(K, dve, T.phase[:, :], t["k"]).then_inc(angles, 1)
            dve.wait_ge(angles, 1)
            exact_exp(K, t["a"], T.decay[:, :], t["em1"], scratch)
            dve.wait_ge(sines, 1)
            link(v.scalar_tensor_tensor(t["cosm1"], t["half"], -2.0, t["half"], ALU.mult, ALU.mult))
            link(v.scalar_tensor_tensor(t["lre"], t["cosm1"], 1.0, t["em1"], ALU.add, ALU.mult))
            link(v.tensor_tensor(t["lre"], t["lre"], t["cosm1"], ALU.add))
            link(v.tensor_tensor(t["lim"], T.decay[:, :], t["sin"], ALU.mult))
            link(v.tensor_tensor(t["inv"], a_re, a_re, ALU.mult))
            link(v.tensor_tensor(t["t"], a_im, a_im, ALU.mult))
            link(v.tensor_tensor(t["inv"], t["inv"], t["t"], ALU.add))
            link(v.reciprocal(t["inv"], t["inv"]))
            for out, p, q, op in (("fre", "lre", "lim", ALU.add), ("fim", "lim", "lre", ALU.subtract)):
                link(v.tensor_tensor(t[out], t[p], a_re, ALU.mult))
                link(v.tensor_tensor(t["t"], t[q], a_im, ALU.mult))
                link(v.tensor_tensor(t[out], t[out], t["t"], op))
                link(v.tensor_tensor(t[out], t[out], t["inv"], ALU.mult))
            for n in ("b_re", "b_im"):
                dve.wait_ge(in_sem[n], 32)
            fre, fim = (t[n].unsqueeze(2).broadcast_to([P, J, 16]) for n in ("fre", "fim"))
            re, im = b_in[0][:, :, :], b_in[1][:, :, :]
            dve.wait_ge(zeroed, 1)
            for i, (p, q, op) in enumerate(((re, im, ALU.subtract), (im, re, ALU.add))):
                link(v.tensor_tensor(b_tmp[0][:, :, :], p, fre, ALU.mult))
                link(v.tensor_tensor(b_tmp[1][:, :, :], q, fim, ALU.mult))
                for g in range(2):
                    rows = slice(64 * g, 64 * g + 64)
                    m = v.tensor_tensor(b_nat[i][rows, :, :, g, :].rearrange("p q j c -> p (q j) c"),
                                        b_tmp[0][rows, :, :], b_tmp[1][rows, :, :], op)
                link(m)
            v.tensor_copy(t["t"], t["inv"]).then_inc(natural, 1)
            for i in range(2):
                banks.ready(dve, c_at[i])
                for g in range(2):
                    rows = slice(64 * g, 64 * g + 64)
                    m = v.tensor_scalar(T.c[i][rows, :, :, g, :], K.ps[3 + i][rows, :].rearrange(
                        "p (q j g c) -> p g q j c", q=Q, j=4, g=2)[:, g], (1.0, -1.0)[i], None, ALU.mult)
                m.then_inc(banks.free[3 + i], 1)
            for i in range(2):
                banks.ready(dve, b_at[i])
                v.tensor_copy(T.b[i][:, :, :].rearrange("p q m -> p (q m)"), K.ps[1 + i][:, :]).then_inc(banks.free[1 + i], 1)


def s5_scan(K, T, u, y):
    nc, banks = K.nc, K.banks
    J, Q = 16, 4
    angles, absolute, tables = (nc.alloc_semaphore("s5_" + n) for n in ("table_angles", "table_abs", "tables_written"))
    bu_written, x_im_written, w_written, s_re_written, s_im_written = (nc.alloc_semaphore("s5_" + n) for n in (
        "bu_written", "x_im_written", "w_written", "s_re_written", "s_im_written"))
    keep_written, y_sum, decays = (nc.alloc_semaphore("s5_" + n) for n in ("pool_part", "y_sums", "decay_rows"))
    bu_at = [[banks.take(b) for b in range(4)] for _ in range(Q)]
    y_at = [banks.take(4 + q) for q in range(Q)]
    memory = K.ring.memory
    cos, sin, work = (memory[:, n * J * S:(n + 1) * J * S].rearrange("p (j t) -> p j t", j=J) for n in range(3))
    rest = memory[:, 3 * J * S:]

    def part(n):
        return rest[:, n * 4 * S:(n + 1) * 4 * S].rearrange("p (j t) -> p j t", j=4)

    bre, bim, xre, xim, wre, wim, decay, t_dve, t_pool = (part(n) for n in range(9))
    sre, sim = xre, xim
    with nc.Block() as block:

        def outputs(pe, q):
            pe.wait_ge(s_re_written, q + 1)
            pe.wait_ge(s_im_written, q + 1)
            banks.vacant(pe, y_at[q])
            for j in range(4):
                for i, s in enumerate((sre, sim)):
                    m = nc.tensor.matmul(K.ps[4 + q][32 * j:32 * j + 32, 0:S], T.c[i][:, q, j, :, :].rearrange("p g c -> p (g c)"),
                                         s[:, j, :], start=i == 0, stop=i == 1)
            m.then_inc(banks.full[4 + q], 1)

        @block.tensor
        def _(pe):
            for q in range(Q):
                for j in range(4):
                    banks.vacant(pe, bu_at[q][j])
                    rows = slice(32 * j, 32 * j + 32)
                    for i in range(2):
                        m = nc.tensor.matmul(K.ps[j][:, i * S:(i + 1) * S], T.b[i][rows, q, :], u[rows, q, :],
                                             start=True, stop=True)
                    m.then_inc(banks.full[j], 1)
                if q:
                    outputs(pe, q - 1)
            outputs(pe, Q - 1)

        @block.scalar
        def _(act):
            act.wait_ge(angles, 1)
            nc.scalar.activation(cos, sin, ACT.Abs).then_inc(absolute, 1)
            act.wait_ge(absolute, 1)
            nc.scalar.activation(cos, cos, ACT.Sin, bias=K.col("half_pi"), scale=-1.0)
            nc.scalar.activation(sin, sin, ACT.Sin).then_inc(tables, 1)
            for q in range(Q):
                if q:
                    act.wait_ge(w_written, q)
                for j in range(4):
                    banks.ready(act, bu_at[q][j])
                    nc.scalar.activation(bre[:, j, :], K.ps[j][:, 0:S], ACT.Copy)
                    nc.scalar.activation(bim[:, j, :], K.ps[j][:, S:2 * S], ACT.Copy).then_inc(banks.free[j], 1)
            act.wait_ge(y_sum, 1)
            nc.scalar.activation(y[:, :, :], y[:, :, :], ACT.Gelu_apprx_tanh)

        def ready_inputs(eng, q):
            for j in range(4):
                banks.read(eng, bu_at[q][j])

        @block.vector
        def _(dve):
            K.vsteps.eng = dve
            link, v = K.vsteps.link, nc.vector
            link(v.tensor_tensor(sin, K.const("times", S).unsqueeze(1).broadcast_to([P, J, S]),
                                 T.phase[:, :].unsqueeze(2).broadcast_to([P, J, S]), ALU.mult))
            reduce_angle(K, dve, sin, work).then_inc(angles, 1)
            dve.wait_ge(tables, 1)
            for q in range(Q):
                c, s = cos[:, 4 * q:4 * q + 4, :], sin[:, 4 * q:4 * q + 4, :]
                ready_inputs(dve, q)
                if q:
                    dve.wait_ge(banks.full[4 + q - 1], y_at[q - 1][2] + 1)
                link(v.tensor_tensor(t_dve, bim, s, ALU.mult))
                link(v.tensor_tensor(xre, bre, c, ALU.mult))
                link(v.tensor_tensor(xre, xre, t_dve, ALU.add))
                link(v.tensor_copy(decay, T.decay[:, 4 * q:4 * q + 4].unsqueeze(2).broadcast_to([P, 4, S])))
                link(v.memset(decay[:, :, 0:1], 0.0))
                if q:
                    dve.wait_ge(s_im_written, q)
                flat = [x.rearrange("p j t -> p (j t)") for x in (decay, xre, xim, wre, wim)]
                v.tensor_tensor_scan(flat[3], flat[0], flat[1], 0.0, ALU.mult, ALU.add)
                dve.wait_ge(x_im_written, q + 1)
                v.tensor_tensor_scan(flat[4], flat[0], flat[2], 0.0, ALU.mult, ALU.add).then_inc(w_written, 1)
                dve.wait_ge(w_written, q + 1)
                link(v.tensor_tensor(t_dve, wim, s, ALU.mult))
                link(v.tensor_tensor(sre, wre, c, ALU.mult))
                v.tensor_tensor(sre, sre, t_dve, ALU.subtract).then_inc(s_re_written, 1)
            for q in range(Q):
                banks.ready(dve, y_at[q])
                v.scalar_tensor_tensor(y[:, q, :], u[:, q, :], K.param("ssm_d", q), K.ps[4 + q][:, 0:S], ALU.mult, ALU.add)\
                    .then_inc(banks.free[4 + q], 1)
            banks.read(dve, y_at[-1])
            v.tensor_copy(K.sums[:, 0:1], K.ones[:, 0:1]).then_inc(y_sum, 1)

        @block.gpsimd
        def _(pool):
            g = nc.gpsimd
            done = [0]

            def link(m):
                done[0] += 1
                m.then_inc(keep_written, 1)
                pool.wait_ge(keep_written, done[0])
            pool.wait_ge(tables, 1)
            for q in range(Q):
                c, s = cos[:, 4 * q:4 * q + 4, :], sin[:, 4 * q:4 * q + 4, :]
                ready_inputs(pool, q)
                if q:
                    pool.wait_ge(banks.full[4 + q - 1], y_at[q - 1][2] + 1)
                link(g.tensor_tensor(t_pool, bre, s, ALU.mult))
                link(g.tensor_tensor(xim, bim, c, ALU.mult))
                g.tensor_tensor(xim, xim, t_pool, ALU.subtract).then_inc(x_im_written, 1)
                pool.wait_ge(w_written, q + 1)
                link(g.tensor_tensor(t_pool, wre, s, ALU.mult))
                link(g.tensor_tensor(sim, wim, c, ALU.mult))
                g.tensor_tensor(sim, sim, t_pool, ALU.add).then_inc(s_im_written, 1)


def s5_gate(K, a, y):
    nc, banks = K.nc, K.banks
    loaded = nc.alloc_semaphore("s5_glu_loaded")
    at = [banks.take(b) for b in range(2)]
    with nc.sbuf_tensor([P, 4, 512], F32) as w, nc.sbuf_tensor([P, 4, S], F32) as gate, nc.Block() as block:

        @block.sync
        def _(sp):
            sp.dma_start(w[:, :, :], a["ssm_w_glu_3"][0].rearrange("(t p) n -> p t n", p=P)).then_inc(loaded, 16)

        @block.tensor
        def _(pe):
            pe.wait_ge(loaded, 16)
            for b in range(2):
                banks.vacant(pe, at[b])
                for i in range(2):
                    t = 2 * b + i
                    for k in range(4):
                        m = nc.tensor.matmul(K.ps[b][:, i * S:(i + 1) * S], w[:, k, t * P:(t + 1) * P], y[:, k, :],
                                             start=k == 0, stop=k == 3)
                m.then_inc(banks.full[b], 1)

        @block.scalar
        def _(act):
            for b in range(2):
                banks.ready(act, at[b])
                for i in range(2):
                    m = nc.scalar.activation(gate[:, 2 * b + i, :], K.ps[b][:, i * S:(i + 1) * S], ACT.Sigmoid,
                                             bias=K.param("ssm_b_glu", 2 * b + i))
                m.then_inc(banks.free[b], 1)

        @block.vector
        def _(dve):
            banks.read(dve, at[0])
            banks.read(dve, at[1])
            nc.vector.tensor_tensor(y[:, :, :], y[:, :, :], gate[:, :, :], ALU.mult)


def two_branches(K, a):
    nc = K.nc
    rmsnorm(K, K.x[:, :, :], K.h, lambda t: K.param("norm_mix_pre", t), DT)
    w_in = a["w_in_3"][0]
    heads = 8
    with ExitStack() as stack:
        def buffer(name, *shape):
            return stack.enter_context(nc.sbuf_tensor(name, [P, *shape], F32))

        gates, u = buffer("branch_gates", 2 * DT, S), buffer("s5_u", 4, S)
        o = buffer("attention_out", 4, S)
        qkv = ExitStack()
        q, k, v = (qkv.enter_context(nc.sbuf_tensor(n, [P, *shape], F32)) for n, shape in (
            ("stick_q", (4, S)), ("stick_k", (4, S)), ("stick_v", (TB, 512))))
        jobs = []

        def copy_to(dst, j):
            return lambda ps: nc.scalar.activation(dst[:, 2 * j:2 * j + 2, :].rearrange("p t s -> p (t s)"), ps[:, :], ACT.Copy)

        def gate(j):
            def finish(ps):
                for i in range(2):
                    m = nc.scalar.activation(gates[:, 2 * j + i, :], ps[:, i * S:(i + 1) * S], ACT.Sigmoid,
                                             bias=K.param("b_gate", 2 * j + i))
                return m
            return finish

        for j in range(16):
            w = w_in[:, j * 256:(j + 1) * 256]
            if j in (4, 5):
                jobs.append((w, True, "act", lambda ps, j=j: nc.scalar.activation(
                    v[:, :, (j - 4) * 256:(j - 3) * 256], ps[:, :].rearrange("p (b n) -> p b n", b=TB), ACT.Copy)))
            else:
                jobs.append((w, False, "act", copy_to((q, k, None, u)[j // 2], j % 2) if j < 8 else gate(j - 8)))
        dense_up(K, K.h, DT, jobs)
        with nc.sbuf_tensor([P, heads * S], F32) as fail, nc.sbuf_tensor([P, heads * S], F32) as keep, \
                nc.sbuf_tensor([P, heads * S], F32) as total:
            stick = StickBreaking(K, 64 ** -0.5, fail, keep)
            stick.total = total
            for qb in range(TB):
                keys = (qb + 1) * P
                tokens = slice(qb * P, (qb + 1) * P)

                def rows(h):
                    return slice(64 * (h % 2), 64 * (h % 2) + 64)
                attention(K, qb, heads, keys, lambda h: [(q[rows(h), h // 2, tokens], k[rows(h), h // 2, 0:keys])],
                          stick, lambda h, kb, half: v[:, kb, h * 64:(h + 1) * 64], 1,
                          lambda ps: [(o[:, :, tokens], ps[0][:, :].rearrange("p (t q) -> p t q", t=4))],
                          order=(0, 2, 4, 6, 1, 3, 5, 7))
        qkv.close()
        y, T = buffer("s5_y", 4, S), S5Operands(
            b=[buffer(f"s5_b{i}", 4, P) for i in range(2)], c=[buffer(f"s5_c{i}", 4, 4, 2, 16) for i in range(2)],
            phase=buffer("s5_phase", 16), decay=buffer("s5_decay", 16))
        s5_matrices(K, a, T)
        s5_scan(K, T, u, y)
        s5_gate(K, a, y)

        def gated(which, add):
            def finish(dve, j, ps):
                part = gates[:, which * DT + 2 * j:which * DT + 2 * j + 2, :].rearrange("p t s -> p (t s)")
                out = K.h[:, 2 * j:2 * j + 2, :].rearrange("p t s -> p (t s)")
                if not add:
                    return nc.vector.tensor_tensor(out, ps[:, :], part, ALU.mult)
                K.vsteps.link(nc.vector.tensor_tensor(part, ps[:, :], part, ALU.mult))
                return nc.vector.tensor_tensor(out, out, part, ALU.add)
            return finish

        dense_down(K, o, a["w_branch_attn_3"][0], 4, gated(0, False))
        dense_down(K, y, a["w_branch_ssm_3"][0], 4, gated(1, True))
    with nc.sbuf_tensor([P, DT, S], F32) as mixed:
        dense_down(K, K.h, a["w_out_3"][0], DT, store_to(K, mixed))
        rmsnorm(K, mixed[:, :, :], None, lambda t: K.param("norm_mix_post", t), DT, add_to=K.x[:, :, :])


def load_feature_major(K, rows, dst):
    nc, banks = K.nc, K.banks
    loaded = nc.alloc_semaphore("rows_loaded")
    at = [banks.take(4 + j) for j in range(4)]
    with nc.sbuf_tensor([P, TB, D], F32) as tokens, nc.Block() as block:

        @block.sync
        def _(sp):
            sp.dma_start(tokens[:, :, :], rows.rearrange("(b p) d -> p b d", p=P)).then_inc(loaded, 16)

        @block.tensor
        def _(pe):
            pe.wait_ge(loaded, 16)
            transpose_tokens(K, pe, tokens, at)

        @block.scalar
        def _(act):
            for j in range(4):
                banks.ready(act, at[j])
                nc.scalar.activation(dst[:, 2 * j:2 * j + 2, :].rearrange("p t s -> p (t s)"), K.ps[4 + j][:, :],
                                     ACT.Copy).then_inc(banks.free[4 + j], 1)


def cross_attention(K, a):
    nc = K.nc
    heads = 4
    with ExitStack() as stack:
        def buffer(name, *shape):
            return stack.enter_context(nc.sbuf_tensor(name, [P, *shape], F32))

        q, k, v = buffer("cross_q", DT, S), buffer("cross_k", DT, S), buffer("cross_v", TB, D)
        mem = buffer("memory", DT, S)
        load_feature_major(K, a["mem_3"][0], mem)
        rmsnorm(K, mem[:, :, :], mem, lambda t: K.param("norm_mem", t), DT)
        dense_down(K, mem, a["xa_wk_3"][0], DT, store_to(K, k))
        w_v = a["xa_wv_3"][0]
        dense_up(K, mem, DT, [(w_v[:, j * 256:(j + 1) * 256], True, "act", lambda ps, j=j: nc.scalar.activation(
            v[:, :, j * 256:(j + 1) * 256], ps[:, :].rearrange("p (b n) -> p b n", b=TB), ACT.Copy)) for j in range(4)])
        rmsnorm(K, K.x[:, :, :], K.h, lambda t: K.param("norm_xa_pre", t), DT)
        dense_down(K, K.h, a["xa_wq_3"][0], DT, store_to(K, q))
        for qb in range(TB):
            tokens = slice(qb * P, (qb + 1) * P)
            attention(K, qb, heads, S, lambda h: [(q[:, 2 * h + i, tokens], k[:, 2 * h + i, :]) for i in range(2)],
                      Softmax(256 ** -0.5), lambda h, kb, half: v[:, kb, h * 256 + half * P:h * 256 + (half + 1) * P], 2,
                      lambda ps: [(K.h[:, 4 * i:4 * i + 4, tokens], ps[i][:, :].rearrange("p (t q) -> p t q", t=4))
                                  for i in range(2)])
        dense_down(K, K.h, a["xa_wo_3"][0], DT, store_to(K, q))
        rmsnorm(K, q[:, :, :], None, lambda t: K.param("norm_xa_post", t), DT, add_to=K.x[:, :, :])


def transformer_blocks(nc, a, const, const_at, out):
    K = Kit(nc, const_at, const.shape[1])
    setup(K, a, const)
    for layer in range(2):
        swiglu(K, a["ffn_w_in"][layer, 0], a["ffn_w_out"][layer, 0], 2 * layer * DT)
        (spatial_gate, pool_mixer)[layer](K, a)
        swiglu(K, a["ffn_w_in"][layer, 1], a["ffn_w_out"][layer, 1], (2 * layer + 1) * DT)
    rmsnorm(K, K.x[:, :, :], K.x, lambda t: K.param("final_norm", t), DT)
    adaptive_columns(K, a)
    mixed_attention(K, a)
    experts(K, a)
    two_branches(K, a)
    cross_attention(K, a)
    conv_feed_forward(K, a)
    store_output(K, out)


def kernel(**inputs):
    import concourse.bacc as bacc
    from concourse.bass_utils import run_bass_kernel_spmd

    nc = bacc.Bacc("TRN2", target_bir_lowering=False, num_devices=1)
    table, const_at = constant_table()
    arrays, aps = {}, {}
    for name, value in [*inputs.items(), ("constant_table", table)]:
        arrays[f"in_{name}"] = value = np.ascontiguousarray(value)
        aps[name] = nc.dram_tensor(f"in_{name}", value.shape, mybir.dt.from_np(value.dtype), kind="ExternalInput").ap()
    out = nc.dram_tensor("out", (1, S, D), F32, kind="ExternalOutput").ap()
    transformer_blocks(nc, aps, aps["constant_table"], const_at, out)
    return run_bass_kernel_spmd(nc, [arrays], core_ids=[0]).results[0]["out"]
```

```python
import math
from contextlib import ExitStack

import numpy as np

import concourse.bass as bass
from concourse import mybir

F32 = mybir.dt.float32
F32R = mybir.dt.float32r
I32 = mybir.dt.int32
U32 = mybir.dt.uint32
ALU = mybir.AluOpType
ACT = mybir.ActivationFunctionType
AX = mybir.AxisListType

P = 128
S = 256
D = 1024
DT = D // P
TB = S // P
FF = 2816
SLOT = 2048
SLOTS = 8
HIGHS = 4
EXPERT_SLOTS = SLOTS + HIGHS
EPS = 1e-6
NEG = -1e30
TWO_PI = 2 * math.pi
ROUND = 1.5 * 2.0 ** 23


class Signal:

    def __init__(self, nc, name, primed=0):
        self.sem, self.base = nc.alloc_semaphore(name), primed

    def __call__(self, n):
        return self.sem, self.base + n

    def done(self, n):
        self.base += n


class Steps:

    def __init__(self, nc, name, primed=0):
        self.sem, self.n, self.shift, self.eng = nc.alloc_semaphore(name), primed, 0, None

    def link(self, instruction):
        self.n += 1
        instruction.then_inc(self.sem, 1)
        self.eng.wait_ge(self.sem, self.n + self.shift)

    def loop(self, i, per):
        self.shift, self.at = i * per, self.n

    def end(self, trips, per):
        assert self.n - self.at == per, (self.n - self.at, per)
        self.shift, self.n = 0, self.n + (trips - 1) * per


def parts_view(nc, name, shape):
    size = 4
    for n in shape[1:]:
        size *= n
    return nc.alloc_sbuf_tensor_at(name, shape, F32R, offset=nc.sbuf_base - size)


class Ring:

    def __init__(self, nc, memory, parts):
        self.memory, self.parts = memory, parts
        self.loaded = [nc.alloc_semaphore(f"slot{i}_loaded") for i in range(SLOTS)]
        self.used = [nc.alloc_semaphore(f"slot{i}_used") for i in range(SLOTS)]
        self.fills = [0] * SLOTS
        self.uses = [0] * SLOTS
        self.last = [None] * SLOTS
        self.next = 0

    def slot(self, s):
        return self.memory[:, s * SLOT:(s + 1) * SLOT]

    def part(self, s):
        return self.parts[:, s * SLOT:(s + 1) * SLOT]

    def take(self, trips=1):
        s = self.next
        self.next = (s + 1) % SLOTS
        fill = self.fills[s]
        self.fills[s] += trips
        return s, fill, self.last[s]

    def freed_by_use(self, s, trips=1):
        n = self.uses[s]
        self.uses[s] += trips
        self.last[s] = (self.used[s], n + trips)
        return n

    def freed_by(self, s, semaphore, value):
        self.last[s] = (semaphore, value)

    def vacant(self, eng, unit):
        if unit[2] is not None:
            eng.wait_ge(*unit[2])

    def arrived(self, eng, unit):
        eng.wait_ge(self.loaded[unit[0]], unit[1] * 16 + 16)


class Banks:

    def __init__(self, nc):
        self.ps = [nc.alloc_psum_tensor(f"bank{i}", [P, 512], F32) for i in range(8)]
        self.full = [nc.alloc_semaphore(f"bank{i}_full") for i in range(8)]
        self.free = [nc.alloc_semaphore(f"bank{i}_free") for i in range(8)]
        self.fulls = [0] * 8
        self.frees = [0] * 8

    def take(self, b, trips=1, signals=True):
        at = b, self.frees[b], self.fulls[b]
        self.frees[b] += trips
        if signals:
            self.fulls[b] += trips
        return at

    def vacant(self, eng, at):
        eng.wait_ge(self.free[at[0]], at[1] + 1)

    def ready(self, eng, at):
        eng.wait_ge(self.full[at[0]], at[2] + 1)

    def read(self, eng, at):
        eng.wait_ge(self.free[at[0]], at[1] + 2)


class Kit:

    def __init__(self, nc, const_at, const_width):
        self.nc = nc
        self.const_at = const_at
        self.consts = nc.alloc_sbuf_tensor("consts", [P, const_width], F32)
        shape = [P, EXPERT_SLOTS * SLOT]
        self.ring = Ring(nc, nc.alloc_sbuf_tensor("weight_slots", shape, F32), parts_view(nc, "weight_parts", shape))
        self.h_high = nc.alloc_sbuf_tensor("h_high", [P, DT, S], F32R)
        self.high_written, self.low_written = Signal(nc, "high_parts_written"), Signal(nc, "low_parts_written")
        self.banks = Banks(nc)
        self.ps = self.banks.ps
        self.x = nc.alloc_sbuf_tensor("x_residual", [P, DT, S], F32)
        self.h = nc.alloc_sbuf_tensor("h_normed", [P, DT, S], F32)
        self.h_low = parts_view(nc, "h_low", [P, DT, S])
        self.ident = self.const("ident", P)
        self.ones = self.const("ones", P)
        self.causal_rows = self.const("seen", 2 * P)
        self.earlier_rows = self.const("all_earlier", 2 * P)
        self.negmax = nc.alloc_sbuf_tensor("negative_maxima", [P, 8], F32)
        self.sums = nc.alloc_sbuf_tensor("exponential_sums", [P, 8], F32)
        self.squares = Signal(nc, "squares_written")
        self.hidden, self.gelus = Signal(nc, "hidden_written"), Signal(nc, "gelu_written")
        self.weights = Signal(nc, "attention_weights_written")
        self.maxima = Signal(nc, "maxima_written")
        self.exps = Signal(nc, "exponentials_written")
        self.pool_done = Signal(nc, "pool_steps")
        self.scaled = Signal(nc, "operand_scaled")
        self.vsteps = Steps(nc, "vector_steps")
        self.asteps = Steps(nc, "scalar_steps")

    def const(self, name, width):
        return self.consts[:, self.const_at[name]:self.const_at[name] + width]

    def col(self, name):
        return self.const(name, 1)

    def param(self, name, t=0, n=1):
        at = self.param_at[name] + t
        return self.params[:, bass.ds(at, n)]


def constant_table():
    at, parts = {}, []

    def add(name, a):
        at[name] = sum(p.shape[1] for p in parts)
        parts.append(np.broadcast_to(np.asarray(a, np.float32), (P, np.shape(a)[-1])))

    i = np.arange(P)
    add("ident", np.eye(P))
    add("stacked", np.concatenate([np.eye(P // 2)] * 2))
    add("before", i[:, None] < i[None, :])
    add("upto", i[:, None] <= i[None, :])
    add("iota", i[None, :])
    add("seen", np.zeros((1, P)))
    add("causal", np.where(i[None, :] <= i[:, None], 0.0, NEG))
    add("all_earlier", np.ones((1, P)))
    add("earlier", i[None, :] < i[:, None])
    t = np.arange(1, S + 1)
    for w in (2, 4, 8, 16):
        add(f"per{w}", (1.0 / np.minimum(t, w))[None, :])
    freq = 10000.0 ** (-np.arange(16, dtype=np.float32) / 16)
    add("freq", np.concatenate([np.zeros(64), freq, freq])[None, :])
    add("times", np.arange(S)[None, :])
    add("sign", np.where(i < 80, -1.0, 1.0)[:, None])
    add("ones", np.ones((1, P)))
    add("index", i[:, None])
    add("half_pi", np.full((1, 1), math.pi / 2))
    add("eps", np.full((1, 1), EPS))
    return np.ascontiguousarray(np.concatenate(parts, 1)), at


def parameter_rows(a):
    rows = []

    def add(name, ap, pattern="(r p) -> r p"):
        rows.append((name, ap.rearrange(pattern, p=P)))

    add("ffn_norm", a["ffn_norm"], "a b (r p) -> (a b r) p")
    add("mix_norm", a["mix_norm"], "a (r p) -> (a r) p")
    add("a_v_norm", a["a_v_norm"][0])
    add("b_scale", a["b_scale"][0])
    add("final_norm", a["final_norm"])
    add("c", a["c_2"][0])
    add("b_ada", a["b_ada_2"][0])
    for n in ("g_pre_mix", "g_post_mix", "g_pre_ffn", "g_post_ffn", "g_q_a", "g_kv_a"):
        add(n, a[n + "_2"][0])
    for n in ("norm_mix_pre", "norm_mix_post", "norm_xa_pre", "norm_xa_post", "norm_mem",
              "norm_ffn_pre", "norm_ffn_post", "b_gate", "ssm_d", "ssm_b_glu", "ffn_conv_b"):
        add(n, a[n + "_3"][0])
    add("conv_w", a["ffn_conv_w_3"][0], "w (r p) -> (w r) p")
    rows.append(("ssm_a_re", a["ssm_a_re_3"][0].rearrange("(j g) n -> j (g n)", g=2)))
    rows.append(("ssm_a_im", a["ssm_a_im_3"][0].rearrange("(j g) n -> j (g n)", g=2)))
    return rows



def transpose_tokens(K, pe, src, banks, width=DT):
    nc = K.nc
    for j, at in enumerate(banks):
        b = at[0]
        K.banks.vacant(pe, at)
        for tile in (2 * j, 2 * j + 1):
            for blk in range(TB):
                col = (tile % 2) * S + blk * P
                last = nc.tensor.transpose(K.ps[b][:, col:col + P], src[:, blk, tile * P:(tile + 1) * P], K.ident)
        last.then_inc(K.banks.full[b], 1)


def rmsnorm(K, src, dst, gain, tiles, shift=None, add_to=None):
    nc = K.nc
    bank = K.banks.take(7)
    with nc.sbuf_tensor([P, tiles, S], F32) as squares, nc.sbuf_tensor([P, S], F32) as rms, \
            nc.sbuf_tensor([P, S], F32) as rstd, nc.Block() as block:

        @block.scalar
        def _(act):
            nc.scalar.activation(squares[:, :, :], src, ACT.Square).then_inc(K.squares.sem, 1)
            K.banks.ready(act, bank)
            nc.scalar.activation(rms[:, :], K.ps[7][:, 0:S], ACT.Sqrt, bias=K.col("eps"),
                                 scale=1.0 / (tiles * P)).then_inc(K.banks.free[7], 1)

        @block.tensor
        def _(pe):
            pe.wait_ge(*K.squares(1))
            K.banks.vacant(pe, bank)
            for t in range(tiles):
                last = nc.tensor.matmul(K.ps[7][:, 0:S], K.ones, squares[:, t, :], start=t == 0, stop=t == tiles - 1)
            last.then_inc(K.banks.full[7], 1)

        @block.vector
        def _(dve):
            K.vsteps.eng = dve
            K.banks.read(dve, bank)
            K.vsteps.link(nc.vector.reciprocal(rstd[:, :], rms[:, :]))
            if add_to is None and shift is None:
                for t in range(tiles):
                    nc.vector.scalar_tensor_tensor(dst[:, t, :], src[:, t, :], gain(t), rstd[:, :], ALU.mult, ALU.mult)
                return
            for t in range(tiles):
                last = nc.vector.scalar_tensor_tensor(squares[:, t, :], src[:, t, :], gain(t), rstd[:, :],
                                                      ALU.mult, ALU.mult)
            K.vsteps.link(last)
            if add_to is not None:
                nc.vector.tensor_tensor(add_to, add_to, squares[:, :, :], ALU.add)
            else:
                for t in range(tiles):
                    nc.vector.tensor_scalar(dst[:, t, :], squares[:, t, :], shift(t), None, ALU.add)
    K.squares.done(1)


def take_accumulators(K, signals=True):
    return [K.banks.take(b, signals=signals and b == 3) for b in range(4)]


def read_accumulators(K, dve, out, finish):
    K.vsteps.eng = dve
    for j, (b, _, _) in enumerate(out):
        finish(dve, j, K.ps[b]).then_inc(K.banks.free[b], 1)


def dense_down(K, src, weights, tiles, finish):
    nc, ring, banks = K.nc, K.ring, K.banks
    view = weights.rearrange("(t p) n -> p t n", p=P)
    units = []
    for u in range(tiles // 2):
        units.append(ring.take())
        ring.freed_by_use(units[-1][0])
    out = take_accumulators(K)
    ring.uses[units[-1][0]] -= 1
    ring.freed_by(units[-1][0], banks.full[3], banks.fulls[3])
    with nc.Block() as block:

        @block.sync
        def _(sp):
            for u, unit in enumerate(units):
                ring.vacant(sp, unit)
                sp.dma_start(ring.slot(unit[0]).rearrange("p (t n) -> p t n", t=2), view[:, 2 * u:2 * u + 2, :])\
                    .then_inc(ring.loaded[unit[0]], 16)

        @block.tensor
        def _(pe):
            for at in out:
                banks.vacant(pe, at)
            for u, unit in enumerate(units):
                ring.arrived(pe, unit)
                last = down_unit(K, ring.slot(unit[0]), lambda kk: src[:, 2 * u + kk, :], u == 0, u == len(units) - 1)
                last.then_inc(ring.used[unit[0]] if u < len(units) - 1 else banks.full[3], 1)

        @block.vector
        def _(dve):
            banks.ready(dve, out[3])
            read_accumulators(K, dve, out, finish)


def down_unit(K, slot, moving, first, last):
    for kk in range(2):
        for c in range(DT):
            m = K.nc.tensor.matmul(K.ps[c // 2][:, (c % 2) * S:(c % 2 + 1) * S],
                                   slot[:, kk * D + c * P:kk * D + (c + 1) * P], moving(kk),
                                   start=first and kk == 0 and c % 2 == 0, stop=last and kk == 1,
                                   skip_group_check=True)
    return m


def add_residual(K, scale=None):
    def finish(dve, j, ps):
        x = K.x[:, 2 * j:2 * j + 2, :].rearrange("p t s -> p (t s)")
        if scale is None:
            return K.nc.vector.tensor_tensor(x, ps[:, :], x, ALU.add)
        return K.nc.vector.scalar_tensor_tensor(x, ps[:, :], scale, x, ALU.mult, ALU.add)
    return finish


def store_to(K, dst):
    def finish(dve, j, ps):
        return K.nc.vector.tensor_copy(dst[:, 2 * j:2 * j + 2, :].rearrange("p t s -> p (t s)"), ps[:, :])
    return finish



def high_place(K, n):
    return K.ring.part(SLOTS + n)


def write_high(K, high, source):
    K.nc.scalar.activation(high, source, ACT.Copy).then_inc(K.high_written.sem, 1)


def leave_low(K, dve, count, place, high, low):
    dve.wait_ge(*count)
    K.nc.vector.tensor_tensor(low, place, high.bitcast(F32), ALU.subtract)\
        .then_inc(K.low_written.sem, 1)


def flat(x):
    return x.rearrange("p t s -> p (t s)")


def multiply_parts(K, out, stationary, moving, start, stop, **flags):
    parts = ((0, 0), (0, 1), (1, 0))
    for n, (a, b) in enumerate(parts):
        m = K.nc.tensor.matmul(out, stationary[a], moving[b], start=start and n == 0, stop=stop and n == 2, **flags)
    return m


def dense_up(K, src, src_low, tiles, jobs):
    nc, ring, banks = K.nc, K.ring, K.banks
    ahead = 2
    units, out = [], []
    for j in range(len(jobs)):
        units.append(ring.take())
        out.append(banks.take(4 + j % 4))
        ring.freed_by(units[j][0], banks.full[out[j][0]], out[j][2] + 1)
    width = tiles * 256

    def weights(j):
        return ring.slot(units[j][0])[:, 0:width]

    def high(j):
        return high_place(K, j % HIGHS)[:, 0:width]

    def in_order(eng, which, split):
        for j in range(len(jobs) + ahead):
            if j < len(jobs):
                split(j)
            if j >= ahead and jobs[j - ahead][2] == which:
                at = out[j - ahead]
                banks.ready(eng, at)
                jobs[j - ahead][3](K.ps[at[0]]).then_inc(banks.free[at[0]], 1)

    with nc.Block() as block:

        @block.sync
        def _(sp):
            for (w, _, _, _), unit in zip(jobs, units):
                ring.vacant(sp, unit)
                sp.dma_start(ring.slot(unit[0])[:, 0:width].rearrange("p (t n) -> p t n", n=256),
                             w.rearrange("(t p) n -> p t n", p=P)).then_inc(ring.loaded[unit[0]], 16)

        @block.tensor
        def _(pe):
            for j, ((_, by_token, _, _), at) in enumerate(zip(jobs, out)):
                pe.wait_ge(*K.low_written(2 + j))
                banks.vacant(pe, at)
                up_unit(K, src_low, (high(j), ring.part(units[j][0])), tiles, K.ps[at[0]], by_token)\
                    .then_inc(banks.full[at[0]], 1)

        @block.scalar
        def _(act):
            def split(j):
                if j >= HIGHS:
                    banks.ready(act, out[j - HIGHS])
                ring.arrived(act, units[j])
                write_high(K, high(j), weights(j))
            write_high(K, flat(K.h_high[:, :, :]), flat(src[:, :, :]))
            in_order(act, "act", split)

        @block.vector
        def _(dve):
            leave_low(K, dve, K.high_written(1), flat(src[:, :, :]), flat(K.h_high[:, :, :]), flat(src_low[:, :, :]))
            in_order(dve, "dve", lambda j: leave_low(K, dve, K.high_written(2 + j), weights(j), high(j),
                                                        ring.part(units[j][0])[:, 0:width]))
    K.high_written.done(1 + len(jobs))
    K.low_written.done(1 + len(jobs))


def up_unit(K, low, weights, tiles, ps, by_token=False):
    for half in range(2):
        for k in range(tiles):
            if by_token:
                a = (K.h_high[:, k, half * P:(half + 1) * P], low[:, k, half * P:(half + 1) * P])
                m = [w[:, k * 256:(k + 1) * 256] for w in weights]
            else:
                a = [w[:, k * 256 + half * P:k * 256 + (half + 1) * P] for w in weights]
                m = (K.h_high[:, k, :], low[:, k, :])
            last = multiply_parts(K, ps[:, half * 256:(half + 1) * 256], a, m, k == 0, k == tiles - 1)
    return last


def feed_forward(K, w_in, w_out, middle, finish):
    nc, ring, banks = K.nc, K.ring, K.banks
    pairs = FF // 256
    trips = (pairs - 1) // 2
    w_in_v = w_in.rearrange("(t p) n -> p t n", p=P)
    w_out_v = w_out.rearrange("(t p) n -> p t n", p=P)

    def plan(first_bank, trips=1):
        units, at = [], []
        for b in (first_bank, first_bank + 1):
            units.append(ring.take(trips))
            at.append(banks.take(b, trips))
            ring.freed_by(units[-1][0], banks.full[b], at[-1][2] + trips)
        return units, at

    first_up = plan(4)
    loop_up = [plan(6, trips), plan(4, trips)]
    down_trips = (pairs - 3) // HIGHS
    first_down, first_uses = [], []
    for _ in range(pairs - HIGHS * down_trips):
        first_down.append(ring.take())
        first_uses.append(ring.freed_by_use(first_down[-1][0]))
    loop_down, loop_uses = [], []
    for _ in range(HIGHS):
        loop_down.append(ring.take(down_trips))
        loop_uses.append(ring.freed_by_use(loop_down[-1][0], down_trips))
    peeled = len(first_down)
    out = take_accumulators(K, signals=False)
    before_down = 1 + 2 * pairs

    shape = [P, FF // P, S]
    with ExitStack() as stack:
        hid = stack.enter_context(nc.sbuf_tensor("hidden", shape, F32, allow_name_mangling=True))
        hid_low = parts_view(nc, f"hidden_low{K.vsteps.n}", shape)
        hid_high = stack.enter_context(nc.sbuf_tensor("hidden_high", shape, F32R, allow_name_mangling=True))
        block = stack.enter_context(nc.Block())

        def load_up(sp, unit, column):
            sp.dma_start(ring.slot(unit[0]).rearrange("p (t n) -> p t n", n=256),
                         w_in_v[:, :, bass.ds(column, 256)]).then_inc(ring.loaded[unit[0]], 16)

        def load_down(sp, u, unit):
            sp.dma_start(ring.slot(unit[0]).rearrange("p (t n) -> p t n", t=2),
                         w_out_v[:, bass.ds(u * 2, 2), :]).then_inc(ring.loaded[unit[0]], 16)

        def loaded(eng, i, unit):
            eng.wait_ge(ring.loaded[unit[0]], i * 16 + (unit[1] * 16 + 16))

        def nth(signal, i, per, n):
            return signal.sem, i * per + (signal.base + n)

        @block.sync
        def _(sp):
            for pair, (units, _) in enumerate([first_up] + loop_up):
                for g, unit in enumerate(units):
                    ring.vacant(sp, unit)
                    load_up(sp, unit, pair * 256 + g * FF)
            with sp.Fori(1, trips) as i:
                for b, (units, at) in enumerate(loop_up):
                    for g, (unit, bank) in enumerate(zip(units, at)):
                        column = sp.snap(i * 512 + ((1 + b) * 256 + g * FF))
                        sp.wait_ge(banks.full[bank[0]], i + bank[2])
                        load_up(sp, unit, column)
            for u, unit in enumerate(first_down + loop_down):
                ring.vacant(sp, unit)
                load_down(sp, u, unit)
            for i in range(1, down_trips):
                for u, (unit, uses) in enumerate(zip(loop_down, loop_uses)):
                    sp.wait_ge(ring.used[unit[0]], uses + i)
                    load_down(sp, peeled + i * HIGHS + u, unit)

        @block.tensor
        def _(pe):
            def up_pair(i, units, at, place, n):
                for g, (unit, bank) in enumerate(zip(units, at)):
                    pe.wait_ge(*nth(K.low_written, i, 4, n + g))
                    pe.wait_ge(banks.free[bank[0]], i + (bank[1] + 1))
                    up_unit(K, K.h_low, (high_place(K, place + g), ring.part(unit[0])), DT, K.ps[bank[0]])\
                        .then_inc(banks.full[bank[0]], 1)

            def down(i, u, unit, place, first=False, last=False):
                pe.wait_ge(*nth(K.hidden, i, HIGHS, u + 1))
                pe.wait_ge(*nth(K.low_written, i, HIGHS, before_down + u + 1))
                parts = high_place(K, place), ring.part(unit[0])
                for kk in range(2):
                    tile = bass.ds(i * (2 * HIGHS) + (2 * u + kk), 1)
                    moving = hid_high[:, tile, :], hid_low[:, tile, :]
                    for c in range(DT):
                        m = multiply_parts(K, K.ps[c // 2][:, (c % 2) * S:(c % 2 + 1) * S],
                                           [w[:, kk * D + c * P:kk * D + (c + 1) * P] for w in parts], moving,
                                           first and kk == 0 and c % 2 == 0, last and kk == 1, skip_group_check=True)
                m.then_inc(ring.used[unit[0]], 1)

            up_pair(0, *first_up, 2, 2)
            with pe.Fori(0, trips) as i:
                for b, (units, at) in enumerate(loop_up):
                    up_pair(i, units, at, 2 * b, 4 + 2 * b)
            for at in out:
                banks.vacant(pe, at)
            for u, unit in enumerate(first_down):
                down(0, u, unit, 1 + u, first=u == 0)
            with pe.Fori(0, down_trips) as i:
                for u, unit in enumerate(loop_down):
                    down(i, peeled + u, unit, u)

        @block.scalar
        def _(act):
            def split(i, unit, place):
                loaded(act, i, unit)
                write_high(K, high_place(K, place), ring.slot(unit[0]))

            write_high(K, flat(K.h_high[:, :, :]), flat(K.h[:, :, :]))
            for g in range(2):
                split(0, first_up[0][g], 2 + g)
            with act.Fori(0, trips) as i:
                for b, (units, at) in enumerate(loop_up):
                    for g in range(2):
                        bank = (at if b == 0 else first_up[1])[g]
                        act.wait_ge(banks.full[bank[0]], i + (bank[2] + b))
                        split(i, units[g], 2 * b + g)
                    middle.act(act, i, b, (first_up[1], loop_up[0][1])[b])
            for u, unit in enumerate(first_down):
                bank, n = (loop_up[0][1][1], trips) if u == 0 else (first_up[1][u - 1], trips + 1)
                act.wait_ge(banks.full[bank[0]], bank[2] + n)
                split(0, unit, 1 + u)
                if u == 0:
                    middle.act(act, trips, 0, first_up[1])
            with act.Fori(0, down_trips) as i:
                for u, (unit, uses) in enumerate(zip(loop_down, loop_uses)):
                    if u:
                        act.wait_ge(ring.used[first_down[u - 1][0]], first_uses[u - 1] + 1)
                    act.wait_ge(ring.used[unit[0]], i + uses)
                    split(i, unit, u)

        @block.vector
        def _(dve):
            K.vsteps.eng = dve

            def split(i, per, n, unit, place):
                leave_low(K, dve, nth(K.high_written, i, per, n), ring.slot(unit[0]), high_place(K, place),
                          ring.part(unit[0]))

            leave_low(K, dve, K.high_written(1), flat(K.h[:, :, :]), flat(K.h_high[:, :, :]), flat(K.h_low[:, :, :]))
            for g in range(2):
                split(0, 0, 2 + g, first_up[0][g], 2 + g)
            with dve.Fori(0, trips) as i:
                K.vsteps.loop(i, 2 * middle.links)
                for b, (units, at) in enumerate(loop_up):
                    for g in range(2):
                        split(i, 4, 4 + 2 * b + g, units[g], 2 * b + g)
                    middle.dve(dve, i, dve.snap(i * 2 + b), b, (first_up[1], loop_up[0][1])[b], hid, hid_high, hid_low)
                K.vsteps.end(trips, 2 * middle.links)
            for u, unit in enumerate(first_down):
                split(0, 0, before_down + 1 + u, unit, 1 + u)
                if u == 0:
                    middle.dve(dve, trips, pairs - 1, 0, first_up[1], hid, hid_high, hid_low)
            with dve.Fori(0, down_trips) as i:
                for u, unit in enumerate(loop_down):
                    split(i, HIGHS, before_down + 1 + peeled + u, unit, u)
            dve.wait_ge(ring.used[loop_down[-1][0]], loop_uses[-1] + down_trips)
            read_accumulators(K, dve, out, finish)
    for signal in (K.high_written, K.low_written):
        signal.done(before_down + pairs)
    K.hidden.done(pairs)


def split_hidden(K, pair, hid, high, low):
    tiles = bass.ds(pair * 2, 2)
    K.vsteps.link(K.nc.vector.tensor_copy(high[:, tiles, :], hid[:, tiles, :]))
    K.nc.vector.tensor_tensor(low[:, tiles, :], hid[:, tiles, :], high[:, tiles, :].bitcast(F32),
                              ALU.subtract).then_inc(K.hidden.sem, 1)


class SiluGate:
    links = 1

    def __init__(self, K, buffer):
        self.K, self.silu = K, buffer

    def act(self, act, i, b, at):
        K, banks, ((gate, _, gate_full), (up, up_free, _)) = self.K, self.K.banks, at
        act.wait_ge(banks.full[gate], i + (gate_full + 1))
        act.wait_ge(banks.free[up], i + (up_free + 1))
        K.nc.scalar.activation(self.silu[:, b, :], K.ps[gate][:, :], ACT.Silu).then_inc(banks.free[gate], 1)

    def dve(self, dve, i, pair, b, at, hid, high, low):
        K, banks, ((gate, gate_free, _), (up, up_free, up_full)) = self.K, self.K.banks, at
        dve.wait_ge(banks.full[up], i + (up_full + 1))
        dve.wait_ge(banks.free[gate], i + (gate_free + 2))
        K.nc.vector.tensor_tensor(hid[:, bass.ds(pair * 2, 2), :], self.silu[:, b, :].rearrange("p (t s) -> p t s", t=2),
                                  K.ps[up][:, :].rearrange("p (t s) -> p t s", t=2), ALU.mult)\
            .then_inc(banks.free[up], 1)
        dve.wait_ge(banks.free[up], i + (up_free + 2))
        split_hidden(K, pair, hid, high, low)


def swiglu(K, w_in, w_out, norm_at):
    rmsnorm(K, K.x[:, :, :], K.h, lambda t: K.param("ffn_norm", norm_at + t), DT)
    with K.nc.sbuf_tensor([P, 2, 512], F32) as silu:
        feed_forward(K, w_in, w_out, SiluGate(K, silu), add_residual(K, 0.5))


class ConvGate:
    links = 4

    def __init__(self, K, buffer):
        self.K, self.buf = K, buffer

    def act(self, act, i, b, at):
        K, (gate, gate_free, _) = self.K, at[0]
        act.wait_ge(K.banks.free[gate], i + (gate_free + 2))
        part = self.buf[:, b, 0:2, :]
        K.nc.scalar.activation(part, part, ACT.Gelu_apprx_tanh).then_inc(K.gelus.sem, 1)

    def dve(self, dve, i, pair, b, at, hid, high, low):
        K, v, banks, ((gate, _, gate_full), (up, _, up_full)) = self.K, self.K.nc.vector, self.K.banks, at
        dve.wait_ge(banks.full[gate], i + (gate_full + 1))
        dve.wait_ge(banks.full[up], i + (up_full + 1))
        def tile_of(n):
            return dve.snap(pair * 2 + n) if not isinstance(pair, int) else pair * 2 + n

        tiles = [(self.buf[:, b, 2 * g + half, :], K.ps[(gate, up)[g]][:, half * S:(half + 1) * S],
                  tile_of(g * (FF // P) + half)) for g in range(2) for half in range(2)]
        for out, ps, tile in tiles:
            m = v.tensor_scalar(out, ps, K.param("conv_w", tile + 2 * 2 * FF // P), K.param("ffn_conv_b", tile),
                                ALU.mult, ALU.add)
        K.vsteps.link(m)
        for out, ps, tile in tiles:
            m = v.scalar_tensor_tensor(out[:, 1:], ps[:, 0:S - 1], K.param("conv_w", tile + 2 * FF // P), out[:, 1:],
                                       ALU.mult, ALU.add)
        K.vsteps.link(m)
        for n, (out, ps, tile) in enumerate(tiles):
            m = v.scalar_tensor_tensor(out[:, 2:], ps[:, 0:S - 2], K.param("conv_w", tile), out[:, 2:], ALU.mult, ALU.add)
            if n % 2:
                m.then_inc(banks.free[(gate, up)[n // 2]], 1)
        dve.wait_ge(banks.free[up], i + (at[1][1] + 2))
        dve.wait_ge(K.gelus.sem, pair + (K.gelus.base + 1))
        K.vsteps.link(v.tensor_tensor(hid[:, bass.ds(pair * 2, 2), :], self.buf[:, b, 0:2, :], self.buf[:, b, 2:4, :],
                                      ALU.mult))
        split_hidden(K, pair, hid, high, low)


def conv_feed_forward(K, a):
    rmsnorm(K, K.x[:, :, :], K.h, lambda t: K.param("norm_ffn_pre", t), DT)
    with K.nc.sbuf_tensor([P, 2, 4, S], F32) as conv:
        feed_forward(K, a["ffn_w_up_3"][0], a["ffn_w_down_3"][0], ConvGate(K, conv), store_to(K, K.h))
    K.gelus.done(FF // 256)
    rmsnorm(K, K.h[:, :, :], None, lambda t: K.param("norm_ffn_post", t), DT, add_to=K.x[:, :, :])


def setup(K, a, const):
    nc, banks = K.nc, K.banks
    rows = parameter_rows(a)
    total = sum(r.shape[0] for _, r in rows)
    groups = -(-total // P)
    K.params = nc.alloc_sbuf_tensor("params", [P, groups * P], F32)
    K.param_at, at, pieces = {}, 0, []
    for name, r in rows:
        K.param_at[name] = at
        done = 0
        while done < r.shape[0]:
            n = min(r.shape[0] - done, P - at % P)
            pieces.append((at // P, at % P, n, r[done:done + n, :]))
            done, at = done + n, at + n
    param_banks = [banks.take(g) for g in range(-(-groups // 4))]
    x_banks = [banks.take(4 + j) for j in range(4)]
    consts_in, x_in, zeroed = (nc.alloc_semaphore(n) for n in ("consts_in", "x_in", "rows_zeroed"))
    rows_in = [nc.alloc_semaphore(f"rows_in{i}") for i in range(4)]
    with nc.sbuf_tensor([P, groups, P], F32) as raw, nc.sbuf_tensor([P, TB, D], F32) as tokens, nc.Block() as block:

        def load_rows(eng, which):
            eng.wait_ge(zeroed, 1)
            for k, (g, p, n, src) in enumerate(pieces[which::4]):
                if k:
                    eng.wait_ge(rows_in[which], 16 * k)
                eng.dma_start(raw[p:p + n, g, :], src).then_inc(rows_in[which], 16)

        @block.sync
        def _(sp):
            sp.dma_start(K.consts[:, :], const).then_inc(consts_in, 16)
            sp.dma_start(tokens[:, :, :], a["x"][0].rearrange("(b p) d -> p b d", p=P)).then_inc(x_in, 16)
            load_rows(sp, 0)
            load_rows(sp, 1)

        @block.gpsimd
        def _(pool):
            nc.gpsimd.memset(raw[:, :, :], 0.0).then_inc(zeroed, 1)
            for sem in banks.free:
                pool.sem_inc(sem, 1)

        @block.scalar
        def _(act):
            load_rows(act, 2)
            load_rows(act, 3)
            for j, at in enumerate(x_banks):
                banks.ready(act, at)
                nc.scalar.activation(K.x[:, 2 * j:2 * j + 2, :].rearrange("p t s -> p (t s)"), K.ps[at[0]][:, :],
                                     ACT.Copy).then_inc(banks.free[at[0]], 1)

        @block.tensor
        def _(pe):
            pe.wait_ge(consts_in, 16)
            pe.wait_ge(x_in, 16)
            transpose_tokens(K, pe, tokens, x_banks)
            for which in range(4):
                pe.wait_ge(rows_in[which], 16 * len(pieces[which::4]))
            for g in range(groups):
                at = param_banks[g // 4]
                if g % 4 == 0:
                    banks.vacant(pe, at)
                m = nc.tensor.transpose(K.ps[at[0]][:, g % 4 * P:(g % 4 + 1) * P], raw[:, g, :], K.ident)
                if g % 4 == 3 or g == groups - 1:
                    m.then_inc(banks.full[at[0]], 1)

        @block.vector
        def _(dve):
            for k, at in enumerate(param_banks):
                banks.ready(dve, at)
                n = min(4, groups - 4 * k) * P
                nc.vector.tensor_copy(K.params[:, k * 512:k * 512 + n], K.ps[at[0]][:, 0:n])\
                    .then_inc(banks.free[at[0]], 1)


def store_output(K, out):
    nc, banks = K.nc, K.banks
    at = [banks.take(j) for j in range(4)]
    out_written = [nc.alloc_semaphore(f"out_written{b}") for b in range(TB)]
    with nc.sbuf_tensor([P, TB, D], F32) as tokens, nc.Block() as block:

        @block.tensor
        def _(pe):
            for j in range(4):
                banks.vacant(pe, at[j])
                for q in range(4):
                    t, blk = (4 * j + q) % DT, j // 2
                    m = nc.tensor.transpose(K.ps[j][:, q * P:(q + 1) * P], K.x[:, t, blk * P:(blk + 1) * P], K.ident)
                m.then_inc(banks.full[j], 1)

        @block.vector
        def _(dve):
            for j in range(4):
                banks.ready(dve, at[j])
                nc.vector.tensor_copy(tokens[:, j // 2, (j % 2) * 512:(j % 2 + 1) * 512], K.ps[j][:, :])\
                    .then_inc(banks.free[j], 1)

        @block.sync
        def _(sp):
            for blk in range(TB):
                banks.read(sp, at[2 * blk + 1])
                sp.dma_start(out[0, blk * P:(blk + 1) * P, :], tokens[:, blk, :]).then_inc(out_written[blk], 16)
            for blk in range(TB):
                sp.wait_ge(out_written[blk], 16)


def spatial_gate(K, a):
    nc, banks = K.nc, K.banks
    heads, wide = 8, 2048
    tiles = wide // P
    rmsnorm(K, K.x[:, :, :], K.h, lambda t: K.param("mix_norm", t), DT)
    w_in, w_s, b_s = a["a_w_in"][0], a["a_w_s"][0], a["a_b_s"][0]
    mix_in, bias_in = nc.alloc_semaphore("mixing_loaded"), nc.alloc_semaphore("mixing_bias_loaded")
    mixed_steps, v_steps = K.vsteps, K.asteps
    with nc.sbuf_tensor([P, tiles, S], F32) as u, nc.sbuf_tensor([P, TB, wide], F32) as v, \
            nc.sbuf_tensor([P, heads, P], F32) as mix:
        jobs = []
        for j in range(8):
            jobs.append((w_in[:, j * 256:(j + 1) * 256], False, "act", lambda ps, j=j: nc.scalar.activation(
                u[:, 2 * j:2 * j + 2, :].rearrange("p t s -> p (t s)"), ps[:, :], ACT.Gelu_apprx_tanh)))
        for j in range(8):
            jobs.append((w_in[:, wide + j * 256:wide + (j + 1) * 256], True, "act",
                         lambda ps, j=j: nc.scalar.activation(v[:, :, j * 256:(j + 1) * 256],
                                                              ps[:, :].rearrange("p (b n) -> p b n", b=TB),
                                                              ACT.Gelu_apprx_tanh)))
        dense_up(K, K.h, K.h_low, DT, jobs)
        mix_at = [banks.take(0), banks.take(1)]
        gate_at = [banks.take(2 + h % 6) for h in range(heads)]
        with nc.sbuf_tensor([P, heads, P], F32) as raw, nc.sbuf_tensor([P, heads, P], F32) as bias, \
                nc.sbuf_tensor([P, wide], F32) as squares, nc.sbuf_tensor([P, TB], F32) as ssq, \
                nc.sbuf_tensor([P, 2, 2, S], F32) as gated, nc.Block() as block:

            @block.sync
            def _(sp):
                sp.dma_start(raw[:, :, :], w_s.rearrange("h t s -> t h s")).then_inc(mix_in, 16)
                sp.dma_start(bias[:, :, :], b_s.unsqueeze(0).broadcast_to([P, heads, P])).then_inc(bias_in, 16)

            @block.scalar
            def _(act):
                v_steps.eng = act
                for b in range(TB):
                    v_steps.link(nc.scalar.activation(squares[:, :], v[:, b, :], ACT.Square, accum_out=ssq[:, b:b + 1]))
                nc.scalar.activation(ssq[:, :], ssq[:, :], ACT.Sqrt, bias=K.col("eps"), scale=1.0 / wide)\
                    .then_inc(K.squares.sem, 1)

            @block.tensor
            def _(pe):
                pe.wait_ge(mix_in, 16)
                for g, at in enumerate(mix_at):
                    banks.vacant(pe, at)
                    for h in range(4):
                        m = nc.tensor.transpose(K.ps[at[0]][:, h * P:(h + 1) * P], raw[:, 4 * g + h, :], K.ident)
                    m.then_inc(banks.full[at[0]], 1)
                banks.read(pe, mix_at[1])
                pe.wait_ge(K.scaled.sem, K.scaled.base + 1)
                for h, at in enumerate(gate_at):
                    banks.vacant(pe, at)
                    for half in range(2):
                        for c in range(TB):
                            m = nc.tensor.matmul(K.ps[at[0]][:, half * S + c * P:half * S + (c + 1) * P],
                                                 v[:, c, h * 256 + half * P:h * 256 + (half + 1) * P], mix[:, h, :],
                                                 start=True, stop=True)
                    m.then_inc(banks.full[at[0]], 1)

            @block.vector
            def _(dve):
                mixed_steps.eng = dve
                for g, at in enumerate(mix_at):
                    banks.ready(dve, at)
                    nc.vector.tensor_tensor(mix[:, 4 * g:4 * g + 4, :],
                                            K.ps[at[0]][:, :].rearrange("p (h t) -> p h t", h=4),
                                            K.const("upto", P).unsqueeze(1).broadcast_to([P, 4, P]), ALU.mult)\
                        .then_inc(banks.free[at[0]], 1)
                dve.wait_ge(*K.squares(1))
                mixed_steps.link(nc.vector.reciprocal(ssq[:, :], ssq[:, :]))
                for b in range(TB):
                    m = nc.vector.tensor_scalar(v[:, b, :], v[:, b, :], ssq[:, b:b + 1], None, ALU.mult)
                m.then_inc(K.scaled.sem, 1)
                dve.wait_ge(bias_in, 16)
                for h, at in enumerate(gate_at):
                    banks.ready(dve, at)
                    for half in range(2):
                        m = nc.vector.scalar_tensor_tensor(
                            gated[:, h % 2, half, :].rearrange("p (c t) -> p c t", c=TB),
                            K.ps[at[0]][:, half * S:(half + 1) * S].rearrange("p (c t) -> p c t", c=TB),
                            K.param("a_v_norm", 2 * h + half),
                            bias[:, h, :].unsqueeze(1).broadcast_to([P, TB, P]), ALU.mult, ALU.add)
                    m.then_inc(banks.free[at[0]], 1)
                    banks.read(dve, at)
                    nc.vector.tensor_tensor(u[:, 2 * h:2 * h + 2, :], u[:, 2 * h:2 * h + 2, :], gated[:, h % 2, :, :],
                                            ALU.mult)
        K.squares.done(1)
        K.scaled.done(1)
        dense_down(K, u, a["a_w_out"][0], tiles, add_residual(K))


def pool_mixer(K, a):
    nc, banks = K.nc, K.banks
    windows = (2, 4, 8, 16)
    rmsnorm(K, K.x[:, :, :], K.h, lambda t: K.param("mix_norm", DT + t), DT)
    with nc.sbuf_tensor([P, DT, S], F32) as p, nc.sbuf_tensor([P, DT, S], F32) as y:
        dense_down(K, K.h, a["b_w_in"][0], DT, store_to(K, p))
        grp_in = nc.alloc_semaphore("group_weights_loaded")
        group_at = [banks.take(g) for g in range(4)]
        with nc.sbuf_tensor([P, DT, S], F32) as even, nc.sbuf_tensor([P, DT, S], F32) as odd, \
                nc.sbuf_tensor([P, 4, 2, 256], F32) as w, nc.Block() as block:

            @block.sync
            def _(sp):
                sp.dma_start(w[:, :, :, :], a["b_w_grp"][0].rearrange("g (k p) d -> p g k d", p=P)).then_inc(grp_in, 16)

            @block.vector
            def _(dve):
                K.vsteps.eng = dve
                link = K.vsteps.link
                src = p
                for g, window in enumerate(windows):
                    back, dst = window // 2, (even, odd)[g % 2]
                    first = 2 * g
                    nc.vector.tensor_copy(dst[:, first:, 0:back], src[:, first:, 0:back])
                    link(nc.vector.tensor_tensor(dst[:, first:, back:], src[:, first:, back:], src[:, first:, 0:S - back],
                                                 ALU.add))
                    mean = dst[:, first:first + 2, :]
                    link(nc.vector.tensor_tensor(mean, mean, K.const(f"per{window}", S).unsqueeze(1)
                                                 .broadcast_to([P, 2, S]), ALU.mult))
                    nc.vector.tensor_tensor(mean, mean, p[:, first:first + 2, :], ALU.subtract)\
                        .then_inc(K.scaled.sem, 1)
                    src = dst
                for g, at in enumerate(group_at):
                    banks.ready(dve, at)
                    for half in range(2):
                        m = nc.vector.tensor_scalar(y[:, 2 * g + half, :], K.ps[at[0]][:, half * S:(half + 1) * S],
                                                    K.param("b_scale", 2 * g + half), None, ALU.mult)
                    m.then_inc(banks.free[at[0]], 1)

            @block.tensor
            def _(pe):
                pe.wait_ge(grp_in, 16)
                for g, at in enumerate(group_at):
                    pe.wait_ge(*K.scaled(g + 1))
                    banks.vacant(pe, at)
                    pooled = (even, odd)[g % 2]
                    for half in range(2):
                        for k in range(2):
                            m = nc.tensor.matmul(K.ps[at[0]][:, half * S:(half + 1) * S],
                                                 w[:, g, k, half * P:(half + 1) * P], pooled[:, 2 * g + k, :],
                                                 start=k == 0, stop=k == 1)
                    m.then_inc(banks.full[at[0]], 1)
        K.scaled.done(4)
        dense_down(K, y, a["b_w_out"][0], DT, add_residual(K))


def adaptive_columns(K, a):
    nc, ring, banks = K.nc, K.ring, K.banks
    tiles = 6 * DT
    trips, per = tiles // 8, 4
    units = [ring.take(trips) for _ in range(per)]
    assert all(units[b][0] + 1 == units[b + 1][0] for b in (0, 2))
    sums, turned = nc.alloc_semaphore("ada_sums_written"), nc.alloc_semaphore("ada_sums_turned")
    for b, unit in enumerate(units):
        ring.freed_by(unit[0], sums, 2 * (trips - 1) + b // 2 + 1)
    at = banks.take(4, signals=False)
    v = nc.vector

    def summed(n, i):
        return sums, i * 2 + n

    w = a["w_ada_2"][0].rearrange("(t p) n -> p t n", p=P)
    mod = nc.alloc_sbuf_tensor("mod_columns", [P, tiles], F32)
    K.gain1, K.gain2, K.gate1, K.gate2 = (nc.alloc_sbuf_tensor(n, [P, DT], F32) for n in
                                          ("gain_mix", "gain_ffn", "gate_mix", "gate_ffn"))
    K.shift1, K.shift2 = mod[:, 0:DT], mod[:, 3 * DT:4 * DT]
    with nc.sbuf_tensor([P, DT], F32) as cond, nc.sbuf_tensor([P, 2, 512], F32) as part, nc.Block() as block:

        @block.sync
        def _(sp):
            for b, unit in enumerate(units):
                ring.vacant(sp, unit)
                sp.dma_start(ring.slot(unit[0]).rearrange("p (t n) -> p t n", n=256), w[:, :, b * 256:(b + 1) * 256])\
                    .then_inc(ring.loaded[unit[0]], 16)
            with sp.Fori(1, trips) as i:
                for b, unit in enumerate(units):
                    column = sp.snap(i * (per * 256) + b * 256)
                    sp.wait_ge(sums, i * 2 + (b // 2 - 1))
                    sp.dma_start(ring.slot(unit[0]).rearrange("p (t n) -> p t n", n=256),
                                 w[:, :, bass.ds(column, 256)]).then_inc(ring.loaded[unit[0]], 16)

        @block.scalar
        def _(act):
            nc.scalar.activation(cond[:, :], K.param("c", 0, DT), ACT.Silu).then_inc(K.squares.sem, 1)

        @block.tensor
        def _(pe):
            banks.vacant(pe, at)
            with pe.Fori(0, trips) as i:
                for pair in range(2):
                    pe.wait_ge(*summed(pair + 1, i))
                    for q in range(4):
                        m = nc.tensor.matmul(K.ps[4][:, bass.ds(i * 8 + (4 * pair + q), 1)],
                                             part[:, pair, q * P:(q + 1) * P], K.ones[:, 0:1], start=True, stop=True)
                    m.then_inc(turned, 1)

        @block.vector
        def _(dve):
            K.vsteps.eng = dve
            link = K.vsteps.link
            dve.wait_ge(*K.squares(1))
            dve.sem_inc(turned, 2)
            with dve.Fori(0, trips) as i:
                K.vsteps.loop(i, 14)
                for pair in range(2):
                    first, second = units[2 * pair:2 * pair + 2]
                    both = K.ring.memory[:, first[0] * SLOT:(first[0] + 2) * SLOT].rearrange("p (u t n) -> p u t n", u=2, t=DT)
                    out = part[:, pair, :].rearrange("p (u n) -> p u n", u=2)
                    for unit in (first, second):
                        dve.wait_ge(ring.loaded[unit[0]], i * 16 + (unit[1] * 16 + 16))
                    dve.wait_ge(turned, i * 2 + (pair + 1))
                    link(v.tensor_scalar(out, both[:, :, 0, :], cond[:, 0:1], None, ALU.mult))
                    for t in range(1, DT - 1):
                        link(v.scalar_tensor_tensor(out, both[:, :, t, :], cond[:, t:t + 1], out, ALU.mult, ALU.add))
                    v.scalar_tensor_tensor(out, both[:, :, DT - 1, :], cond[:, DT - 1:DT], out, ALU.mult, ALU.add)\
                        .then_inc(sums, 1)
                K.vsteps.end(1, 14)
            K.vsteps.n += 14 * (trips - 1)
            dve.wait_ge(turned, 2 + 2 * trips)
            K.vsteps.link(nc.vector.tensor_tensor(mod[:, :], K.ps[4][:, 0:tiles], K.param("b_ada", 0, tiles), ALU.add))
            for out, g, q in ((K.gain1, "g_pre_mix", 1), (K.gain2, "g_pre_ffn", 4)):
                nc.vector.scalar_tensor_tensor(out[:, :], mod[:, q * DT:(q + 1) * DT], 1.0, K.param(g, 0, DT),
                                               ALU.add, ALU.mult)
            for out, g, q in ((K.gate1, "g_post_mix", 2), (K.gate2, "g_post_ffn", 5)):
                m = nc.vector.tensor_tensor(out[:, :], mod[:, q * DT:(q + 1) * DT], K.param(g, 0, DT), ALU.mult)
            m.then_inc(banks.free[4], 1)
    K.squares.done(1)


def attention(K, qb, heads, keys, scores, weights, values, halves, out, order=range(8)):
    nc, banks = K.nc, K.banks
    blocks = keys // P
    per_bank = 512 // keys
    score_at = [banks.take(b) for b in range(-(-heads // per_bank))]
    turned = heads * blocks
    turned_at = [banks.take(4 + b) for b in range(turned // 4)]
    out_banks = 1 if halves == 1 else 2
    out_at = [banks.take(b) for b in range(out_banks)]
    with nc.sbuf_tensor([P, heads, keys], F32) as w, nc.sbuf_tensor([P, turned, P], F32) as w_t, nc.Block() as block:
        weights.begin(K, qb, heads, keys, w, score_at)

        @block.tensor
        def _(pe):
            for b, at in enumerate(score_at):
                banks.vacant(pe, at)
                for h in range(b * per_bank, min(heads, (b + 1) * per_bank)):
                    ops = scores(order[h])
                    col = (h - b * per_bank) * keys
                    for k, (lhs, rhs) in enumerate(ops):
                        m = nc.tensor.matmul(K.ps[at[0]][:, col:col + keys], lhs, rhs, start=k == 0,
                                             stop=k == len(ops) - 1)
                m.then_inc(banks.full[at[0]], 1)
            pe.wait_ge(*K.weights(1))
            for b, at in enumerate(turned_at):
                banks.vacant(pe, at)
                for q in range(4):
                    h, kb = divmod(4 * b + q, blocks)
                    m = nc.tensor.transpose(K.ps[at[0]][:, q * P:(q + 1) * P], w[:, h, kb * P:(kb + 1) * P], K.ident)
                m.then_inc(banks.full[at[0]], 1)
            for at in turned_at:
                banks.read(pe, at)
            for at in out_at:
                banks.vacant(pe, at)
            for h in range(heads):
                for half in range(halves):
                    if halves == 1:
                        row, tile = order[h] % 2, order[h] // 2
                        ps = K.ps[0][64 * row:64 * row + 64, tile * P:(tile + 1) * P]
                    else:
                        tile = 2 * h + half
                        ps = K.ps[tile // 4][:, tile % 4 * P:(tile % 4 + 1) * P]
                    for kb in range(blocks):
                        m = nc.tensor.matmul(ps, values(order[h], kb, half), w_t[:, h * blocks + kb, :], start=kb == 0,
                                             stop=kb == blocks - 1)
                if h == heads - 1 or halves == 2 and h % 2:
                    m.then_inc(banks.full[0 if halves == 1 else h // 2], 1)

        @block.scalar
        def _(act):
            weights.act(act)
            for b, at in enumerate(turned_at):
                banks.ready(act, at)
                nc.scalar.activation(w_t[:, 4 * b:4 * b + 4, :].rearrange("p a q -> p (a q)"), K.ps[at[0]][:, :],
                                     ACT.Copy).then_inc(banks.free[at[0]], 1)

        @block.gpsimd
        def _(pool):
            weights.pool(pool)

        @block.vector
        def _(dve):
            K.vsteps.eng = dve
            weights.dve(dve)
            for at, (dst, src) in zip(out_at, out([K.ps[at[0]] for at in out_at])):
                banks.ready(dve, at)
                nc.vector.tensor_copy(dst, src).then_inc(banks.free[at[0]], 1)
    K.weights.done(1)
    weights.end()


class Softmax:

    def __init__(self, scale, bias=None, slopes=None, distance=None):
        self.scale, self.bias, self.slopes, self.distance = scale, bias, slopes, distance

    def begin(self, K, qb, heads, keys, w, at):
        self.K, self.qb, self.heads, self.keys, self.w, self.at = K, qb, heads, keys, w, at

    def pool(self, pool):
        pass

    def act(self, act):
        K, nc = self.K, self.K.nc
        act.wait_ge(*K.maxima(1))
        for h in range(self.heads):
            m = nc.scalar.activation(self.w[:, h, :], self.w[:, h, :], ACT.Exp, bias=K.negmax[:, h:h + 1],
                                     accum_out=K.sums[:, h:h + 1])
        m.then_inc(K.exps.sem, 1)

    def dve(self, dve):
        K, nc, w, keys = self.K, self.K.nc, self.w, self.keys
        link = K.vsteps.link
        per_bank = 512 // keys
        if self.slopes is not None:
            for h in range(self.heads):
                m = nc.vector.scalar_tensor_tensor(w[:, h, :], self.distance[:, self.qb, 0:keys], -self.slopes[h],
                                                   self.bias[:, self.qb, 0:keys], ALU.mult, ALU.add)
            link(m)
        for b, at in enumerate(self.at):
            K.banks.ready(dve, at)
            h0, n = b * per_bank, min(per_bank, self.heads - b * per_bank)
            ps = K.ps[at[0]][:, 0:n * keys].rearrange("p (h k) -> p h k", h=n)
            part = w[:, h0:h0 + n, :]
            if self.slopes is not None:
                m = nc.vector.scalar_tensor_tensor(part, ps, self.scale, part, ALU.mult, ALU.add)
            elif self.bias is not None:
                m = nc.vector.scalar_tensor_tensor(part, ps, self.scale, self.bias[self.qb].unsqueeze(1)
                                                   .broadcast_to([P, n, keys]), ALU.mult, ALU.add)
            else:
                m = nc.vector.tensor_scalar(part, ps, self.scale, None, ALU.mult)
            m.then_inc(K.banks.free[at[0]], 1)
        K.banks.read(dve, self.at[-1])
        nc.vector.tensor_reduce(K.negmax[:, 0:self.heads], w[:, :, :], AX.X, ALU.max, negate=True)\
            .then_inc(K.maxima.sem, 1)
        dve.wait_ge(*K.exps(1))
        link(nc.vector.reciprocal(K.sums[:, 0:self.heads], K.sums[:, 0:self.heads]))
        nc.vector.tensor_tensor(w[:, :, :], w[:, :, :], K.sums[:, 0:self.heads].unsqueeze(2)
                                .broadcast_to([P, self.heads, keys]), ALU.mult).then_inc(K.weights.sem, 1)

    def end(self):
        self.K.maxima.done(1)
        self.K.exps.done(1)


def reduce_angle(K, dve, angle, turns):
    nc, link = K.nc, K.vsteps.link
    c1 = 6.28125
    c2 = float(np.float32(np.round((TWO_PI - c1) * 2 ** 21) / 2 ** 21))
    c3 = float(np.float32(TWO_PI - c1 - c2))
    link(nc.vector.tensor_scalar(turns, angle, 1.0 / TWO_PI, ROUND, ALU.mult, ALU.add))
    link(nc.vector.tensor_scalar(turns, turns, ROUND, None, ALU.subtract))
    for c in (c1, c2, c3):
        link(nc.vector.scalar_tensor_tensor(angle, turns, -c, angle, ALU.mult, ALU.add))
    limit = 3.1415925
    return nc.vector.tensor_scalar(angle, angle, limit, -limit, ALU.min, ALU.max)


def mixed_attention(K, a):
    nc, banks = K.nc, K.banks
    rmsnorm(K, K.x[:, :, :], K.h, lambda t: K.gain1[:, t:t + 1], DT, shift=lambda t: K.shift1[:, t:t + 1])
    heads, width = 8, 1480
    memory = K.ring.memory
    at = [0]

    def part(n, pattern, **sizes):
        at[0] += n
        return memory[:, at[0] - n:at[0]].rearrange(pattern, **sizes)

    w_in = part(DT * width, "p (k n) -> p k n", k=DT)
    w_q = part(2 * 768, "p (k n) -> p k n", k=2)
    w_q_swapped = part(2 * 768, "p (k n) -> p k n", k=2)
    w_kv = part(1024, "p (k n) -> p k n", k=1)
    w_k_swapped = part(DT * 96, "p (k n) -> p k n", k=DT)
    w_q_pairs = part(DT * 512, "p (k n) -> p k n", k=DT)
    w_k_four = part(DT * P, "p (k n) -> p k n", k=DT)
    with ExitStack() as stack:
        def buffer(name, *shape):
            return stack.enter_context(nc.sbuf_tensor(name, [P, *shape], F32))

        c_q, c_kv = buffer("c_q", 2, S), buffer("c_kv", 1, S)
        q, k, v = buffer("mla_q", heads, S), buffer("mla_k", heads, S), buffer("mla_v", TB, 512)
        q_d, k_d, v_d = buffer("sparse_q", 4, S), buffer("sparse_k", S), buffer("sparse_v", TB, P)
        q_i, k_i, w_i = buffer("index_q", 2, S), buffer("index_k", S), buffer("index_w", TB, 8)
        mix, cos, sin = buffer("mixed", DT, S), buffer("rotary_cos", S), buffer("rotary_sin", S)
        distance, selected = buffer("distance", TB, S), buffer("selected", TB, S)
        project_inputs(K, a, heads, w_in, w_q, w_q_swapped, w_kv, w_k_swapped, w_q_pairs, w_k_four, c_q, c_kv, k, q_d, k_d, v_d,
                       q_i, k_i, w_i, cos, sin, distance)
        rmsnorm(K, c_q[:, :, :], c_q, lambda t: K.param("g_q_a", t), 2)
        rmsnorm(K, c_kv[:, :, :], c_kv, lambda t: K.param("g_kv_a", t), 1)
        expand_latents(K, heads, w_q, w_q_swapped, w_kv, c_q, c_kv, cos, sin, q, k, v)
        select_keys(K, q_i, k_i, w_i, selected)
        causal = {0: K.const("causal", P), 1: K.causal_rows}
        for qb in range(TB):
            keys = (qb + 1) * P
            tokens = slice(qb * P, (qb + 1) * P)
            attention(K, qb, heads, keys, lambda h: [(q[0:96, h, tokens], k[0:96, h, 0:keys])],
                      Softmax(96 ** -0.5, bias=causal), lambda h, kb, half: v[:, kb, h * 64:(h + 1) * 64], 1,
                      lambda ps: [(mix[:, 0:4, tokens], ps[0][:, :].rearrange("p (t q) -> p t q", t=4))])
            slopes = [2.0 ** (-8.0 * (h + 1) / heads) for h in range(heads)]

            def sparse_scores(h):
                g, j = divmod(h, 4)
                rows = slice(64 * g, 64 * g + 64)
                return [(q_d[rows, j, tokens], k_d[rows, 0:keys])]

            attention(K, qb, heads, keys, sparse_scores,
                      Softmax(64 ** -0.5, bias=selected, slopes=slopes, distance=distance),
                      lambda h, kb, half: v_d[:, kb, (h // 4) * 64:(h // 4 + 1) * 64], 1,
                      lambda ps: [(mix[:, 4:8, tokens], ps[0][:, :].rearrange("p (t q) -> p t q", t=4))])
        dense_down(K, mix, a["w_o_2"][0], DT, store_to(K, K.h))
    rmsnorm(K, K.h[:, :, :], None, lambda t: K.gate1[:, t:t + 1], DT, add_to=K.x[:, :, :])


def project_inputs(K, a, heads, w_in, w_q, w_q_swapped, w_kv, w_k_swapped, w_q_pairs, w_k_four, c_q, c_kv, k, q_d, k_d, v_d,
                   q_i, k_i, w_i, cos, sin, distance):
    nc, banks = K.nc, K.banks
    w_in_loaded = [nc.alloc_semaphore(f"w_in_loaded{i}") for i in range(2)]
    w_q_loaded, w_kv_loaded, pos_loaded, row_loaded = (nc.alloc_semaphore(n) for n in (
        "w_q_loaded", "w_kv_loaded", "positions_loaded", "position_row_loaded"))
    arranged = nc.alloc_semaphore("projection_weights_arranged")
    pos_done, angle_done, abs_done = (nc.alloc_semaphore(n) for n in ("positions_float", "angles_reduced", "abs_angle"))
    with nc.sbuf_tensor([P, S], I32) as pos_int, nc.sbuf_tensor([P, S], F32) as pos, \
            nc.sbuf_tensor([P, TB], F32) as pos_col, nc.sbuf_tensor([P, S], F32) as turns, \
            nc.sbuf_tensor([P, 2, S], F32) as k_rope:
        angle_at = [banks.take(7), banks.take(6)]
        result_at = [banks.take(b) for b in range(6)] + [banks.take(6), banks.take(7)]
        with nc.Block() as block:

            @block.sync
            def _(sp):
                view = a["w_in_2"][0].rearrange("(t p) n -> p t n", p=P)
                sp.dma_start(pos_int[:, :], a["positions_2"].broadcast_to([P, S])).then_inc(pos_loaded, 16)
                for i in range(2):
                    sp.dma_start(w_in[:, 4 * i:4 * i + 4, :], view[:, 4 * i:4 * i + 4, :]).then_inc(w_in_loaded[i], 16)
                sp.dma_start(w_q, a["w_q_b_2"][0].rearrange("(t p) n -> p t n", p=P)).then_inc(w_q_loaded, 16)
                sp.dma_start(w_kv, a["w_kv_b_2"][0].rearrange("(t p) n -> p t n", p=P)).then_inc(w_kv_loaded, 16)

            @block.tensor
            def _(pe):
                pe.wait_ge(pos_done, 1)
                for b in angle_at:
                    banks.vacant(pe, b)
                nc.tensor.matmul(K.ps[7][0:96, 0:S], K.const("freq", 96)[0:1, :], pos[0:1, :], start=True, stop=True)\
                    .then_inc(banks.full[7], 1)
                for b in range(TB):
                    m = nc.tensor.matmul(K.ps[6][:, b:b + 1], pos[0:1, b * P:(b + 1) * P], K.ones[0:1, 0:1],
                                         start=True, stop=True)
                m.then_inc(banks.full[6], 1)

                def project(ps, cols, by_token=None):
                    for t in range(DT):
                        lhs, rhs = (cols(t), K.h[:, t, :]) if by_token is None else \
                            (K.h[:, t, by_token * P:(by_token + 1) * P], cols(t))
                        m = nc.tensor.matmul(ps, lhs, rhs, start=t == 0, stop=t == DT - 1)
                    return m

                def columns(lo, n):
                    return lambda t: w_in[:, t, lo:lo + n]

                for i in range(2):
                    pe.wait_ge(w_in_loaded[i], 16)
                for at_ in result_at[:6]:
                    banks.vacant(pe, at_)
                ps = K.ps
                project(ps[0][:, 0:S], columns(0, P))
                project(ps[0][:, S:2 * S], columns(P, P)).then_inc(banks.full[0], 1)
                project(ps[1][:, 0:S], columns(256, P))
                project(ps[1][0:96, S:2 * S], columns(320, 96)).then_inc(banks.full[1], 1)
                pe.wait_ge(*K.scaled(1))
                project(ps[2][0:96, 0:S], lambda t: w_k_swapped[:, t, :])
                project(ps[2][:, S:2 * S], columns(928, P)).then_inc(banks.full[2], 1)
                pe.wait_ge(arranged, 1)
                for j in range(4):
                    m = project(ps[3 + j // 2][:, (j % 2) * S:(j % 2 + 1) * S],
                                lambda t: w_q_pairs[:, t, j * P:(j + 1) * P])
                    if j % 2:
                        m.then_inc(banks.full[3 + j // 2], 1)
                for b in range(TB):
                    m = project(ps[5][:, b * P:(b + 1) * P], columns(1056, P), b)
                m.then_inc(banks.full[5], 1)
                for at_ in result_at[6:]:
                    banks.vacant(pe, at_)
                project(ps[6][:, 0:S], columns(1184, P))
                project(ps[6][:, S:2 * S], columns(1312, P)).then_inc(banks.full[6], 1)
                project(ps[7][:, 0:S], lambda t: w_k_four[:, t, :])
                for b in range(TB):
                    m = project(ps[7][:, S + 8 * b:S + 8 * b + 8], columns(1472, 8), b)
                m.then_inc(banks.full[7], 1)
                pe.wait_ge(w_kv_loaded, 16)

            @block.gpsimd
            def _(pool):
                for i in range(2):
                    pool.wait_ge(w_in_loaded[i], 16)
                pairs = w_q_pairs.rearrange("p k (j g d) -> p k j g d", j=4, g=2)
                own = w_in[:, :, 416:928].rearrange("p k (g j d) -> p k g j d", g=2, j=4)
                for j in range(4):
                    nc.gpsimd.tensor_copy(pairs[:, :, j], own[:, :, :, j])
                nc.gpsimd.tensor_copy(w_k_four.rearrange("p k (r d) -> p k r d", r=4),
                                      w_in[:, :, 1440:1472].unsqueeze(2).broadcast_to([P, DT, 4, 32])).then_inc(arranged, 1)

            @block.scalar
            def _(act):
                for b in range(TB):
                    act.wait_ge(*K.maxima(b + 1))
                    nc.scalar.activation(distance[:, b, :], distance[:, b, :], ACT.Abs)
                act.wait_ge(angle_done, 1)
                nc.scalar.activation(turns[0:96, :], sin[0:96, :], ACT.Abs).then_inc(abs_done, 1)
                act.wait_ge(abs_done, 1)
                nc.scalar.activation(cos[0:96, :], turns[0:96, :], ACT.Sin, bias=K.col("half_pi")[0:96, :], scale=-1.0)
                nc.scalar.activation(sin[0:96, :], sin[0:96, :], ACT.Sin).then_inc(abs_done, 1)
                for b, at_, dst, src in (
                        (0, result_at[0], c_q[:, :, :].rearrange("p t s -> p (t s)"), K.ps[0][:, :]),
                        (3, result_at[3], q_d[:, 0:2, :].rearrange("p t s -> p (t s)"), K.ps[3][:, :]),
                        (4, result_at[4], q_d[:, 2:4, :].rearrange("p t s -> p (t s)"), K.ps[4][:, :]),
                        (5, result_at[5], v_d[:, :, :].rearrange("p t s -> p (t s)"), K.ps[5][:, 0:2 * P])):
                    banks.ready(act, at_)
                    nc.scalar.activation(dst, src, ACT.Copy).then_inc(banks.free[b], 1)

            @block.vector
            def _(dve):
                K.vsteps.eng = dve
                link = K.vsteps.link
                dve.wait_ge(pos_loaded, 16)
                nc.vector.tensor_copy(pos[:, :], pos_int[:, :]).then_inc(pos_done, 1)
                for i in range(2):
                    dve.wait_ge(w_in_loaded[i], 16)
                nc.vector.tensor_copy(w_k_swapped[:, :, 0:64], w_in[:, :, 320:384])
                nc.vector.tensor_copy(w_k_swapped[:, :, 64:80], w_in[:, :, 400:416])
                nc.vector.tensor_copy(w_k_swapped[:, :, 80:96], w_in[:, :, 384:400]).then_inc(K.scaled.sem, 1)
                banks.ready(dve, angle_at[0])
                nc.vector.tensor_copy(sin[0:96, :], K.ps[7][0:96, 0:S]).then_inc(banks.free[7], 1)
                banks.ready(dve, angle_at[1])
                nc.vector.tensor_copy(pos_col[:, :], K.ps[6][:, 0:TB]).then_inc(banks.free[6], 1)
                banks.read(dve, angle_at[1])
                for b in range(TB):
                    nc.vector.tensor_scalar(distance[:, b, :], pos[:, :], pos_col[:, b:b + 1], None, ALU.subtract)\
                        .then_inc(K.maxima.sem, 1)
                reduce_angle(K, dve, sin[0:96, :], turns[0:96, :]).then_inc(angle_done, 1)
                dve.wait_ge(w_q_loaded, 16)
                own, swapped = (w.rearrange("p k (h n) -> p (k h) n", n=96) for w in (w_q, w_q_swapped))
                nc.vector.tensor_copy(swapped[:, :, 0:64], own[:, :, 0:64])
                nc.vector.tensor_copy(swapped[:, :, 64:80], own[:, :, 80:96])
                nc.vector.tensor_copy(swapped[:, :, 80:96], own[:, :, 64:80])
                dve.wait_ge(abs_done, 2)
                link(nc.vector.tensor_scalar(sin[0:96, :], sin[0:96, :], K.col("sign")[0:96, :], None, ALU.mult))
                banks.ready(dve, result_at[1])
                nc.vector.tensor_copy(c_kv[:, 0, :], K.ps[1][:, 0:S])
                nc.vector.tensor_tensor(k_rope[64:96, 0, :], K.ps[1][64:96, S:2 * S], cos[64:96, :], ALU.mult)\
                    .then_inc(banks.free[1], 1)
                banks.ready(dve, result_at[2])
                nc.vector.tensor_copy(k_d[:, :], K.ps[2][:, S:2 * S])
                nc.vector.tensor_tensor(k_rope[64:96, 1, :], K.ps[2][64:96, 0:S], sin[64:96, :], ALU.mult)\
                    .then_inc(banks.free[2], 1)
                banks.read(dve, result_at[2])
                for h in range(heads):
                    nc.vector.tensor_tensor(k[64:96, h, :], k_rope[64:96, 0, :], k_rope[64:96, 1, :], ALU.add)
                banks.ready(dve, result_at[6])
                nc.vector.tensor_scalar(q_i[:, :, :].rearrange("p t s -> p (t s)"), K.ps[6][:, :], 32 ** -0.5, None,
                                        ALU.mult).then_inc(banks.free[6], 1)
                banks.ready(dve, result_at[7])
                nc.vector.tensor_copy(k_i[:, :], K.ps[7][:, 0:S])
                nc.vector.tensor_scalar(w_i[:, :, :].rearrange("p b h -> p (b h)"), K.ps[7][:, S:S + 16], 8 ** -0.5,
                                        None, ALU.mult).then_inc(banks.free[7], 1)
        K.scaled.done(1)
        K.maxima.done(TB)


def expand_latents(K, heads, w_q, w_q_swapped, w_kv, c_q, c_kv, cos, sin, q, k, v):
    nc, banks = K.nc, K.banks
    plain_at = [banks.take(b) for b in (0, 1, 2, 3)]
    swapped_at = [banks.take(b) for b in (4, 5, 6, 7)]
    k_at = [banks.take(b) for b in (0, 1, 2, 3)]
    v_at = [banks.take(b) for b in (4, 5)]
    with nc.sbuf_tensor([P, 2, 2, S], F32) as turned, nc.Block() as block:

        @block.tensor
        def _(pe):
            for w, at in ((w_q, plain_at), (w_q_swapped, swapped_at)):
                for j in range(4):
                    banks.vacant(pe, at[j])
                    for i in range(2):
                        h = 2 * j + i
                        for t in range(2):
                            m = nc.tensor.matmul(K.ps[at[j][0]][0:96, i * S:(i + 1) * S], w[:, t, h * 96:(h + 1) * 96],
                                                 c_q[:, t, :], start=t == 0, stop=t == 1)
                    m.then_inc(banks.full[at[j][0]], 1)
            for j in range(4):
                banks.vacant(pe, k_at[j])
                for i in range(2):
                    h = 2 * j + i
                    m = nc.tensor.matmul(K.ps[j][0:64, i * S:(i + 1) * S], w_kv[:, 0, h * P:h * P + 64], c_kv[:, 0, :],
                                         start=True, stop=True)
                m.then_inc(banks.full[j], 1)
            for b, at in enumerate(v_at):
                banks.vacant(pe, at)
                nc.tensor.matmul(K.ps[at[0]][:, :], c_kv[:, 0, b * P:(b + 1) * P],
                                 w_kv[:, 0, :].rearrange("p (h n) -> p h n", h=heads)[:, :, 64:P],
                                 start=True, stop=True).then_inc(banks.full[at[0]], 1)

        @block.vector
        def _(dve):
            K.vsteps.eng = dve
            link = K.vsteps.link

            def table(t):
                return t[64:96, :].unsqueeze(1).broadcast_to([32, 2, S])
            for j in range(4):
                banks.ready(dve, plain_at[j])
                ps = K.ps[j][:, :].rearrange("p (h s) -> p h s", h=2)
                nc.vector.tensor_copy(q[0:64, 2 * j:2 * j + 2, :], ps[0:64])
                nc.vector.tensor_tensor(turned[64:96, 0, :, :], ps[64:96], table(cos), ALU.mult)\
                    .then_inc(banks.free[j], 1)
                banks.ready(dve, swapped_at[j])
                nc.vector.tensor_tensor(turned[64:96, 1, :, :],
                                        K.ps[4 + j][:, :].rearrange("p (h s) -> p h s", h=2)[64:96], table(sin),
                                        ALU.mult).then_inc(banks.free[4 + j], 1)
                banks.read(dve, swapped_at[j])
                link(nc.vector.tensor_tensor(q[64:96, 2 * j:2 * j + 2, :], turned[64:96, 0, :, :],
                                             turned[64:96, 1, :, :], ALU.add))
            for b, at in enumerate(v_at):
                banks.ready(dve, at)
                nc.vector.tensor_copy(v[:, b, :], K.ps[at[0]][:, :]).then_inc(banks.free[at[0]], 1)

        @block.scalar
        def _(act):
            for j in range(4):
                banks.ready(act, k_at[j])
                nc.scalar.activation(k[0:64, 2 * j:2 * j + 2, :], K.ps[j][0:64, :].rearrange("p (h s) -> p h s", h=2),
                                     ACT.Copy).then_inc(banks.free[j], 1)


def select_keys(K, q_i, k_i, w_i, selected):
    nc, banks = K.nc, K.banks
    taken = -3e38
    at = [[banks.take(4 * (qb % 2) + r) for r in range(4)] for qb in range(TB)]
    with nc.sbuf_tensor([P, TB, 8, S], F32) as rel, nc.sbuf_tensor([P, TB, S], F32) as score, \
            nc.sbuf_tensor([P, TB, 8], F32) as top, nc.Block() as block:

        @block.tensor
        def _(pe):
            for qb in range(TB):
                keys = (qb + 1) * P
                for r in range(4):
                    banks.vacant(pe, at[qb][r])
                    for i in range(2):
                        rows = slice(32 * r, 32 * r + 32)
                        m = nc.tensor.matmul(K.ps[at[qb][r][0]][:, i * keys:(i + 1) * keys],
                                             q_i[rows, i, qb * P:(qb + 1) * P], k_i[rows, 0:keys], start=True, stop=True)
                    m.then_inc(banks.full[at[qb][r][0]], 1)

        @block.scalar
        def _(act):
            for qb in range(TB):
                keys = (qb + 1) * P
                for r in range(4):
                    banks.ready(act, at[qb][r])
                    nc.scalar.activation(rel[:, qb, 2 * r:2 * r + 2, 0:keys],
                                         K.ps[at[qb][r][0]][:, 0:2 * keys].rearrange("p (h s) -> p h s", h=2),
                                         ACT.Relu).then_inc(banks.free[at[qb][r][0]], 1)

        @block.vector
        def _(dve):
            K.vsteps.eng = dve
            link = K.vsteps.link
            for qb in range(TB):
                keys = (qb + 1) * P
                acc = score[:, qb, 0:keys]
                for r in range(4):
                    banks.read(dve, at[qb][r])
                    for i in range(2):
                        w = w_i[:, qb, 4 * i + r:4 * i + r + 1]
                        part = rel[:, qb, 2 * r + i, 0:keys]
                        if r == i == 0:
                            link(nc.vector.tensor_scalar(acc, part, w, 0.0, ALU.mult, ALU.add))
                        else:
                            link(nc.vector.scalar_tensor_tensor(acc, part, w, acc, ALU.mult, ALU.add))
                causal = K.const("causal", P) if qb == 0 else K.causal_rows
                link(nc.vector.tensor_tensor(acc, acc, causal, ALU.add))
                for _ in range(64 // 8):
                    link(nc.vector.max(top[:, qb, :], acc))
                    link(nc.vector.match_replace(acc, top[:, qb, :], acc, taken))
                link(nc.vector.tensor_scalar(acc, acc, taken / 2, NEG, ALU.is_gt, ALU.mult))
                nc.vector.tensor_tensor(selected[:, qb, 0:keys], acc, causal, ALU.add)


EXPERTS, CHOSEN = 32, 4
CAP = 64
ITEMS = 48


def route(K, a, M):
    nc, banks = K.nc, K.banks
    router_in, bias_in, b1_in, b2_in = (nc.alloc_semaphore(n) for n in (
        "router_loaded", "router_bias_loaded", "expert_b1_loaded", "expert_b2_loaded"))
    chosen, softmaxed, tables = (nc.alloc_semaphore(n) for n in ("experts_chosen", "gates_exp", "item_tables"))
    logits_at = banks.take(0)
    token_at = [banks.take(4 + j) for j in range(4)]
    rank_at, turn_at, start_at, item_at, b1_at = banks.take(1), banks.take(2), banks.take(3), banks.take(0), banks.take(1)
    b2_at = [banks.take(4 + j) for j in range(4)]
    E = EXPERTS
    with ExitStack() as stack:
        def buffer(name, *shape, dt=F32):
            return stack.enter_context(nc.sbuf_tensor(name, list(shape), dt))

        w, bias = buffer("router_w", P, DT, E), buffer("router_b", P, E)
        b1, b2 = buffer("b1_rows", E, 2 * D), buffer("b2_rows", E, D)
        logits, top, negtop = buffer("logits", P, TB, E), buffer("top_logits", P, TB, 8), buffer("neg_top", P, TB)
        index_u, index = buffer("top_index", P, TB, 8, dt=U32), buffer("top_index_f", P, TB, 8)
        gates4, total = buffer("gates4", P, TB, CHOSEN), buffer("gate_sums", P, TB)
        hit, mask, gates = buffer("hit", P, TB, E), buffer("expert_mask", P, TB, E), buffer("expert_gates", P, TB, E)
        ranks = buffer("ranks", P, TB, E)
        rank_t, gate_t = buffer("rank_t", E, S), buffer("gate_t", E, S)
        count, items, over, start = (buffer(n, E, 1) for n in ("expert_counts", "expert_items", "over", "first_item"))
        since, inside, offset = (buffer(n, E, ITEMS) for n in ("since_first", "item_of_expert", "slot_offset"))
        block = stack.enter_context(nc.Block())

        @block.sync
        def _(sp):
            sp.dma_start(w[:, :, :], a["w_router_2"][0].rearrange("(t p) n -> p t n", p=P)).then_inc(router_in, 16)
            sp.dma_start(bias[:, :], a["b_router_2"].broadcast_to([P, E])).then_inc(bias_in, 16)
            sp.dma_start(b1[:, :], a["b_mlp1_2"][0]).then_inc(b1_in, 16)
            sp.dma_start(b2[:, :], a["b_mlp2_2"][0]).then_inc(b2_in, 16)

        @block.tensor
        def _(pe):
            ps = K.ps
            pe.wait_ge(router_in, 16)
            banks.vacant(pe, logits_at)
            for b in range(TB):
                for t in range(DT):
                    m = nc.tensor.matmul(ps[0][:, b * E:(b + 1) * E], K.h[:, t, b * P:(b + 1) * P], w[:, t, :],
                                         start=t == 0, stop=t == DT - 1)
            m.then_inc(banks.full[0], 1)
            for j, at in enumerate(token_at):
                banks.vacant(pe, at)
                for q in range(4):
                    t = 4 * (j % 2) + q
                    m = nc.tensor.transpose(ps[4 + j][:, q * P:(q + 1) * P], K.h[:, t, j // 2 * P:(j // 2 + 1) * P], K.ident)
                m.then_inc(banks.full[4 + j], 1)
            pe.wait_ge(chosen, 1)
            banks.vacant(pe, rank_at)
            before = K.const("before", P)
            nc.tensor.matmul(ps[1][:, 0:E], before, mask[:, 0, :], start=True, stop=True)
            nc.tensor.matmul(ps[1][:, E:2 * E], before, mask[:, 1, :], start=True, stop=False)
            nc.tensor.matmul(ps[1][:, E:2 * E], K.ones, mask[:, 0, :], start=False, stop=True)
            for b in range(TB):
                m = nc.tensor.matmul(ps[1][0:E, 2 * E:2 * E + 1], mask[:, b, :], K.ones[:, 0:1], start=b == 0, stop=b == TB - 1)
            m.then_inc(banks.full[1], 1)
            pe.wait_ge(chosen, 2)
            banks.vacant(pe, turn_at)
            for b in range(TB):
                nc.tensor.transpose(ps[2][0:E, b * P:(b + 1) * P], ranks[:, b, :], K.ident)
                m = nc.tensor.transpose(ps[2][0:E, S + b * P:S + (b + 1) * P], gates[:, b, :], K.ident)
            m.then_inc(banks.full[2], 1)
            pe.wait_ge(chosen, 3)
            banks.vacant(pe, start_at)
            nc.tensor.matmul(ps[3][0:E, 0:1], before[0:E, 0:E], items[:, :], start=True, stop=True)
            nc.tensor.matmul(ps[3][0:1, 1:2], items[:, :], K.ones[0:E, 0:1], start=True, stop=True)\
                .then_inc(banks.full[3], 1)
            pe.wait_ge(b1_in, 16)
            banks.vacant(pe, b1_at)
            pairs = b1[:, :].rearrange("e (t p two) -> e two t p", two=2, p=P)
            for q in range(2 * DT):
                m = nc.tensor.transpose(ps[1][:, q * E:(q + 1) * E], pairs[:, q // DT, q % DT, :], K.ident[0:E, 0:E])
            m.then_inc(banks.full[1], 1)
            pe.wait_ge(tables, 1)
            banks.vacant(pe, item_at)
            for b in range(TB):
                tokens = slice(b * P, (b + 1) * P)
                nc.tensor.matmul(ps[0][:, b * ITEMS:(b + 1) * ITEMS], rank_t[:, tokens], inside[:, :], start=True, stop=False)
                nc.tensor.matmul(ps[0][:, b * ITEMS:(b + 1) * ITEMS], K.ones[0:E, :], offset[:, :], start=False, stop=True)
                nc.tensor.matmul(ps[0][:, (2 + b) * ITEMS:(3 + b) * ITEMS], gate_t[:, tokens], inside[:, :], start=True, stop=True)
            nc.tensor.matmul(ps[0][0:1, 4 * ITEMS:5 * ITEMS], K.col("index")[0:E, :], inside[:, :], start=True, stop=True)\
                .then_inc(banks.full[0], 1)
            pe.wait_ge(b2_in, 16)
            for j, at in enumerate(b2_at):
                banks.vacant(pe, at)
                for i in range(2):
                    t = 2 * j + i
                    m = nc.tensor.matmul(ps[4 + j][:, i * S:(i + 1) * S], b2[:, t * P:(t + 1) * P], gate_t[:, :],
                                         start=True, stop=True)
                m.then_inc(banks.full[4 + j], 1)

        @block.scalar
        def _(act):
            for j, at in enumerate(token_at):
                banks.ready(act, at)
                nc.scalar.activation(M.tokens[:, j // 2, (j % 2) * 512:(j % 2 + 1) * 512], K.ps[4 + j][:, :], ACT.Copy)\
                    .then_inc(banks.free[4 + j], 1)
            act.wait_ge(softmaxed, 1)
            for b in range(TB):
                m = nc.scalar.activation(gates4[:, b, :], top[:, b, 0:CHOSEN], ACT.Exp, bias=negtop[:, b:b + 1],
                                         accum_out=total[:, b:b + 1])
            m.then_inc(softmaxed, 1)

        @block.vector
        def _(dve):
            K.vsteps.eng = dve
            link, v = K.vsteps.link, nc.vector
            dve.wait_ge(bias_in, 16)
            banks.ready(dve, logits_at)
            v.tensor_tensor(logits[:, :, :], K.ps[0][:, 0:TB * E].rearrange("p (b e) -> p b e", b=TB),
                            bias[:, :].unsqueeze(1).broadcast_to([P, TB, E]), ALU.add).then_inc(banks.free[0], 1)
            banks.read(dve, logits_at)
            for b in range(TB):
                link(v.max(top[:, b, :], logits[:, b, :]))
                link(v.max_index(index_u[:, b, :], top[:, b, :], logits[:, b, :]))
            v.tensor_scalar(negtop[:, :], top[:, :, 0], -1.0, None, ALU.mult).then_inc(softmaxed, 1)
            link(v.tensor_copy(index[:, :, :], index_u[:, :, :]))
            dve.wait_ge(softmaxed, 2)
            link(v.reciprocal(total[:, :], total[:, :]))
            link(v.tensor_tensor(gates4[:, :, :], gates4[:, :, :], total[:, :].unsqueeze(2).broadcast_to([P, TB, CHOSEN]), ALU.mult))
            number = K.const("iota", E)
            for b in range(TB):
                for k in range(CHOSEN):
                    pick = index[:, b, k:k + 1]
                    if k == 0:
                        v.tensor_scalar(mask[:, b, :], number, pick, None, ALU.is_equal)
                        link(v.tensor_scalar(gates[:, b, :], number, pick, gates4[:, b, k:k + 1], ALU.is_equal, ALU.mult))
                        continue
                    v.scalar_tensor_tensor(mask[:, b, :], number, pick, mask[:, b, :], ALU.is_equal, ALU.add)
                    link(v.tensor_scalar(hit[:, b, :], number, pick, gates4[:, b, k:k + 1], ALU.is_equal, ALU.mult))
                    link(v.tensor_tensor(gates[:, b, :], gates[:, b, :], hit[:, b, :], ALU.add))
            v.tensor_copy(hit[:, :, :], mask[:, :, :]).then_inc(chosen, 1)
            banks.ready(dve, rank_at)
            link(v.tensor_copy(count[:, :], K.ps[1][0:E, 2 * E:2 * E + 1]))
            link(v.scalar_tensor_tensor(ranks[:, :, :], K.ps[1][:, 0:TB * E].rearrange("p (b e) -> p b e", b=TB), 1000.0,
                                        mask[:, :, :], ALU.add, ALU.mult))
            v.tensor_scalar(ranks[:, :, :], ranks[:, :, :], -1000.0, None, ALU.add).then_inc(banks.free[1], 1)
            banks.read(dve, rank_at)
            v.tensor_copy(hit[:, :, :], ranks[:, :, :]).then_inc(chosen, 1)
            link(v.tensor_scalar(items[:, :], count[:, :], 0.0, None, ALU.is_gt))
            for r in range(1, S // CAP):
                link(v.tensor_scalar(over[:, :], count[:, :], float(r * CAP), None, ALU.is_gt))
                link(v.tensor_tensor(items[:, :], items[:, :], over[:, :], ALU.add))
            v.tensor_copy(over[:, :], items[:, :]).then_inc(chosen, 1)
            banks.ready(dve, turn_at)
            v.tensor_copy(rank_t[:, :], K.ps[2][0:E, 0:S])
            v.tensor_copy(gate_t[:, :], K.ps[2][0:E, S:2 * S]).then_inc(banks.free[2], 1)
            banks.ready(dve, start_at)
            link(v.tensor_copy(start[:, :], K.ps[3][0:E, 0:1]))
            v.tensor_copy(M.number[0:1, :], K.ps[3][0:1, 1:2]).then_inc(banks.free[3], 1)
            item = K.const("iota", ITEMS)[0:E, :]
            link(v.tensor_scalar(since[:, :], item, start[:, :], None, ALU.subtract))
            link(v.tensor_scalar(inside[:, :], since[:, :], 0.0, None, ALU.is_ge))
            link(v.scalar_tensor_tensor(inside[:, :], since[:, :], items[:, :], inside[:, :], ALU.is_lt, ALU.mult))
            banks.read(dve, turn_at)
            v.scalar_tensor_tensor(offset[:, :], since[:, :], -float(CAP), inside[:, :], ALU.mult, ALU.mult)\
                .then_inc(tables, 1)
            banks.ready(dve, b1_at)
            v.tensor_copy(M.b1[:, :], K.ps[1][:, :]).then_inc(banks.free[1], 1)
            banks.ready(dve, item_at)
            v.tensor_copy(M.rank[:, :, :], K.ps[0][:, 0:2 * ITEMS].rearrange("p (b j) -> p b j", b=TB))
            v.tensor_copy(M.gate[:, :, :], K.ps[0][:, 2 * ITEMS:4 * ITEMS].rearrange("p (b j) -> p b j", b=TB))
            v.tensor_copy(M.expert[0:1, :], K.ps[0][0:1, 4 * ITEMS:5 * ITEMS]).then_inc(banks.free[0], 1)
            for j, at in enumerate(b2_at):
                banks.ready(dve, at)
                v.tensor_copy(M.sum[:, 2 * j:2 * j + 2, :].rearrange("p t s -> p (t s)"), K.ps[4 + j][:, :])\
                    .then_inc(banks.free[4 + j], 1)


def experts(K, a):
    nc = K.nc
    rmsnorm(K, K.x[:, :, :], K.h, lambda t: K.gain2[:, t:t + 1], DT, shift=lambda t: K.shift2[:, t:t + 1])
    with ExitStack() as stack:
        def buffer(name, *shape, dt=F32):
            return stack.enter_context(nc.sbuf_tensor(name, list(shape), dt))

        M = ExpertMemory(
            tokens=buffer("h_by_token", P, TB, D), number=buffer("item_number", P, 1, dt=I32),
            rank=buffer("item_rank", P, TB, ITEMS), gate=buffer("item_gate", P, TB, ITEMS),
            expert=buffer("item_expert", P, ITEMS, dt=I32), b1=buffer("b1_columns", P, 2 * DT * EXPERTS),
            sum=buffer("expert_sum", P, DT, S))
        route(K, a, M)
        run_items(K, a, M)
        rmsnorm(K, M.sum[:, :, :], None, lambda t: K.gate2[:, t:t + 1], DT, add_to=K.x[:, :, :])


class ExpertMemory:

    def __init__(self, tokens, number, rank, gate, expert, b1, sum):
        self.tokens, self.number, self.rank, self.gate = tokens, number, rank, gate
        self.expert, self.b1, self.sum = expert, b1, sum


class ItemSignals:

    def __init__(self, nc):
        self.slots_selected = nc.alloc_semaphore("item_slots_selected")
        self.gathered = nc.alloc_semaphore("item_gathered")
        self.gathered_written = nc.alloc_semaphore("item_gathered_written")
        self.low_gathered_written = nc.alloc_semaphore("item_low_gathered_written")
        self.hidden_done = nc.alloc_semaphore("item_hidden_done")
        self.hidden_written = nc.alloc_semaphore("item_hidden_written")
        self.gated_turned = nc.alloc_semaphore("item_gated_turned")
        self.linear_turned = nc.alloc_semaphore("item_linear_turned")
        self.gated_ready = nc.alloc_semaphore("item_gated_ready")
        self.sigmoid_written = nc.alloc_semaphore("item_sigmoid_written")
        self.act_written = nc.alloc_semaphore("item_act_written")
        self.gate_rows_written = nc.alloc_semaphore("item_gate_rows_written")
        self.gates_turned = nc.alloc_semaphore("item_gates_turned")
        self.gates_written = nc.alloc_semaphore("item_gates_written")
        self.output_done = nc.alloc_semaphore("item_output_done")
        self.output_written = nc.alloc_semaphore("item_output_written")
        self.scattered = nc.alloc_semaphore("item_scattered")
        self.added = nc.alloc_semaphore("item_added")
        self.high_written = nc.alloc_semaphore("item_weights_high_written")
        self.low_written = nc.alloc_semaphore("item_weights_low_written")


def run_items(K, a, M):
    nc, ring, ps = K.nc, K.ring, K.ps
    w1 = a["w_mlp1_2"][0].rearrange("e (t p) n -> e p t n", p=P)
    w2 = a["w_mlp2_2"][0].rearrange("e (t p) n -> e p t n", p=P)
    sem = ItemSignals(nc)
    loaded = [nc.alloc_semaphore(f"expert_slot{s}_loaded") for s in range(EXPERT_SLOTS)]
    used = [sem.hidden_done if s == 7 else sem.output_done if s == 11 else nc.alloc_semaphore(f"expert_slot{s}_used")
            for s in range(EXPERT_SLOTS)]
    steps = Steps(nc, "item_vector_steps")
    HIGH = 5
    split_slots = (0, 1, 2, 3, 4, 5, 6, 8, 9, 10)
    SPLITS = len(split_slots)
    number_in_turn = {s: k for k, s in enumerate(split_slots)}
    FIRST, LAST = SPLITS - 7, -7
    LINKS = 6
    with ExitStack() as stack:
        def buffer(name, *shape, dt=F32):
            return stack.enter_context(nc.sbuf_tensor(name, [P, *shape], dt))

        x, x_last = buffer("item_x", DT, 2, CAP, dt=F32R), buffer("item_x_last", CAP)
        act_t, act_split = buffer("item_act", DT, CAP), buffer("item_act_split", DT - 2, 2, CAP, dt=F32R)
        hid, y = buffer("item_hidden", 2 * D), buffer("item_y", D)
        sel, gated_sel, gates_t = buffer("item_select", TB, CAP), buffer("item_gated_select", TB, 2, CAP), buffer("item_gates_t", S)
        glu, sig, lin = buffer("item_glu", DT, CAP), buffer("item_sigmoid", DT, CAP), buffer("item_linear", DT, CAP)
        highs = [buffer(f"weights_high{j}", SLOT, dt=F32R)[:, :] for j in range(HIGH - 2)]
        highs += [flat(K.h_low[:, :, :]), flat(K.h_high[:, :, :])]
        block = stack.enter_context(nc.Block())

        def high(s):
            return highs[number_in_turn[s] % HIGH]

        def low(s):
            return ring.part(s)

        def number_of(eng):
            return eng.value_load(M.number[0:1, 0:1], min_val=S * CHOSEN // CAP, max_val=ITEMS - 1)

        def expert_of(eng, i):
            return eng.value_load(M.expert[0:1, bass.ds(i, 1)], min_val=0, max_val=EXPERTS - 1)

        @block.sync
        def _(sp):
            n = number_of(sp)

            def load_first(i):
                e = expert_of(sp, i)
                for s in range(8):
                    if not isinstance(i, int):
                        sp.wait_ge(used[s], i)
                    sp.dma_start(ring.slot(s), w1[bass.ds(e, 1), :, s, :].rearrange("e p n -> p (e n)")).then_inc(loaded[s], 16)

            def load_second(i):
                e = expert_of(sp, sp.snap(i - 1))
                for s in range(8, 12):
                    sp.wait_ge(used[s], i)
                    sp.dma_start(ring.slot(s).rearrange("p (t n) -> p t n", t=2),
                                 w2[bass.ds(e, 1), :, 2 * (s - 8):2 * (s - 8) + 2, :].rearrange("e p t n -> p (e t) n"))\
                        .then_inc(loaded[s], 16)

            load_first(0)
            with sp.Fori(1, n) as i:
                load_first(i)
                load_second(i)
            load_second(n)

        @block.tensor
        def _(pe):
            def gather(i):
                pe.wait_ge(sem.slots_selected, i + 1)
                pe.wait_ge(sem.added, i * 4 + 1)
                for t in range(DT):
                    for b in range(TB):
                        m = nc.tensor.matmul(ps[4][:, t * CAP:(t + 1) * CAP], M.tokens[:, b, t * P:(t + 1) * P],
                                             sel[:, b, :], start=b == 0, stop=b == TB - 1)
                m.then_inc(sem.gathered, 1)

            def wait_split(i, s, shift):
                pe.wait_ge(sem.low_written, i * SPLITS + (number_in_turn[s] + 1 + shift))

            def first_product(i, shift=0):
                pe.wait_ge(sem.low_gathered_written, i + 1)
                for s in range(7):
                    wait_split(i, s, shift)
                    for part, weights in enumerate((high(s), low(s))):
                        for c in range(4):
                            m = nc.tensor.matmul(ps[c][:, :], x[:, s, :, :].rearrange("p two s -> p (two s)"),
                                                 weights[:, c * 512:(c + 1) * 512], start=s == 0 and part == 0,
                                                 stop=s == 6 and part == 1)
                    m.then_inc(used[s], 1)
                pe.wait_ge(loaded[7], i * 16 + 16)
                for c in range(4):
                    m = nc.tensor.matmul(ps[c][0:CAP, :], x_last[:, :], ring.slot(7)[:, c * 512:(c + 1) * 512],
                                         start=False, stop=True, skip_group_check=True)
                m.then_inc(used[7], 1)

            def turn_hidden(i):
                pairs = hid[:, :].rearrange("s (t p two) -> s two t p", two=2, p=P)
                pe.wait_ge(sem.hidden_written, i)
                pe.wait_ge(sem.added, i * 4 + 4)
                for q in range(2):
                    for t in range(DT):
                        m = nc.tensor.matmul(ps[6 - q][:, t * CAP:(t + 1) * CAP], pairs[:, q, t, :], K.const("stacked", CAP),
                                             start=True, stop=True)
                    m.then_inc((sem.gated_turned, sem.linear_turned)[q], 1)
                pe.wait_ge(sem.gate_rows_written, i)
                for b in range(TB):
                    m = nc.tensor.transpose(ps[7][:, b * P:(b + 1) * P], gated_sel[:, b, :, :].rearrange("p two s -> p (two s)"),
                                            K.ident)
                m.then_inc(sem.gates_turned, 1)

            def finish_item(i, shift=0):
                pe.wait_ge(sem.act_written, i)
                for s in range(8, 11):
                    wait_split(i, s, shift)
                    for kk in range(2):
                        k = 2 * (s - 8) + kk
                        for part, weights in enumerate((high(s), low(s))):
                            for c in range(2):
                                m = nc.tensor.matmul(ps[4 + c][:, :], act_split[:, k, :, :].rearrange("p two s -> p (two s)"),
                                                     weights[:, kk * D + c * 512:kk * D + (c + 1) * 512],
                                                     start=k == 0 and part == 0, stop=k == 5 and part == 1)
                    m.then_inc(used[s], 1)
                pe.wait_ge(loaded[11], i * 16)
                for kk in range(2):
                    for c in range(2):
                        m = nc.tensor.matmul(ps[4 + c][0:CAP, :], act_t[:, 6 + kk, :],
                                             ring.slot(11)[:, kk * D + c * 512:kk * D + (c + 1) * 512],
                                             start=False, stop=kk == 1, skip_group_check=True)
                m.then_inc(used[11], 1)
                pe.wait_ge(sem.output_written, i)
                pe.wait_ge(sem.gates_written, i)
                for j in range(4):
                    for half in range(2):
                        t = 2 * j + half
                        m = nc.tensor.matmul(ps[4 + j][:, half * S:(half + 1) * S], y[:, t * P:(t + 1) * P], gates_t[:, :],
                                             start=True, stop=True)
                    m.then_inc(sem.scattered, 1)

            n = number_of(pe)
            pe.sem_inc(sem.scattered, 8)
            for s in range(8, 12):
                pe.sem_inc(used[s], 1)
            gather(0)
            first_product(0, FIRST)
            with pe.Fori(1, n) as i:
                gather(i)
                turn_hidden(i)
                first_product(i)
                finish_item(i)
            turn_hidden(n)
            finish_item(n, LAST)

        def split_vacant(eng, i, s):
            k = number_in_turn[s]
            if k >= HIGH:
                eng.wait_ge(used[split_slots[k - HIGH]], i + 1)
                return
            if isinstance(i, int) and i == 0:
                return
            eng.wait_ge(used[split_slots[k - HIGH + SPLITS]], i)
            if k + HIGH >= number_in_turn[8]:
                eng.wait_ge(used[s], i)

        @block.scalar
        def _(act):
            copy = ACT.Copy

            def write_high(i, *slots):
                for s in slots:
                    split_vacant(act, i, s)
                    act.wait_ge(loaded[s], i * 16 + 16 if s < 8 else i * 16)
                    nc.scalar.activation(high(s), ring.slot(s), copy).then_inc(sem.high_written, 1)

            def write_gathered(i):
                act.wait_ge(sem.gathered, i + 1)
                nc.scalar.activation(x[:, :, 0, :], ps[4][:, :].rearrange("p (t s) -> p t s", t=DT), copy)
                nc.scalar.activation(x_last[:, :], ps[4][:, 7 * CAP:], copy).then_inc(sem.gathered_written, 1)

            def write_hidden(i):
                act.wait_ge(sem.hidden_done, i)
                for c in range(4):
                    m = nc.scalar.activation(hid[:, c * 512:(c + 1) * 512], ps[c][:, :], copy)
                m.then_inc(sem.hidden_written, 1)

            def sigmoid(i):
                act.wait_ge(sem.gated_ready, i)
                nc.scalar.activation(sig[:, :, :], glu[:, :, :], ACT.Sigmoid, scale=1.702).then_inc(sem.sigmoid_written, 1)
                act.wait_ge(sem.gates_turned, i)
                nc.scalar.activation(gates_t[:, :], ps[7][:, 0:S], copy).then_inc(sem.gates_written, 1)

            def write_output(i):
                act.wait_ge(sem.output_done, i)
                for c in range(2):
                    m = nc.scalar.activation(y[:, c * 512:(c + 1) * 512], ps[4 + c][:, :], copy)
                m.then_inc(sem.output_written, 1)

            def turn(i, first=False):
                write_high(i, 0, 1)
                write_hidden(i)
                write_high(i, 2, 3, 4)
                if not first:
                    write_output(i)
                write_gathered(i)
                sigmoid(i)
                write_high(i, 5, 6, 8, 9, 10)

            n = number_of(act)
            act.sem_inc(sem.high_written, FIRST)
            write_high(0, 0, 1, 2, 3, 4)
            write_gathered(0)
            write_high(0, 5, 6)
            turn(1, first=True)
            with act.Fori(2, n) as i:
                turn(i)
            write_hidden(n)
            for s in range(8, 11):
                act.wait_ge(used[s], n)
                act.wait_ge(loaded[s], n * 16)
                nc.scalar.activation(high(s), ring.slot(s), copy).then_inc(sem.high_written, 1)
            write_output(n)
            sigmoid(n)
            write_output(n + 1)

        @block.vector
        def _(dve):
            v = nc.vector
            steps.eng = dve
            link = steps.link

            def select(i):
                for b in range(TB):
                    m = v.tensor_scalar(sel[:, b, :], K.const("iota", CAP), M.rank[:, b, bass.ds(i, 1)], None, ALU.is_equal)
                m.then_inc(sem.slots_selected, 1)

            def leave_low(i, *slots, shift=0):
                for s in slots:
                    dve.wait_ge(sem.high_written, i * SPLITS + (number_in_turn[s] + 1 + shift))
                    v.tensor_tensor(low(s), ring.slot(s), high(s).bitcast(F32), ALU.subtract).then_inc(sem.low_written, 1)

            def write_low_gathered(i):
                dve.wait_ge(sem.gathered_written, i + 1)
                v.tensor_tensor(x[:, :, 1, :], ps[4][:, :].rearrange("p (t s) -> p t s", t=DT),
                                x[:, :, 0, :].bitcast(F32), ALU.subtract).then_inc(sem.low_gathered_written, 1)

            def activate(i):
                before = dve.snap(i - 1)
                bias_at = dve.value_load(M.expert[0:1, bass.ds(before, 1)], min_val=0, max_val=EXPERTS - 1)
                columns = M.b1[:, :].rearrange("p (q t e) -> p q t e", q=2, e=EXPERTS)

                def bias(q):
                    return columns[:, q, :, bass.ds(bias_at, 1)].broadcast_to([P, DT, CAP])

                dve.wait_ge(sem.gated_turned, i)
                link(v.tensor_tensor(glu[:, :, :], ps[6][:, :].rearrange("p (t s) -> p t s", t=DT), bias(0), ALU.add))
                v.tensor_scalar(glu[:, :, :], glu[:, :, :], 7.0, None, ALU.min).then_inc(sem.gated_ready, 1)
                for b in range(TB):
                    m = v.tensor_scalar(gated_sel[:, b, :, :], K.const("iota", CAP).unsqueeze(1).broadcast_to([P, 2, CAP]),
                                        M.rank[:, b, bass.ds(before, 1)], M.gate[:, b, bass.ds(before, 1)],
                                        ALU.is_equal, ALU.mult)
                m.then_inc(sem.gate_rows_written, 1)
                dve.wait_ge(sem.linear_turned, i)
                link(v.tensor_tensor(lin[:, :, :], ps[5][:, :].rearrange("p (t s) -> p t s", t=DT), bias(1), ALU.add))
                link(v.tensor_scalar(lin[:, :, :], lin[:, :, :], -7.0, 7.0, ALU.max, ALU.min))
                dve.wait_ge(sem.gated_ready, i)
                link(v.scalar_tensor_tensor(lin[:, :, :], lin[:, :, :], 1.0, glu[:, :, :], ALU.add, ALU.mult))
                dve.wait_ge(sem.sigmoid_written, i)
                link(v.tensor_tensor(act_t[:, :, :], lin[:, :, :], sig[:, :, :], ALU.mult))
                link(v.tensor_copy(act_split[:, :, 0, :], act_t[:, 0:6, :]))
                v.tensor_tensor(act_split[:, :, 1, :], act_t[:, 0:6, :], act_split[:, :, 0, :].bitcast(F32), ALU.subtract)\
                    .then_inc(sem.act_written, 1)

            def add_scattered(i, shift=0):
                for j in range(4):
                    dve.wait_ge(sem.scattered, i * 4 + (j + 1 + shift))
                    part = M.sum[:, 2 * j:2 * j + 2, :].rearrange("p t s -> p (t s)")
                    v.tensor_tensor(part, ps[4 + j][:, :], part, ALU.add).then_inc(sem.added, 1)

            def turn(i, first=False):
                steps.loop(i, LINKS)
                leave_low(i, 0, 1, 2, 3, 4)
                if not first:
                    add_scattered(i)
                write_low_gathered(i)
                select(i + 1)
                activate(i)
                leave_low(i, 5, 6, 8, 9, 10)
                steps.n = 0

            n = number_of(dve)
            dve.sem_inc(steps.sem, LINKS)
            dve.sem_inc(sem.added, 8)
            dve.sem_inc(sem.low_written, FIRST)
            select(0)
            leave_low(0, 0, 1, 2, 3, 4, shift=FIRST)
            write_low_gathered(0)
            select(1)
            leave_low(0, 5, 6, shift=FIRST)
            turn(1, first=True)
            with dve.Fori(2, n) as i:
                turn(i)
            leave_low(n, 8, 9, 10, shift=LAST)
            add_scattered(n)
            steps.loop(n, LINKS)
            activate(n)
            add_scattered(n, shift=4)


class StickBreaking:

    def __init__(self, K, scale, fail, keep, total):
        self.K, self.scale, self.fail_buffer, self.keep_buffer, self.total = K, scale, fail, keep, total

    def begin(self, K, qb, heads, keys, w, at):
        self.qb, self.heads, self.keys, self.w, self.at = qb, heads, keys, w, at
        self.fail = self.fail_buffer[:, 0:heads * keys].rearrange("p (h k) -> p h k", h=heads)
        self.keep = self.keep_buffer[:, 0:heads * keys].rearrange("p (h k) -> p h k", h=heads)

    def pool(self, pool):
        K, nc = self.K, self.K.nc
        nc.gpsimd.memset(self.keep, 1.0).then_inc(K.pool_done.sem, 1)
        pool.wait_ge(*K.pool_done(1))
        nc.gpsimd.memset(self.keep[:, :, self.keys - 1:self.keys], 0.0).then_inc(K.pool_done.sem, 1)
        pool.wait_ge(*K.exps(2))
        nc.gpsimd.affine_select(out=self.w[:, :, :], in_=self.w[:, :, :], compare_op=ALU.is_gt, fill=0.0,
                                base=self.qb * P, pattern=[[0, self.heads], [-1, self.keys]], channel_multiplier=1)\
            .then_inc(K.weights.sem, 1)

    def act(self, act):
        K, nc = self.K, self.K.nc
        K.asteps.eng = act
        link = K.asteps.link
        act.wait_ge(*K.maxima(1))
        link(nc.scalar.activation(self.fail, self.w[:, :, :], ACT.Abs))
        link(nc.scalar.activation(self.fail, self.fail, ACT.Exp, scale=-1.0))
        nc.scalar.activation(self.fail, self.fail, ACT.Ln, bias=K.ones[:, 0:1]).then_inc(K.exps.sem, 1)
        act.wait_ge(*K.maxima(2))
        nc.scalar.activation(self.w[:, :, :], self.w[:, :, :], ACT.Exp).then_inc(K.exps.sem, 1)

    def dve(self, dve):
        K, v, w, keys, fail = self.K, self.K.nc.vector, self.w, self.keys, self.fail
        link = K.vsteps.link
        per_bank = 512 // keys
        for b, at in enumerate(self.at):
            K.banks.ready(dve, at)
            v.tensor_scalar(w[:, b * per_bank:(b + 1) * per_bank, :].rearrange("p h k -> p (h k)"), K.ps[at[0]][:, :],
                            self.scale, None, ALU.mult).then_inc(K.banks.free[at[0]], 1)
        K.banks.read(dve, self.at[-1])
        v.tensor_copy(K.sums[:, 0:1], K.ones[:, 0:1]).then_inc(K.maxima.sem, 1)
        dve.wait_ge(*K.exps(1))
        link(v.scalar_tensor_tensor(fail, w[:, :, :], 0.0, fail, ALU.max, ALU.add))
        earlier = K.const("earlier", P) if self.qb == 0 else K.earlier_rows
        link(v.scalar_tensor_tensor(fail, fail, -1.0, earlier.unsqueeze(1).broadcast_to([P, self.heads, keys]),
                                    ALU.mult, ALU.mult))
        dve.wait_ge(*K.pool_done(2))
        n = self.heads * keys
        total = self.total[:, 0:n]
        link(v.tensor_tensor_scan(total[:, ::-1], self.keep_buffer[:, 0:n][:, ::-1], self.fail_buffer[:, 0:n][:, ::-1],
                                  0.0, ALU.mult, ALU.add))
        v.tensor_tensor(w[:, :, :], w[:, :, :], total.rearrange("p (h k) -> p h k", h=self.heads), ALU.add)\
            .then_inc(K.maxima.sem, 1)

    def end(self):
        self.K.pool_done.done(2)
        self.K.maxima.done(2)
        self.K.exps.done(2)


def exact_exp(K, x, out, minus_one, s):
    v, link = K.nc.vector, K.vsteps.link
    k, r, power = s
    ln2_hi = 0.693359375
    ln2_lo = math.log(2.0) - ln2_hi
    link(v.tensor_scalar(r, x, -87.0, 88.0, ALU.max, ALU.min))
    link(v.tensor_scalar(k, r, 1.0 / math.log(2.0), ROUND, ALU.mult, ALU.add))
    link(v.tensor_scalar(k, k, ROUND, None, ALU.subtract))
    link(v.scalar_tensor_tensor(r, k, -ln2_hi, r, ALU.mult, ALU.add))
    link(v.scalar_tensor_tensor(r, k, -ln2_lo, r, ALU.mult, ALU.add))
    link(v.tensor_scalar(power, k, 127.0, 2.0 ** 23, ALU.add, ALU.mult))
    link(v.tensor_scalar(k, r, 1.0 / math.factorial(8), None, ALU.mult))
    for n in range(7, 0, -1):
        link(v.scalar_tensor_tensor(k, k, 1.0 / math.factorial(n), r, ALU.add, ALU.mult))
    scale = power.bitcast(F32)
    if out is not None:
        link(v.scalar_tensor_tensor(out, k, 1.0, scale, ALU.add, ALU.mult))
    if minus_one is not None:
        link(v.tensor_tensor(k, k, scale, ALU.mult))
        link(v.scalar_tensor_tensor(minus_one, scale, -1.0, k, ALU.add, ALU.add))


class S5Operands:

    def __init__(self, b, c, phase, decay):
        self.b, self.c, self.phase, self.decay = b, c, phase, decay


def s5_matrices(K, a, T):
    nc, banks = K.nc, K.banks
    J, Q = 16, 4
    in_sem = {n: nc.alloc_semaphore("s5_" + n + "_loaded") for n in ("dt", "b_re", "b_im", "c_re", "c_im")}
    dt_ready, angles, sines, zeroed, natural = (nc.alloc_semaphore("s5_" + n) for n in (
        "dt_rows", "angles_reduced", "sines_written", "zeroed", "natural_ready"))
    dt_at = banks.take(0)
    b_at, c_at = [banks.take(1), banks.take(2)], [banks.take(3), banks.take(4)]
    with ExitStack() as stack:
        def buffer(name, *shape, dt=F32):
            return stack.enter_context(nc.sbuf_tensor(name, list(shape), dt))

        dt_pair, dt_rows = buffer("dt_pairs", J, 2), buffer("dt_rows", J, 2, 64)
        small = {n: buffer("s5_" + n, P, J) for n in (
            "dt", "a", "k", "r", "em1", "sin", "half", "cos", "cosm1", "lre", "lim", "fre", "fim", "inv", "t")}
        power = buffer("s5_power", P, J, dt=I32)
        b_in = [buffer(f"s5_b_in{i}", P, J, 16) for i in range(2)]
        b_tmp = [buffer(f"s5_b_tmp{i}", P, J, 16) for i in range(2)]
        b_nat = [buffer(f"s5_b_natural{i}", P, Q, 4, 2, 16) for i in range(2)]
        c_in = [buffer(f"s5_c_in{i}", P, Q, 2, 64) for i in range(2)]
        block = stack.enter_context(nc.Block())

        @block.sync
        def _(sp):
            sp.dma_start(dt_pair[:, :], a["ssm_log_dt_3"][0].rearrange("(j g) -> j g", g=2)).then_inc(in_sem["dt"], 16)
            for i, n in enumerate(("b_re", "b_im")):
                for g in range(2):
                    sp.dma_start(b_in[i][64 * g:64 * g + 64, :, :], a[f"ssm_{n}_3"][0].rearrange("(j g) n c -> g n j c", g=2)[g])\
                        .then_inc(in_sem[n], 16)
                    sp.wait_ge(in_sem[n], 16 * (g + 1))
            for i, n in enumerate(("c_re", "c_im")):
                for g in range(2):
                    sp.dma_start(c_in[i][:, :, g, :], a[f"ssm_{n}_3"][0].rearrange("(q g) c n -> (g c) q n", q=Q))\
                        .then_inc(in_sem[n], 16)
                    sp.wait_ge(in_sem[n], 16 * (g + 1))

        @block.gpsimd
        def _(pool):
            for i in range(2):
                nc.gpsimd.memset(b_nat[i][:, :, :, :, :], 0.0)
                m = nc.gpsimd.memset(T.c[i][:, :, :, :, :], 0.0)
            m.then_inc(zeroed, 1)

        @block.tensor
        def _(pe):
            pe.wait_ge(dt_ready, 1)
            banks.vacant(pe, dt_at)
            nc.tensor.transpose(K.ps[0][:, 0:J], dt_rows[:, :, :].rearrange("j g n -> j (g n)"), K.ident[0:J, 0:J])\
                .then_inc(banks.full[0], 1)
            for i, n in enumerate(("c_re", "c_im")):
                pe.wait_ge(in_sem[n], 32)
                banks.vacant(pe, c_at[i])
                for q in range(Q):
                    m = nc.tensor.transpose(K.ps[3 + i][:, q * P:(q + 1) * P], c_in[i][:, q, :, :].rearrange("p g n -> p (g n)"),
                                            K.ident)
                m.then_inc(banks.full[3 + i], 1)
            pe.wait_ge(natural, 1)
            for i in range(2):
                banks.vacant(pe, b_at[i])
                for q in range(Q):
                    m = nc.tensor.transpose(K.ps[1 + i][:, q * P:(q + 1) * P],
                                            b_nat[i][:, q, :, :, :].rearrange("p j g c -> p (j g c)"), K.ident)
                m.then_inc(banks.full[1 + i], 1)

        @block.scalar
        def _(act):
            act.wait_ge(angles, 1)
            nc.scalar.activation(small["half"][:, :], T.phase[:, :], ACT.Sin, scale=0.5)
            nc.scalar.activation(small["sin"][:, :], T.phase[:, :], ACT.Sin).then_inc(sines, 1)

        @block.vector
        def _(dve):
            K.vsteps.eng = dve
            link, v = K.vsteps.link, nc.vector
            a_re, a_im = K.param("ssm_a_re", 0, J), K.param("ssm_a_im", 0, J)
            t = {n: b[:, :] for n, b in small.items()}
            scratch = (t["k"], t["r"], power[:, :])
            dve.wait_ge(in_sem["dt"], 16)
            v.tensor_copy(dt_rows[:, :, :], dt_pair[:, :].unsqueeze(2).broadcast_to([J, 2, 64])).then_inc(dt_ready, 1)
            banks.ready(dve, dt_at)
            v.tensor_copy(t["dt"], K.ps[0][:, 0:J]).then_inc(banks.free[0], 1)
            banks.read(dve, dt_at)
            exact_exp(K, t["dt"], t["dt"], None, scratch)
            link(v.tensor_tensor(T.phase[:, :], a_im, t["dt"], ALU.mult))
            link(v.tensor_tensor(t["a"], a_re, t["dt"], ALU.mult))
            reduce_angle(K, dve, T.phase[:, :], t["k"]).then_inc(angles, 1)
            dve.wait_ge(angles, 1)
            exact_exp(K, t["a"], T.decay[:, :], t["em1"], scratch)
            dve.wait_ge(sines, 1)
            link(v.scalar_tensor_tensor(t["cosm1"], t["half"], -2.0, t["half"], ALU.mult, ALU.mult))
            link(v.scalar_tensor_tensor(t["lre"], t["cosm1"], 1.0, t["em1"], ALU.add, ALU.mult))
            link(v.tensor_tensor(t["lre"], t["lre"], t["cosm1"], ALU.add))
            link(v.tensor_tensor(t["lim"], T.decay[:, :], t["sin"], ALU.mult))
            link(v.tensor_tensor(t["inv"], a_re, a_re, ALU.mult))
            link(v.tensor_tensor(t["t"], a_im, a_im, ALU.mult))
            link(v.tensor_tensor(t["inv"], t["inv"], t["t"], ALU.add))
            link(v.reciprocal(t["inv"], t["inv"]))
            for out, p, q, op in (("fre", "lre", "lim", ALU.add), ("fim", "lim", "lre", ALU.subtract)):
                link(v.tensor_tensor(t[out], t[p], a_re, ALU.mult))
                link(v.tensor_tensor(t["t"], t[q], a_im, ALU.mult))
                link(v.tensor_tensor(t[out], t[out], t["t"], op))
                link(v.tensor_tensor(t[out], t[out], t["inv"], ALU.mult))
            for n in ("b_re", "b_im"):
                dve.wait_ge(in_sem[n], 32)
            fre, fim = (t[n].unsqueeze(2).broadcast_to([P, J, 16]) for n in ("fre", "fim"))
            re, im = b_in[0][:, :, :], b_in[1][:, :, :]
            dve.wait_ge(zeroed, 1)
            for i, (p, q, op) in enumerate(((re, im, ALU.subtract), (im, re, ALU.add))):
                link(v.tensor_tensor(b_tmp[0][:, :, :], p, fre, ALU.mult))
                link(v.tensor_tensor(b_tmp[1][:, :, :], q, fim, ALU.mult))
                for g in range(2):
                    rows = slice(64 * g, 64 * g + 64)
                    m = v.tensor_tensor(b_nat[i][rows, :, :, g, :].rearrange("p q j c -> p (q j) c"),
                                        b_tmp[0][rows, :, :], b_tmp[1][rows, :, :], op)
                link(m)
            v.tensor_copy(t["t"], t["inv"]).then_inc(natural, 1)
            for i in range(2):
                banks.ready(dve, c_at[i])
                for g in range(2):
                    rows = slice(64 * g, 64 * g + 64)
                    m = v.tensor_scalar(T.c[i][rows, :, :, g, :], K.ps[3 + i][rows, :].rearrange(
                        "p (q j g c) -> p g q j c", q=Q, j=4, g=2)[:, g], (1.0, -1.0)[i], None, ALU.mult)
                m.then_inc(banks.free[3 + i], 1)
            for i in range(2):
                banks.ready(dve, b_at[i])
                v.tensor_copy(T.b[i][:, :, :].rearrange("p q m -> p (q m)"), K.ps[1 + i][:, :]).then_inc(banks.free[1 + i], 1)


def s5_scan(K, T, u, y):
    nc, banks = K.nc, K.banks
    J, Q = 16, 4
    angles, absolute, tables = (nc.alloc_semaphore("s5_" + n) for n in ("table_angles", "table_abs", "tables_written"))
    bu_written, x_im_written, w_written, s_re_written, s_im_written = (nc.alloc_semaphore("s5_" + n) for n in (
        "bu_written", "x_im_written", "w_written", "s_re_written", "s_im_written"))
    keep_written, y_sum, decays = (nc.alloc_semaphore("s5_" + n) for n in ("pool_part", "y_sums", "decay_rows"))
    bu_at = [[banks.take(b) for b in range(4)] for _ in range(Q)]
    y_at = [banks.take(4 + q) for q in range(Q)]
    memory = K.ring.memory
    cos, sin, work = (memory[:, n * J * S:(n + 1) * J * S].rearrange("p (j t) -> p j t", j=J) for n in range(3))
    rest = memory[:, 3 * J * S:]

    def part(n):
        return rest[:, n * 4 * S:(n + 1) * 4 * S].rearrange("p (j t) -> p j t", j=4)

    bre, bim, xre, xim, wre, wim, decay, t_dve, t_pool = (part(n) for n in range(9))
    sre, sim = xre, xim
    with nc.Block() as block:

        def outputs(pe, q):
            pe.wait_ge(s_re_written, q + 1)
            pe.wait_ge(s_im_written, q + 1)
            banks.vacant(pe, y_at[q])
            for j in range(4):
                for i, s in enumerate((sre, sim)):
                    m = nc.tensor.matmul(K.ps[4 + q][32 * j:32 * j + 32, 0:S], T.c[i][:, q, j, :, :].rearrange("p g c -> p (g c)"),
                                         s[:, j, :], start=i == 0, stop=i == 1)
            m.then_inc(banks.full[4 + q], 1)

        @block.tensor
        def _(pe):
            for q in range(Q):
                for j in range(4):
                    banks.vacant(pe, bu_at[q][j])
                    rows = slice(32 * j, 32 * j + 32)
                    for i in range(2):
                        m = nc.tensor.matmul(K.ps[j][:, i * S:(i + 1) * S], T.b[i][rows, q, :], u[rows, q, :],
                                             start=True, stop=True)
                    m.then_inc(banks.full[j], 1)
                if q:
                    outputs(pe, q - 1)
            outputs(pe, Q - 1)

        @block.scalar
        def _(act):
            act.wait_ge(angles, 1)
            nc.scalar.activation(cos, sin, ACT.Abs).then_inc(absolute, 1)
            act.wait_ge(absolute, 1)
            nc.scalar.activation(cos, cos, ACT.Sin, bias=K.col("half_pi"), scale=-1.0)
            nc.scalar.activation(sin, sin, ACT.Sin).then_inc(tables, 1)
            for q in range(Q):
                if q:
                    act.wait_ge(w_written, q)
                for j in range(4):
                    banks.ready(act, bu_at[q][j])
                    nc.scalar.activation(bre[:, j, :], K.ps[j][:, 0:S], ACT.Copy)
                    nc.scalar.activation(bim[:, j, :], K.ps[j][:, S:2 * S], ACT.Copy).then_inc(banks.free[j], 1)
            act.wait_ge(y_sum, 1)
            nc.scalar.activation(y[:, :, :], y[:, :, :], ACT.Gelu_apprx_tanh)

        def ready_inputs(eng, q):
            for j in range(4):
                banks.read(eng, bu_at[q][j])

        @block.vector
        def _(dve):
            K.vsteps.eng = dve
            link, v = K.vsteps.link, nc.vector
            link(v.tensor_tensor(sin, K.const("times", S).unsqueeze(1).broadcast_to([P, J, S]),
                                 T.phase[:, :].unsqueeze(2).broadcast_to([P, J, S]), ALU.mult))
            reduce_angle(K, dve, sin, work).then_inc(angles, 1)
            dve.wait_ge(tables, 1)
            for q in range(Q):
                c, s = cos[:, 4 * q:4 * q + 4, :], sin[:, 4 * q:4 * q + 4, :]
                ready_inputs(dve, q)
                if q:
                    dve.wait_ge(banks.full[4 + q - 1], y_at[q - 1][2] + 1)
                link(v.tensor_tensor(t_dve, bim, s, ALU.mult))
                link(v.tensor_tensor(xre, bre, c, ALU.mult))
                link(v.tensor_tensor(xre, xre, t_dve, ALU.add))
                link(v.tensor_copy(decay, T.decay[:, 4 * q:4 * q + 4].unsqueeze(2).broadcast_to([P, 4, S])))
                link(v.memset(decay[:, :, 0:1], 0.0))
                if q:
                    dve.wait_ge(s_im_written, q)
                flat = [x.rearrange("p j t -> p (j t)") for x in (decay, xre, xim, wre, wim)]
                v.tensor_tensor_scan(flat[3], flat[0], flat[1], 0.0, ALU.mult, ALU.add)
                dve.wait_ge(x_im_written, q + 1)
                v.tensor_tensor_scan(flat[4], flat[0], flat[2], 0.0, ALU.mult, ALU.add).then_inc(w_written, 1)
                dve.wait_ge(w_written, q + 1)
                link(v.tensor_tensor(t_dve, wim, s, ALU.mult))
                link(v.tensor_tensor(sre, wre, c, ALU.mult))
                v.tensor_tensor(sre, sre, t_dve, ALU.subtract).then_inc(s_re_written, 1)
            for q in range(Q):
                banks.ready(dve, y_at[q])
                v.scalar_tensor_tensor(y[:, q, :], u[:, q, :], K.param("ssm_d", q), K.ps[4 + q][:, 0:S], ALU.mult, ALU.add)\
                    .then_inc(banks.free[4 + q], 1)
            banks.read(dve, y_at[-1])
            v.tensor_copy(K.sums[:, 0:1], K.ones[:, 0:1]).then_inc(y_sum, 1)

        @block.gpsimd
        def _(pool):
            g = nc.gpsimd
            done = [0]

            def link(m):
                done[0] += 1
                m.then_inc(keep_written, 1)
                pool.wait_ge(keep_written, done[0])
            pool.wait_ge(tables, 1)
            for q in range(Q):
                c, s = cos[:, 4 * q:4 * q + 4, :], sin[:, 4 * q:4 * q + 4, :]
                ready_inputs(pool, q)
                if q:
                    pool.wait_ge(banks.full[4 + q - 1], y_at[q - 1][2] + 1)
                link(g.tensor_tensor(t_pool, bre, s, ALU.mult))
                link(g.tensor_tensor(xim, bim, c, ALU.mult))
                g.tensor_tensor(xim, xim, t_pool, ALU.subtract).then_inc(x_im_written, 1)
                pool.wait_ge(w_written, q + 1)
                link(g.tensor_tensor(t_pool, wre, s, ALU.mult))
                link(g.tensor_tensor(sim, wim, c, ALU.mult))
                g.tensor_tensor(sim, sim, t_pool, ALU.add).then_inc(s_im_written, 1)


def s5_gate(K, a, y):
    nc, banks = K.nc, K.banks
    loaded = nc.alloc_semaphore("s5_glu_loaded")
    at = [banks.take(b) for b in range(2)]
    with nc.sbuf_tensor([P, 4, 512], F32) as w, nc.sbuf_tensor([P, 4, S], F32) as gate, nc.Block() as block:

        @block.sync
        def _(sp):
            sp.dma_start(w[:, :, :], a["ssm_w_glu_3"][0].rearrange("(t p) n -> p t n", p=P)).then_inc(loaded, 16)

        @block.tensor
        def _(pe):
            pe.wait_ge(loaded, 16)
            for b in range(2):
                banks.vacant(pe, at[b])
                for i in range(2):
                    t = 2 * b + i
                    for k in range(4):
                        m = nc.tensor.matmul(K.ps[b][:, i * S:(i + 1) * S], w[:, k, t * P:(t + 1) * P], y[:, k, :],
                                             start=k == 0, stop=k == 3)
                m.then_inc(banks.full[b], 1)

        @block.scalar
        def _(act):
            for b in range(2):
                banks.ready(act, at[b])
                for i in range(2):
                    m = nc.scalar.activation(gate[:, 2 * b + i, :], K.ps[b][:, i * S:(i + 1) * S], ACT.Sigmoid,
                                             bias=K.param("ssm_b_glu", 2 * b + i))
                m.then_inc(banks.free[b], 1)

        @block.vector
        def _(dve):
            banks.read(dve, at[0])
            banks.read(dve, at[1])
            nc.vector.tensor_tensor(y[:, :, :], y[:, :, :], gate[:, :, :], ALU.mult)


def two_branches(K, a):
    nc = K.nc
    rmsnorm(K, K.x[:, :, :], K.h, lambda t: K.param("norm_mix_pre", t), DT)
    w_in = a["w_in_3"][0]
    heads = 8
    with ExitStack() as stack:
        def buffer(name, *shape):
            return stack.enter_context(nc.sbuf_tensor(name, [P, *shape], F32))

        gates, u = buffer("branch_gates", 2 * DT, S), buffer("s5_u", 4, S)
        o = buffer("attention_out", 4, S)
        qkv = ExitStack()
        q, k, v = (qkv.enter_context(nc.sbuf_tensor(n, [P, *shape], F32)) for n, shape in (
            ("stick_q", (4, S)), ("stick_k", (4, S)), ("stick_v", (TB, 512))))
        jobs = []

        def copy_to(dst, j):
            return lambda ps: nc.scalar.activation(dst[:, 2 * j:2 * j + 2, :].rearrange("p t s -> p (t s)"), ps[:, :], ACT.Copy)

        def gate(j):
            def finish(ps):
                for i in range(2):
                    m = nc.scalar.activation(gates[:, 2 * j + i, :], ps[:, i * S:(i + 1) * S], ACT.Sigmoid,
                                             bias=K.param("b_gate", 2 * j + i))
                return m
            return finish

        for j in range(16):
            w = w_in[:, j * 256:(j + 1) * 256]
            if j in (4, 5):
                jobs.append((w, True, "act", lambda ps, j=j: nc.scalar.activation(
                    v[:, :, (j - 4) * 256:(j - 3) * 256], ps[:, :].rearrange("p (b n) -> p b n", b=TB), ACT.Copy)))
            else:
                jobs.append((w, False, "act", copy_to((q, k, None, u)[j // 2], j % 2) if j < 8 else gate(j - 8)))
        dense_up(K, K.h, K.h_low, DT, jobs)
        n = heads * S
        fail, keep, total = (K.ring.memory[:, i * n:(i + 1) * n] for i in range(3))
        stick = StickBreaking(K, 64 ** -0.5, fail, keep, total)
        for qb in range(TB):
            keys = (qb + 1) * P
            tokens = slice(qb * P, (qb + 1) * P)

            def rows(h):
                return slice(64 * (h % 2), 64 * (h % 2) + 64)
            attention(K, qb, heads, keys, lambda h: [(q[rows(h), h // 2, tokens], k[rows(h), h // 2, 0:keys])],
                      stick, lambda h, kb, half: v[:, kb, h * 64:(h + 1) * 64], 1,
                      lambda ps: [(o[:, :, tokens], ps[0][:, :].rearrange("p (t q) -> p t q", t=4))],
                      order=(0, 2, 4, 6, 1, 3, 5, 7))
        qkv.close()
        y, T = buffer("s5_y", 4, S), S5Operands(
            b=[buffer(f"s5_b{i}", 4, P) for i in range(2)], c=[buffer(f"s5_c{i}", 4, 4, 2, 16) for i in range(2)],
            phase=buffer("s5_phase", 16), decay=buffer("s5_decay", 16))
        s5_matrices(K, a, T)
        s5_scan(K, T, u, y)
        s5_gate(K, a, y)

        def gated(which, add):
            def finish(dve, j, ps):
                part = gates[:, which * DT + 2 * j:which * DT + 2 * j + 2, :].rearrange("p t s -> p (t s)")
                out = K.h[:, 2 * j:2 * j + 2, :].rearrange("p t s -> p (t s)")
                if not add:
                    return nc.vector.tensor_tensor(out, ps[:, :], part, ALU.mult)
                K.vsteps.link(nc.vector.tensor_tensor(part, ps[:, :], part, ALU.mult))
                return nc.vector.tensor_tensor(out, out, part, ALU.add)
            return finish

        dense_down(K, o, a["w_branch_attn_3"][0], 4, gated(0, False))
        dense_down(K, y, a["w_branch_ssm_3"][0], 4, gated(1, True))
    with nc.sbuf_tensor([P, DT, S], F32) as mixed:
        dense_down(K, K.h, a["w_out_3"][0], DT, store_to(K, mixed))
        rmsnorm(K, mixed[:, :, :], None, lambda t: K.param("norm_mix_post", t), DT, add_to=K.x[:, :, :])


def load_feature_major(K, rows, dst):
    nc, banks = K.nc, K.banks
    loaded = nc.alloc_semaphore("rows_loaded")
    at = [banks.take(4 + j) for j in range(4)]
    with nc.sbuf_tensor([P, TB, D], F32) as tokens, nc.Block() as block:

        @block.sync
        def _(sp):
            sp.dma_start(tokens[:, :, :], rows.rearrange("(b p) d -> p b d", p=P)).then_inc(loaded, 16)

        @block.tensor
        def _(pe):
            pe.wait_ge(loaded, 16)
            transpose_tokens(K, pe, tokens, at)

        @block.scalar
        def _(act):
            for j in range(4):
                banks.ready(act, at[j])
                nc.scalar.activation(dst[:, 2 * j:2 * j + 2, :].rearrange("p t s -> p (t s)"), K.ps[4 + j][:, :],
                                     ACT.Copy).then_inc(banks.free[4 + j], 1)


def cross_attention(K, a):
    nc = K.nc
    heads = 4
    with ExitStack() as stack:
        def buffer(name, *shape):
            return stack.enter_context(nc.sbuf_tensor(name, [P, *shape], F32))

        q, k, v = buffer("cross_q", DT, S), buffer("cross_k", DT, S), buffer("cross_v", TB, D)
        mem = buffer("memory", DT, S)
        mem_low = parts_view(nc, "memory_low", [P, DT, S])
        load_feature_major(K, a["mem_3"][0], mem)
        rmsnorm(K, mem[:, :, :], mem, lambda t: K.param("norm_mem", t), DT)
        dense_down(K, mem, a["xa_wk_3"][0], DT, store_to(K, k))
        w_v = a["xa_wv_3"][0]
        dense_up(K, mem, mem_low, DT, [(w_v[:, j * 256:(j + 1) * 256], True, "act", lambda ps, j=j: nc.scalar.activation(
            v[:, :, j * 256:(j + 1) * 256], ps[:, :].rearrange("p (b n) -> p b n", b=TB), ACT.Copy)) for j in range(4)])
        rmsnorm(K, K.x[:, :, :], K.h, lambda t: K.param("norm_xa_pre", t), DT)
        dense_down(K, K.h, a["xa_wq_3"][0], DT, store_to(K, q))
        for qb in range(TB):
            tokens = slice(qb * P, (qb + 1) * P)
            attention(K, qb, heads, S, lambda h: [(q[:, 2 * h + i, tokens], k[:, 2 * h + i, :]) for i in range(2)],
                      Softmax(256 ** -0.5), lambda h, kb, half: v[:, kb, h * 256 + half * P:h * 256 + (half + 1) * P], 2,
                      lambda ps: [(K.h[:, 4 * i:4 * i + 4, tokens], ps[i][:, :].rearrange("p (t q) -> p t q", t=4))
                                  for i in range(2)])
        dense_down(K, K.h, a["xa_wo_3"][0], DT, store_to(K, q))
        rmsnorm(K, q[:, :, :], None, lambda t: K.param("norm_xa_post", t), DT, add_to=K.x[:, :, :])


def transformer_blocks(nc, a, const, const_at, out):
    K = Kit(nc, const_at, const.shape[1])
    setup(K, a, const)
    for layer in range(2):
        swiglu(K, a["ffn_w_in"][layer, 0], a["ffn_w_out"][layer, 0], 2 * layer * DT)
        (spatial_gate, pool_mixer)[layer](K, a)
        swiglu(K, a["ffn_w_in"][layer, 1], a["ffn_w_out"][layer, 1], (2 * layer + 1) * DT)
    rmsnorm(K, K.x[:, :, :], K.x, lambda t: K.param("final_norm", t), DT)
    adaptive_columns(K, a)
    mixed_attention(K, a)
    experts(K, a)
    two_branches(K, a)
    cross_attention(K, a)
    conv_feed_forward(K, a)
    store_output(K, out)


def kernel(**inputs):
    import concourse.bacc as bacc
    from concourse.bass_utils import run_bass_kernel_spmd

    nc = bacc.Bacc("TRN2", target_bir_lowering=False, num_devices=1)
    table, const_at = constant_table()
    arrays, aps = {}, {}
    for name, value in [*inputs.items(), ("constant_table", table)]:
        arrays[f"in_{name}"] = value = np.ascontiguousarray(value)
        aps[name] = nc.dram_tensor(f"in_{name}", value.shape, mybir.dt.from_np(value.dtype), kind="ExternalInput").ap()
    out = nc.dram_tensor("out", (1, S, D), F32, kind="ExternalOutput").ap()
    transformer_blocks(nc, aps, aps["constant_table"], const_at, out)
    return run_bass_kernel_spmd(nc, [arrays], core_ids=[0]).results[0]["out"]
```

```python
import math
from contextlib import ExitStack

import numpy as np

import concourse.bass as bass
from concourse import mybir

F32 = mybir.dt.float32
F32R = mybir.dt.float32r
I32 = mybir.dt.int32
U32 = mybir.dt.uint32
ALU = mybir.AluOpType
ACT = mybir.ActivationFunctionType
AX = mybir.AxisListType

P = 128
S = 256
D = 1024
DT = D // P
TB = S // P
FF = 2816
SLOT = 2048
SLOTS = 8
HIGHS = 4
EXPERT_SLOTS = SLOTS + HIGHS
EPS = 1e-6
NEG = -1e30
TWO_PI = 2 * math.pi
ROUND = 1.5 * 2.0 ** 23


class Signal:

    def __init__(self, nc, name, primed=0):
        self.sem, self.base = nc.alloc_semaphore(name), primed

    def __call__(self, n):
        return self.sem, self.base + n

    def done(self, n):
        self.base += n


class Steps:

    def __init__(self, nc, name, primed=0):
        self.sem, self.n, self.shift, self.eng = nc.alloc_semaphore(name), primed, 0, None

    def link(self, instruction):
        self.n += 1
        instruction.then_inc(self.sem, 1)
        self.eng.wait_ge(self.sem, self.n + self.shift)

    def loop(self, i, per):
        self.shift, self.at = i * per, self.n

    def end(self, trips, per):
        assert self.n - self.at == per, (self.n - self.at, per)
        self.shift, self.n = 0, self.n + (trips - 1) * per


def parts_view(nc, name, shape):
    size = 4
    for n in shape[1:]:
        size *= n
    return nc.alloc_sbuf_tensor_at(name, shape, F32R, offset=nc.sbuf_base - size)


class Ring:

    def __init__(self, nc, memory, parts):
        self.memory, self.parts = memory, parts
        self.loaded = [nc.alloc_semaphore(f"slot{i}_loaded") for i in range(SLOTS)]
        self.used = [nc.alloc_semaphore(f"slot{i}_used") for i in range(SLOTS)]
        self.fills = [0] * SLOTS
        self.uses = [0] * SLOTS
        self.last = [None] * SLOTS
        self.next = 0

    def slot(self, s):
        return self.memory[:, s * SLOT:(s + 1) * SLOT]

    def part(self, s):
        return self.parts[:, s * SLOT:(s + 1) * SLOT]

    def take(self, trips=1):
        s = self.next
        self.next = (s + 1) % SLOTS
        fill = self.fills[s]
        self.fills[s] += trips
        return s, fill, self.last[s]

    def freed_by_use(self, s, trips=1):
        n = self.uses[s]
        self.uses[s] += trips
        self.last[s] = (self.used[s], n + trips)
        return n

    def freed_by(self, s, semaphore, value):
        self.last[s] = (semaphore, value)

    def vacant(self, eng, unit):
        if unit[2] is not None:
            eng.wait_ge(*unit[2])

    def arrived(self, eng, unit):
        eng.wait_ge(self.loaded[unit[0]], unit[1] * 16 + 16)


class Banks:

    def __init__(self, nc):
        self.ps = [nc.alloc_psum_tensor(f"bank{i}", [P, 512], F32) for i in range(8)]
        self.full = [nc.alloc_semaphore(f"bank{i}_full") for i in range(8)]
        self.free = [nc.alloc_semaphore(f"bank{i}_free") for i in range(8)]
        self.fulls = [0] * 8
        self.frees = [0] * 8

    def take(self, b, trips=1, signals=True):
        at = b, self.frees[b], self.fulls[b]
        self.frees[b] += trips
        if signals:
            self.fulls[b] += trips
        return at

    def vacant(self, eng, at):
        eng.wait_ge(self.free[at[0]], at[1] + 1)

    def ready(self, eng, at):
        eng.wait_ge(self.full[at[0]], at[2] + 1)

    def read(self, eng, at):
        eng.wait_ge(self.free[at[0]], at[1] + 2)


class Kit:

    def __init__(self, nc, const_at, const_width):
        self.nc = nc
        self.const_at = const_at
        self.consts = nc.alloc_sbuf_tensor("consts", [P, const_width], F32)
        shape = [P, EXPERT_SLOTS * SLOT]
        self.ring = Ring(nc, nc.alloc_sbuf_tensor("weight_slots", shape, F32), parts_view(nc, "weight_parts", shape))
        self.h_high = nc.alloc_sbuf_tensor("h_high", [P, DT, S], F32R)
        self.high_written, self.low_written = Signal(nc, "high_parts_written"), Signal(nc, "low_parts_written")
        self.banks = Banks(nc)
        self.ps = self.banks.ps
        self.x = nc.alloc_sbuf_tensor("x_residual", [P, DT, S], F32)
        self.h = nc.alloc_sbuf_tensor("h_normed", [P, DT, S], F32)
        self.h_low = parts_view(nc, "h_low", [P, DT, S])
        self.ident = self.const("ident", P)
        self.ones = self.const("ones", P)
        self.causal_rows = self.const("seen", 2 * P)
        self.earlier_rows = self.const("all_earlier", 2 * P)
        self.negmax = nc.alloc_sbuf_tensor("negative_maxima", [P, 8], F32)
        self.sums = nc.alloc_sbuf_tensor("exponential_sums", [P, 8], F32)
        self.squares = Signal(nc, "squares_written")
        self.hidden, self.gelus = Signal(nc, "hidden_written"), Signal(nc, "gelu_written")
        self.weights = Signal(nc, "attention_weights_written")
        self.maxima = Signal(nc, "maxima_written")
        self.exps = Signal(nc, "exponentials_written")
        self.pool_done = Signal(nc, "pool_steps")
        self.scaled = Signal(nc, "operand_scaled")
        self.vsteps = Steps(nc, "vector_steps")
        self.asteps = Steps(nc, "scalar_steps")

    def const(self, name, width):
        return self.consts[:, self.const_at[name]:self.const_at[name] + width]

    def col(self, name):
        return self.const(name, 1)

    def param(self, name, t=0, n=1):
        at = self.param_at[name] + t
        return self.params[:, bass.ds(at, n)]


def constant_table():
    at, parts = {}, []

    def add(name, a):
        at[name] = sum(p.shape[1] for p in parts)
        parts.append(np.broadcast_to(np.asarray(a, np.float32), (P, np.shape(a)[-1])))

    i = np.arange(P)
    add("ident", np.eye(P))
    add("stacked", np.concatenate([np.eye(P // 2)] * 2))
    add("before", i[:, None] < i[None, :])
    add("upto", i[:, None] <= i[None, :])
    add("iota", i[None, :])
    add("seen", np.zeros((1, P)))
    add("causal", np.where(i[None, :] <= i[:, None], 0.0, NEG))
    add("all_earlier", np.ones((1, P)))
    add("earlier", i[None, :] < i[:, None])
    t = np.arange(1, S + 1)
    for w in (2, 4, 8, 16):
        add(f"per{w}", (1.0 / np.minimum(t, w))[None, :])
    freq = 10000.0 ** (-np.arange(16, dtype=np.float32) / 16)
    add("freq", np.concatenate([np.zeros(64), freq, freq])[None, :])
    add("times", np.arange(S)[None, :])
    add("sign", np.where(i < 80, -1.0, 1.0)[:, None])
    add("ones", np.ones((1, P)))
    add("index", i[:, None])
    add("half_pi", np.full((1, 1), math.pi / 2))
    add("eps", np.full((1, 1), EPS))
    return np.ascontiguousarray(np.concatenate(parts, 1)), at


def parameter_rows(a):
    rows = []

    def add(name, ap, pattern="(r p) -> r p"):
        rows.append((name, ap.rearrange(pattern, p=P)))

    add("ffn_norm", a["ffn_norm"], "a b (r p) -> (a b r) p")
    add("mix_norm", a["mix_norm"], "a (r p) -> (a r) p")
    add("a_v_norm", a["a_v_norm"][0])
    add("b_scale", a["b_scale"][0])
    add("final_norm", a["final_norm"])
    add("c", a["c_2"][0])
    add("b_ada", a["b_ada_2"][0])
    for n in ("g_pre_mix", "g_post_mix", "g_pre_ffn", "g_post_ffn", "g_q_a", "g_kv_a"):
        add(n, a[n + "_2"][0])
    for n in ("norm_mix_pre", "norm_mix_post", "norm_xa_pre", "norm_xa_post", "norm_mem",
              "norm_ffn_pre", "norm_ffn_post", "b_gate", "ssm_d", "ssm_b_glu", "ffn_conv_b"):
        add(n, a[n + "_3"][0])
    add("conv_w", a["ffn_conv_w_3"][0], "w (r p) -> (w r) p")
    rows.append(("ssm_a_re", a["ssm_a_re_3"][0].rearrange("(j g) n -> j (g n)", g=2)))
    rows.append(("ssm_a_im", a["ssm_a_im_3"][0].rearrange("(j g) n -> j (g n)", g=2)))
    return rows



def transpose_tokens(K, pe, src, banks, width=DT):
    nc = K.nc
    for j, at in enumerate(banks):
        b = at[0]
        K.banks.vacant(pe, at)
        for tile in (2 * j, 2 * j + 1):
            for blk in range(TB):
                col = (tile % 2) * S + blk * P
                last = nc.tensor.transpose(K.ps[b][:, col:col + P], src[:, blk, tile * P:(tile + 1) * P], K.ident)
        last.then_inc(K.banks.full[b], 1)


def rmsnorm(K, src, dst, gain, tiles, shift=None, add_to=None, loads=None):
    nc = K.nc
    bank = K.banks.take(7)
    chunks = 4 if tiles == DT else 1
    per = tiles // chunks
    with nc.sbuf_tensor([P, tiles, S], F32) as squares, nc.sbuf_tensor([P, S], F32) as rms, \
            nc.sbuf_tensor([P, S], F32) as rstd, nc.Block() as block:

        @block.sync
        def _(sp):
            if loads is not None:
                loads(sp)

        @block.scalar
        def _(act):
            for c in range(chunks):
                part = slice(c * per, (c + 1) * per)
                nc.scalar.activation(squares[:, part, :], src[:, part, :], ACT.Square).then_inc(K.squares.sem, 1)
            K.banks.ready(act, bank)
            nc.scalar.activation(rms[:, :], K.ps[7][:, 0:S], ACT.Sqrt, bias=K.col("eps"),
                                 scale=1.0 / (tiles * P)).then_inc(K.banks.free[7], 1)

        @block.tensor
        def _(pe):
            K.banks.vacant(pe, bank)
            for t in range(tiles):
                if t % per == 0:
                    pe.wait_ge(*K.squares(t // per + 1))
                last = nc.tensor.matmul(K.ps[7][:, 0:S], K.ones, squares[:, t, :], start=t == 0, stop=t == tiles - 1)
            last.then_inc(K.banks.full[7], 1)

        @block.vector
        def _(dve):
            K.vsteps.eng = dve
            K.banks.read(dve, bank)
            K.vsteps.link(nc.vector.reciprocal(rstd[:, :], rms[:, :]))
            if add_to is None and shift is None:
                for t in range(tiles):
                    nc.vector.scalar_tensor_tensor(dst[:, t, :], src[:, t, :], gain(t), rstd[:, :], ALU.mult, ALU.mult)
                return
            for t in range(tiles):
                last = nc.vector.scalar_tensor_tensor(squares[:, t, :], src[:, t, :], gain(t), rstd[:, :],
                                                      ALU.mult, ALU.mult)
            K.vsteps.link(last)
            if add_to is not None:
                nc.vector.tensor_tensor(add_to, add_to, squares[:, :, :], ALU.add)
            else:
                for t in range(tiles):
                    nc.vector.tensor_scalar(dst[:, t, :], squares[:, t, :], shift(t), None, ALU.add)
    K.squares.done(chunks)


def take_accumulators(K, signals=True):
    return [K.banks.take(b, signals=signals and b == 3) for b in range(4)]


def read_accumulators(K, dve, out, finish):
    K.vsteps.eng = dve
    for j, (b, _, _) in enumerate(out):
        finish(dve, j, K.ps[b]).then_inc(K.banks.free[b], 1)


class DownWeights:

    def __init__(self, K, weights, tiles):
        self.ring, self.tiles, self.view, self.issued = K.ring, tiles, weights.rearrange("(t p) n -> p t n", p=P), False
        self.units, self.uses = [], []
        for u in range(tiles // 2):
            self.units.append(self.ring.take())
            self.uses.append(self.ring.freed_by_use(self.units[-1][0]))

    def issue(self, sp):
        if self.issued:
            return
        self.issued = True
        for u, unit in enumerate(self.units):
            self.ring.vacant(sp, unit)
            sp.dma_start(self.ring.slot(unit[0]).rearrange("p (t n) -> p t n", t=2), self.view[:, 2 * u:2 * u + 2, :])\
                .then_inc(self.ring.loaded[unit[0]], 16)


def dense_down(K, src, weights, finish, following=None):
    nc, ring, banks = K.nc, K.ring, K.banks
    tiles, units, uses = weights.tiles, weights.units, weights.uses
    count = len(units)
    out = take_accumulators(K, signals=False)
    with ExitStack() as stack:
        def buffer():
            return stack.enter_context(nc.sbuf_tensor("source_part", [P, tiles - 2, S], F32R, allow_name_mangling=True))

        low = buffer()
        high = K.h_high[:, 0:tiles - 2, :] if tiles - 2 <= DT else buffer()[:, :, :]
        block = stack.enter_context(nc.Block())

        @block.sync
        def _(sp):
            weights.issue(sp)
            if following is not None:
                following.issue(sp)

        @block.tensor
        def _(pe):
            for at in out:
                banks.vacant(pe, at)
            for u, unit in enumerate(units):
                if u == 0:
                    ring.arrived(pe, unit)
                    m = down_unit(K, ring.slot(unit[0]), lambda kk: src[:, kk, :], True, count == 1)
                else:
                    pe.wait_ge(*K.low_written(max(2, u + 1)))
                    m = down_unit_by_parts(K, (high_place(K, (u - 1) % HIGHS), ring.part(unit[0])),
                                           lambda kk: (high[:, 2 * u - 2 + kk, :], low[:, 2 * u - 2 + kk, :]),
                                           False, u == count - 1)
                m.then_inc(ring.used[unit[0]], 1)

        @block.scalar
        def _(act):
            for u in range(1, count):
                if u > HIGHS:
                    act.wait_ge(ring.used[units[u - HIGHS][0]], uses[u - HIGHS] + 1)
                ring.arrived(act, units[u])
                write_high(K, high_place(K, (u - 1) % HIGHS), ring.slot(units[u][0]))
                if u == 1:
                    write_high(K, high, src[:, 2:, :])

        @block.vector
        def _(dve):
            for u in range(1, count):
                slot = units[u][0]
                leave_low(K, dve, K.high_written(max(1, u + (u > 1))), ring.slot(slot), high_place(K, (u - 1) % HIGHS),
                          ring.part(slot))
                if u == 1:
                    leave_low(K, dve, K.high_written(2), src[:, 2:, :], high, low[:, :, :])
            dve.wait_ge(ring.used[units[-1][0]], uses[-1] + 1)
            read_accumulators(K, dve, out, finish)
    for signal in (K.high_written, K.low_written):
        signal.done(count if count > 1 else 0)


def down_unit(K, slot, moving, first, last):
    for kk in range(2):
        for c in range(DT):
            m = K.nc.tensor.matmul(K.ps[c // 2][:, (c % 2) * S:(c % 2 + 1) * S],
                                   slot[:, kk * D + c * P:kk * D + (c + 1) * P], moving(kk),
                                   start=first and kk == 0 and c % 2 == 0, stop=last and kk == 1,
                                   skip_group_check=True)
    return m


def down_unit_by_parts(K, weights, moving, first, last):
    for kk in range(2):
        for c in range(DT):
            m = multiply_parts(K, K.ps[c // 2][:, (c % 2) * S:(c % 2 + 1) * S],
                               [w[:, kk * D + c * P:kk * D + (c + 1) * P] for w in weights], moving(kk),
                               first and kk == 0 and c % 2 == 0, last and kk == 1, skip_group_check=True)
    return m


def add_residual(K, scale=None):
    def finish(dve, j, ps):
        x = K.x[:, 2 * j:2 * j + 2, :].rearrange("p t s -> p (t s)")
        if scale is None:
            return K.nc.vector.tensor_tensor(x, ps[:, :], x, ALU.add)
        return K.nc.vector.scalar_tensor_tensor(x, ps[:, :], scale, x, ALU.mult, ALU.add)
    return finish


def store_to(K, dst):
    def finish(dve, j, ps):
        return K.nc.vector.tensor_copy(dst[:, 2 * j:2 * j + 2, :].rearrange("p t s -> p (t s)"), ps[:, :])
    return finish



def high_place(K, n):
    return K.ring.part(SLOTS + n)


def write_high(K, high, source):
    K.nc.scalar.activation(high, source, ACT.Copy).then_inc(K.high_written.sem, 1)


def leave_low(K, dve, count, place, high, low):
    dve.wait_ge(*count)
    K.nc.vector.tensor_tensor(low, place, high.bitcast(F32), ALU.subtract)\
        .then_inc(K.low_written.sem, 1)


def flat(x):
    return x.rearrange("p t s -> p (t s)")


def multiply_parts(K, out, stationary, moving, start, stop, **flags):
    parts = ((0, 0), (0, 1), (1, 0))
    for n, (a, b) in enumerate(parts):
        m = K.nc.tensor.matmul(out, stationary[a], moving[b], start=start and n == 0, stop=stop and n == 2, **flags)
    return m


def dense_up(K, src, tiles, jobs, before=None):
    nc, ring, banks = K.nc, K.ring, K.banks
    ahead = 2
    width = tiles * 256
    units, out = [ring.take() for _ in jobs[:SLOTS]], []

    def loads(sp, first=0):
        for (w, _, _, _), unit in list(zip(jobs, units))[first:]:
            ring.vacant(sp, unit)
            sp.dma_start(ring.slot(unit[0])[:, 0:width].rearrange("p (t n) -> p t n", n=256),
                         w.rearrange("(t p) n -> p t n", p=P)).then_inc(ring.loaded[unit[0]], 16)

    if before is not None:
        before(loads)
    issued = len(units) if before is not None else 0
    for j in range(len(jobs)):
        if j >= SLOTS:
            units.append(ring.take())
        out.append(banks.take(4 + j % 4))
        ring.freed_by(units[j][0], banks.full[out[j][0]], out[j][2] + 1)

    def weights(j):
        return ring.slot(units[j][0])[:, 0:width]

    def high(j):
        return high_place(K, j % HIGHS)[:, 0:width]

    def in_order(eng, which, split):
        for j in range(len(jobs) + ahead):
            if j < len(jobs):
                split(j)
            if j >= ahead and jobs[j - ahead][2] == which:
                at = out[j - ahead]
                banks.ready(eng, at)
                jobs[j - ahead][3](K.ps[at[0]]).then_inc(banks.free[at[0]], 1)

    with nc.sbuf_tensor([P, tiles, S], F32R) as low, nc.Block() as block:

        @block.sync
        def _(sp):
            loads(sp, issued)

        @block.tensor
        def _(pe):
            for j, ((_, by_token, _, _), at) in enumerate(zip(jobs, out)):
                banks.vacant(pe, at)
                if j == 0:
                    ring.arrived(pe, units[0])
                    m = up_unit(K, src, weights(0), tiles, K.ps[at[0]], by_token)
                else:
                    pe.wait_ge(*K.low_written(max(2, j + 1)))
                    m = up_unit_by_parts(K, (K.h_high, low), (high(j), ring.part(units[j][0])), tiles, K.ps[at[0]],
                                         by_token)
                m.then_inc(banks.full[at[0]], 1)

        @block.scalar
        def _(act):
            def split(j):
                if j > HIGHS:
                    banks.ready(act, out[j - HIGHS])
                if j:
                    ring.arrived(act, units[j])
                    write_high(K, high(j), weights(j))
                if j == 1:
                    write_high(K, flat(K.h_high[:, :, :]), flat(src[:, :, :]))
            in_order(act, "act", split)

        @block.vector
        def _(dve):
            def split(j):
                if j:
                    leave_low(K, dve, K.high_written(j + (j > 1)), weights(j), high(j), ring.part(units[j][0])[:, 0:width])
                if j == 1:
                    leave_low(K, dve, K.high_written(2), flat(src[:, :, :]), flat(K.h_high[:, :, :]), flat(low[:, :, :]))
            in_order(dve, "dve", split)
    K.high_written.done(len(jobs))
    K.low_written.done(len(jobs))


def up_unit(K, src, slot, tiles, ps, by_token=False):
    for half in range(2):
        for k in range(tiles):
            if by_token:
                a, m = src[:, k, half * P:(half + 1) * P], slot[:, k * 256:(k + 1) * 256]
            else:
                a, m = slot[:, k * 256 + half * P:k * 256 + (half + 1) * P], src[:, k, :]
            last = K.nc.tensor.matmul(ps[:, half * 256:(half + 1) * 256], a, m, start=k == 0, stop=k == tiles - 1)
    return last


def up_unit_by_parts(K, src, weights, tiles, ps, by_token=False):
    for half in range(2):
        for k in range(tiles):
            if by_token:
                a = [x[:, k, half * P:(half + 1) * P] for x in src]
                m = [w[:, k * 256:(k + 1) * 256] for w in weights]
            else:
                a = [w[:, k * 256 + half * P:k * 256 + (half + 1) * P] for w in weights]
                m = [x[:, k, :] for x in src]
            last = multiply_parts(K, ps[:, half * 256:(half + 1) * 256], a, m, k == 0, k == tiles - 1)
    return last


def feed_forward(K, w_in, w_out, middle, finish, before, following=None):
    nc, ring, banks = K.nc, K.ring, K.banks
    pairs = FF // 256
    trips = (pairs - 1) // 2
    w_in_v = w_in.rearrange("(t p) n -> p t n", p=P)
    w_out_v = w_out.rearrange("(t p) n -> p t n", p=P)

    def load_up(sp, unit, column):
        sp.dma_start(ring.slot(unit[0]).rearrange("p (t n) -> p t n", n=256),
                     w_in_v[:, :, bass.ds(column, 256)]).then_inc(ring.loaded[unit[0]], 16)

    up_units = [[ring.take(n) for _ in range(2)] for n in (1, trips, trips)]

    def loads(sp):
        for pair, units in enumerate(up_units):
            for g, unit in enumerate(units):
                ring.vacant(sp, unit)
                load_up(sp, unit, pair * 256 + g * FF)

    before(loads)

    def banks_of(units, first_bank, trips=1):
        at = []
        for unit, b in zip(units, (first_bank, first_bank + 1)):
            at.append(banks.take(b, trips))
            ring.freed_by(unit[0], banks.full[b], at[-1][2] + trips)
        return units, at

    first_up = banks_of(up_units[0], 4)
    loop_up = [banks_of(up_units[1], 6, trips), banks_of(up_units[2], 4, trips)]
    down_trips = (pairs - 3) // HIGHS
    first_down, first_uses = [], []
    for _ in range(pairs - HIGHS * down_trips):
        first_down.append(ring.take())
        first_uses.append(ring.freed_by_use(first_down[-1][0]))
    loop_down, loop_uses = [], []
    for _ in range(HIGHS):
        loop_down.append(ring.take(down_trips))
        loop_uses.append(ring.freed_by_use(loop_down[-1][0], down_trips))
    peeled = len(first_down)
    out = take_accumulators(K, signals=False)
    before_down = 2 * pairs

    next_weights = None if following is None else following()
    shape = [P, FF // P, S]
    with ExitStack() as stack:
        hid = stack.enter_context(nc.sbuf_tensor("hidden", shape, F32, allow_name_mangling=True))
        hid_low = parts_view(nc, f"hidden_low{K.vsteps.n}", shape)
        h_low = stack.enter_context(nc.sbuf_tensor("h_part", [P, DT, S], F32R, allow_name_mangling=True))
        hid_high = stack.enter_context(nc.sbuf_tensor("hidden_high", shape, F32R, allow_name_mangling=True))
        block = stack.enter_context(nc.Block())

        def load_down(sp, u, unit):
            sp.dma_start(ring.slot(unit[0]).rearrange("p (t n) -> p t n", t=2),
                         w_out_v[:, bass.ds(u * 2, 2), :]).then_inc(ring.loaded[unit[0]], 16)

        def loaded(eng, i, unit):
            eng.wait_ge(ring.loaded[unit[0]], i * 16 + (unit[1] * 16 + 16))

        def nth(signal, i, per, n):
            return signal.sem, i * per + (signal.base + n)

        @block.sync
        def _(sp):
            with sp.Fori(1, trips) as i:
                for b, (units, at) in enumerate(loop_up):
                    for g, (unit, bank) in enumerate(zip(units, at)):
                        column = sp.snap(i * 512 + ((1 + b) * 256 + g * FF))
                        sp.wait_ge(banks.full[bank[0]], i + bank[2])
                        load_up(sp, unit, column)
            for u, unit in enumerate(first_down + loop_down):
                ring.vacant(sp, unit)
                load_down(sp, u, unit)
            for i in range(1, down_trips):
                for u, (unit, uses) in enumerate(zip(loop_down, loop_uses)):
                    sp.wait_ge(ring.used[unit[0]], uses + i)
                    load_down(sp, peeled + i * HIGHS + u, unit)
            if next_weights is not None:
                next_weights.issue(sp)

        @block.tensor
        def _(pe):
            def up_parts(i, unit, bank, place, n):
                pe.wait_ge(*nth(K.low_written, i, 4, n))
                pe.wait_ge(banks.free[bank[0]], i + (bank[1] + 1))
                up_unit_by_parts(K, (K.h_high, h_low), (high_place(K, place), ring.part(unit[0])), DT, K.ps[bank[0]])\
                    .then_inc(banks.full[bank[0]], 1)

            def down(i, u, unit, place, first=False, last=False):
                pe.wait_ge(*nth(K.hidden, i, HIGHS, u + 1))
                pe.wait_ge(*nth(K.low_written, i, HIGHS, before_down + u + 1))
                tile = [bass.ds(i * (2 * HIGHS) + (2 * u + kk), 1) for kk in range(2)]
                down_unit_by_parts(K, (high_place(K, place), ring.part(unit[0])),
                                   lambda kk: (hid_high[:, tile[kk], :], hid_low[:, tile[kk], :]),
                                   first, last).then_inc(ring.used[unit[0]], 1)

            (gate, up), (gate_bank, up_bank) = first_up
            ring.arrived(pe, gate)
            banks.vacant(pe, gate_bank)
            up_unit(K, K.h, ring.slot(gate[0]), DT, K.ps[gate_bank[0]]).then_inc(banks.full[gate_bank[0]], 1)
            up_parts(0, up, up_bank, 3, 2)
            with pe.Fori(0, trips) as i:
                for b, (units, at) in enumerate(loop_up):
                    for g in range(2):
                        up_parts(i, units[g], at[g], 2 * b + g, 3 + 2 * b + g)
            for at in out:
                banks.vacant(pe, at)
            for u, unit in enumerate(first_down):
                down(0, u, unit, 1 + u, first=u == 0)
            with pe.Fori(0, down_trips) as i:
                for u, unit in enumerate(loop_down):
                    down(i, peeled + u, unit, u)

        @block.scalar
        def _(act):
            def split(i, unit, place):
                loaded(act, i, unit)
                write_high(K, high_place(K, place), ring.slot(unit[0]))

            split(0, first_up[0][1], 3)
            write_high(K, flat(K.h_high[:, :, :]), flat(K.h[:, :, :]))
            with act.Fori(0, trips) as i:
                for b, (units, at) in enumerate(loop_up):
                    for g in range(2):
                        bank = (at if b == 0 else first_up[1])[g]
                        act.wait_ge(banks.full[bank[0]], i + (bank[2] + b))
                        split(i, units[g], 2 * b + g)
                    middle.act(act, i, b, (first_up[1], loop_up[0][1])[b])
            for u, unit in enumerate(first_down):
                bank, n = (loop_up[0][1][1], trips) if u == 0 else (first_up[1][u - 1], trips + 1)
                act.wait_ge(banks.full[bank[0]], bank[2] + n)
                split(0, unit, 1 + u)
                if u == 0:
                    middle.act(act, trips, 0, first_up[1])
            with act.Fori(0, down_trips) as i:
                for u, (unit, uses) in enumerate(zip(loop_down, loop_uses)):
                    if u:
                        act.wait_ge(ring.used[first_down[u - 1][0]], first_uses[u - 1] + 1)
                    act.wait_ge(ring.used[unit[0]], i + uses)
                    split(i, unit, u)

        @block.vector
        def _(dve):
            K.vsteps.eng = dve

            def split(i, per, n, unit, place):
                leave_low(K, dve, nth(K.high_written, i, per, n), ring.slot(unit[0]), high_place(K, place),
                          ring.part(unit[0]))

            split(0, 0, 1, first_up[0][1], 3)
            leave_low(K, dve, K.high_written(2), flat(K.h[:, :, :]), flat(K.h_high[:, :, :]), flat(h_low[:, :, :]))
            with dve.Fori(0, trips) as i:
                K.vsteps.loop(i, 2 * middle.links)
                for b, (units, at) in enumerate(loop_up):
                    for g in range(2):
                        split(i, 4, 3 + 2 * b + g, units[g], 2 * b + g)
                    middle.dve(dve, i, dve.snap(i * 2 + b), b, (first_up[1], loop_up[0][1])[b], hid, hid_high, hid_low)
                K.vsteps.end(trips, 2 * middle.links)
            for u, unit in enumerate(first_down):
                split(0, 0, before_down + 1 + u, unit, 1 + u)
                if u == 0:
                    middle.dve(dve, trips, pairs - 1, 0, first_up[1], hid, hid_high, hid_low)
            with dve.Fori(0, down_trips) as i:
                for u, unit in enumerate(loop_down):
                    split(i, HIGHS, before_down + 1 + peeled + u, unit, u)
            dve.wait_ge(ring.used[loop_down[-1][0]], loop_uses[-1] + down_trips)
            read_accumulators(K, dve, out, finish)
    for signal in (K.high_written, K.low_written):
        signal.done(before_down + pairs)
    K.hidden.done(pairs)


def split_hidden(K, pair, hid, high, low):
    tiles = bass.ds(pair * 2, 2)
    K.vsteps.link(K.nc.vector.tensor_copy(high[:, tiles, :], hid[:, tiles, :]))
    K.nc.vector.tensor_tensor(low[:, tiles, :], hid[:, tiles, :], high[:, tiles, :].bitcast(F32),
                              ALU.subtract).then_inc(K.hidden.sem, 1)


class SiluGate:
    links = 1

    def __init__(self, K, buffer):
        self.K, self.silu = K, buffer

    def act(self, act, i, b, at):
        K, banks, ((gate, _, gate_full), (up, up_free, _)) = self.K, self.K.banks, at
        act.wait_ge(banks.full[gate], i + (gate_full + 1))
        act.wait_ge(banks.free[up], i + (up_free + 1))
        K.nc.scalar.activation(self.silu[:, b, :], K.ps[gate][:, :], ACT.Silu).then_inc(banks.free[gate], 1)

    def dve(self, dve, i, pair, b, at, hid, high, low):
        K, banks, ((gate, gate_free, _), (up, up_free, up_full)) = self.K, self.K.banks, at
        dve.wait_ge(banks.full[up], i + (up_full + 1))
        dve.wait_ge(banks.free[gate], i + (gate_free + 2))
        K.nc.vector.tensor_tensor(hid[:, bass.ds(pair * 2, 2), :], self.silu[:, b, :].rearrange("p (t s) -> p t s", t=2),
                                  K.ps[up][:, :].rearrange("p (t s) -> p t s", t=2), ALU.mult)\
            .then_inc(banks.free[up], 1)
        dve.wait_ge(banks.free[up], i + (up_free + 2))
        split_hidden(K, pair, hid, high, low)


def swiglu(K, w_in, w_out, norm_at, following=None):
    def norm(loads):
        rmsnorm(K, K.x[:, :, :], K.h, lambda t: K.param("ffn_norm", norm_at + t), DT, loads=loads)

    with K.nc.sbuf_tensor([P, 2, 512], F32) as silu:
        feed_forward(K, w_in, w_out, SiluGate(K, silu), add_residual(K, 0.5), norm, following)


class ConvGate:
    links = 4

    def __init__(self, K, buffer):
        self.K, self.buf = K, buffer

    def act(self, act, i, b, at):
        K, (gate, gate_free, _) = self.K, at[0]
        act.wait_ge(K.banks.free[gate], i + (gate_free + 2))
        part = self.buf[:, b, 0:2, :]
        K.nc.scalar.activation(part, part, ACT.Gelu_apprx_tanh).then_inc(K.gelus.sem, 1)

    def dve(self, dve, i, pair, b, at, hid, high, low):
        K, v, banks, ((gate, _, gate_full), (up, _, up_full)) = self.K, self.K.nc.vector, self.K.banks, at
        dve.wait_ge(banks.full[gate], i + (gate_full + 1))
        dve.wait_ge(banks.full[up], i + (up_full + 1))
        def tile_of(n):
            return dve.snap(pair * 2 + n) if not isinstance(pair, int) else pair * 2 + n

        tiles = [(self.buf[:, b, 2 * g + half, :], K.ps[(gate, up)[g]][:, half * S:(half + 1) * S],
                  tile_of(g * (FF // P) + half)) for g in range(2) for half in range(2)]
        for out, ps, tile in tiles:
            m = v.tensor_scalar(out, ps, K.param("conv_w", tile + 2 * 2 * FF // P), K.param("ffn_conv_b", tile),
                                ALU.mult, ALU.add)
        K.vsteps.link(m)
        for out, ps, tile in tiles:
            m = v.scalar_tensor_tensor(out[:, 1:], ps[:, 0:S - 1], K.param("conv_w", tile + 2 * FF // P), out[:, 1:],
                                       ALU.mult, ALU.add)
        K.vsteps.link(m)
        for n, (out, ps, tile) in enumerate(tiles):
            m = v.scalar_tensor_tensor(out[:, 2:], ps[:, 0:S - 2], K.param("conv_w", tile), out[:, 2:], ALU.mult, ALU.add)
            if n % 2:
                m.then_inc(banks.free[(gate, up)[n // 2]], 1)
        dve.wait_ge(banks.free[up], i + (at[1][1] + 2))
        dve.wait_ge(K.gelus.sem, pair + (K.gelus.base + 1))
        K.vsteps.link(v.tensor_tensor(hid[:, bass.ds(pair * 2, 2), :], self.buf[:, b, 0:2, :], self.buf[:, b, 2:4, :],
                                      ALU.mult))
        split_hidden(K, pair, hid, high, low)


def conv_feed_forward(K, a):
    def norm(loads):
        rmsnorm(K, K.x[:, :, :], K.h, lambda t: K.param("norm_ffn_pre", t), DT, loads=loads)

    with K.nc.sbuf_tensor([P, 2, 4, S], F32) as conv:
        feed_forward(K, a["ffn_w_up_3"][0], a["ffn_w_down_3"][0], ConvGate(K, conv), store_to(K, K.h), norm)
    K.gelus.done(FF // 256)
    rmsnorm(K, K.h[:, :, :], None, lambda t: K.param("norm_ffn_post", t), DT, add_to=K.x[:, :, :])


def setup(K, a, const):
    nc, banks = K.nc, K.banks
    rows = parameter_rows(a)
    total = sum(r.shape[0] for _, r in rows)
    groups = -(-total // P)
    K.params = nc.alloc_sbuf_tensor("params", [P, groups * P], F32)
    K.param_at, at, pieces = {}, 0, []
    for name, r in rows:
        K.param_at[name] = at
        done = 0
        while done < r.shape[0]:
            n = min(r.shape[0] - done, P - at % P)
            pieces.append((at // P, at % P, n, r[done:done + n, :]))
            done, at = done + n, at + n
    param_banks = [banks.take(g) for g in range(-(-groups // 4))]
    x_banks = [banks.take(4 + j) for j in range(4)]
    consts_in, x_in, zeroed = (nc.alloc_semaphore(n) for n in ("consts_in", "x_in", "rows_zeroed"))
    CHAINS = 12
    rows_in = [nc.alloc_semaphore(f"rows_in{i}") for i in range(CHAINS)]
    with nc.sbuf_tensor([P, groups, P], F32) as raw, nc.sbuf_tensor([P, TB, D], F32) as tokens, nc.Block() as block:

        def load_rows(eng, half):
            eng.wait_ge(zeroed, 1)
            for n_piece, (g, p, n, src) in enumerate(pieces):
                k, chain = divmod(n_piece, CHAINS)
                if chain % 2 == half:
                    if k:
                        eng.wait_ge(rows_in[chain], 16 * k)
                    eng.dma_start(raw[p:p + n, g, :], src).then_inc(rows_in[chain], 16)

        @block.sync
        def _(sp):
            sp.dma_start(K.consts[:, :], const).then_inc(consts_in, 16)
            sp.dma_start(tokens[:, :, :], a["x"][0].rearrange("(b p) d -> p b d", p=P)).then_inc(x_in, 16)
            load_rows(sp, 0)

        @block.gpsimd
        def _(pool):
            nc.gpsimd.memset(raw[:, :, :], 0.0).then_inc(zeroed, 1)
            for sem in banks.free:
                pool.sem_inc(sem, 1)

        @block.scalar
        def _(act):
            load_rows(act, 1)
            for j, at in enumerate(x_banks):
                banks.ready(act, at)
                nc.scalar.activation(K.x[:, 2 * j:2 * j + 2, :].rearrange("p t s -> p (t s)"), K.ps[at[0]][:, :],
                                     ACT.Copy).then_inc(banks.free[at[0]], 1)

        @block.tensor
        def _(pe):
            pe.wait_ge(consts_in, 16)
            pe.wait_ge(x_in, 16)
            transpose_tokens(K, pe, tokens, x_banks)
            for chain in range(CHAINS):
                pe.wait_ge(rows_in[chain], 16 * len(pieces[chain::CHAINS]))
            for g in range(groups):
                at = param_banks[g // 4]
                if g % 4 == 0:
                    banks.vacant(pe, at)
                m = nc.tensor.transpose(K.ps[at[0]][:, g % 4 * P:(g % 4 + 1) * P], raw[:, g, :], K.ident)
                if g % 4 == 3 or g == groups - 1:
                    m.then_inc(banks.full[at[0]], 1)

        @block.vector
        def _(dve):
            for k, at in enumerate(param_banks):
                banks.ready(dve, at)
                n = min(4, groups - 4 * k) * P
                nc.vector.tensor_copy(K.params[:, k * 512:k * 512 + n], K.ps[at[0]][:, 0:n])\
                    .then_inc(banks.free[at[0]], 1)


def store_output(K, out):
    nc, banks = K.nc, K.banks
    at = [banks.take(j) for j in range(4)]
    out_written = [nc.alloc_semaphore(f"out_written{b}") for b in range(TB)]
    with nc.sbuf_tensor([P, TB, D], F32) as tokens, nc.Block() as block:

        @block.tensor
        def _(pe):
            for j in range(4):
                banks.vacant(pe, at[j])
                for q in range(4):
                    t, blk = (4 * j + q) % DT, j // 2
                    m = nc.tensor.transpose(K.ps[j][:, q * P:(q + 1) * P], K.x[:, t, blk * P:(blk + 1) * P], K.ident)
                m.then_inc(banks.full[j], 1)

        @block.vector
        def _(dve):
            for j in range(4):
                banks.ready(dve, at[j])
                nc.vector.tensor_copy(tokens[:, j // 2, (j % 2) * 512:(j % 2 + 1) * 512], K.ps[j][:, :])\
                    .then_inc(banks.free[j], 1)

        @block.sync
        def _(sp):
            for blk in range(TB):
                banks.read(sp, at[2 * blk + 1])
                sp.dma_start(out[0, blk * P:(blk + 1) * P, :], tokens[:, blk, :]).then_inc(out_written[blk], 16)
            for blk in range(TB):
                sp.wait_ge(out_written[blk], 16)


def spatial_gate(K, a):
    nc, banks = K.nc, K.banks
    heads, wide = 8, 2048
    tiles = wide // P
    w_in, w_s, b_s = a["a_w_in"][0], a["a_w_s"][0], a["a_b_s"][0]
    mix_in, bias_in = nc.alloc_semaphore("mixing_loaded"), nc.alloc_semaphore("mixing_bias_loaded")
    mixed_steps, v_steps = K.vsteps, K.asteps
    with nc.sbuf_tensor([P, tiles, S], F32) as u, nc.sbuf_tensor([P, TB, wide], F32) as v, \
            nc.sbuf_tensor([P, heads, P], F32) as mix:
        jobs = []
        for j in range(8):
            jobs.append((w_in[:, j * 256:(j + 1) * 256], False, "act", lambda ps, j=j: nc.scalar.activation(
                u[:, 2 * j:2 * j + 2, :].rearrange("p t s -> p (t s)"), ps[:, :], ACT.Gelu_apprx_tanh)))
        for j in range(8):
            jobs.append((w_in[:, wide + j * 256:wide + (j + 1) * 256], True, "act",
                         lambda ps, j=j: nc.scalar.activation(v[:, :, j * 256:(j + 1) * 256],
                                                              ps[:, :].rearrange("p (b n) -> p b n", b=TB),
                                                              ACT.Gelu_apprx_tanh)))
        dense_up(K, K.h, DT, jobs, lambda loads: rmsnorm(
            K, K.x[:, :, :], K.h, lambda t: K.param("mix_norm", t), DT, loads=loads))
        w_out = DownWeights(K, a["a_w_out"][0], tiles)
        mix_at = [banks.take(0), banks.take(1)]
        gate_at = [banks.take(2 + h % 6) for h in range(heads)]
        with nc.sbuf_tensor([P, heads, P], F32) as raw, nc.sbuf_tensor([P, heads, P], F32) as bias, \
                nc.sbuf_tensor([P, wide], F32) as squares, nc.sbuf_tensor([P, TB], F32) as ssq, \
                nc.sbuf_tensor([P, 2, 2, S], F32) as gated, nc.Block() as block:

            @block.sync
            def _(sp):
                sp.dma_start(raw[:, :, :], w_s.rearrange("h t s -> t h s")).then_inc(mix_in, 16)
                sp.dma_start(bias[:, :, :], b_s.unsqueeze(0).broadcast_to([P, heads, P])).then_inc(bias_in, 16)
                w_out.issue(sp)

            @block.scalar
            def _(act):
                v_steps.eng = act
                for b in range(TB):
                    v_steps.link(nc.scalar.activation(squares[:, :], v[:, b, :], ACT.Square, accum_out=ssq[:, b:b + 1]))
                nc.scalar.activation(ssq[:, :], ssq[:, :], ACT.Sqrt, bias=K.col("eps"), scale=1.0 / wide)\
                    .then_inc(K.squares.sem, 1)

            @block.tensor
            def _(pe):
                pe.wait_ge(mix_in, 16)
                for g, at in enumerate(mix_at):
                    banks.vacant(pe, at)
                    for h in range(4):
                        m = nc.tensor.transpose(K.ps[at[0]][:, h * P:(h + 1) * P], raw[:, 4 * g + h, :], K.ident)
                    m.then_inc(banks.full[at[0]], 1)
                banks.read(pe, mix_at[1])
                pe.wait_ge(K.scaled.sem, K.scaled.base + 1)
                for h, at in enumerate(gate_at):
                    banks.vacant(pe, at)
                    for half in range(2):
                        for c in range(TB):
                            m = nc.tensor.matmul(K.ps[at[0]][:, half * S + c * P:half * S + (c + 1) * P],
                                                 v[:, c, h * 256 + half * P:h * 256 + (half + 1) * P], mix[:, h, :],
                                                 start=True, stop=True)
                    m.then_inc(banks.full[at[0]], 1)

            @block.vector
            def _(dve):
                mixed_steps.eng = dve
                for g, at in enumerate(mix_at):
                    banks.ready(dve, at)
                    nc.vector.tensor_tensor(mix[:, 4 * g:4 * g + 4, :],
                                            K.ps[at[0]][:, :].rearrange("p (h t) -> p h t", h=4),
                                            K.const("upto", P).unsqueeze(1).broadcast_to([P, 4, P]), ALU.mult)\
                        .then_inc(banks.free[at[0]], 1)
                dve.wait_ge(*K.squares(1))
                mixed_steps.link(nc.vector.reciprocal(ssq[:, :], ssq[:, :]))
                for b in range(TB):
                    m = nc.vector.tensor_scalar(v[:, b, :], v[:, b, :], ssq[:, b:b + 1], None, ALU.mult)
                m.then_inc(K.scaled.sem, 1)
                dve.wait_ge(bias_in, 16)
                for h, at in enumerate(gate_at):
                    banks.ready(dve, at)
                    for half in range(2):
                        m = nc.vector.scalar_tensor_tensor(
                            gated[:, h % 2, half, :].rearrange("p (c t) -> p c t", c=TB),
                            K.ps[at[0]][:, half * S:(half + 1) * S].rearrange("p (c t) -> p c t", c=TB),
                            K.param("a_v_norm", 2 * h + half),
                            bias[:, h, :].unsqueeze(1).broadcast_to([P, TB, P]), ALU.mult, ALU.add)
                    m.then_inc(banks.free[at[0]], 1)
                    banks.read(dve, at)
                    nc.vector.tensor_tensor(u[:, 2 * h:2 * h + 2, :], u[:, 2 * h:2 * h + 2, :], gated[:, h % 2, :, :],
                                            ALU.mult)
        K.squares.done(1)
        K.scaled.done(1)
        dense_down(K, u, w_out, add_residual(K))


def pool_mixer(K, a):
    nc, banks = K.nc, K.banks
    windows = (2, 4, 8, 16)
    with nc.sbuf_tensor([P, DT, S], F32) as p, nc.sbuf_tensor([P, DT, S], F32) as y:
        w_in, w_out = DownWeights(K, a["b_w_in"][0], DT), DownWeights(K, a["b_w_out"][0], DT)
        rmsnorm(K, K.x[:, :, :], K.h, lambda t: K.param("mix_norm", DT + t), DT, loads=w_in.issue)
        dense_down(K, K.h, w_in, store_to(K, p))
        grp_in = nc.alloc_semaphore("group_weights_loaded")
        group_at = [banks.take(g) for g in range(4)]
        with nc.sbuf_tensor([P, DT, S], F32) as even, nc.sbuf_tensor([P, DT, S], F32) as odd, \
                nc.sbuf_tensor([P, 4, 2, 256], F32) as w, nc.Block() as block:

            @block.sync
            def _(sp):
                sp.dma_start(w[:, :, :, :], a["b_w_grp"][0].rearrange("g (k p) d -> p g k d", p=P)).then_inc(grp_in, 16)
                w_out.issue(sp)

            @block.vector
            def _(dve):
                K.vsteps.eng = dve
                link = K.vsteps.link
                src = p
                for g, window in enumerate(windows):
                    back, dst = window // 2, (even, odd)[g % 2]
                    first = 2 * g
                    nc.vector.tensor_copy(dst[:, first:, 0:back], src[:, first:, 0:back])
                    link(nc.vector.tensor_tensor(dst[:, first:, back:], src[:, first:, back:], src[:, first:, 0:S - back],
                                                 ALU.add))
                    mean = dst[:, first:first + 2, :]
                    link(nc.vector.tensor_tensor(mean, mean, K.const(f"per{window}", S).unsqueeze(1)
                                                 .broadcast_to([P, 2, S]), ALU.mult))
                    nc.vector.tensor_tensor(mean, mean, p[:, first:first + 2, :], ALU.subtract)\
                        .then_inc(K.scaled.sem, 1)
                    src = dst
                for g, at in enumerate(group_at):
                    banks.ready(dve, at)
                    for half in range(2):
                        m = nc.vector.tensor_scalar(y[:, 2 * g + half, :], K.ps[at[0]][:, half * S:(half + 1) * S],
                                                    K.param("b_scale", 2 * g + half), None, ALU.mult)
                    m.then_inc(banks.free[at[0]], 1)

            @block.tensor
            def _(pe):
                pe.wait_ge(grp_in, 16)
                for g, at in enumerate(group_at):
                    pe.wait_ge(*K.scaled(g + 1))
                    banks.vacant(pe, at)
                    pooled = (even, odd)[g % 2]
                    for half in range(2):
                        for k in range(2):
                            m = nc.tensor.matmul(K.ps[at[0]][:, half * S:(half + 1) * S],
                                                 w[:, g, k, half * P:(half + 1) * P], pooled[:, 2 * g + k, :],
                                                 start=k == 0, stop=k == 1)
                    m.then_inc(banks.full[at[0]], 1)
        K.scaled.done(4)
        dense_down(K, y, w_out, add_residual(K))


class AdaptiveWeights:

    def __init__(self, K, a):
        self.ring = K.ring
        self.trips = 6 * D // 256 // SLOTS
        self.view = a["w_ada_2"][0].rearrange("(t p) n -> p t n", p=P)
        self.sums, self.turned = K.nc.alloc_semaphore("ada_sums_written"), K.nc.alloc_semaphore("ada_sums_turned")
        self.units = sorted(K.ring.take(self.trips) for _ in range(SLOTS))
        for b, unit in enumerate(self.units):
            K.ring.freed_by(unit[0], self.turned, 2 + SLOTS // 2 * (self.trips - 1) + b // 2 + 1)

    def load(self, sp, b, column):
        slot = self.units[b][0]
        sp.dma_start(self.ring.slot(slot).rearrange("p (t n) -> p t n", n=256), self.view[:, :, bass.ds(column, 256)])\
            .then_inc(self.ring.loaded[slot], 16)

    def issue(self, sp):
        for b, unit in enumerate(self.units):
            self.ring.vacant(sp, unit)
            self.load(sp, b, b * 256)


def adaptive_columns(K, a, weights):
    nc, ring, banks = K.nc, K.ring, K.banks
    tiles = 6 * DT
    trips, units, sums, turned = weights.trips, weights.units, weights.sums, weights.turned
    pairs = SLOTS // 2
    direct = 2
    at = banks.take(4, signals=False)
    v = nc.vector
    mod = nc.alloc_sbuf_tensor("mod_columns", [P, tiles], F32)
    K.gain1, K.gain2, K.gate1, K.gate2 = (nc.alloc_sbuf_tensor(n, [P, DT], F32) for n in
                                          ("gain_mix", "gain_ffn", "gate_mix", "gate_ffn"))
    K.shift1, K.shift2 = mod[:, 0:DT], mod[:, 3 * DT:4 * DT]
    with nc.sbuf_tensor([P, DT], F32) as cond, nc.sbuf_tensor([P, 2, 512], F32) as part, nc.Block() as block:

        @block.sync
        def _(sp):
            with sp.Fori(1, trips) as i:
                for b in range(SLOTS):
                    column = sp.snap(i * (SLOTS * 256) + b * 256)
                    sp.wait_ge(turned, i * pairs + (b // 2 + 3 - pairs))
                    weights.load(sp, b, column)

        @block.scalar
        def _(act):
            nc.scalar.activation(cond[:, :], K.param("c", 0, DT), ACT.Silu).then_inc(K.squares.sem, 1)

        @block.tensor
        def _(pe):
            banks.vacant(pe, at)
            pe.wait_ge(*K.squares(1))
            with pe.Fori(0, trips) as i:
                for pair in range(pairs):
                    pe.wait_ge(sums, i * pairs + (pair + 1))
                    for unit in units[2 * pair:2 * pair + 2]:
                        pe.wait_ge(ring.loaded[unit[0]], i * 16 + (unit[1] * 16 + 16))
                    for q in range(4):
                        out = K.ps[4][:, bass.ds(i * (4 * pairs) + (4 * pair + q), 1)]
                        slot = ring.slot(units[2 * pair + q // 2][0])
                        for t in range(DT - direct, DT):
                            nc.tensor.matmul(out, slot[:, t * 256 + q % 2 * P:t * 256 + (q % 2 + 1) * P], cond[:, t:t + 1],
                                             start=t == DT - direct, stop=False)
                        m = nc.tensor.matmul(out, part[:, pair % 2, q * P:(q + 1) * P], K.ones[:, 0:1], start=False, stop=True)
                    m.then_inc(turned, 1)

        @block.vector
        def _(dve):
            K.vsteps.eng = dve
            link = K.vsteps.link
            dve.wait_ge(*K.squares(1))
            dve.sem_inc(turned, 2)
            last = DT - direct - 1
            links = last
            with dve.Fori(0, trips) as i:
                K.vsteps.loop(i, links * pairs)
                for pair in range(pairs):
                    first, second = units[2 * pair:2 * pair + 2]
                    both = K.ring.memory[:, first[0] * SLOT:(first[0] + 2) * SLOT].rearrange("p (u t n) -> p u t n", u=2, t=DT)
                    out = part[:, pair % 2, :].rearrange("p (u n) -> p u n", u=2)
                    for unit in (first, second):
                        dve.wait_ge(ring.loaded[unit[0]], i * 16 + (unit[1] * 16 + 16))
                    dve.wait_ge(turned, i * pairs + (pair + 1))
                    link(v.tensor_scalar(out, both[:, :, 0, :], cond[:, 0:1], None, ALU.mult))
                    for t in range(1, last):
                        link(v.scalar_tensor_tensor(out, both[:, :, t, :], cond[:, t:t + 1], out, ALU.mult, ALU.add))
                    v.scalar_tensor_tensor(out, both[:, :, last, :], cond[:, last:last + 1], out, ALU.mult, ALU.add)\
                        .then_inc(sums, 1)
                K.vsteps.end(trips, links * pairs)
            dve.wait_ge(turned, 2 + pairs * trips)
            K.vsteps.link(nc.vector.tensor_tensor(mod[:, :], K.ps[4][:, 0:tiles], K.param("b_ada", 0, tiles), ALU.add))
            for out, g, q in ((K.gain1, "g_pre_mix", 1), (K.gain2, "g_pre_ffn", 4)):
                nc.vector.scalar_tensor_tensor(out[:, :], mod[:, q * DT:(q + 1) * DT], 1.0, K.param(g, 0, DT),
                                               ALU.add, ALU.mult)
            for out, g, q in ((K.gate1, "g_post_mix", 2), (K.gate2, "g_post_ffn", 5)):
                m = nc.vector.tensor_tensor(out[:, :], mod[:, q * DT:(q + 1) * DT], K.param(g, 0, DT), ALU.mult)
            m.then_inc(banks.free[4], 1)
    K.squares.done(1)


def attention(K, qb, heads, keys, scores, weights, values, halves, out, order=range(8),
              loads=None):
    nc, banks = K.nc, K.banks
    blocks = keys // P
    per_bank = 512 // keys
    score_at = [banks.take(b) for b in range(-(-heads // per_bank))]
    turned = heads * blocks
    turned_at = [banks.take(4 + b) for b in range(turned // 4)]
    out_banks = 1 if halves == 1 else 2
    out_at = [banks.take(b) for b in range(out_banks)]
    with nc.sbuf_tensor([P, heads, keys], F32) as w, nc.sbuf_tensor([P, turned, P], F32) as w_t, nc.Block() as block:
        weights.begin(K, qb, heads, keys, w, score_at)

        @block.sync
        def _(sp):
            if loads is not None:
                loads(sp)

        @block.tensor
        def _(pe):
            for b, at in enumerate(score_at):
                banks.vacant(pe, at)
                for h in range(b * per_bank, min(heads, (b + 1) * per_bank)):
                    ops = scores(order[h])
                    col = (h - b * per_bank) * keys
                    for k, (lhs, rhs) in enumerate(ops):
                        m = nc.tensor.matmul(K.ps[at[0]][:, col:col + keys], lhs, rhs, start=k == 0,
                                             stop=k == len(ops) - 1)
                m.then_inc(banks.full[at[0]], 1)
            for b, at in enumerate(turned_at):
                pe.wait_ge(*K.weights(b * weights.parts // len(turned_at) + 1))
                banks.vacant(pe, at)
                for q in range(4):
                    h, kb = divmod(4 * b + q, blocks)
                    m = nc.tensor.transpose(K.ps[at[0]][:, q * P:(q + 1) * P], w[:, h, kb * P:(kb + 1) * P], K.ident)
                m.then_inc(banks.full[at[0]], 1)
            for at in turned_at:
                banks.read(pe, at)
            for at in out_at:
                banks.vacant(pe, at)
            for h in range(heads):
                for half in range(halves):
                    if halves == 1:
                        row, tile = order[h] % 2, order[h] // 2
                        ps = K.ps[0][64 * row:64 * row + 64, tile * P:(tile + 1) * P]
                    else:
                        tile = 2 * h + half
                        ps = K.ps[tile // 4][:, tile % 4 * P:(tile % 4 + 1) * P]
                    for kb in range(blocks):
                        m = nc.tensor.matmul(ps, values(order[h], kb, half), w_t[:, h * blocks + kb, :], start=kb == 0,
                                             stop=kb == blocks - 1)
                if h == heads - 1 or halves == 2 and h % 2:
                    m.then_inc(banks.full[0 if halves == 1 else h // 2], 1)

        @block.scalar
        def _(act):
            weights.act(act)
            for b, at in enumerate(turned_at):
                banks.ready(act, at)
                nc.scalar.activation(w_t[:, 4 * b:4 * b + 4, :].rearrange("p a q -> p (a q)"), K.ps[at[0]][:, :],
                                     ACT.Copy).then_inc(banks.free[at[0]], 1)

        @block.gpsimd
        def _(pool):
            weights.pool(pool)

        @block.vector
        def _(dve):
            K.vsteps.eng = dve
            weights.dve(dve)
            for at, (dst, src) in zip(out_at, out([K.ps[at[0]] for at in out_at])):
                banks.ready(dve, at)
                nc.vector.tensor_copy(dst, src).then_inc(banks.free[at[0]], 1)
    K.weights.done(weights.parts)
    weights.end()


class Softmax:

    def __init__(self, scale, bias=None, slopes=None, distance=None):
        self.scale, self.bias, self.slopes, self.distance = scale, bias, slopes, distance

    def begin(self, K, qb, heads, keys, w, at):
        self.K, self.qb, self.heads, self.keys, self.w, self.at = K, qb, heads, keys, w, at
        self.parts = len(at)
        self.per_bank = heads // self.parts

    def heads_of(self, b):
        return slice(b * self.per_bank, (b + 1) * self.per_bank)

    def pool(self, pool):
        pass

    def act(self, act):
        K, nc = self.K, self.K.nc
        for b in range(self.parts):
            act.wait_ge(*K.maxima(b + 1))
            for h in range(b * self.per_bank, (b + 1) * self.per_bank):
                m = nc.scalar.activation(self.w[:, h, :], self.w[:, h, :], ACT.Exp, bias=K.negmax[:, h:h + 1],
                                         accum_out=K.sums[:, h:h + 1])
            m.then_inc(K.exps.sem, 1)

    def dve(self, dve):
        K, nc, w, keys = self.K, self.K.nc, self.w, self.keys
        link = K.vsteps.link
        if self.slopes is not None:
            for h in range(self.heads):
                m = nc.vector.scalar_tensor_tensor(w[:, h, :], self.distance[:, self.qb, 0:keys], -self.slopes[h],
                                                   self.bias[:, self.qb, 0:keys], ALU.mult, ALU.add)
            link(m)
        for b, at in enumerate(self.at):
            K.banks.ready(dve, at)
            heads = self.heads_of(b)
            ps = K.ps[at[0]][:, 0:self.per_bank * keys].rearrange("p (h k) -> p h k", k=keys)
            part = w[:, heads, :]
            if self.slopes is not None:
                m = nc.vector.scalar_tensor_tensor(part, ps, self.scale, part, ALU.mult, ALU.add)
            elif self.bias is not None:
                m = nc.vector.scalar_tensor_tensor(part, ps, self.scale, self.bias[self.qb].unsqueeze(1)
                                                   .broadcast_to([P, self.per_bank, keys]), ALU.mult, ALU.add)
            else:
                m = nc.vector.tensor_scalar(part, ps, self.scale, None, ALU.mult)
            m.then_inc(K.banks.free[at[0]], 1)
            K.banks.read(dve, at)
            nc.vector.tensor_reduce(K.negmax[:, heads], part, AX.X, ALU.max, negate=True).then_inc(K.maxima.sem, 1)
        for b in range(self.parts):
            heads = self.heads_of(b)
            dve.wait_ge(*K.exps(b + 1))
            link(nc.vector.reciprocal(K.sums[:, heads], K.sums[:, heads]))
            nc.vector.tensor_tensor(w[:, heads, :], w[:, heads, :], K.sums[:, heads].unsqueeze(2)
                                    .broadcast_to([P, self.per_bank, keys]), ALU.mult).then_inc(K.weights.sem, 1)

    def end(self):
        self.K.maxima.done(self.parts)
        self.K.exps.done(self.parts)


def reduce_angle(K, dve, angle, turns):
    nc, link = K.nc, K.vsteps.link
    c1 = 6.28125
    c2 = float(np.float32(np.round((TWO_PI - c1) * 2 ** 21) / 2 ** 21))
    c3 = float(np.float32(TWO_PI - c1 - c2))
    link(nc.vector.tensor_scalar(turns, angle, 1.0 / TWO_PI, ROUND, ALU.mult, ALU.add))
    link(nc.vector.tensor_scalar(turns, turns, ROUND, None, ALU.subtract))
    for c in (c1, c2, c3):
        link(nc.vector.scalar_tensor_tensor(angle, turns, -c, angle, ALU.mult, ALU.add))
    limit = 3.1415925
    return nc.vector.tensor_scalar(angle, angle, limit, -limit, ALU.min, ALU.max)


def mixed_attention(K, a):
    nc, banks = K.nc, K.banks
    heads, width = 8, 1480
    memory = K.ring.memory
    at = [0]

    def part(n, pattern, **sizes):
        at[0] += n
        return memory[:, at[0] - n:at[0]].rearrange(pattern, **sizes)

    w_in = part(DT * width, "p (k n) -> p k n", k=DT)
    w_q = part(2 * 768, "p (k n) -> p k n", k=2)
    w_q_swapped = part(2 * 768, "p (k n) -> p k n", k=2)
    w_kv = part(1024, "p (k n) -> p k n", k=1)
    w_k_swapped = part(DT * 96, "p (k n) -> p k n", k=DT)
    w_q_pairs = part(DT * 512, "p (k n) -> p k n", k=DT)
    w_k_four = part(DT * P, "p (k n) -> p k n", k=DT)
    w_in_loaded = [nc.alloc_semaphore(f"w_in_loaded{i}") for i in range(2)]
    w_q_loaded, w_kv_loaded = nc.alloc_semaphore("w_q_loaded"), nc.alloc_semaphore("w_kv_loaded")

    def loads(sp):
        view = a["w_in_2"][0].rearrange("(t p) n -> p t n", p=P)
        for i in range(2):
            sp.dma_start(w_in[:, 4 * i:4 * i + 4, :], view[:, 4 * i:4 * i + 4, :]).then_inc(w_in_loaded[i], 16)
        sp.dma_start(w_q, a["w_q_b_2"][0].rearrange("(t p) n -> p t n", p=P)).then_inc(w_q_loaded, 16)
        sp.dma_start(w_kv, a["w_kv_b_2"][0].rearrange("(t p) n -> p t n", p=P)).then_inc(w_kv_loaded, 16)

    rmsnorm(K, K.x[:, :, :], K.h, lambda t: K.gain1[:, t:t + 1], DT, shift=lambda t: K.shift1[:, t:t + 1], loads=loads)
    with ExitStack() as stack:
        def buffer(name, *shape):
            return stack.enter_context(nc.sbuf_tensor(name, [P, *shape], F32))

        c_q, c_kv = buffer("c_q", 2, S), buffer("c_kv", 1, S)
        q, k, v = buffer("mla_q", heads, S), buffer("mla_k", heads, S), buffer("mla_v", TB, 512)
        q_d, k_d, v_d = buffer("sparse_q", 4, S), buffer("sparse_k", S), buffer("sparse_v", TB, P)
        q_i, k_i, w_i = buffer("index_q", 2, S), buffer("index_k", S), buffer("index_w", TB, 8)
        mix, cos, sin = buffer("mixed", DT, S), buffer("rotary_cos", S), buffer("rotary_sin", S)
        distance, selected = buffer("distance", TB, S), buffer("selected", TB, S)
        project_inputs(K, a, heads, w_in, w_q, w_q_swapped, w_kv, w_k_swapped, w_q_pairs, w_k_four, c_q, c_kv, k, q_d, k_d, v_d,
                       q_i, k_i, w_i, cos, sin, distance, w_in_loaded, w_q_loaded, w_kv_loaded)
        rmsnorm(K, c_q[:, :, :], c_q, lambda t: K.param("g_q_a", t), 2)
        rmsnorm(K, c_kv[:, :, :], c_kv, lambda t: K.param("g_kv_a", t), 1)
        expand_latents(K, heads, w_q, w_q_swapped, w_kv, c_q, c_kv, cos, sin, q, k, v)
        select_keys(K, q_i, k_i, w_i, selected)
        causal = {0: K.const("causal", P), 1: K.causal_rows}
        w_o = DownWeights(K, a["w_o_2"][0], DT)
        for qb in range(TB):
            keys = (qb + 1) * P
            tokens = slice(qb * P, (qb + 1) * P)
            attention(K, qb, heads, keys, lambda h: [(q[0:96, h, tokens], k[0:96, h, 0:keys])],
                      Softmax(96 ** -0.5, bias=causal), lambda h, kb, half: v[:, kb, h * 64:(h + 1) * 64], 1,
                      lambda ps: [(mix[:, 0:4, tokens], ps[0][:, :].rearrange("p (t q) -> p t q", t=4))], loads=w_o.issue)
            slopes = [2.0 ** (-8.0 * (h + 1) / heads) for h in range(heads)]

            def sparse_scores(h):
                g, j = divmod(h, 4)
                rows = slice(64 * g, 64 * g + 64)
                return [(q_d[rows, j, tokens], k_d[rows, 0:keys])]

            attention(K, qb, heads, keys, sparse_scores,
                      Softmax(64 ** -0.5, bias=selected, slopes=slopes, distance=distance),
                      lambda h, kb, half: v_d[:, kb, (h // 4) * 64:(h // 4 + 1) * 64], 1,
                      lambda ps: [(mix[:, 4:8, tokens], ps[0][:, :].rearrange("p (t q) -> p t q", t=4))])
        dense_down(K, mix, w_o, store_to(K, K.h))
    rmsnorm(K, K.h[:, :, :], None, lambda t: K.gate1[:, t:t + 1], DT, add_to=K.x[:, :, :])


def project_inputs(K, a, heads, w_in, w_q, w_q_swapped, w_kv, w_k_swapped, w_q_pairs, w_k_four, c_q, c_kv, k, q_d, k_d, v_d,
                   q_i, k_i, w_i, cos, sin, distance, w_in_loaded, w_q_loaded, w_kv_loaded):
    nc, banks = K.nc, K.banks
    pos_loaded = nc.alloc_semaphore("positions_loaded")
    arranged = nc.alloc_semaphore("projection_weights_arranged")
    pos_done, angle_done, abs_done = (nc.alloc_semaphore(n) for n in ("positions_float", "angles_reduced", "abs_angle"))
    with nc.sbuf_tensor([P, S], I32) as pos_int, nc.sbuf_tensor([P, S], F32) as pos, \
            nc.sbuf_tensor([P, TB], F32) as pos_col, nc.sbuf_tensor([P, S], F32) as turns, \
            nc.sbuf_tensor([P, 2, S], F32) as k_rope:
        angle_at = [banks.take(7), banks.take(6)]
        result_at = [banks.take(b) for b in range(6)] + [banks.take(6), banks.take(7)]
        with nc.Block() as block:

            @block.sync
            def _(sp):
                sp.dma_start(pos_int[:, :], a["positions_2"].broadcast_to([P, S])).then_inc(pos_loaded, 16)

            @block.tensor
            def _(pe):
                pe.wait_ge(pos_done, 1)
                for b in angle_at:
                    banks.vacant(pe, b)
                nc.tensor.matmul(K.ps[7][0:96, 0:S], K.const("freq", 96)[0:1, :], pos[0:1, :], start=True, stop=True)\
                    .then_inc(banks.full[7], 1)
                for b in range(TB):
                    m = nc.tensor.matmul(K.ps[6][:, b:b + 1], pos[0:1, b * P:(b + 1) * P], K.ones[0:1, 0:1],
                                         start=True, stop=True)
                m.then_inc(banks.full[6], 1)

                def project(ps, cols, by_token=None):
                    for t in range(DT):
                        lhs, rhs = (cols(t), K.h[:, t, :]) if by_token is None else \
                            (K.h[:, t, by_token * P:(by_token + 1) * P], cols(t))
                        m = nc.tensor.matmul(ps, lhs, rhs, start=t == 0, stop=t == DT - 1)
                    return m

                def columns(lo, n):
                    return lambda t: w_in[:, t, lo:lo + n]

                for i in range(2):
                    pe.wait_ge(w_in_loaded[i], 16)
                for at_ in result_at[:6]:
                    banks.vacant(pe, at_)
                ps = K.ps
                project(ps[0][:, 0:S], columns(0, P))
                project(ps[0][:, S:2 * S], columns(P, P)).then_inc(banks.full[0], 1)
                project(ps[1][:, 0:S], columns(256, P))
                project(ps[1][0:96, S:2 * S], columns(320, 96)).then_inc(banks.full[1], 1)
                pe.wait_ge(*K.scaled(1))
                project(ps[2][0:96, 0:S], lambda t: w_k_swapped[:, t, :])
                project(ps[2][:, S:2 * S], columns(928, P)).then_inc(banks.full[2], 1)
                pe.wait_ge(arranged, 1)
                for j in range(4):
                    m = project(ps[3 + j // 2][:, (j % 2) * S:(j % 2 + 1) * S],
                                lambda t: w_q_pairs[:, t, j * P:(j + 1) * P])
                    if j % 2:
                        m.then_inc(banks.full[3 + j // 2], 1)
                for b in range(TB):
                    m = project(ps[5][:, b * P:(b + 1) * P], columns(1056, P), b)
                m.then_inc(banks.full[5], 1)
                for at_ in result_at[6:]:
                    banks.vacant(pe, at_)
                project(ps[6][:, 0:S], columns(1184, P))
                project(ps[6][:, S:2 * S], columns(1312, P)).then_inc(banks.full[6], 1)
                project(ps[7][:, 0:S], lambda t: w_k_four[:, t, :])
                for b in range(TB):
                    m = project(ps[7][:, S + 8 * b:S + 8 * b + 8], columns(1472, 8), b)
                m.then_inc(banks.full[7], 1)
                pe.wait_ge(w_kv_loaded, 16)

            @block.gpsimd
            def _(pool):
                for i in range(2):
                    pool.wait_ge(w_in_loaded[i], 16)
                pairs = w_q_pairs.rearrange("p k (j g d) -> p k j g d", j=4, g=2)
                own = w_in[:, :, 416:928].rearrange("p k (g j d) -> p k g j d", g=2, j=4)
                for j in range(4):
                    nc.gpsimd.tensor_copy(pairs[:, :, j], own[:, :, :, j])
                nc.gpsimd.tensor_copy(w_k_four.rearrange("p k (r d) -> p k r d", r=4),
                                      w_in[:, :, 1440:1472].unsqueeze(2).broadcast_to([P, DT, 4, 32])).then_inc(arranged, 1)

            @block.scalar
            def _(act):
                for b in range(TB):
                    act.wait_ge(*K.maxima(b + 1))
                    nc.scalar.activation(distance[:, b, :], distance[:, b, :], ACT.Abs)
                act.wait_ge(angle_done, 1)
                nc.scalar.activation(turns[0:96, :], sin[0:96, :], ACT.Abs).then_inc(abs_done, 1)
                act.wait_ge(abs_done, 1)
                nc.scalar.activation(cos[0:96, :], turns[0:96, :], ACT.Sin, bias=K.col("half_pi")[0:96, :], scale=-1.0)
                nc.scalar.activation(sin[0:96, :], sin[0:96, :], ACT.Sin).then_inc(abs_done, 1)
                for b, at_, dst, src in (
                        (0, result_at[0], c_q[:, :, :].rearrange("p t s -> p (t s)"), K.ps[0][:, :]),
                        (3, result_at[3], q_d[:, 0:2, :].rearrange("p t s -> p (t s)"), K.ps[3][:, :]),
                        (4, result_at[4], q_d[:, 2:4, :].rearrange("p t s -> p (t s)"), K.ps[4][:, :]),
                        (5, result_at[5], v_d[:, :, :].rearrange("p t s -> p (t s)"), K.ps[5][:, 0:2 * P])):
                    banks.ready(act, at_)
                    nc.scalar.activation(dst, src, ACT.Copy).then_inc(banks.free[b], 1)

            @block.vector
            def _(dve):
                K.vsteps.eng = dve
                link = K.vsteps.link
                dve.wait_ge(pos_loaded, 16)
                nc.vector.tensor_copy(pos[:, :], pos_int[:, :]).then_inc(pos_done, 1)
                for i in range(2):
                    dve.wait_ge(w_in_loaded[i], 16)
                nc.vector.tensor_copy(w_k_swapped[:, :, 0:64], w_in[:, :, 320:384])
                nc.vector.tensor_copy(w_k_swapped[:, :, 64:80], w_in[:, :, 400:416])
                nc.vector.tensor_copy(w_k_swapped[:, :, 80:96], w_in[:, :, 384:400]).then_inc(K.scaled.sem, 1)
                banks.ready(dve, angle_at[0])
                nc.vector.tensor_copy(sin[0:96, :], K.ps[7][0:96, 0:S]).then_inc(banks.free[7], 1)
                banks.ready(dve, angle_at[1])
                nc.vector.tensor_copy(pos_col[:, :], K.ps[6][:, 0:TB]).then_inc(banks.free[6], 1)
                banks.read(dve, angle_at[1])
                for b in range(TB):
                    nc.vector.tensor_scalar(distance[:, b, :], pos[:, :], pos_col[:, b:b + 1], None, ALU.subtract)\
                        .then_inc(K.maxima.sem, 1)
                reduce_angle(K, dve, sin[0:96, :], turns[0:96, :]).then_inc(angle_done, 1)
                dve.wait_ge(w_q_loaded, 16)
                own, swapped = (w.rearrange("p k (h n) -> p (k h) n", n=96) for w in (w_q, w_q_swapped))
                nc.vector.tensor_copy(swapped[:, :, 0:64], own[:, :, 0:64])
                nc.vector.tensor_copy(swapped[:, :, 64:80], own[:, :, 80:96])
                nc.vector.tensor_copy(swapped[:, :, 80:96], own[:, :, 64:80])
                dve.wait_ge(abs_done, 2)
                link(nc.vector.tensor_scalar(sin[0:96, :], sin[0:96, :], K.col("sign")[0:96, :], None, ALU.mult))
                banks.ready(dve, result_at[1])
                nc.vector.tensor_copy(c_kv[:, 0, :], K.ps[1][:, 0:S])
                nc.vector.tensor_tensor(k_rope[64:96, 0, :], K.ps[1][64:96, S:2 * S], cos[64:96, :], ALU.mult)\
                    .then_inc(banks.free[1], 1)
                banks.ready(dve, result_at[2])
                nc.vector.tensor_copy(k_d[:, :], K.ps[2][:, S:2 * S])
                nc.vector.tensor_tensor(k_rope[64:96, 1, :], K.ps[2][64:96, 0:S], sin[64:96, :], ALU.mult)\
                    .then_inc(banks.free[2], 1)
                banks.read(dve, result_at[2])
                for h in range(heads):
                    nc.vector.tensor_tensor(k[64:96, h, :], k_rope[64:96, 0, :], k_rope[64:96, 1, :], ALU.add)
                banks.ready(dve, result_at[6])
                nc.vector.tensor_scalar(q_i[:, :, :].rearrange("p t s -> p (t s)"), K.ps[6][:, :], 32 ** -0.5, None,
                                        ALU.mult).then_inc(banks.free[6], 1)
                banks.ready(dve, result_at[7])
                nc.vector.tensor_copy(k_i[:, :], K.ps[7][:, 0:S])
                nc.vector.tensor_scalar(w_i[:, :, :].rearrange("p b h -> p (b h)"), K.ps[7][:, S:S + 16], 8 ** -0.5,
                                        None, ALU.mult).then_inc(banks.free[7], 1)
        K.scaled.done(1)
        K.maxima.done(TB)


def expand_latents(K, heads, w_q, w_q_swapped, w_kv, c_q, c_kv, cos, sin, q, k, v):
    nc, banks = K.nc, K.banks
    plain_at = [banks.take(b) for b in (0, 1, 2, 3)]
    swapped_at = [banks.take(b) for b in (4, 5, 6, 7)]
    k_at = [banks.take(b) for b in (0, 1, 2, 3)]
    v_at = [banks.take(b) for b in (4, 5)]
    with nc.sbuf_tensor([P, 2, 2, S], F32) as turned, nc.Block() as block:

        @block.tensor
        def _(pe):
            for w, at in ((w_q, plain_at), (w_q_swapped, swapped_at)):
                for j in range(4):
                    banks.vacant(pe, at[j])
                    for i in range(2):
                        h = 2 * j + i
                        for t in range(2):
                            m = nc.tensor.matmul(K.ps[at[j][0]][0:96, i * S:(i + 1) * S], w[:, t, h * 96:(h + 1) * 96],
                                                 c_q[:, t, :], start=t == 0, stop=t == 1)
                    m.then_inc(banks.full[at[j][0]], 1)
            for j in range(4):
                banks.vacant(pe, k_at[j])
                for i in range(2):
                    h = 2 * j + i
                    m = nc.tensor.matmul(K.ps[j][0:64, i * S:(i + 1) * S], w_kv[:, 0, h * P:h * P + 64], c_kv[:, 0, :],
                                         start=True, stop=True)
                m.then_inc(banks.full[j], 1)
            for b, at in enumerate(v_at):
                banks.vacant(pe, at)
                nc.tensor.matmul(K.ps[at[0]][:, :], c_kv[:, 0, b * P:(b + 1) * P],
                                 w_kv[:, 0, :].rearrange("p (h n) -> p h n", h=heads)[:, :, 64:P],
                                 start=True, stop=True).then_inc(banks.full[at[0]], 1)

        @block.vector
        def _(dve):
            K.vsteps.eng = dve
            link = K.vsteps.link

            def table(t):
                return t[64:96, :].unsqueeze(1).broadcast_to([32, 2, S])
            for j in range(4):
                banks.ready(dve, plain_at[j])
                ps = K.ps[j][:, :].rearrange("p (h s) -> p h s", h=2)
                nc.vector.tensor_copy(q[0:64, 2 * j:2 * j + 2, :], ps[0:64])
                nc.vector.tensor_tensor(turned[64:96, 0, :, :], ps[64:96], table(cos), ALU.mult)\
                    .then_inc(banks.free[j], 1)
                banks.ready(dve, swapped_at[j])
                nc.vector.tensor_tensor(turned[64:96, 1, :, :],
                                        K.ps[4 + j][:, :].rearrange("p (h s) -> p h s", h=2)[64:96], table(sin),
                                        ALU.mult).then_inc(banks.free[4 + j], 1)
                banks.read(dve, swapped_at[j])
                link(nc.vector.tensor_tensor(q[64:96, 2 * j:2 * j + 2, :], turned[64:96, 0, :, :],
                                             turned[64:96, 1, :, :], ALU.add))
            for b, at in enumerate(v_at):
                banks.ready(dve, at)
                nc.vector.tensor_copy(v[:, b, :], K.ps[at[0]][:, :]).then_inc(banks.free[at[0]], 1)

        @block.scalar
        def _(act):
            for j in range(4):
                banks.ready(act, k_at[j])
                nc.scalar.activation(k[0:64, 2 * j:2 * j + 2, :], K.ps[j][0:64, :].rearrange("p (h s) -> p h s", h=2),
                                     ACT.Copy).then_inc(banks.free[j], 1)


def select_keys(K, q_i, k_i, w_i, selected):
    nc, banks = K.nc, K.banks
    taken = -3e38
    at = [[banks.take(4 * (qb % 2) + r) for r in range(4)] for qb in range(TB)]
    with nc.sbuf_tensor([P, TB, 8, S], F32) as rel, nc.sbuf_tensor([P, TB, S], F32) as score, \
            nc.sbuf_tensor([P, TB, 8], F32) as top, nc.Block() as block:

        @block.tensor
        def _(pe):
            for qb in range(TB):
                keys = (qb + 1) * P
                for r in range(4):
                    banks.vacant(pe, at[qb][r])
                    for i in range(2):
                        rows = slice(32 * r, 32 * r + 32)
                        m = nc.tensor.matmul(K.ps[at[qb][r][0]][:, i * keys:(i + 1) * keys],
                                             q_i[rows, i, qb * P:(qb + 1) * P], k_i[rows, 0:keys], start=True, stop=True)
                    m.then_inc(banks.full[at[qb][r][0]], 1)

        @block.scalar
        def _(act):
            for qb in range(TB):
                keys = (qb + 1) * P
                for r in range(4):
                    banks.ready(act, at[qb][r])
                    nc.scalar.activation(rel[:, qb, 2 * r:2 * r + 2, 0:keys],
                                         K.ps[at[qb][r][0]][:, 0:2 * keys].rearrange("p (h s) -> p h s", h=2),
                                         ACT.Relu).then_inc(banks.free[at[qb][r][0]], 1)

        @block.vector
        def _(dve):
            K.vsteps.eng = dve
            link = K.vsteps.link
            for qb in range(TB):
                keys = (qb + 1) * P
                acc = score[:, qb, 0:keys]
                for r in range(4):
                    banks.read(dve, at[qb][r])
                    for i in range(2):
                        w = w_i[:, qb, 4 * i + r:4 * i + r + 1]
                        part = rel[:, qb, 2 * r + i, 0:keys]
                        if r == i == 0:
                            link(nc.vector.tensor_scalar(acc, part, w, 0.0, ALU.mult, ALU.add))
                        else:
                            link(nc.vector.scalar_tensor_tensor(acc, part, w, acc, ALU.mult, ALU.add))
                causal = K.const("causal", P) if qb == 0 else K.causal_rows
                link(nc.vector.tensor_tensor(acc, acc, causal, ALU.add))
                for _ in range(64 // 8):
                    link(nc.vector.max(top[:, qb, :], acc))
                    link(nc.vector.match_replace(acc, top[:, qb, :], acc, taken))
                link(nc.vector.tensor_scalar(acc, acc, taken / 2, NEG, ALU.is_gt, ALU.mult))
                nc.vector.tensor_tensor(selected[:, qb, 0:keys], acc, causal, ALU.add)


EXPERTS, CHOSEN = 32, 4
CAP = 64
ITEMS = 48


def route(K, a, M):
    nc, banks = K.nc, K.banks
    router_in, bias_in, b1_in, b2_in = (nc.alloc_semaphore(n) for n in (
        "router_loaded", "router_bias_loaded", "expert_b1_loaded", "expert_b2_loaded"))
    chosen, softmaxed, tables = (nc.alloc_semaphore(n) for n in ("experts_chosen", "gates_exp", "item_tables"))
    logits_at = banks.take(0)
    token_at = [banks.take(4 + j) for j in range(4)]
    rank_at, turn_at, start_at, item_at, b1_at = banks.take(1), banks.take(2), banks.take(3), banks.take(0), banks.take(1)
    b2_at = [banks.take(4 + j) for j in range(4)]
    E = EXPERTS
    with ExitStack() as stack:
        def buffer(name, *shape, dt=F32):
            return stack.enter_context(nc.sbuf_tensor(name, list(shape), dt))

        w, bias = buffer("router_w", P, DT, E), buffer("router_b", P, E)
        b1, b2 = buffer("b1_rows", E, 2 * D), buffer("b2_rows", E, D)
        logits, top, negtop = buffer("logits", P, TB, E), buffer("top_logits", P, TB, 8), buffer("neg_top", P, TB)
        index_u, index = buffer("top_index", P, TB, 8, dt=U32), buffer("top_index_f", P, TB, 8)
        gates4, total = buffer("gates4", P, TB, CHOSEN), buffer("gate_sums", P, TB)
        hit, mask, gates = buffer("hit", P, TB, E), buffer("expert_mask", P, TB, E), buffer("expert_gates", P, TB, E)
        ranks = buffer("ranks", P, TB, E)
        rank_t, gate_t = buffer("rank_t", E, S), buffer("gate_t", E, S)
        count, items, over, start = (buffer(n, E, 1) for n in ("expert_counts", "expert_items", "over", "first_item"))
        since, inside, offset = (buffer(n, E, ITEMS) for n in ("since_first", "item_of_expert", "slot_offset"))
        block = stack.enter_context(nc.Block())

        @block.sync
        def _(sp):
            sp.dma_start(w[:, :, :], a["w_router_2"][0].rearrange("(t p) n -> p t n", p=P)).then_inc(router_in, 16)
            sp.dma_start(bias[:, :], a["b_router_2"].broadcast_to([P, E])).then_inc(bias_in, 16)
            sp.dma_start(b1[:, :], a["b_mlp1_2"][0]).then_inc(b1_in, 16)
            sp.dma_start(b2[:, :], a["b_mlp2_2"][0]).then_inc(b2_in, 16)
            w1 = a["w_mlp1_2"][0, 0].rearrange("(t p) n -> p t n", p=P)
            w2 = a["w_mlp2_2"][0, 0].rearrange("(t p) n -> p t n", p=P)
            for s in range(8):
                sp.dma_start(K.ring.slot(s), w1[:, s, :]).then_inc(M.loaded[s], 16)
            for s in range(8, EXPERT_SLOTS):
                sp.dma_start(K.ring.slot(s).rearrange("p (t n) -> p t n", t=2), w2[:, 2 * s - 16:2 * s - 14, :])\
                    .then_inc(M.loaded[s], 16)

        @block.tensor
        def _(pe):
            ps = K.ps
            pe.wait_ge(router_in, 16)
            banks.vacant(pe, logits_at)
            for b in range(TB):
                for t in range(DT):
                    m = nc.tensor.matmul(ps[0][:, b * E:(b + 1) * E], K.h[:, t, b * P:(b + 1) * P], w[:, t, :],
                                         start=t == 0, stop=t == DT - 1)
            m.then_inc(banks.full[0], 1)
            for j, at in enumerate(token_at):
                banks.vacant(pe, at)
                for q in range(4):
                    t = 4 * (j % 2) + q
                    m = nc.tensor.transpose(ps[4 + j][:, q * P:(q + 1) * P], K.h[:, t, j // 2 * P:(j // 2 + 1) * P], K.ident)
                m.then_inc(banks.full[4 + j], 1)
            pe.wait_ge(chosen, 1)
            banks.vacant(pe, rank_at)
            before = K.const("before", P)
            nc.tensor.matmul(ps[1][:, 0:E], before, mask[:, 0, :], start=True, stop=True)
            nc.tensor.matmul(ps[1][:, E:2 * E], before, mask[:, 1, :], start=True, stop=False)
            nc.tensor.matmul(ps[1][:, E:2 * E], K.ones, mask[:, 0, :], start=False, stop=True)
            for b in range(TB):
                m = nc.tensor.matmul(ps[1][0:E, 2 * E:2 * E + 1], mask[:, b, :], K.ones[:, 0:1], start=b == 0, stop=b == TB - 1)
            m.then_inc(banks.full[1], 1)
            pe.wait_ge(chosen, 2)
            banks.vacant(pe, turn_at)
            for b in range(TB):
                nc.tensor.transpose(ps[2][0:E, b * P:(b + 1) * P], ranks[:, b, :], K.ident)
                m = nc.tensor.transpose(ps[2][0:E, S + b * P:S + (b + 1) * P], gates[:, b, :], K.ident)
            m.then_inc(banks.full[2], 1)
            pe.wait_ge(chosen, 3)
            banks.vacant(pe, start_at)
            nc.tensor.matmul(ps[3][0:E, 0:1], before[0:E, 0:E], items[:, :], start=True, stop=True)
            nc.tensor.matmul(ps[3][0:1, 1:2], items[:, :], K.ones[0:E, 0:1], start=True, stop=True)\
                .then_inc(banks.full[3], 1)
            pe.wait_ge(b1_in, 16)
            banks.vacant(pe, b1_at)
            pairs = b1[:, :].rearrange("e (t p two) -> e two t p", two=2, p=P)
            for q in range(2 * DT):
                m = nc.tensor.transpose(ps[1][:, q * E:(q + 1) * E], pairs[:, q // DT, q % DT, :], K.ident[0:E, 0:E])
            m.then_inc(banks.full[1], 1)
            pe.wait_ge(tables, 1)
            banks.vacant(pe, item_at)
            for b in range(TB):
                tokens = slice(b * P, (b + 1) * P)
                nc.tensor.matmul(ps[0][:, b * ITEMS:(b + 1) * ITEMS], rank_t[:, tokens], inside[:, :], start=True, stop=False)
                nc.tensor.matmul(ps[0][:, b * ITEMS:(b + 1) * ITEMS], K.ones[0:E, :], offset[:, :], start=False, stop=True)
                nc.tensor.matmul(ps[0][:, (2 + b) * ITEMS:(3 + b) * ITEMS], gate_t[:, tokens], inside[:, :], start=True, stop=True)
            nc.tensor.matmul(ps[0][0:1, 4 * ITEMS:5 * ITEMS], K.col("index")[0:E, :], inside[:, :], start=True, stop=True)\
                .then_inc(banks.full[0], 1)
            pe.wait_ge(b2_in, 16)
            for j, at in enumerate(b2_at):
                banks.vacant(pe, at)
                for i in range(2):
                    t = 2 * j + i
                    m = nc.tensor.matmul(ps[4 + j][:, i * S:(i + 1) * S], b2[:, t * P:(t + 1) * P], gate_t[:, :],
                                         start=True, stop=True)
                m.then_inc(banks.full[4 + j], 1)

        @block.scalar
        def _(act):
            for j, at in enumerate(token_at):
                banks.ready(act, at)
                nc.scalar.activation(M.tokens[:, j // 2, (j % 2) * 512:(j % 2 + 1) * 512], K.ps[4 + j][:, :], ACT.Copy)\
                    .then_inc(banks.free[4 + j], 1)
            act.wait_ge(softmaxed, 1)
            for b in range(TB):
                m = nc.scalar.activation(gates4[:, b, :], top[:, b, 0:CHOSEN], ACT.Exp, bias=negtop[:, b:b + 1],
                                         accum_out=total[:, b:b + 1])
            m.then_inc(softmaxed, 1)

        @block.vector
        def _(dve):
            K.vsteps.eng = dve
            link, v = K.vsteps.link, nc.vector
            dve.wait_ge(bias_in, 16)
            banks.ready(dve, logits_at)
            v.tensor_tensor(logits[:, :, :], K.ps[0][:, 0:TB * E].rearrange("p (b e) -> p b e", b=TB),
                            bias[:, :].unsqueeze(1).broadcast_to([P, TB, E]), ALU.add).then_inc(banks.free[0], 1)
            banks.read(dve, logits_at)
            for b in range(TB):
                link(v.max(top[:, b, :], logits[:, b, :]))
                link(v.max_index(index_u[:, b, :], top[:, b, :], logits[:, b, :]))
            v.tensor_scalar(negtop[:, :], top[:, :, 0], -1.0, None, ALU.mult).then_inc(softmaxed, 1)
            link(v.tensor_copy(index[:, :, :], index_u[:, :, :]))
            dve.wait_ge(softmaxed, 2)
            link(v.reciprocal(total[:, :], total[:, :]))
            link(v.tensor_tensor(gates4[:, :, :], gates4[:, :, :], total[:, :].unsqueeze(2).broadcast_to([P, TB, CHOSEN]), ALU.mult))
            number = K.const("iota", E)
            for b in range(TB):
                for k in range(CHOSEN):
                    pick = index[:, b, k:k + 1]
                    if k == 0:
                        v.tensor_scalar(mask[:, b, :], number, pick, None, ALU.is_equal)
                        link(v.tensor_scalar(gates[:, b, :], number, pick, gates4[:, b, k:k + 1], ALU.is_equal, ALU.mult))
                        continue
                    v.scalar_tensor_tensor(mask[:, b, :], number, pick, mask[:, b, :], ALU.is_equal, ALU.add)
                    link(v.tensor_scalar(hit[:, b, :], number, pick, gates4[:, b, k:k + 1], ALU.is_equal, ALU.mult))
                    link(v.tensor_tensor(gates[:, b, :], gates[:, b, :], hit[:, b, :], ALU.add))
            v.tensor_copy(hit[:, :, :], mask[:, :, :]).then_inc(chosen, 1)
            banks.ready(dve, rank_at)
            link(v.tensor_copy(count[:, :], K.ps[1][0:E, 2 * E:2 * E + 1]))
            link(v.scalar_tensor_tensor(ranks[:, :, :], K.ps[1][:, 0:TB * E].rearrange("p (b e) -> p b e", b=TB), 1000.0,
                                        mask[:, :, :], ALU.add, ALU.mult))
            v.tensor_scalar(ranks[:, :, :], ranks[:, :, :], -1000.0, None, ALU.add).then_inc(banks.free[1], 1)
            banks.read(dve, rank_at)
            v.tensor_copy(hit[:, :, :], ranks[:, :, :]).then_inc(chosen, 1)
            link(v.tensor_copy(items[:, :], K.ones[0:E, 0:1]))
            for r in range(1, S // CAP):
                link(v.tensor_scalar(over[:, :], count[:, :], float(r * CAP), None, ALU.is_gt))
                link(v.tensor_tensor(items[:, :], items[:, :], over[:, :], ALU.add))
            v.tensor_copy(over[:, :], items[:, :]).then_inc(chosen, 1)
            banks.ready(dve, turn_at)
            v.tensor_copy(rank_t[:, :], K.ps[2][0:E, 0:S])
            v.tensor_copy(gate_t[:, :], K.ps[2][0:E, S:2 * S]).then_inc(banks.free[2], 1)
            banks.ready(dve, start_at)
            link(v.tensor_copy(start[:, :], K.ps[3][0:E, 0:1]))
            v.tensor_copy(M.number[0:1, :], K.ps[3][0:1, 1:2]).then_inc(banks.free[3], 1)
            item = K.const("iota", ITEMS)[0:E, :]
            link(v.tensor_scalar(since[:, :], item, start[:, :], None, ALU.subtract))
            link(v.tensor_scalar(inside[:, :], since[:, :], 0.0, None, ALU.is_ge))
            link(v.scalar_tensor_tensor(inside[:, :], since[:, :], items[:, :], inside[:, :], ALU.is_lt, ALU.mult))
            banks.read(dve, turn_at)
            v.scalar_tensor_tensor(offset[:, :], since[:, :], -float(CAP), inside[:, :], ALU.mult, ALU.mult)\
                .then_inc(tables, 1)
            banks.ready(dve, b1_at)
            v.tensor_copy(M.b1[:, :], K.ps[1][:, :]).then_inc(banks.free[1], 1)
            banks.ready(dve, item_at)
            v.tensor_copy(M.rank[:, :, :], K.ps[0][:, 0:2 * ITEMS].rearrange("p (b j) -> p b j", b=TB))
            v.tensor_copy(M.gate[:, :, :], K.ps[0][:, 2 * ITEMS:4 * ITEMS].rearrange("p (b j) -> p b j", b=TB))
            v.tensor_copy(M.expert[0:1, :], K.ps[0][0:1, 4 * ITEMS:5 * ITEMS]).then_inc(banks.free[0], 1)
            for j, at in enumerate(b2_at):
                banks.ready(dve, at)
                v.tensor_copy(M.sum[:, 2 * j:2 * j + 2, :].rearrange("p t s -> p (t s)"), K.ps[4 + j][:, :])\
                    .then_inc(banks.free[4 + j], 1)


def experts(K, a):
    nc = K.nc
    rmsnorm(K, K.x[:, :, :], K.h, lambda t: K.gain2[:, t:t + 1], DT, shift=lambda t: K.shift2[:, t:t + 1])
    with ExitStack() as stack:
        def buffer(name, *shape, dt=F32):
            return stack.enter_context(nc.sbuf_tensor(name, list(shape), dt))

        M = ExpertMemory(
            nc, tokens=buffer("h_by_token", P, TB, D), number=buffer("item_number", P, 1, dt=I32),
            rank=buffer("item_rank", P, TB, ITEMS), gate=buffer("item_gate", P, TB, ITEMS),
            expert=buffer("item_expert", P, ITEMS, dt=I32), b1=buffer("b1_columns", P, 2 * DT * EXPERTS),
            sum=buffer("expert_sum", P, DT, S))
        route(K, a, M)
        run_items(K, a, M)
        rmsnorm(K, M.sum[:, :, :], None, lambda t: K.gate2[:, t:t + 1], DT, add_to=K.x[:, :, :])


class ExpertMemory:

    def __init__(self, nc, tokens, number, rank, gate, expert, b1, sum):
        self.loaded = [nc.alloc_semaphore(f"expert_slot{s}_loaded") for s in range(EXPERT_SLOTS)]
        self.tokens, self.number, self.rank, self.gate = tokens, number, rank, gate
        self.expert, self.b1, self.sum = expert, b1, sum


class ItemSignals:

    def __init__(self, nc):
        self.slots_selected = nc.alloc_semaphore("item_slots_selected")
        self.gathered = nc.alloc_semaphore("item_gathered")
        self.gathered_written = nc.alloc_semaphore("item_gathered_written")
        self.low_gathered_written = nc.alloc_semaphore("item_low_gathered_written")
        self.hidden_done = nc.alloc_semaphore("item_hidden_done")
        self.hidden_written = nc.alloc_semaphore("item_hidden_written")
        self.gated_turned = nc.alloc_semaphore("item_gated_turned")
        self.linear_turned = nc.alloc_semaphore("item_linear_turned")
        self.gated_ready = nc.alloc_semaphore("item_gated_ready")
        self.sigmoid_written = nc.alloc_semaphore("item_sigmoid_written")
        self.act_written = nc.alloc_semaphore("item_act_written")
        self.gate_rows_written = nc.alloc_semaphore("item_gate_rows_written")
        self.gates_turned = nc.alloc_semaphore("item_gates_turned")
        self.gates_written = nc.alloc_semaphore("item_gates_written")
        self.output_done = nc.alloc_semaphore("item_output_done")
        self.output_written = nc.alloc_semaphore("item_output_written")
        self.scattered = nc.alloc_semaphore("item_scattered")
        self.added = nc.alloc_semaphore("item_added")
        self.high_written = nc.alloc_semaphore("item_weights_high_written")
        self.low_written = nc.alloc_semaphore("item_weights_low_written")


def run_items(K, a, M):
    nc, ring, ps = K.nc, K.ring, K.ps
    w1 = a["w_mlp1_2"][0].rearrange("e (t p) n -> e p t n", p=P)
    w2 = a["w_mlp2_2"][0].rearrange("e (t p) n -> e p t n", p=P)
    sem = ItemSignals(nc)
    loaded = M.loaded
    used = [sem.hidden_done if s == 7 else sem.output_done if s == 11 else nc.alloc_semaphore(f"expert_slot{s}_used")
            for s in range(EXPERT_SLOTS)]
    steps = Steps(nc, "item_vector_steps")
    HIGH = 5
    split_slots = (0, 1, 2, 3, 4, 5, 6, 8, 9, 10)
    SPLITS = len(split_slots)
    number_in_turn = {s: k for k, s in enumerate(split_slots)}
    FIRST, LAST = SPLITS - 7, -7
    LINKS = 6
    with ExitStack() as stack:
        def buffer(name, *shape, dt=F32):
            return stack.enter_context(nc.sbuf_tensor(name, [P, *shape], dt))

        x, x_last = buffer("item_x", DT, 2, CAP, dt=F32R), buffer("item_x_last", CAP)
        act_t, act_split = buffer("item_act", DT, CAP), buffer("item_act_split", DT - 2, 2, CAP, dt=F32R)
        hid, y = buffer("item_hidden", 2 * D), buffer("item_y", D)
        sel, gated_sel, gates_t = buffer("item_select", TB, CAP), buffer("item_gated_select", TB, 2, CAP), buffer("item_gates_t", S)
        glu, sig, lin = buffer("item_glu", DT, CAP), buffer("item_sigmoid", DT, CAP), buffer("item_linear", DT, CAP)
        highs = [buffer(f"weights_high{j}", SLOT, dt=F32R)[:, :] for j in range(HIGH - 2)]
        highs += [flat(K.h_low[:, :, :]), flat(K.h_high[:, :, :])]
        block = stack.enter_context(nc.Block())

        def high(s):
            return highs[number_in_turn[s] % HIGH]

        def low(s):
            return ring.part(s)

        def number_of(eng):
            return eng.value_load(M.number[0:1, 0:1], min_val=EXPERTS, max_val=ITEMS - 1)

        def expert_of(eng, i):
            return eng.value_load(M.expert[0:1, bass.ds(i, 1)], min_val=0, max_val=EXPERTS - 1)

        @block.sync
        def _(sp):
            n = number_of(sp)

            def load_first(i):
                e = expert_of(sp, i)
                for s in range(8):
                    sp.wait_ge(used[s], i)
                    sp.dma_start(ring.slot(s), w1[bass.ds(e, 1), :, s, :].rearrange("e p n -> p (e n)")).then_inc(loaded[s], 16)

            def load_second(i):
                e = expert_of(sp, sp.snap(i - 1))
                for s in range(8, 12):
                    sp.wait_ge(used[s], i)
                    sp.dma_start(ring.slot(s).rearrange("p (t n) -> p t n", t=2),
                                 w2[bass.ds(e, 1), :, 2 * (s - 8):2 * (s - 8) + 2, :].rearrange("e p t n -> p (e t) n"))\
                        .then_inc(loaded[s], 16)

            load_first(1)
            with sp.Fori(2, n) as i:
                load_first(i)
                load_second(i)
            load_second(n)

        @block.tensor
        def _(pe):
            def gather(i):
                pe.wait_ge(sem.slots_selected, i + 1)
                pe.wait_ge(sem.added, i * 4 + 1)
                for t in range(DT):
                    for b in range(TB):
                        m = nc.tensor.matmul(ps[4][:, t * CAP:(t + 1) * CAP], M.tokens[:, b, t * P:(t + 1) * P],
                                             sel[:, b, :], start=b == 0, stop=b == TB - 1)
                m.then_inc(sem.gathered, 1)

            def wait_split(i, s, shift):
                pe.wait_ge(sem.low_written, i * SPLITS + (number_in_turn[s] + 1 + shift))

            def first_product(i, shift=0):
                pe.wait_ge(sem.low_gathered_written, i + 1)
                for s in range(7):
                    wait_split(i, s, shift)
                    for part, weights in enumerate((high(s), low(s))):
                        for c in range(4):
                            m = nc.tensor.matmul(ps[c][:, :], x[:, s, :, :].rearrange("p two s -> p (two s)"),
                                                 weights[:, c * 512:(c + 1) * 512], start=s == 0 and part == 0,
                                                 stop=s == 6 and part == 1)
                    m.then_inc(used[s], 1)
                pe.wait_ge(loaded[7], i * 16 + 16)
                for c in range(4):
                    m = nc.tensor.matmul(ps[c][0:CAP, :], x_last[:, :], ring.slot(7)[:, c * 512:(c + 1) * 512],
                                         start=False, stop=True, skip_group_check=True)
                m.then_inc(used[7], 1)

            def turn_hidden(i):
                pairs = hid[:, :].rearrange("s (t p two) -> s two t p", two=2, p=P)
                pe.wait_ge(sem.hidden_written, i)
                pe.wait_ge(sem.added, i * 4 + 4)
                for q in range(2):
                    for t in range(DT):
                        m = nc.tensor.matmul(ps[6 - q][:, t * CAP:(t + 1) * CAP], pairs[:, q, t, :], K.const("stacked", CAP),
                                             start=True, stop=True)
                    m.then_inc((sem.gated_turned, sem.linear_turned)[q], 1)
                pe.wait_ge(sem.gate_rows_written, i)
                for b in range(TB):
                    m = nc.tensor.transpose(ps[7][:, b * P:(b + 1) * P], gated_sel[:, b, :, :].rearrange("p two s -> p (two s)"),
                                            K.ident)
                m.then_inc(sem.gates_turned, 1)

            def finish_item(i, shift=0):
                pe.wait_ge(sem.act_written, i)
                for s in range(8, 11):
                    wait_split(i, s, shift)
                    for kk in range(2):
                        k = 2 * (s - 8) + kk
                        for part, weights in enumerate((high(s), low(s))):
                            for c in range(2):
                                m = nc.tensor.matmul(ps[4 + c][:, :], act_split[:, k, :, :].rearrange("p two s -> p (two s)"),
                                                     weights[:, kk * D + c * 512:kk * D + (c + 1) * 512],
                                                     start=k == 0 and part == 0, stop=k == 5 and part == 1)
                    m.then_inc(used[s], 1)
                pe.wait_ge(loaded[11], i * 16)
                for kk in range(2):
                    for c in range(2):
                        m = nc.tensor.matmul(ps[4 + c][0:CAP, :], act_t[:, 6 + kk, :],
                                             ring.slot(11)[:, kk * D + c * 512:kk * D + (c + 1) * 512],
                                             start=False, stop=kk == 1, skip_group_check=True)
                m.then_inc(used[11], 1)
                pe.wait_ge(sem.output_written, i)
                pe.wait_ge(sem.gates_written, i)
                for j in range(4):
                    for half in range(2):
                        t = 2 * j + half
                        m = nc.tensor.matmul(ps[4 + j][:, half * S:(half + 1) * S], y[:, t * P:(t + 1) * P], gates_t[:, :],
                                             start=True, stop=True)
                    m.then_inc(sem.scattered, 1)

            n = number_of(pe)
            pe.sem_inc(sem.scattered, 8)
            for s in range(8, 12):
                pe.sem_inc(used[s], 1)
            gather(0)
            first_product(0, FIRST)
            with pe.Fori(1, n) as i:
                gather(i)
                turn_hidden(i)
                first_product(i)
                finish_item(i)
            turn_hidden(n)
            finish_item(n, LAST)

        def split_vacant(eng, i, s):
            k = number_in_turn[s]
            if k >= HIGH:
                eng.wait_ge(used[split_slots[k - HIGH]], i + 1)
                return
            if isinstance(i, int) and i == 0:
                return
            eng.wait_ge(used[split_slots[k - HIGH + SPLITS]], i)
            if k + HIGH >= number_in_turn[8]:
                eng.wait_ge(used[s], i)

        @block.scalar
        def _(act):
            copy = ACT.Copy

            def write_high(i, *slots):
                for s in slots:
                    split_vacant(act, i, s)
                    act.wait_ge(loaded[s], i * 16 + 16 if s < 8 else i * 16)
                    nc.scalar.activation(high(s), ring.slot(s), copy).then_inc(sem.high_written, 1)

            def write_gathered(i):
                act.wait_ge(sem.gathered, i + 1)
                nc.scalar.activation(x[:, :, 0, :], ps[4][:, :].rearrange("p (t s) -> p t s", t=DT), copy)
                nc.scalar.activation(x_last[:, :], ps[4][:, 7 * CAP:], copy).then_inc(sem.gathered_written, 1)

            def write_hidden(i):
                act.wait_ge(sem.hidden_done, i)
                for c in range(4):
                    m = nc.scalar.activation(hid[:, c * 512:(c + 1) * 512], ps[c][:, :], copy)
                m.then_inc(sem.hidden_written, 1)

            def sigmoid(i):
                act.wait_ge(sem.gated_ready, i)
                nc.scalar.activation(sig[:, :, :], glu[:, :, :], ACT.Sigmoid, scale=1.702).then_inc(sem.sigmoid_written, 1)
                act.wait_ge(sem.gates_turned, i)
                nc.scalar.activation(gates_t[:, :], ps[7][:, 0:S], copy).then_inc(sem.gates_written, 1)

            def write_output(i):
                act.wait_ge(sem.output_done, i)
                for c in range(2):
                    m = nc.scalar.activation(y[:, c * 512:(c + 1) * 512], ps[4 + c][:, :], copy)
                m.then_inc(sem.output_written, 1)

            def turn(i, first=False):
                write_high(i, 0, 1)
                write_hidden(i)
                write_high(i, 2, 3, 4)
                if not first:
                    write_output(i)
                write_gathered(i)
                sigmoid(i)
                write_high(i, 5, 6, 8, 9, 10)

            n = number_of(act)
            act.sem_inc(sem.high_written, FIRST)
            write_high(0, 0, 1, 2, 3, 4)
            write_gathered(0)
            write_high(0, 5, 6)
            turn(1, first=True)
            with act.Fori(2, n) as i:
                turn(i)
            write_hidden(n)
            for s in range(8, 11):
                act.wait_ge(used[s], n)
                act.wait_ge(loaded[s], n * 16)
                nc.scalar.activation(high(s), ring.slot(s), copy).then_inc(sem.high_written, 1)
            write_output(n)
            sigmoid(n)
            write_output(n + 1)

        @block.vector
        def _(dve):
            v = nc.vector
            steps.eng = dve
            link = steps.link

            def select(i):
                for b in range(TB):
                    m = v.tensor_scalar(sel[:, b, :], K.const("iota", CAP), M.rank[:, b, bass.ds(i, 1)], None, ALU.is_equal)
                m.then_inc(sem.slots_selected, 1)

            def leave_low(i, *slots, shift=0):
                for s in slots:
                    dve.wait_ge(sem.high_written, i * SPLITS + (number_in_turn[s] + 1 + shift))
                    v.tensor_tensor(low(s), ring.slot(s), high(s).bitcast(F32), ALU.subtract).then_inc(sem.low_written, 1)

            def write_low_gathered(i):
                dve.wait_ge(sem.gathered_written, i + 1)
                v.tensor_tensor(x[:, :, 1, :], ps[4][:, :].rearrange("p (t s) -> p t s", t=DT),
                                x[:, :, 0, :].bitcast(F32), ALU.subtract).then_inc(sem.low_gathered_written, 1)

            def activate(i):
                before = dve.snap(i - 1)
                bias_at = dve.value_load(M.expert[0:1, bass.ds(before, 1)], min_val=0, max_val=EXPERTS - 1)
                columns = M.b1[:, :].rearrange("p (q t e) -> p q t e", q=2, e=EXPERTS)

                def bias(q):
                    return columns[:, q, :, bass.ds(bias_at, 1)].broadcast_to([P, DT, CAP])

                dve.wait_ge(sem.gated_turned, i)
                link(v.tensor_tensor(glu[:, :, :], ps[6][:, :].rearrange("p (t s) -> p t s", t=DT), bias(0), ALU.add))
                v.tensor_scalar(glu[:, :, :], glu[:, :, :], 7.0, None, ALU.min).then_inc(sem.gated_ready, 1)
                for b in range(TB):
                    m = v.tensor_scalar(gated_sel[:, b, :, :], K.const("iota", CAP).unsqueeze(1).broadcast_to([P, 2, CAP]),
                                        M.rank[:, b, bass.ds(before, 1)], M.gate[:, b, bass.ds(before, 1)],
                                        ALU.is_equal, ALU.mult)
                m.then_inc(sem.gate_rows_written, 1)
                dve.wait_ge(sem.linear_turned, i)
                link(v.tensor_tensor(lin[:, :, :], ps[5][:, :].rearrange("p (t s) -> p t s", t=DT), bias(1), ALU.add))
                link(v.tensor_scalar(lin[:, :, :], lin[:, :, :], -7.0, 7.0, ALU.max, ALU.min))
                dve.wait_ge(sem.gated_ready, i)
                link(v.scalar_tensor_tensor(lin[:, :, :], lin[:, :, :], 1.0, glu[:, :, :], ALU.add, ALU.mult))
                dve.wait_ge(sem.sigmoid_written, i)
                link(v.tensor_tensor(act_t[:, :, :], lin[:, :, :], sig[:, :, :], ALU.mult))
                link(v.tensor_copy(act_split[:, :, 0, :], act_t[:, 0:6, :]))
                v.tensor_tensor(act_split[:, :, 1, :], act_t[:, 0:6, :], act_split[:, :, 0, :].bitcast(F32), ALU.subtract)\
                    .then_inc(sem.act_written, 1)

            def add_scattered(i, shift=0):
                for j in range(4):
                    dve.wait_ge(sem.scattered, i * 4 + (j + 1 + shift))
                    part = M.sum[:, 2 * j:2 * j + 2, :].rearrange("p t s -> p (t s)")
                    v.tensor_tensor(part, ps[4 + j][:, :], part, ALU.add).then_inc(sem.added, 1)

            def turn(i, first=False):
                steps.loop(i, LINKS)
                leave_low(i, 0, 1, 2, 3, 4)
                if not first:
                    add_scattered(i)
                write_low_gathered(i)
                select(i + 1)
                activate(i)
                leave_low(i, 5, 6, 8, 9, 10)
                steps.n = 0

            n = number_of(dve)
            dve.sem_inc(steps.sem, LINKS)
            dve.sem_inc(sem.added, 8)
            dve.sem_inc(sem.low_written, FIRST)
            select(0)
            leave_low(0, 0, 1, 2, 3, 4, shift=FIRST)
            write_low_gathered(0)
            select(1)
            leave_low(0, 5, 6, shift=FIRST)
            turn(1, first=True)
            with dve.Fori(2, n) as i:
                turn(i)
            leave_low(n, 8, 9, 10, shift=LAST)
            add_scattered(n)
            steps.loop(n, LINKS)
            activate(n)
            add_scattered(n, shift=4)


class StickBreaking:

    def __init__(self, K, scale, fail, keep, total):
        self.K, self.scale, self.fail_buffer, self.keep_buffer, self.total = K, scale, fail, keep, total

    def begin(self, K, qb, heads, keys, w, at):
        self.qb, self.heads, self.keys, self.w, self.at = qb, heads, keys, w, at
        self.parts = 2
        self.fail, self.keep = (x[:, 0:heads * keys].rearrange("p (h k) -> p h k", h=heads)
                                for x in (self.fail_buffer, self.keep_buffer))

    def heads_of(self, part):
        half = self.heads // self.parts
        return slice(part * half, (part + 1) * half)

    def pool(self, pool):
        K, nc = self.K, self.K.nc
        nc.gpsimd.memset(self.keep, 1.0).then_inc(K.pool_done.sem, 1)
        pool.wait_ge(*K.pool_done(1))
        nc.gpsimd.memset(self.keep[:, :, self.keys - 1:self.keys], 0.0).then_inc(K.pool_done.sem, 1)
        for part in range(self.parts):
            pool.wait_ge(*K.exps(self.parts + part + 1))
            w = self.w[:, self.heads_of(part), :]
            nc.gpsimd.affine_select(out=w, in_=w, compare_op=ALU.is_gt, fill=0.0, base=self.qb * P,
                                    pattern=[[0, self.heads // self.parts], [-1, self.keys]], channel_multiplier=1)\
                .then_inc(K.weights.sem, 1)

    def act(self, act):
        K, nc = self.K, self.K.nc
        K.asteps.eng = act
        link = K.asteps.link
        for part in range(self.parts):
            act.wait_ge(*K.maxima(part + 1))
            heads = self.heads_of(part)
            fail = self.fail[:, heads, :]
            link(nc.scalar.activation(fail, self.w[:, heads, :], ACT.Abs))
            link(nc.scalar.activation(fail, fail, ACT.Exp, scale=-1.0))
            nc.scalar.activation(fail, fail, ACT.Ln, bias=K.ones[:, 0:1]).then_inc(K.exps.sem, 1)
        for part in range(self.parts):
            act.wait_ge(*K.maxima(self.parts + part + 1))
            w = self.w[:, self.heads_of(part), :]
            nc.scalar.activation(w, w, ACT.Exp).then_inc(K.exps.sem, 1)

    def dve(self, dve):
        K, v, keys = self.K, self.K.nc.vector, self.keys
        link = K.vsteps.link
        per_bank, half = 512 // keys, self.heads // self.parts
        for b, at in enumerate(self.at):
            K.banks.ready(dve, at)
            v.tensor_scalar(self.w[:, b * per_bank:(b + 1) * per_bank, :].rearrange("p h k -> p (h k)"), K.ps[at[0]][:, :],
                            self.scale, None, ALU.mult).then_inc(K.banks.free[at[0]], 1)
            if (b + 1) * per_bank % half == 0:
                K.banks.read(dve, at)
                v.tensor_copy(K.sums[:, 0:1], K.ones[:, 0:1]).then_inc(K.maxima.sem, 1)
        earlier = K.const("earlier", P) if self.qb == 0 else K.earlier_rows
        for part in range(self.parts):
            heads = self.heads_of(part)
            w, fail = self.w[:, heads, :], self.fail[:, heads, :]
            dve.wait_ge(*K.exps(part + 1))
            link(v.scalar_tensor_tensor(fail, w, 0.0, fail, ALU.max, ALU.add))
            link(v.scalar_tensor_tensor(fail, fail, -1.0, earlier.unsqueeze(1).broadcast_to([P, half, keys]),
                                        ALU.mult, ALU.mult))
            dve.wait_ge(*K.pool_done(2))
            columns = slice(part * half * keys, (part + 1) * half * keys)
            total = self.total[:, columns]
            link(v.tensor_tensor_scan(total[:, ::-1], self.keep_buffer[:, columns][:, ::-1],
                                      self.fail_buffer[:, columns][:, ::-1], 0.0, ALU.mult, ALU.add))
            v.tensor_tensor(w, w, total.rearrange("p (h k) -> p h k", h=half), ALU.add).then_inc(K.maxima.sem, 1)

    def end(self):
        self.K.pool_done.done(2)
        self.K.maxima.done(2 * self.parts)
        self.K.exps.done(2 * self.parts)


def exact_exp(K, x, out, minus_one, s):
    v, link = K.nc.vector, K.vsteps.link
    k, r, power = s
    ln2_hi = 0.693359375
    ln2_lo = math.log(2.0) - ln2_hi
    link(v.tensor_scalar(r, x, -87.0, 88.0, ALU.max, ALU.min))
    link(v.tensor_scalar(k, r, 1.0 / math.log(2.0), ROUND, ALU.mult, ALU.add))
    link(v.tensor_scalar(k, k, ROUND, None, ALU.subtract))
    link(v.scalar_tensor_tensor(r, k, -ln2_hi, r, ALU.mult, ALU.add))
    link(v.scalar_tensor_tensor(r, k, -ln2_lo, r, ALU.mult, ALU.add))
    link(v.tensor_scalar(power, k, 127.0, 2.0 ** 23, ALU.add, ALU.mult))
    link(v.tensor_scalar(k, r, 1.0 / math.factorial(8), None, ALU.mult))
    for n in range(7, 0, -1):
        link(v.scalar_tensor_tensor(k, k, 1.0 / math.factorial(n), r, ALU.add, ALU.mult))
    scale = power.bitcast(F32)
    if out is not None:
        link(v.scalar_tensor_tensor(out, k, 1.0, scale, ALU.add, ALU.mult))
    if minus_one is not None:
        link(v.tensor_tensor(k, k, scale, ALU.mult))
        link(v.scalar_tensor_tensor(minus_one, scale, -1.0, k, ALU.add, ALU.add))


class S5Operands:

    def __init__(self, b, c, phase, decay):
        self.b, self.c, self.phase, self.decay = b, c, phase, decay


def s5_matrices(K, a, T):
    nc, banks = K.nc, K.banks
    J, Q = 16, 4
    in_sem = {n: nc.alloc_semaphore("s5_" + n + "_loaded") for n in ("dt", "b_re", "b_im", "c_re", "c_im")}
    dt_ready, angles, sines, zeroed, natural = (nc.alloc_semaphore("s5_" + n) for n in (
        "dt_rows", "angles_reduced", "sines_written", "zeroed", "natural_ready"))
    dt_at = banks.take(0)
    b_at, c_at = [banks.take(1), banks.take(2)], [banks.take(3), banks.take(4)]
    with ExitStack() as stack:
        def buffer(name, *shape, dt=F32):
            return stack.enter_context(nc.sbuf_tensor(name, list(shape), dt))

        dt_pair, dt_rows = buffer("dt_pairs", J, 2), buffer("dt_rows", J, 2, 64)
        small = {n: buffer("s5_" + n, P, J) for n in (
            "dt", "a", "k", "r", "em1", "sin", "half", "cos", "cosm1", "lre", "lim", "fre", "fim", "inv", "t")}
        power = buffer("s5_power", P, J, dt=I32)
        b_in = [buffer(f"s5_b_in{i}", P, J, 16) for i in range(2)]
        b_tmp = [buffer(f"s5_b_tmp{i}", P, J, 16) for i in range(2)]
        b_nat = [buffer(f"s5_b_natural{i}", P, Q, 4, 2, 16) for i in range(2)]
        c_in = [buffer(f"s5_c_in{i}", P, Q, 2, 64) for i in range(2)]
        block = stack.enter_context(nc.Block())

        @block.sync
        def _(sp):
            sp.dma_start(dt_pair[:, :], a["ssm_log_dt_3"][0].rearrange("(j g) -> j g", g=2)).then_inc(in_sem["dt"], 16)
            for i, n in enumerate(("b_re", "b_im")):
                for g in range(2):
                    sp.dma_start(b_in[i][64 * g:64 * g + 64, :, :], a[f"ssm_{n}_3"][0].rearrange("(j g) n c -> g n j c", g=2)[g])\
                        .then_inc(in_sem[n], 16)
                    sp.wait_ge(in_sem[n], 16 * (g + 1))
            for i, n in enumerate(("c_re", "c_im")):
                for g in range(2):
                    sp.dma_start(c_in[i][:, :, g, :], a[f"ssm_{n}_3"][0].rearrange("(q g) c n -> (g c) q n", q=Q))\
                        .then_inc(in_sem[n], 16)
                    sp.wait_ge(in_sem[n], 16 * (g + 1))

        @block.gpsimd
        def _(pool):
            for i in range(2):
                nc.gpsimd.memset(b_nat[i][:, :, :, :, :], 0.0)
                m = nc.gpsimd.memset(T.c[i][:, :, :, :, :], 0.0)
            m.then_inc(zeroed, 1)

        @block.tensor
        def _(pe):
            pe.wait_ge(dt_ready, 1)
            banks.vacant(pe, dt_at)
            nc.tensor.transpose(K.ps[0][:, 0:J], dt_rows[:, :, :].rearrange("j g n -> j (g n)"), K.ident[0:J, 0:J])\
                .then_inc(banks.full[0], 1)
            for i, n in enumerate(("c_re", "c_im")):
                pe.wait_ge(in_sem[n], 32)
                banks.vacant(pe, c_at[i])
                for q in range(Q):
                    m = nc.tensor.transpose(K.ps[3 + i][:, q * P:(q + 1) * P], c_in[i][:, q, :, :].rearrange("p g n -> p (g n)"),
                                            K.ident)
                m.then_inc(banks.full[3 + i], 1)
            pe.wait_ge(natural, 1)
            for i in range(2):
                banks.vacant(pe, b_at[i])
                for q in range(Q):
                    m = nc.tensor.transpose(K.ps[1 + i][:, q * P:(q + 1) * P],
                                            b_nat[i][:, q, :, :, :].rearrange("p j g c -> p (j g c)"), K.ident)
                m.then_inc(banks.full[1 + i], 1)

        @block.scalar
        def _(act):
            act.wait_ge(angles, 1)
            nc.scalar.activation(small["half"][:, :], T.phase[:, :], ACT.Sin, scale=0.5)
            nc.scalar.activation(small["sin"][:, :], T.phase[:, :], ACT.Sin).then_inc(sines, 1)

        @block.vector
        def _(dve):
            K.vsteps.eng = dve
            link, v = K.vsteps.link, nc.vector
            a_re, a_im = K.param("ssm_a_re", 0, J), K.param("ssm_a_im", 0, J)
            t = {n: b[:, :] for n, b in small.items()}
            scratch = (t["k"], t["r"], power[:, :])
            dve.wait_ge(in_sem["dt"], 16)
            v.tensor_copy(dt_rows[:, :, :], dt_pair[:, :].unsqueeze(2).broadcast_to([J, 2, 64])).then_inc(dt_ready, 1)
            banks.ready(dve, dt_at)
            v.tensor_copy(t["dt"], K.ps[0][:, 0:J]).then_inc(banks.free[0], 1)
            banks.read(dve, dt_at)
            exact_exp(K, t["dt"], t["dt"], None, scratch)
            link(v.tensor_tensor(T.phase[:, :], a_im, t["dt"], ALU.mult))
            link(v.tensor_tensor(t["a"], a_re, t["dt"], ALU.mult))
            reduce_angle(K, dve, T.phase[:, :], t["k"]).then_inc(angles, 1)
            dve.wait_ge(angles, 1)
            exact_exp(K, t["a"], T.decay[:, :], t["em1"], scratch)
            dve.wait_ge(sines, 1)
            link(v.scalar_tensor_tensor(t["cosm1"], t["half"], -2.0, t["half"], ALU.mult, ALU.mult))
            link(v.scalar_tensor_tensor(t["lre"], t["cosm1"], 1.0, t["em1"], ALU.add, ALU.mult))
            link(v.tensor_tensor(t["lre"], t["lre"], t["cosm1"], ALU.add))
            link(v.tensor_tensor(t["lim"], T.decay[:, :], t["sin"], ALU.mult))
            link(v.tensor_tensor(t["inv"], a_re, a_re, ALU.mult))
            link(v.tensor_tensor(t["t"], a_im, a_im, ALU.mult))
            link(v.tensor_tensor(t["inv"], t["inv"], t["t"], ALU.add))
            link(v.reciprocal(t["inv"], t["inv"]))
            for out, p, q, op in (("fre", "lre", "lim", ALU.add), ("fim", "lim", "lre", ALU.subtract)):
                link(v.tensor_tensor(t[out], t[p], a_re, ALU.mult))
                link(v.tensor_tensor(t["t"], t[q], a_im, ALU.mult))
                link(v.tensor_tensor(t[out], t[out], t["t"], op))
                link(v.tensor_tensor(t[out], t[out], t["inv"], ALU.mult))
            for n in ("b_re", "b_im"):
                dve.wait_ge(in_sem[n], 32)
            fre, fim = (t[n].unsqueeze(2).broadcast_to([P, J, 16]) for n in ("fre", "fim"))
            re, im = b_in[0][:, :, :], b_in[1][:, :, :]
            dve.wait_ge(zeroed, 1)
            for i, (p, q, op) in enumerate(((re, im, ALU.subtract), (im, re, ALU.add))):
                link(v.tensor_tensor(b_tmp[0][:, :, :], p, fre, ALU.mult))
                link(v.tensor_tensor(b_tmp[1][:, :, :], q, fim, ALU.mult))
                for g in range(2):
                    rows = slice(64 * g, 64 * g + 64)
                    m = v.tensor_tensor(b_nat[i][rows, :, :, g, :].rearrange("p q j c -> p (q j) c"),
                                        b_tmp[0][rows, :, :], b_tmp[1][rows, :, :], op)
                link(m)
            v.tensor_copy(t["t"], t["inv"]).then_inc(natural, 1)
            for i in range(2):
                banks.ready(dve, c_at[i])
                for g in range(2):
                    rows = slice(64 * g, 64 * g + 64)
                    m = v.tensor_scalar(T.c[i][rows, :, :, g, :], K.ps[3 + i][rows, :].rearrange(
                        "p (q j g c) -> p g q j c", q=Q, j=4, g=2)[:, g], (1.0, -1.0)[i], None, ALU.mult)
                m.then_inc(banks.free[3 + i], 1)
            for i in range(2):
                banks.ready(dve, b_at[i])
                v.tensor_copy(T.b[i][:, :, :].rearrange("p q m -> p (q m)"), K.ps[1 + i][:, :]).then_inc(banks.free[1 + i], 1)


def s5_scan(K, T, u, y):
    nc, banks = K.nc, K.banks
    J, Q = 16, 4
    angles, absolute, tables = (nc.alloc_semaphore("s5_" + n) for n in ("table_angles", "table_abs", "tables_written"))
    bu_written, x_im_written, w_written, s_re_written, s_im_written = (nc.alloc_semaphore("s5_" + n) for n in (
        "bu_written", "x_im_written", "w_written", "s_re_written", "s_im_written"))
    keep_written, y_sum, turned_im = (nc.alloc_semaphore("s5_" + n) for n in ("pool_part", "y_sums", "w_im_turned"))
    bu_at = [[banks.take(b) for b in range(4)] for _ in range(Q)]
    y_at = [banks.take(4 + q) for q in range(Q)]
    memory = K.ring.memory
    cos, sin, work = (memory[:, n * J * S:(n + 1) * J * S].rearrange("p (j t) -> p j t", j=J) for n in range(3))
    rest = memory[:, 3 * J * S:]

    def part(n):
        return rest[:, n * 4 * S:(n + 1) * 4 * S].rearrange("p (j t) -> p j t", j=4)

    bre, bim, xre, xim, wre, wim, decay, t_dve, t_pool = (part(n) for n in range(9))
    sre, sim = xre, xim
    with nc.Block() as block:

        def outputs(pe, q):
            pe.wait_ge(s_re_written, q + 1)
            pe.wait_ge(s_im_written, q + 1)
            banks.vacant(pe, y_at[q])
            for j in range(4):
                for i, s in enumerate((sre, sim)):
                    m = nc.tensor.matmul(K.ps[4 + q][32 * j:32 * j + 32, 0:S], T.c[i][:, q, j, :, :].rearrange("p g c -> p (g c)"),
                                         s[:, j, :], start=i == 0, stop=i == 1)
            m.then_inc(banks.full[4 + q], 1)

        @block.tensor
        def _(pe):
            for q in range(Q):
                for j in range(4):
                    banks.vacant(pe, bu_at[q][j])
                    rows = slice(32 * j, 32 * j + 32)
                    for i in range(2):
                        m = nc.tensor.matmul(K.ps[j][:, i * S:(i + 1) * S], T.b[i][rows, q, :], u[rows, q, :],
                                             start=True, stop=True)
                    m.then_inc(banks.full[j], 1)
                if q:
                    outputs(pe, q - 1)
            outputs(pe, Q - 1)

        @block.scalar
        def _(act):
            for q in range(Q):
                c, s = cos[:, 4 * q:4 * q + 4, :], sin[:, 4 * q:4 * q + 4, :]
                act.wait_ge(angles, q + 1)
                nc.scalar.activation(c, s, ACT.Abs).then_inc(absolute, 1)
                act.wait_ge(absolute, q + 1)
                nc.scalar.activation(c, c, ACT.Sin, bias=K.col("half_pi"), scale=-1.0)
                nc.scalar.activation(s, s, ACT.Sin).then_inc(tables, 1)
                if q:
                    act.wait_ge(w_written, q)
                for j in range(4):
                    banks.ready(act, bu_at[q][j])
                    nc.scalar.activation(bre[:, j, :], K.ps[j][:, 0:S], ACT.Copy)
                    nc.scalar.activation(bim[:, j, :], K.ps[j][:, S:2 * S], ACT.Copy).then_inc(banks.free[j], 1)
            act.wait_ge(y_sum, 1)
            nc.scalar.activation(y[:, :, :], y[:, :, :], ACT.Gelu_apprx_tanh)

        def ready_inputs(eng, q):
            for j in range(4):
                banks.read(eng, bu_at[q][j])

        @block.vector
        def _(dve):
            K.vsteps.eng = dve
            link, v = K.vsteps.link, nc.vector

            def write_angles(q):
                tiles = slice(4 * q, 4 * q + 4)
                link(v.tensor_tensor(sin[:, tiles, :], K.const("times", S).unsqueeze(1).broadcast_to([P, 4, S]),
                                     T.phase[:, tiles].unsqueeze(2).broadcast_to([P, 4, S]), ALU.mult))
                reduce_angle(K, dve, sin[:, tiles, :], work[:, tiles, :]).then_inc(angles, 1)

            write_angles(0)
            for q in range(Q):
                c, s = cos[:, 4 * q:4 * q + 4, :], sin[:, 4 * q:4 * q + 4, :]
                ready_inputs(dve, q)
                dve.wait_ge(tables, q + 1)
                if q:
                    dve.wait_ge(banks.full[4 + q - 1], y_at[q - 1][2] + 1)
                link(v.tensor_tensor(t_dve, bim, s, ALU.mult))
                link(v.tensor_tensor(xre, bre, c, ALU.mult))
                link(v.tensor_tensor(xre, xre, t_dve, ALU.add))
                link(v.tensor_copy(decay, T.decay[:, 4 * q:4 * q + 4].unsqueeze(2).broadcast_to([P, 4, S])))
                link(v.memset(decay[:, :, 0:1], 0.0))
                if q < Q - 1:
                    write_angles(q + 1)
                if q:
                    dve.wait_ge(s_im_written, q)
                flat = [x.rearrange("p j t -> p (j t)") for x in (decay, xre, xim, wre, wim)]
                v.tensor_tensor_scan(flat[3], flat[0], flat[1], 0.0, ALU.mult, ALU.add)
                dve.wait_ge(x_im_written, q + 1)
                v.tensor_tensor_scan(flat[4], flat[0], flat[2], 0.0, ALU.mult, ALU.add).then_inc(w_written, 1)
                dve.wait_ge(w_written, q + 1)
                v.tensor_tensor(sim, wim, c, ALU.mult).then_inc(turned_im, 1)
                link(v.tensor_tensor(t_dve, wim, s, ALU.mult))
                link(v.tensor_tensor(sre, wre, c, ALU.mult))
                v.tensor_tensor(sre, sre, t_dve, ALU.subtract).then_inc(s_re_written, 1)
            for q in range(Q):
                banks.ready(dve, y_at[q])
                v.scalar_tensor_tensor(y[:, q, :], u[:, q, :], K.param("ssm_d", q), K.ps[4 + q][:, 0:S], ALU.mult, ALU.add)\
                    .then_inc(banks.free[4 + q], 1)
            banks.read(dve, y_at[-1])
            v.tensor_copy(K.sums[:, 0:1], K.ones[:, 0:1]).then_inc(y_sum, 1)

        @block.gpsimd
        def _(pool):
            g = nc.gpsimd
            done = [0]

            def link(m):
                done[0] += 1
                m.then_inc(keep_written, 1)
                pool.wait_ge(keep_written, done[0])
            for q in range(Q):
                c, s = cos[:, 4 * q:4 * q + 4, :], sin[:, 4 * q:4 * q + 4, :]
                ready_inputs(pool, q)
                pool.wait_ge(tables, q + 1)
                if q:
                    pool.wait_ge(banks.full[4 + q - 1], y_at[q - 1][2] + 1)
                link(g.tensor_tensor(t_pool, bre, s, ALU.mult))
                link(g.tensor_tensor(xim, bim, c, ALU.mult))
                g.tensor_tensor(xim, xim, t_pool, ALU.subtract).then_inc(x_im_written, 1)
                pool.wait_ge(w_written, q + 1)
                link(g.tensor_tensor(t_pool, wre, s, ALU.mult))
                pool.wait_ge(turned_im, q + 1)
                g.tensor_tensor(sim, sim, t_pool, ALU.add).then_inc(s_im_written, 1)


def s5_gate(K, a, y, following):
    nc, banks = K.nc, K.banks
    loaded = nc.alloc_semaphore("s5_glu_loaded")
    at = [banks.take(b) for b in range(2)]
    with nc.sbuf_tensor([P, 4, 512], F32) as w, nc.sbuf_tensor([P, 4, S], F32) as gate, nc.Block() as block:

        @block.sync
        def _(sp):
            sp.dma_start(w[:, :, :], a["ssm_w_glu_3"][0].rearrange("(t p) n -> p t n", p=P)).then_inc(loaded, 16)
            following.issue(sp)

        @block.tensor
        def _(pe):
            pe.wait_ge(loaded, 16)
            for b in range(2):
                banks.vacant(pe, at[b])
                for i in range(2):
                    t = 2 * b + i
                    for k in range(4):
                        m = nc.tensor.matmul(K.ps[b][:, i * S:(i + 1) * S], w[:, k, t * P:(t + 1) * P], y[:, k, :],
                                             start=k == 0, stop=k == 3)
                m.then_inc(banks.full[b], 1)

        @block.scalar
        def _(act):
            for b in range(2):
                banks.ready(act, at[b])
                for i in range(2):
                    m = nc.scalar.activation(gate[:, 2 * b + i, :], K.ps[b][:, i * S:(i + 1) * S], ACT.Sigmoid,
                                             bias=K.param("ssm_b_glu", 2 * b + i))
                m.then_inc(banks.free[b], 1)

        @block.vector
        def _(dve):
            banks.read(dve, at[0])
            banks.read(dve, at[1])
            nc.vector.tensor_tensor(y[:, :, :], y[:, :, :], gate[:, :, :], ALU.mult)


def two_branches(K, a):
    nc = K.nc
    w_in = a["w_in_3"][0]
    heads = 8
    with ExitStack() as stack:
        def buffer(name, *shape):
            return stack.enter_context(nc.sbuf_tensor(name, [P, *shape], F32))

        gates, u = buffer("branch_gates", 2 * DT, S), buffer("s5_u", 4, S)
        o = buffer("attention_out", 4, S)
        qkv = ExitStack()
        q, k, v = (qkv.enter_context(nc.sbuf_tensor(n, [P, *shape], F32)) for n, shape in (
            ("stick_q", (4, S)), ("stick_k", (4, S)), ("stick_v", (TB, 512))))
        jobs = []

        def copy_to(dst, j):
            return lambda ps: nc.scalar.activation(dst[:, 2 * j:2 * j + 2, :].rearrange("p t s -> p (t s)"), ps[:, :], ACT.Copy)

        def gate(j):
            def finish(ps):
                for i in range(2):
                    m = nc.scalar.activation(gates[:, 2 * j + i, :], ps[:, i * S:(i + 1) * S], ACT.Sigmoid,
                                             bias=K.param("b_gate", 2 * j + i))
                return m
            return finish

        for j in range(16):
            w = w_in[:, j * 256:(j + 1) * 256]
            if j in (4, 5):
                jobs.append((w, True, "act", lambda ps, j=j: nc.scalar.activation(
                    v[:, :, (j - 4) * 256:(j - 3) * 256], ps[:, :].rearrange("p (b n) -> p b n", b=TB), ACT.Copy)))
            else:
                jobs.append((w, False, "act", copy_to((q, k, None, u)[j // 2], j % 2) if j < 8 else gate(j - 8)))
        dense_up(K, K.h, DT, jobs, lambda loads: rmsnorm(
            K, K.x[:, :, :], K.h, lambda t: K.param("norm_mix_pre", t), DT, loads=loads))
        n = heads * S
        fail, keep, total = (K.ring.memory[:, i * n:(i + 1) * n] for i in range(3))
        stick = StickBreaking(K, 64 ** -0.5, fail, keep, total)
        for qb in range(TB):
            keys = (qb + 1) * P
            tokens = slice(qb * P, (qb + 1) * P)

            def rows(h):
                return slice(64 * (h % 2), 64 * (h % 2) + 64)
            attention(K, qb, heads, keys, lambda h: [(q[rows(h), h // 2, tokens], k[rows(h), h // 2, 0:keys])],
                      stick, lambda h, kb, half: v[:, kb, h * 64:(h + 1) * 64], 1,
                      lambda ps: [(o[:, :, tokens], ps[0][:, :].rearrange("p (t q) -> p t q", t=4))],
                      order=(0, 2, 4, 6, 1, 3, 5, 7))
        qkv.close()
        y, T = buffer("s5_y", 4, S), S5Operands(
            b=[buffer(f"s5_b{i}", 4, P) for i in range(2)], c=[buffer(f"s5_c{i}", 4, 4, 2, 16) for i in range(2)],
            phase=buffer("s5_phase", 16), decay=buffer("s5_decay", 16))
        s5_matrices(K, a, T)
        s5_scan(K, T, u, y)
        w_attention, w_ssm, w_out = (DownWeights(K, a[n][0], tiles) for n, tiles in (
            ("w_branch_attn_3", 4), ("w_branch_ssm_3", 4), ("w_out_3", DT)))
        s5_gate(K, a, y, w_attention)

        def gated(which, add):
            def finish(dve, j, ps):
                part = gates[:, which * DT + 2 * j:which * DT + 2 * j + 2, :].rearrange("p t s -> p (t s)")
                out = K.h[:, 2 * j:2 * j + 2, :].rearrange("p t s -> p (t s)")
                if not add:
                    return nc.vector.tensor_tensor(out, ps[:, :], part, ALU.mult)
                K.vsteps.link(nc.vector.tensor_tensor(part, ps[:, :], part, ALU.mult))
                return nc.vector.tensor_tensor(out, out, part, ALU.add)
            return finish

        dense_down(K, o, w_attention, gated(0, False), w_ssm)
        dense_down(K, y, w_ssm, gated(1, True), w_out)
    with nc.sbuf_tensor([P, DT, S], F32) as mixed:
        dense_down(K, K.h, w_out, store_to(K, mixed))
        rmsnorm(K, mixed[:, :, :], None, lambda t: K.param("norm_mix_post", t), DT, add_to=K.x[:, :, :])


def load_feature_major(K, rows, dst):
    nc, banks = K.nc, K.banks
    loaded = nc.alloc_semaphore("rows_loaded")
    at = [banks.take(4 + j) for j in range(4)]
    with nc.sbuf_tensor([P, TB, D], F32) as tokens, nc.Block() as block:

        @block.sync
        def _(sp):
            sp.dma_start(tokens[:, :, :], rows.rearrange("(b p) d -> p b d", p=P)).then_inc(loaded, 16)

        @block.tensor
        def _(pe):
            pe.wait_ge(loaded, 16)
            transpose_tokens(K, pe, tokens, at)

        @block.scalar
        def _(act):
            for j in range(4):
                banks.ready(act, at[j])
                nc.scalar.activation(dst[:, 2 * j:2 * j + 2, :].rearrange("p t s -> p (t s)"), K.ps[4 + j][:, :],
                                     ACT.Copy).then_inc(banks.free[4 + j], 1)


def cross_attention(K, a):
    nc = K.nc
    heads = 4
    with ExitStack() as stack:
        def buffer(name, *shape):
            return stack.enter_context(nc.sbuf_tensor(name, [P, *shape], F32))

        q, k, v = buffer("cross_q", DT, S), buffer("cross_k", DT, S), buffer("cross_v", TB, D)
        mem = buffer("memory", DT, S)
        load_feature_major(K, a["mem_3"][0], mem)
        w_k = DownWeights(K, a["xa_wk_3"][0], DT)
        rmsnorm(K, mem[:, :, :], mem, lambda t: K.param("norm_mem", t), DT, loads=w_k.issue)
        dense_down(K, mem, w_k, store_to(K, k))
        w_v = a["xa_wv_3"][0]
        dense_up(K, mem, DT, [(w_v[:, j * 256:(j + 1) * 256], True, "act", lambda ps, j=j: nc.scalar.activation(
            v[:, :, j * 256:(j + 1) * 256], ps[:, :].rearrange("p (b n) -> p b n", b=TB), ACT.Copy)) for j in range(4)])
        w_q = DownWeights(K, a["xa_wq_3"][0], DT)
        rmsnorm(K, K.x[:, :, :], K.h, lambda t: K.param("norm_xa_pre", t), DT, loads=w_q.issue)
        w_o = DownWeights(K, a["xa_wo_3"][0], DT)
        dense_down(K, K.h, w_q, store_to(K, q), w_o)
        for qb in range(TB):
            tokens = slice(qb * P, (qb + 1) * P)
            attention(K, qb, heads, S, lambda h: [(q[:, 2 * h + i, tokens], k[:, 2 * h + i, :]) for i in range(2)],
                      Softmax(256 ** -0.5), lambda h, kb, half: v[:, kb, h * 256 + half * P:h * 256 + (half + 1) * P], 2,
                      lambda ps: [(K.h[:, 4 * i:4 * i + 4, tokens], ps[i][:, :].rearrange("p (t q) -> p t q", t=4))
                                  for i in range(2)])
        dense_down(K, K.h, w_o, store_to(K, q))
        rmsnorm(K, q[:, :, :], None, lambda t: K.param("norm_xa_post", t), DT, add_to=K.x[:, :, :])


def transformer_blocks(nc, a, const, const_at, out):
    K = Kit(nc, const_at, const.shape[1])
    setup(K, a, const)
    ada = []

    def adaptive_weights():
        ada.append(AdaptiveWeights(K, a))
        return ada[0]

    for layer in range(2):
        swiglu(K, a["ffn_w_in"][layer, 0], a["ffn_w_out"][layer, 0], 2 * layer * DT)
        (spatial_gate, pool_mixer)[layer](K, a)
        swiglu(K, a["ffn_w_in"][layer, 1], a["ffn_w_out"][layer, 1], (2 * layer + 1) * DT,
               following=adaptive_weights if layer == 1 else None)
    rmsnorm(K, K.x[:, :, :], K.x, lambda t: K.param("final_norm", t), DT)
    adaptive_columns(K, a, ada[0])
    mixed_attention(K, a)
    experts(K, a)
    two_branches(K, a)
    cross_attention(K, a)
    conv_feed_forward(K, a)
    store_output(K, out)


def kernel(**inputs):
    import concourse.bacc as bacc
    from concourse.bass_utils import run_bass_kernel_spmd

    nc = bacc.Bacc("TRN2", target_bir_lowering=False, num_devices=1)
    table, const_at = constant_table()
    arrays, aps = {}, {}
    for name, value in [*inputs.items(), ("constant_table", table)]:
        arrays[f"in_{name}"] = value = np.ascontiguousarray(value)
        aps[name] = nc.dram_tensor(f"in_{name}", value.shape, mybir.dt.from_np(value.dtype), kind="ExternalInput").ap()
    out = nc.dram_tensor("out", (1, S, D), F32, kind="ExternalOutput").ap()
    transformer_blocks(nc, aps, aps["constant_table"], const_at, out)
    return run_bass_kernel_spmd(nc, [arrays], core_ids=[0]).results[0]["out"]
```
